# Optimizing a Trainium2 kernel written in Bass

```python
import jax, jax.numpy as jnp
from jax import lax
import numpy as np
import math

D_MODEL = 1024
BATCH = 1
SEQ = 2048
DEPTH = 2

MIX_WIDTH = D_MODEL
BRANCH = MIX_WIDTH // 2
GLA_HEADS = 4
GLA_DK = BRANCH // 2 // GLA_HEADS
GLA_DV = BRANCH // GLA_HEADS
GLA_RANK = 16
GLA_TAU = 16.0
GLA_CHUNK = 64
SGU_GROUPS = 4
SGU_CHUNK = 128
SGU_CH = BRANCH // SGU_GROUPS
RET_HEADS = 4
RET_DK = BRANCH // 2 // RET_HEADS
RET_DV = BRANCH // RET_HEADS
RET_CHUNK = 128
ROPE_BASE = 10000.0
POOL_WINDOWS = (2, 4, 8, 16)
POOL_CH = BRANCH // len(POOL_WINDOWS)
DN_ALPHA = (2 * DEPTH) ** 0.25
DN_BETA = (8 * DEPTH) ** -0.25
LN_EPS = 1e-5

EVEN_SIZES = (GLA_HEADS * GLA_DK, GLA_HEADS * GLA_DK, BRANCH, BRANCH, GLA_RANK,
              BRANCH, BRANCH, BRANCH)
ODD_SIZES = (RET_HEADS * RET_DK, RET_HEADS * RET_DK, BRANCH, BRANCH,
             BRANCH, BRANCH)


def _split(h, sizes):
    idx = [int(i) for i in np.cumsum(sizes)[:-1]]
    return jnp.split(h, idx, axis=-1)

def _layer_norm(x, g, b):
    xf = x.astype(jnp.float32)
    mu = jnp.mean(xf, axis=-1, keepdims=True)
    var = jnp.mean(jnp.square(xf - mu), axis=-1, keepdims=True)
    return ((xf - mu) * lax.rsqrt(var + LN_EPS) * g + b).astype(x.dtype)

def _head_rmsnorm(o, g):
    of = o.astype(jnp.float32)
    return of * lax.rsqrt(jnp.mean(jnp.square(of), axis=-1, keepdims=True) + LN_EPS) * g

def _head_groupnorm(o, g):
    of = o.astype(jnp.float32)
    mu = jnp.mean(of, axis=-1, keepdims=True)
    var = jnp.mean(jnp.square(of - mu), axis=-1, keepdims=True)
    return (of - mu) * lax.rsqrt(var + LN_EPS) * g

def _chunk_scan(decay, chunk_state):
    def step(s_prev, inp):
        dec, cs = inp
        return dec * s_prev + cs, s_prev
    init = jnp.zeros(chunk_state.shape[1:], jnp.float32)
    _, s_in = lax.scan(step, init, (decay, chunk_state))
    return s_in

def _gla(q, k, v, log_a):
    B, S, H, dk = q.shape
    dv = v.shape[-1]
    C = GLA_CHUNK
    n = S // C
    f32 = jnp.float32
    q = q.astype(f32).reshape(B, n, C, H, dk) * (dk ** -0.5)
    k = k.astype(f32).reshape(B, n, C, H, dk)
    v = v.astype(f32).reshape(B, n, C, H, dv)
    b = jnp.cumsum(log_a.astype(f32).reshape(B, n, C, H, dk), axis=2)
    q_dec = q * jnp.exp(b)
    k_dec = k * jnp.exp(-b)
    causal = jnp.tril(jnp.ones((C, C), dtype=bool))
    scores = jnp.einsum('bnihd,bnjhd->bnhij', q_dec, k_dec)
    scores = jnp.where(causal, scores, 0.0)
    o_intra = jnp.einsum('bnhij,bnjhe->bnihe', scores, v)
    b_last = b[:, :, -1]
    k_state = k * jnp.exp(b_last[:, :, None] - b)
    chunk_state = jnp.einsum('bnjhd,bnjhe->bnhde', k_state, v)
    decay = jnp.exp(b_last)[..., None]
    s_in = _chunk_scan(jnp.moveaxis(decay, 1, 0), jnp.moveaxis(chunk_state, 1, 0))
    s_in = jnp.moveaxis(s_in, 0, 1)
    o_inter = jnp.einsum('bnihd,bnhde->bnihe', q_dec, s_in)
    return (o_intra + o_inter).reshape(B, S, H, dv)

def _spatial_gating(u, sv, ln_g, ln_b, w_s, b_s):
    B, S, _ = u.shape
    n = S // SGU_CHUNK
    svr = sv.reshape(B, n, SGU_CHUNK, SGU_GROUPS, SGU_CH)
    svr = _layer_norm(svr, ln_g, ln_b)
    w = jnp.where(jnp.tril(jnp.ones((SGU_CHUNK, SGU_CHUNK), dtype=bool)), w_s, 0.0)
    s = jnp.einsum('gts,bnsgc->bntgc', w, svr) + jnp.transpose(b_s)[None, None, :, :, None]
    return u * s.reshape(B, S, BRANCH).astype(u.dtype)

def _rotary(x, positions):
    half = x.shape[-1] // 2
    inv = ROPE_BASE ** (-jnp.arange(half, dtype=jnp.float32) / half)
    ang = positions.astype(jnp.float32)[..., None] * inv
    cos = jnp.cos(ang)[:, :, None, :]
    sin = jnp.sin(ang)[:, :, None, :]
    xf = x.astype(jnp.float32)
    x1, x2 = xf[..., :half], xf[..., half:]
    return jnp.concatenate([x1 * cos - x2 * sin, x1 * sin + x2 * cos], axis=-1)

def _retention(q, k, v):
    B, S, H, dk = q.shape
    dv = v.shape[-1]
    C = RET_CHUNK
    n = S // C
    f32 = jnp.float32
    log_gamma = jnp.log(1.0 - 2.0 ** (-5.0 - jnp.arange(H, dtype=f32)))
    q = q.astype(f32).reshape(B, n, C, H, dk) * (dk ** -0.5)
    k = k.astype(f32).reshape(B, n, C, H, dk)
    v = v.astype(f32).reshape(B, n, C, H, dv)
    idx = jnp.arange(C, dtype=f32)
    rel = idx[:, None] - idx[None, :]
    dmat = jnp.where(rel >= 0, jnp.exp(jnp.maximum(rel, 0.0)[None] * log_gamma[:, None, None]), 0.0)
    scores = jnp.einsum('bnihd,bnjhd->bnhij', q, k) * dmat
    o_intra = jnp.einsum('bnhij,bnjhe->bnihe', scores, v)
    w_state = jnp.exp((C - 1.0 - idx)[None] * log_gamma[:, None])
    chunk_state = jnp.einsum('bnjhd,hj,bnjhe->bnhde', k, w_state, v)
    chunk_decay = jnp.exp(C * log_gamma)[None, None, :, None, None]
    chunk_decay = jnp.broadcast_to(chunk_decay, (B, n, H, 1, 1))
    s_in = _chunk_scan(jnp.moveaxis(chunk_decay, 1, 0), jnp.moveaxis(chunk_state, 1, 0))
    s_in = jnp.moveaxis(s_in, 0, 1)
    w_inter = jnp.exp((idx + 1.0)[None] * log_gamma[:, None])
    o_inter = jnp.einsum('bnihd,hi,bnhde->bnihe', q, w_inter, s_in)
    return (o_intra + o_inter).reshape(B, S, H, dv)

def _multiscale_pool(p, w_pool, scale):
    B, S, _ = p.shape
    pf = p.astype(jnp.float32)
    cs = jnp.concatenate([jnp.zeros((B, 1, BRANCH), jnp.float32), jnp.cumsum(pf, axis=1)], axis=1)
    t = jnp.arange(S)
    outs = []
    for g, w in enumerate(POOL_WINDOWS):
        lo, hi = g * POOL_CH, (g + 1) * POOL_CH
        start = jnp.maximum(t + 1 - w, 0)
        win_sum = cs[:, 1:, lo:hi] - cs[:, start, lo:hi]
        cnt = jnp.minimum(t + 1, w).astype(jnp.float32)[None, :, None]
        outs.append(win_sum / cnt - pf[..., lo:hi])
    pooled = jnp.concatenate(outs, axis=-1).reshape(B, S, len(POOL_WINDOWS), POOL_CH)
    y = jnp.einsum('bsgc,gcd->bsgd', pooled, w_pool).reshape(B, S, BRANCH) * scale
    return y.astype(p.dtype)

def _even_layer(x, w_in, w_a2, b_a, gla_norm_g, sgu_ln_g, sgu_ln_b, w_s, b_s, w_out, ln_g, ln_b):
    B, S, _ = x.shape
    h = x @ w_in
    q, k, v, g_a, a_lr, u, sv, g_b = _split(h, EVEN_SIZES)
    log_a = jax.nn.log_sigmoid((a_lr @ w_a2 + b_a).astype(jnp.float32)) / GLA_TAU
    o = _gla(q.reshape(B, S, GLA_HEADS, GLA_DK), k.reshape(B, S, GLA_HEADS, GLA_DK),
             v.reshape(B, S, GLA_HEADS, GLA_DV), log_a.reshape(B, S, GLA_HEADS, GLA_DK))
    o_a = _head_rmsnorm(o, gla_norm_g).reshape(B, S, BRANCH).astype(x.dtype) * jax.nn.silu(g_a)
    o_b = _spatial_gating(jax.nn.gelu(u), jax.nn.gelu(sv), sgu_ln_g, sgu_ln_b, w_s, b_s) * jax.nn.silu(g_b)
    y = jnp.concatenate([o_a, o_b], axis=-1) @ w_out
    return _layer_norm(DN_ALPHA * x + y, ln_g, ln_b)

def _odd_layer(x, positions, w_in, ret_norm_g, w_pool, pool_scale, w_out, ln_g, ln_b):
    B, S, _ = x.shape
    h = x @ w_in
    q, k, v, g_c, p, g_d = _split(h, ODD_SIZES)
    qr = _rotary(q.reshape(B, S, RET_HEADS, RET_DK), positions)
    kr = _rotary(k.reshape(B, S, RET_HEADS, RET_DK), positions)
    o = _retention(qr, kr, v.reshape(B, S, RET_HEADS, RET_DV))
    o_c = _head_groupnorm(o, ret_norm_g).reshape(B, S, BRANCH).astype(x.dtype) * jax.nn.silu(g_c)
    o_d = _multiscale_pool(p, w_pool, pool_scale) * jax.nn.silu(g_d)
    y = jnp.concatenate([o_c, o_d], axis=-1) @ w_out
    return _layer_norm(DN_ALPHA * x + y, ln_g, ln_b)

def first_inputs(seed: int = 0) -> dict:
    key = jax.random.key(seed)
    ks = jax.random.split(key, 24)
    f32 = jnp.float32
    nrm = lambda k, shape, s: jax.random.normal(k, shape, f32) * s
    d_even = sum(EVEN_SIZES)
    d_odd = sum(ODD_SIZES)
    return {
        "x": jax.random.normal(ks[0], (BATCH, SEQ, D_MODEL), f32),
        "positions": jnp.broadcast_to(jnp.arange(SEQ, dtype=jnp.int32), (BATCH, SEQ)),
        "l0_w_in": nrm(ks[1], (D_MODEL, d_even), D_MODEL ** -0.5),
        "l0_w_a2": nrm(ks[2], (GLA_RANK, GLA_HEADS * GLA_DK), GLA_RANK ** -0.5),
        "l0_b_a": nrm(ks[3], (GLA_HEADS * GLA_DK,), 0.1),
        "l0_gla_norm_g": 1.0 + nrm(ks[4], (GLA_HEADS, GLA_DV), 0.1),
        "l0_sgu_ln_g": 1.0 + nrm(ks[5], (SGU_GROUPS, SGU_CH), 0.1),
        "l0_sgu_ln_b": nrm(ks[6], (SGU_GROUPS, SGU_CH), 0.02),
        "l0_w_s": nrm(ks[7], (SGU_GROUPS, SGU_CHUNK, SGU_CHUNK), 0.5 * SGU_CHUNK ** -0.5),
        "l0_b_s": 1.0 + nrm(ks[8], (SGU_GROUPS, SGU_CHUNK), 0.1),
        "l0_w_out": nrm(ks[9], (MIX_WIDTH, D_MODEL), DN_BETA * MIX_WIDTH ** -0.5),
        "l0_ln_g": 1.0 + nrm(ks[10], (D_MODEL,), 0.1),
        "l0_ln_b": nrm(ks[11], (D_MODEL,), 0.02),
        "l1_w_in": nrm(ks[12], (D_MODEL, d_odd), D_MODEL ** -0.5),
        "l1_ret_norm_g": 1.0 + nrm(ks[13], (RET_HEADS, RET_DV), 0.1),
        "l1_w_pool": nrm(ks[14], (len(POOL_WINDOWS), POOL_CH, POOL_CH), POOL_CH ** -0.5),
        "l1_pool_scale": 0.5 + nrm(ks[15], (BRANCH,), 0.05),
        "l1_w_out": nrm(ks[16], (MIX_WIDTH, D_MODEL), DN_BETA * MIX_WIDTH ** -0.5),
        "l1_ln_g": 1.0 + nrm(ks[17], (D_MODEL,), 0.1),
        "l1_ln_b": nrm(ks[18], (D_MODEL,), 0.02),
    }

def first_block(x, positions, l0_w_in, l0_w_a2, l0_b_a, l0_gla_norm_g, l0_sgu_ln_g, l0_sgu_ln_b,
              l0_w_s, l0_b_s, l0_w_out, l0_ln_g, l0_ln_b, l1_w_in, l1_ret_norm_g, l1_w_pool,
              l1_pool_scale, l1_w_out, l1_ln_g, l1_ln_b):
    even_params = [(l0_w_in, l0_w_a2, l0_b_a, l0_gla_norm_g, l0_sgu_ln_g, l0_sgu_ln_b,
                    l0_w_s, l0_b_s, l0_w_out, l0_ln_g, l0_ln_b)]
    odd_params = [(l1_w_in, l1_ret_norm_g, l1_w_pool, l1_pool_scale, l1_w_out, l1_ln_g, l1_ln_b)]
    for layer in range(DEPTH):
        if layer % 2 == 0:
            x = _even_layer(x, *even_params[layer // 2])
        else:
            x = _odd_layer(x, positions, *odd_params[layer // 2])
    return x


DEPTH_2 = 1

H_A = 4
DK_A = 128
DV_A = 128
W_A = H_A * DV_A
CONV_W = 4
CHUNK = 64
H_B = 4
R_KV = 128
DV_B = 128
W_B = H_B * DV_B
H_IDX = 8
D_IDX = 64
TOPK_MAX = 256
Q_BLOCK = 128
N_BUCKETS = 32
MAX_EXACT = 16
MAX_DIST = 128
EPS = 1e-6
SPLITS = (3 * W_A, W_A, H_A, H_A, H_B * R_KV, R_KV, W_B, H_IDX * D_IDX, D_IDX, H_IDX)
SPLIT_OFFSETS = (3072 // 2, 2048, 2052, 2056, 2568, 2696, 3208, 3720, 3784)
D_IN = 3792


def rmsnorm(x, g):
    xf = x.astype(jnp.float32)
    xf = xf * lax.rsqrt(jnp.mean(xf * xf, axis=-1, keepdims=True) + EPS)
    return xf.astype(x.dtype) * g

def l2norm(x):
    return x * lax.rsqrt(jnp.sum(x * x, axis=-1, keepdims=True) + EPS)

def causal_conv(u, w):
    L = u.shape[1]
    up = jnp.pad(u, ((0, 0), (CONV_W - 1, 0), (0, 0)))
    out = up[:, 0:L] * w[0]
    for j in range(1, CONV_W):
        out = out + up[:, j:j + L] * w[j]
    return out

def t5_bucket(dist):
    n = jnp.maximum(dist, 0)
    nf = jnp.maximum(n, 1).astype(jnp.float32)
    large = MAX_EXACT + (jnp.log(nf / MAX_EXACT) / math.log(MAX_DIST / MAX_EXACT)
                         * (N_BUCKETS - MAX_EXACT)).astype(jnp.int32)
    large = jnp.minimum(large, N_BUCKETS - 1)
    return jnp.where(n < MAX_EXACT, n, large)

def gated_deltanet(qkv, z, b, a, conv_w, a_log, dt_bias, g_norm):
    Bsz, L, _ = qkv.shape
    n_chunks = L // CHUNK
    qkv = jax.nn.silu(causal_conv(qkv, conv_w))
    q, k, v = jnp.split(qkv, 3, axis=-1)

    def heads(t, d):
        t = t.reshape(Bsz, L, H_A, d).transpose(0, 2, 1, 3).astype(jnp.float32)
        return t.reshape(Bsz, H_A, n_chunks, CHUNK, d)

    q = l2norm(heads(q, DK_A)) * (DK_A ** -0.5)
    k = l2norm(heads(k, DK_A))
    v = heads(v, DV_A)
    beta = jax.nn.sigmoid(b.astype(jnp.float32)).transpose(0, 2, 1).reshape(Bsz, H_A, n_chunks, CHUNK)
    g = -jnp.exp(a_log.astype(jnp.float32)) * jax.nn.softplus(a.astype(jnp.float32) + dt_bias.astype(jnp.float32))
    g = g.transpose(0, 2, 1).reshape(Bsz, H_A, n_chunks, CHUNK)
    gc = jnp.cumsum(g, axis=-1)
    pos = jnp.arange(CHUNK)
    causal = pos[:, None] >= pos[None, :]
    strict = pos[:, None] > pos[None, :]
    decay = jnp.exp(jnp.where(causal, gc[..., :, None] - gc[..., None, :], -jnp.inf))
    kb = k * beta[..., None]
    vb = v * beta[..., None]
    lmat = jnp.where(strict, jnp.einsum('bhnik,bhnjk->bhnij', kb, k) * decay, 0.0)
    eye = jnp.eye(CHUNK, dtype=jnp.float32)
    tmat = lax.linalg.triangular_solve(lmat + eye, jnp.broadcast_to(eye, lmat.shape),
                                       left_side=True, lower=True, unit_diagonal=True)
    u = jnp.einsum('bhnij,bhnjd->bhnid', tmat, vb)
    w = jnp.einsum('bhnij,bhnjd->bhnid', tmat, kb * jnp.exp(gc)[..., None])
    attn = jnp.einsum('bhnik,bhnjk->bhnij', q, k) * decay
    qg = q * jnp.exp(gc)[..., None]
    kg = k * jnp.exp(gc[..., -1:] - gc)[..., None]
    glast = jnp.exp(gc[..., -1])
    xs = tuple(jnp.moveaxis(t, 2, 0) for t in (qg, kg, u, w, attn, glast))

    def step(S, inp):
        qg_c, kg_c, u_c, w_c, attn_c, gl_c = inp
        v_new = u_c - jnp.einsum('bhck,bhkv->bhcv', w_c, S)
        o = jnp.einsum('bhck,bhkv->bhcv', qg_c, S) + jnp.einsum('bhij,bhjv->bhiv', attn_c, v_new)
        S = S * gl_c[..., None, None] + jnp.einsum('bhck,bhcv->bhkv', kg_c, v_new)
        return S, o

    S0 = jnp.zeros((Bsz, H_A, DK_A, DV_A), jnp.float32)
    _, o = lax.scan(step, S0, xs)
    o = jnp.moveaxis(o, 0, 2).reshape(Bsz, H_A, L, DV_A).transpose(0, 2, 1, 3)
    o = rmsnorm(o, g_norm.astype(jnp.float32))
    o = o.reshape(Bsz, L, W_A) * jax.nn.silu(z.astype(jnp.float32))
    return o.astype(qkv.dtype)

def dsa_sparse_attention(q_b, ckv, iq, ik, iw, g_kv, w_uv, rel_bias, z):
    Bsz, L, _ = q_b.shape
    n_blocks = L // Q_BLOCK
    k_top = min(TOPK_MAX, L // 4)
    ckv = rmsnorm(ckv, g_kv)
    q_b = q_b.reshape(Bsz, L, H_B, R_KV)
    iq = iq.reshape(Bsz, L, H_IDX, D_IDX)
    iw = iw * (H_IDX ** -0.5 * D_IDX ** -0.5)
    key_pos = jnp.arange(L, dtype=jnp.int32)

    def to_blocks(t):
        return jnp.moveaxis(t.reshape((Bsz, n_blocks, Q_BLOCK) + t.shape[2:]), 1, 0)

    def block(args):
        qb, iqb, iwb, t0 = args
        t = t0 + jnp.arange(Q_BLOCK, dtype=jnp.int32)
        rel = jnp.einsum('bqhd,bsd->bqhs', iqb, ik)
        score = jnp.einsum('bqh,bqhs->bqs', iwb.astype(jnp.float32), jax.nn.relu(rel).astype(jnp.float32))
        score = jnp.where(key_pos[None, None, :] <= t[None, :, None], score, -jnp.inf)
        _, sel = lax.top_k(score, k_top)
        kv_sel = jax.vmap(lambda kv, i: kv[i])(ckv, sel)
        dist = t[None, :, None] - sel
        bias = jnp.moveaxis(rel_bias[t5_bucket(dist)], 3, 2)
        logits = (jnp.einsum('bqhr,bqkr->bqhk', qb, kv_sel).astype(jnp.float32) * (R_KV ** -0.5)
                  + bias.astype(jnp.float32))
        logits = jnp.where((dist >= 0)[:, :, None, :], logits, -jnp.inf)
        p = jax.nn.softmax(logits, axis=-1).astype(kv_sel.dtype)
        return jnp.einsum('bqhk,bqkr->bqhr', p, kv_sel)

    t0s = jnp.arange(n_blocks, dtype=jnp.int32) * Q_BLOCK
    o = lax.map(block, (to_blocks(q_b), to_blocks(iq), to_blocks(iw), t0s))
    o = jnp.moveaxis(o, 0, 1).reshape(Bsz, L, H_B, R_KV)
    o = jnp.einsum('blhr,hrd->blhd', o, w_uv).reshape(Bsz, L, W_B)
    return o * jax.nn.silu(z)

def second_inputs(seed: int = 0) -> dict:
    key = jax.random.key(seed)
    ks = jax.random.split(key, 16)
    nrm = jax.random.normal
    x = nrm(ks[0], (BATCH, SEQ, D_MODEL), jnp.float32)
    c = nrm(ks[1], (BATCH, D_MODEL), jnp.float32)
    w_ada = nrm(ks[2], (DEPTH_2, D_MODEL, 3 * D_MODEL), jnp.float32) * (0.5 * D_MODEL ** -0.5)
    b_ada = 0.01 * nrm(ks[3], (DEPTH_2, 3 * D_MODEL), jnp.float32)
    g_pre = 1.0 + 0.05 * nrm(ks[4], (DEPTH_2, D_MODEL), jnp.float32)
    w_in = nrm(ks[5], (DEPTH_2, D_MODEL, D_IN), jnp.float32) * (D_MODEL ** -0.5)
    conv_w = nrm(ks[6], (DEPTH_2, CONV_W, 3 * W_A), jnp.float32) * (CONV_W ** -0.5)
    a_log = jnp.log(jax.random.uniform(ks[7], (DEPTH_2, H_A), jnp.float32, 1.0, 16.0))
    dt = jnp.exp(jax.random.uniform(ks[8], (DEPTH_2, H_A), jnp.float32, math.log(1e-3), math.log(1e-1)))
    dt_bias = dt + jnp.log(-jnp.expm1(-dt))
    g_gdn = 1.0 + 0.05 * nrm(ks[9], (DEPTH_2, DV_A), jnp.float32)
    g_kv = 1.0 + 0.05 * nrm(ks[10], (DEPTH_2, R_KV), jnp.float32)
    w_uv = nrm(ks[11], (DEPTH_2, H_B, R_KV, DV_B), jnp.float32) * (R_KV ** -0.5)
    rel_bias = 0.5 * nrm(ks[12], (N_BUCKETS, H_B), jnp.float32)
    w_out = nrm(ks[13], (DEPTH_2, W_A + W_B, D_MODEL), jnp.float32) * ((W_A + W_B) ** -0.5)
    g_post = 1.0 + 0.05 * nrm(ks[14], (DEPTH_2, D_MODEL), jnp.float32)
    return {'x': x, 'c': c, 'w_ada': w_ada, 'b_ada': b_ada, 'g_pre': g_pre, 'w_in': w_in,
            'conv_w': conv_w, 'a_log': a_log, 'dt_bias': dt_bias, 'g_gdn': g_gdn, 'g_kv': g_kv,
            'w_uv': w_uv, 'rel_bias': rel_bias, 'w_out': w_out, 'g_post': g_post}

def second_block(x, c, w_ada, b_ada, g_pre, w_in, conv_w, a_log, dt_bias, g_gdn, g_kv, w_uv, rel_bias, w_out, g_post):
    for layer in range(DEPTH_2):
        mod = jax.nn.silu(c) @ w_ada[layer] + b_ada[layer]
        shift, scale, gate = jnp.split(mod, 3, axis=-1)
        h = rmsnorm(x, g_pre[layer]) * (1.0 + scale[:, None, :]) + shift[:, None, :]
        proj = h @ w_in[layer]
        (qkv_a, z_a, b_a, a_a, q_b, ckv, z_b, iq, ik, iw) = jnp.split(proj, list(SPLIT_OFFSETS), axis=-1)
        o_a = gated_deltanet(qkv_a, z_a, b_a, a_a, conv_w[layer], a_log[layer], dt_bias[layer], g_gdn[layer])
        o_b = dsa_sparse_attention(q_b, ckv, iq, ik, iw, g_kv[layer], w_uv[layer], rel_bias, z_b)
        mix = jnp.concatenate([o_a, o_b], axis=-1) @ w_out[layer]
        x = x + gate[:, None, :] * rmsnorm(mix, g_post[layer])
    return x


def setup_inputs(seed=0):
    out = dict(first_inputs(seed))
    for name, value in second_inputs(seed + 1).items():
        if name != "x":
            out[name + "_2"] = value
    return out


def reference(
    x, positions, l0_w_in, l0_w_a2, l0_b_a, l0_gla_norm_g, l0_sgu_ln_g, l0_sgu_ln_b, l0_w_s,
    l0_b_s, l0_w_out, l0_ln_g, l0_ln_b, l1_w_in, l1_ret_norm_g, l1_w_pool, l1_pool_scale,
    l1_w_out, l1_ln_g, l1_ln_b, c_2, w_ada_2, b_ada_2, g_pre_2, w_in_2, conv_w_2, a_log_2,
    dt_bias_2, g_gdn_2, g_kv_2, w_uv_2, rel_bias_2, w_out_2, g_post_2,
):
    x = first_block(
        x, positions, l0_w_in, l0_w_a2, l0_b_a, l0_gla_norm_g, l0_sgu_ln_g, l0_sgu_ln_b, l0_w_s,
        l0_b_s, l0_w_out, l0_ln_g, l0_ln_b, l1_w_in, l1_ret_norm_g, l1_w_pool, l1_pool_scale,
        l1_w_out, l1_ln_g, l1_ln_b,
    )
    return second_block(
        x, c_2, w_ada_2, b_ada_2, g_pre_2, w_in_2, conv_w_2, a_log_2, dt_bias_2, g_gdn_2,
        g_kv_2, w_uv_2, rel_bias_2, w_out_2, g_post_2,
    )


_drawn_inputs = setup_inputs


def setup_inputs(seed=0):
    import zlib

    import numpy as np

    out = dict(_drawn_inputs(seed))
    spreads = {}
    factors = {'l0_w_a2': 3.321,
     'l0_b_a': 7.945,
     'l0_gla_norm_g': 3.48,
     'l0_sgu_ln_g': 8.0,
     'l0_sgu_ln_b': 8.0,
     'l0_b_s': 5.332,
     'l1_ret_norm_g': 3.554,
     'l1_pool_scale': 7.653,
     'b_ada_2': 4.463,
     'g_gdn_2': 14.971,
     'g_kv_2': 8.0,
     'rel_bias_2': 5.045,
     'g_post_2': 3.889}
    for name, (base, spread) in spreads.items():
        noise = np.random.default_rng([zlib.crc32(name.encode()), seed]).standard_normal(out[name].shape)
        drawn = base * np.exp(spread * noise) if base else spread * noise
        out[name] = __import__('jax').numpy.asarray(drawn.astype(out[name].dtype))
    for name, factor in factors.items():
        out[name] = (out[name] * factor).astype(out[name].dtype)
    return out
```

```python
import math
from contextlib import ExitStack

import numpy as np
import concourse.bass as bass
from concourse import mybir

F32 = mybir.dt.float32
I32 = mybir.dt.int32
ALU = mybir.AluOpType
ACT = mybir.ActivationFunctionType
AX = mybir.AxisListType

P = 128
SEQ, D = 2048, 1024
BLOCKS = SEQ // P
KT = D // P
HEADS = 4
LN_EPS = 1e-5
RMS_EPS = 1e-6
ALPHA = 4 ** 0.25
GELU_C = math.sqrt(2 / math.pi)
GELU_A = math.sqrt(0.044715)
TABLES = "natural_log_exp_and_others"


class Signal:

    def __init__(self, sem, per=1):
        self.sem, self.per = sem, per

    def inc(self):
        return self.sem, 1

    def upto(self, i, k=None):
        return self.sem, i * self.per + (self.per if k is None else k)

    def before(self, i):
        return self.sem, i * self.per


class Semaphores:

    def __init__(self, nc, prefix):
        self.nc, self.prefix, self.taken = nc, prefix, []

    def __enter__(self):
        return self

    def __call__(self, name):
        self.taken.append(self.nc.alloc_semaphore(name=self.prefix + name))
        return self.taken[-1]

    def __exit__(self, *_):
        self.nc.clear_and_free_semaphores(self.taken)
        self.nc.all_engine_barrier()


class Order:

    def __init__(self, eng, sem):
        self.eng, self.sem, self.count = eng, sem, 0

    def inc(self):
        self.count += 1
        return self.sem, 1

    def settle(self):
        self.eng.wait_ge(self.sem, self.count)

    def end_block(self):
        self.settle()
        self.eng.sem_clear(self.sem)
        self.count = 0


class Blk:

    def __init__(self, r, p, last=False):
        self.r, self.p, self.i, self.last = r, p, 2 * r + p, last
        self.q = 1 - p


def over_blocks(eng, body):
    with eng.Fori(0, BLOCKS // 2 - 1) as r:
        body(Blk(r, 0))
        body(Blk(r, 1))
    body(Blk(BLOCKS // 2 - 1, 0))
    body(Blk(BLOCKS // 2 - 1, 1, last=True))


def spread(ap, n):
    return ap.unsqueeze(2).broadcast_to([ap.shape[0], ap.shape[1], n])


def over_heads(ap, g):
    return ap.unsqueeze(1).broadcast_to([ap.shape[0], g, ap.shape[1]])


def row(ap, n=P):
    return ap.unsqueeze(0).broadcast_to([n, ap.shape[0]])


GLA_CHUNK = 64


def even_layer(nc, x, w_in, w_a2, b_a, gla_g, sgu_g, sgu_b, w_s, b_s, w_out, ln_g, ln_b, consts, x_next):
    ident_d, chunk_d, causal_d, tril_d = consts
    O_QK, O_V, O_GA, O_ALR, O_USV, O_GB = 0, 512, 1024, 1536, 1552, 2576
    W = w_in.shape[1]
    wv = w_in.rearrange("(k p) n -> p k n", p=P)
    with ExitStack() as ctx:
        sem = ctx.enter_context(Semaphores(nc, "e_"))

        def sb(name, shape, dt=F32):
            return ctx.enter_context(nc.sbuf_tensor("e_" + name, shape, dt))

        def sig(name, per=1):
            return Signal(sem(name), per)

        W_in = sb("w_in", [P, KT, W])
        W_out = sb("w_out", [P, KT, D])
        xb = sb("xb", [P, 2, D])
        xT = sb("xT", [P, KT * P])
        qk = sb("qk", [P, 512])
        v = sb("v", [P, 2, 512])
        gates = sb("gates", [P, 2, 1024])
        usv = sb("usv", [P, 2, 1024])
        alrT = sb("alrT", [17, 2, P])
        w2 = sb("w2", [17, 256])
        ident = sb("ident", [P, P])
        chunkm = sb("chunkm", [P, 2, P])
        causal = sb("causal", [P, P])
        tril = sb("tril", [P, P])
        gla_row = sb("gla_row", [P, 512])
        sgu_grow = sb("sgu_grow", [P, 512])
        sgu_brow = sb("sgu_brow", [P, 512])
        ln_grow = sb("ln_grow", [P, D])
        ln_brow = sb("ln_brow", [P, D])
        wsT = sb("wsT", [P, 4, P])
        bsT = sb("bsT", [P, 4])
        eps = sb("eps", [P, 1])
        la = sb("la", [P, 256])
        lt = sb("lt", [P, 256])
        eks = sb("eks", [P, 256])
        ebT = sb("ebT", [P, 2, P])
        enT = sb("enT", [P, 2, P])
        qz = sb("qz", [P, 4, P])
        kdT = sb("kdT", [P, 2, P])
        kst = sb("kst", [P, 256])
        probs = sb("probs", [P, 4, P])
        S = sb("S", [P, 2, P])
        Smid = sb("Smid", [P, 2, P])
        gt = sb("gt", [P, 1024])
        gl = sb("gl", [P, 1024])
        catT, cat = gt, gl
        sq = sb("sq", [P, 512])
        ws_in = sq[:].rearrange("p (g s) -> p g s", g=4)
        ss = sb("ss", [P, 4])
        rs = sb("rs", [P, 4])
        st6 = sb("st6", [P, 4, 6])
        mv = sb("mv", [P, 4, 2])
        rs2 = sb("rs2", [P, 4])
        lnst = sb("lnst", [P, 2, 6])
        lnmv = sb("lnmv", [P, 2])
        lnrs = sb("lnrs", [P, 1])
        bank = [ctx.enter_context(nc.psum_tensor(f"e_ps{n}", [P, 512], F32)) for n in range(8)]
        zk, bTp, qkTp, scp, Up, op = bank[2], bank[3], bank[4], bank[5], bank[6], bank[7]
        Uc = Up[:, 0:256], bTp[:, 256:512]

        loaded, wloaded = sig("loaded"), sig("wloaded")
        x_in = [sig("x_in0"), sig("x_in1")]
        stored = sig("stored")
        setup = sig("setup")
        ws_turned, ws_ready = sig("ws_turned"), sig("ws_ready")
        xT_made, xT_ready = sig("xT_made", 2), sig("xT_ready", 2)
        proj_made, proj_ready = sig("proj_made", 7), sig("proj_ready", 7)
        z_made, lse_ready, la_ready = sig("z_made"), sig("lse"), sig("la_ready")
        decay_made, decay_ready = sig("decay_made"), sig("decay_ready", 3)
        qkT_made, qkd_ready, kst_ready = sig("qkT_made"), sig("qkd_ready"), sig("kst_ready")
        sc_made, probs_ready = sig("sc_made"), sig("probs_ready")
        U_made, Smid_ready, S_ready = sig("U_made"), sig("Smid_ready"), sig("S_ready")
        o_made, sq_ready, ss_ready, rs_ready = sig("o_made"), sig("sq_ready"), sig("ss_ready"), sig("rs_ready")
        gexp_ready, gsig_ready, gate_ready = sig("gexp"), sig("gsig"), sig("gate_ready")
        usq_ready, inner_ready, uexp_ready, usig_ready, gelu_ready = (
            sig("usq"), sig("inner"), sig("uexp"), sig("usig"), sig("gelu_ready"))
        mv_ready, rs2_ready, norm_ready, sn_ready = sig("mv_ready"), sig("rs2_ready"), sig("norm_ready"), sig("sn_ready")
        s_made, ob_ready, oa_ready, cb_ready = sig("s_made"), sig("ob_ready"), sig("oa_ready"), sig("cb_ready")
        catT_made, catT_ready = sig("catT_made", 2), sig("catT_ready", 2)
        y_made, r_ready, lnmv_ready, lnrs_ready, lnn_ready, out_ready = (
            sig("y_made"), sig("r_ready"), sig("lnmv"), sig("lnrs"), sig("lnn"), sig("out_ready"))
        orders = {n: sem("order_" + n) for n in ("act", "dve", "pool")}

        def chunks(p):
            return [
                (O_V, v[:, p, :]), (O_GA, gates[:, p, 0:512]), (O_GB, gates[:, p, 512:1024]),
                (O_USV, usv[:, p, 0:512]), (O_USV + 512, usv[:, p, 512:1024]), (O_QK, qk[:]),
            ]

        block = ctx.enter_context(nc.Block())
        small = [(ident[:], ident_d), (chunkm[:], chunk_d), (causal[:], causal_d), (tril[:], tril_d), (w2[0:16, :], w_a2),
                 (w2[16:17, :], b_a.unsqueeze(0)), (gla_row[:], row(gla_g.rearrange("h e -> (h e)"))),
                 (sgu_grow[:], row(sgu_g.rearrange("h e -> (h e)"))), (sgu_brow[:], row(sgu_b.rearrange("h e -> (h e)"))),
                 (ln_grow[:], row(ln_g)), (ln_brow[:], row(ln_b)), (ws_in, w_s.rearrange("g t s -> t g s")),
                 (bsT[:], b_s.rearrange("g t -> t g"))]
        NSMALL = 16 * len(small)

        @block.sync
        def _(sp):
            sp.dma_start(xb[:, 0, :], x[0:P, :]).then_inc(x_in[0].sem, 16)
            sp.dma_start(xb[:, 1, :], x[P:2 * P, :]).then_inc(x_in[1].sem, 16)
            with nc.allow_non_contiguous_dma(reason="small tables"):
                for dst, src in small:
                    sp.dma_start(dst, src).then_inc(loaded.sem, 16)
            for k in range(KT):
                sp.dma_start(W_in[:, k, :], wv[:, k, :]).then_inc(wloaded.sem, 16)
            sp.dma_start(W_out[:], w_out.rearrange("(k p) n -> p k n", p=P)).then_inc(wloaded.sem, 16)

            def body(b, load=True):
                sp.wait_ge(*out_ready.upto(b.i))
                sp.dma_start(x_next[bass.ds(b.i * P, P), :], xb[:, b.p, :]).then_inc(stored.sem, 16)
                if load:
                    sp.wait_ge(stored.sem, b.i * 16 + 16)
                    sp.dma_start(xb[:, b.p, :], x[bass.ds(b.i * P + 2 * P, P), :]).then_inc(x_in[b.p].sem, 16)

            with sp.Fori(0, BLOCKS // 2 - 1) as r:
                body(Blk(r, 0))
                body(Blk(r, 1))
            body(Blk(BLOCKS // 2 - 1, 0), load=False)
            body(Blk(BLOCKS // 2 - 1, 1), load=False)
            sp.wait_ge(stored.sem, 16 * BLOCKS)

        @block.tensor
        def _(pe):
            def turn_x(i, r, p):
                pe.wait_ge(x_in[p].sem, 16 * r + 16)
                for half in range(2):
                    pe.wait_ge(*proj_ready.before(i))
                    for k in range(4):
                        t = 4 * half + k
                        m = pe.transpose(bank[half][:, k * P:(k + 1) * P], xb[:, p, t * P:(t + 1) * P], ident[:])
                    m.then_inc(*xT_made.inc())

            def project(i, p, c):
                if c < 6:
                    off, _ = chunks(p)[c]
                    if c < 2:
                        pe.wait_ge(*xT_ready.upto(i))
                    else:
                        pe.wait_ge(*proj_ready.upto(i, c - 1))
                    for k in range(KT):
                        m = pe.matmul(bank[c % 2][:], xT[:, k * P:(k + 1) * P], W_in[:, k, off:off + 512],
                                      start=(k == 0), stop=(k == KT - 1))
                    m.then_inc(*proj_made.inc())
                else:
                    pe.wait_ge(*proj_ready.upto(i, 5))
                    for k in range(KT):
                        m = pe.matmul(bank[0][0:16, 0:P], W_in[:, k, O_ALR:O_ALR + 16], xT[:, k * P:(k + 1) * P],
                                      start=(k == 0), stop=(k == KT - 1))
                    m.then_inc(*proj_made.inc())

            pe.wait_ge(loaded.sem, NSMALL)
            for g in range(4):
                m = pe.transpose(bank[2][:, g * P:(g + 1) * P], ws_in[:, g, :], ident[:])
            m.then_inc(*ws_turned.inc())
            turn_x(0, 0, 0)
            pe.wait_ge(wloaded.sem, 16 * (KT + 1))
            for c in range(7):
                project(0, 0, c)
            pe.wait_ge(*setup.upto(0))
            pe.wait_ge(*ws_ready.upto(0))

            def body(b):
                i, p = b.i, b.p
                nxt = []
                if not b.last:
                    r1, i1 = (b.r, b.i + 1) if p == 0 else (b.r + 1, b.i + 1)
                    nxt = [lambda: turn_x(i1, r1, b.q)] + [(lambda c=c: project(i1, b.q, c)) for c in range(7)]

                def fill():
                    if nxt:
                        nxt.pop(0)()

                pe.wait_ge(*proj_ready.upto(i))
                pe.wait_ge(*r_ready.before(i))
                pe.matmul(zk[:, 0:256], alrT[:, p, :], w2[:], start=True, stop=True).then_inc(*z_made.inc())
                fill()
                for g in range(4):
                    m = pe.transpose(qkTp[:, g * P:(g + 1) * P], qk[:, g * P:(g + 1) * P], ident[:])
                m.then_inc(*qkT_made.inc())
                fill()
                pe.wait_ge(*la_ready.upto(i))
                pe.matmul(zk[:, 256:512], chunkm[:, 1, :], la[:], start=True, stop=True)
                for g in range(2):
                    m = pe.matmul(bTp[:, g * P:(g + 1) * P], la[:, g * P:(g + 1) * P], chunkm[:, 0, :],
                                  start=True, stop=True)
                m.then_inc(*decay_made.inc())
                fill()
                pe.wait_ge(*kst_ready.upto(i))
                pe.wait_ge(*qkd_ready.upto(i))
                for h in range(4):
                    m = pe.matmul(scp[:, h * P:(h + 1) * P], kdT[:, h // 2, :], qz[:, h, :], start=True, stop=True)
                m.then_inc(*sc_made.inc())
                for c in range(2):
                    for h in range(4):
                        a, g = 64 * (h % 2), h // 2
                        m = pe.matmul(Uc[c][a:a + 64, g * P:(g + 1) * P],
                                      kst[64 * c:64 * c + 64, h * 64:h * 64 + 64],
                                      v[64 * c:64 * c + 64, p, h * P:(h + 1) * P], start=True, stop=True)
                m.then_inc(*U_made.inc())
                fill()
                pe.wait_ge(*probs_ready.upto(i))
                pe.wait_ge(*Smid_ready.upto(i))
                for h in range(4):
                    g = h // 2
                    pe.matmul(op[:, h * P:(h + 1) * P], probs[:, h, :], v[:, p, h * P:(h + 1) * P],
                              start=True, stop=False, skip_group_check=True)
                    pe.matmul(op[0:64, h * P:(h + 1) * P], qz[:, h, 0:64], S[:, g, :],
                              start=False, stop=False, skip_group_check=True)
                    m = pe.matmul(op[64:128, h * P:(h + 1) * P], qz[:, h, 64:128], Smid[:, g, :],
                                  start=False, stop=True, skip_group_check=True)
                m.then_inc(*o_made.inc())
                fill()
                pe.wait_ge(*sn_ready.upto(i))
                pe.wait_ge(*S_ready.upto(i))
                for g in range(4):
                    m = pe.matmul(Up[:, g * P:(g + 1) * P], wsT[:, g, :], usv[:, p, 512 + g * P:512 + (g + 1) * P],
                                  start=True, stop=True)
                m.then_inc(*s_made.inc())
                fill()
                for half, ready in enumerate((oa_ready, cb_ready)):
                    pe.wait_ge(*ready.upto(i))
                    for k in range(4):
                        t = 4 * half + k
                        m = pe.transpose((qkTp, scp)[half][:, k * P:(k + 1) * P], cat[:, t * P:(t + 1) * P], ident[:])
                    m.then_inc(*catT_made.inc())
                    fill()
                pe.wait_ge(*catT_ready.upto(i))
                for half in range(2):
                    for k in range(KT):
                        m = pe.matmul((zk, bTp)[half][:], catT[:, k * P:(k + 1) * P],
                                      W_out[:, k, half * 512:(half + 1) * 512], start=(k == 0), stop=(k == KT - 1))
                m.then_inc(*y_made.inc())
                while nxt:
                    fill()

            over_blocks(pe, body)

        @block.scalar
        def _(act):
            o = Order(act, orders["act"])
            act.preload_act_table_set(TABLES)

            def turn_x(i, p):
                for half in range(2):
                    act.wait_ge(*xT_made.upto(i, half + 1))
                    act.activation(xT[:, half * 512:(half + 1) * 512], bank[half][:], ACT.Copy).then_inc(*xT_ready.inc())

            def project(i, p, c):
                act.wait_ge(*proj_made.upto(i, c + 1))
                if c == 5:
                    act.wait_ge(*kst_ready.before(i))
                if c < 6:
                    act.activation(chunks(p)[c][1], bank[c % 2][:], ACT.Copy).then_inc(*proj_ready.inc())
                else:
                    act.activation(alrT[0:16, p, :], bank[0][0:16, 0:P], ACT.Copy).then_inc(*proj_ready.inc())

            turn_x(0, 0)
            act.wait_ge(*setup.upto(0))
            for c in range(7):
                project(0, 0, c)

            def body(b):
                i, p = b.i, b.p
                nxt = []
                if not b.last:
                    nxt = [lambda: turn_x(b.i + 1, b.q)] + [(lambda c=c: project(b.i + 1, b.q, c)) for c in range(7)]

                def fill():
                    if nxt:
                        nxt.pop(0)()

                act.wait_ge(*y_made.before(i))
                act.wait_ge(*z_made.upto(i))
                act.activation(lt[:], zk[:, 0:256], ACT.Abs).then_inc(*o.inc())
                o.settle()
                act.activation(eks[:], lt[:], ACT.Exp, scale=-1.0).then_inc(*o.inc())
                o.settle()
                act.activation(lt[:], eks[:], ACT.Ln, bias=1.0).then_inc(*lse_ready.inc())
                fill()
                act.wait_ge(*proj_ready.upto(i))
                act.activation(gt[:], gates[:, p, :], ACT.Exp, scale=-1.0).then_inc(*gexp_ready.inc())
                act.activation(gl[:], usv[:, p, :], ACT.Square, scale=GELU_A).then_inc(*usq_ready.inc())
                fill()
                act.wait_ge(*decay_made.upto(i))
                act.activation(eks[:], zk[:, 256:512], ACT.Exp).then_inc(*decay_ready.inc())
                act.activation(ebT[:], bTp[:, 0:256].rearrange("p (g t) -> p g t", g=2), ACT.Exp).then_inc(*decay_ready.inc())
                act.activation(enT[:], bTp[:, 0:256].rearrange("p (g t) -> p g t", g=2), ACT.Exp, scale=-1.0)\
                   .then_inc(*decay_ready.inc())
                act.wait_ge(*inner_ready.upto(i))
                act.activation(gl[:], gl[:], ACT.Exp, scale=-2.0 * GELU_C).then_inc(*uexp_ready.inc())
                fill()
                fill()
                act.wait_ge(*o_made.upto(i))
                act.activation(sq[:], op[:], ACT.Square).then_inc(*sq_ready.inc())
                act.wait_ge(*mv_ready.upto(i))
                act.activation(rs2[:], mv[:, :, 1], ACT.Ln, bias=eps[:, 0:1]).then_inc(*o.inc())
                o.settle()
                act.activation(rs2[:], rs2[:], ACT.Exp, scale=-0.5).then_inc(*rs2_ready.inc())
                act.wait_ge(*ss_ready.upto(i))
                act.activation(rs[:], ss[:], ACT.Ln, bias=eps[:, 0:1], scale=1.0 / P).then_inc(*o.inc())
                o.settle()
                act.activation(rs[:], rs[:], ACT.Exp, scale=-0.5).then_inc(*rs_ready.inc())
                fill()
                fill()
                for half in range(2):
                    act.wait_ge(*catT_made.upto(i, half + 1))
                    act.activation(catT[:, half * 512:(half + 1) * 512], (qkTp, scp)[half][:], ACT.Copy)\
                       .then_inc(*catT_ready.inc())
                    fill()
                act.wait_ge(*lnmv_ready.upto(i))
                act.activation(lnrs[:], lnmv[:, 1:2], ACT.Ln, bias=eps[:, 0:1]).then_inc(*o.inc())
                o.settle()
                act.activation(lnrs[:], lnrs[:], ACT.Exp, scale=-0.5).then_inc(*lnrs_ready.inc())
                while nxt:
                    fill()
                o.end_block()

            over_blocks(act, body)

        @block.vector
        def _(dve):
            o = Order(dve, orders["dve"])
            dve.memset(S[:], 0.0).then_inc(*o.inc())
            dve.memset(qz[:], 0.0).then_inc(*o.inc())
            dve.memset(eps[:], LN_EPS).then_inc(*o.inc())
            dve.memset(alrT[:], 1.0).then_inc(*o.inc())
            o.settle()
            dve.memset(st6[:], 0.0).then_inc(*setup.inc())
            dve.wait_ge(*ws_turned.upto(0))
            dve.wait_ge(loaded.sem, NSMALL)
            dve.tensor_tensor(wsT[:], bank[2][:].rearrange("p (g t) -> p g t", g=4), over_heads(tril[:, :], 4),
                              ALU.mult).then_inc(*ws_ready.inc())
            o.end_block()

            def body(b):
                i, p = b.i, b.p
                dve.wait_ge(*lse_ready.upto(i))
                dve.scalar_tensor_tensor(la[:], zk[:, 0:256], 0.0, lt[:], ALU.min, ALU.subtract).then_inc(*la_ready.inc())
                dve.wait_ge(*gexp_ready.upto(i))
                dve.tensor_scalar_add(gt[:], gt[:], 1.0).then_inc(*o.inc())
                o.settle()
                dve.reciprocal(gt[:], gt[:]).then_inc(*gsig_ready.inc())
                dve.wait_ge(*qkT_made.upto(i))
                dve.wait_ge(*decay_ready.upto(i))
                for a in (0, 64):
                    dve.scalar_tensor_tensor(qz[a:a + 64].rearrange("p (g b) t -> p b g t", b=2)[:, a // 64],
                                             qkTp[a:a + 64, 0:256].rearrange("p (g t) -> p g t", g=2), 0.125,
                                             ebT[a:a + 64], ALU.mult, ALU.mult).then_inc(*o.inc())
                dve.tensor_tensor(kdT[:], qkTp[:, 256:512].rearrange("p (g t) -> p g t", g=2), enT[:], ALU.mult)\
                   .then_inc(*qkd_ready.inc())
                dve.wait_ge(*uexp_ready.upto(i))
                dve.tensor_scalar_add(gl[:], gl[:], 1.0).then_inc(*o.inc())
                o.settle()
                dve.reciprocal(gl[:], gl[:]).then_inc(*usig_ready.inc())
                dve.wait_ge(*sc_made.upto(i))
                dve.tensor_tensor(probs[:], scp[:].rearrange("p (h t) -> p h t", h=4), over_heads(causal[:, :], 4),
                                  ALU.mult).then_inc(*probs_ready.inc())
                dve.wait_ge(*U_made.upto(i))
                for g in range(2):
                    dve.scalar_tensor_tensor(Smid[:, g, :], S[:, g, :], ebT[:, g, 63:64], Uc[0][:, g * P:(g + 1) * P],
                                             ALU.mult, ALU.add).then_inc(*(Smid_ready if g else o).inc())
                dve.wait_ge(*gelu_ready.upto(i))
                for g in range(4):
                    dve.bn_stats(st6[:, g, :], usv[:, p, 512 + g * P:512 + (g + 1) * P]).then_inc(*o.inc())
                o.settle()
                for g in range(4):
                    dve.bn_aggr(mv[:, g, :], st6[:, g, :]).then_inc(*(mv_ready if g == 3 else o).inc())
                dve.wait_ge(*rs2_ready.upto(i))
                for g in range(4):
                    dve.tensor_scalar(usv[:, p, 512 + g * P:512 + (g + 1) * P], usv[:, p, 512 + g * P:512 + (g + 1) * P], mv[:, g, 0:1],
                                      rs2[:, g:g + 1], ALU.subtract, ALU.mult)\
                       .then_inc(*(norm_ready if g == 3 else o).inc())
                dve.wait_ge(*o_made.upto(i))
                for g in range(2):
                    dve.scalar_tensor_tensor(S[:, g, :], Smid[:, g, :], ebT[:, g, 127:128],
                                             Uc[1][:, g * P:(g + 1) * P], ALU.mult, ALU.add)\
                       .then_inc(*(S_ready if g else o).inc())
                dve.wait_ge(*sq_ready.upto(i))
                dve.tensor_reduce(ss[:], sq[:].rearrange("p (h e) -> p h e", h=4), AX.X, ALU.add).then_inc(*ss_ready.inc())
                dve.wait_ge(*rs_ready.upto(i))
                dve.wait_ge(*gate_ready.upto(i))
                for h in range(4):
                    dve.scalar_tensor_tensor(cat[:, h * P:(h + 1) * P], op[:, h * P:(h + 1) * P], rs[:, h:h + 1],
                                             gates[:, p, h * P:(h + 1) * P], ALU.mult, ALU.mult)\
                       .then_inc(*(oa_ready if h == 3 else o).inc())
                dve.wait_ge(*s_made.upto(i))
                for g in range(4):
                    dve.scalar_tensor_tensor(cat[:, 512 + g * P:512 + (g + 1) * P], Up[:, g * P:(g + 1) * P], bsT[:, g:g + 1],
                                             usv[:, p, g * P:(g + 1) * P], ALU.add, ALU.mult)\
                       .then_inc(*(ob_ready if g == 3 else o).inc())
                dve.wait_ge(*y_made.upto(i))
                for half in range(2):
                    dve.scalar_tensor_tensor(xb[:, p, half * 512:(half + 1) * 512], xb[:, p, half * 512:(half + 1) * 512],
                                             ALPHA, (zk, bTp)[half][:], ALU.mult, ALU.add)\
                       .then_inc(*(r_ready if half else o).inc())
                dve.wait_ge(*r_ready.upto(i))
                for half in range(2):
                    dve.bn_stats(lnst[:, half, :], xb[:, p, half * 512:(half + 1) * 512]).then_inc(*o.inc())
                o.settle()
                dve.bn_aggr(lnmv[:], lnst[:].rearrange("p a b -> p (a b)")).then_inc(*lnmv_ready.inc())
                dve.wait_ge(*lnrs_ready.upto(i))
                dve.tensor_scalar(xb[:, p, :], xb[:, p, :], lnmv[:, 0:1], lnrs[:, 0:1], ALU.subtract, ALU.mult)\
                   .then_inc(*lnn_ready.inc())
                o.end_block()

            over_blocks(dve, body)

        @block.gpsimd
        def _(pool):
            o = Order(pool, orders["pool"])
            pool.wait_ge(loaded.sem, NSMALL)

            def body(b):
                i, p = b.i, b.p
                pool.wait_ge(*usq_ready.upto(i))
                pool.tensor_tensor(gl[:], gl[:], usv[:, p, :], ALU.mult).then_inc(*o.inc())
                o.settle()
                pool.tensor_tensor(gl[:], gl[:], usv[:, p, :], ALU.add).then_inc(*inner_ready.inc())
                pool.wait_ge(*decay_ready.upto(i, 1))
                pool.tensor_tensor(kst[:], qk[:, 256:512], eks[:], ALU.mult).then_inc(*kst_ready.inc())
                pool.wait_ge(*usig_ready.upto(i))
                pool.tensor_tensor(usv[:, p, :], usv[:, p, :], gl[:], ALU.mult).then_inc(*gelu_ready.inc())
                pool.wait_ge(*gsig_ready.upto(i))
                pool.tensor_tensor(gates[:, p, :], gates[:, p, :], gt[:], ALU.mult).then_inc(*o.inc())
                o.settle()
                pool.tensor_tensor(gates[:, p, 0:512], gates[:, p, 0:512], gla_row[:], ALU.mult).then_inc(*gate_ready.inc())
                pool.wait_ge(*norm_ready.upto(i))
                pool.tensor_tensor(usv[:, p, 512:1024], usv[:, p, 512:1024], sgu_grow[:], ALU.mult).then_inc(*o.inc())
                o.settle()
                pool.tensor_tensor(usv[:, p, 512:1024], usv[:, p, 512:1024], sgu_brow[:], ALU.add).then_inc(*sn_ready.inc())
                pool.wait_ge(*ob_ready.upto(i))
                pool.tensor_tensor(cat[:, 512:1024], cat[:, 512:1024], gates[:, p, 512:1024], ALU.mult).then_inc(*cb_ready.inc())
                pool.wait_ge(*lnn_ready.upto(i))
                pool.tensor_tensor(xb[:, p, :], xb[:, p, :], ln_grow[:], ALU.mult).then_inc(*o.inc())
                o.settle()
                pool.tensor_tensor(xb[:, p, :], xb[:, p, :], ln_brow[:], ALU.add).then_inc(*out_ready.inc())
                o.end_block()

            over_blocks(pool, body)


POOL_WINDOWS = (2, 4, 8, 16)
TWO_PI = 2 * math.pi
PI_A = 6.28125
PI_B = float(np.float32(TWO_PI - PI_A) // np.float32(2 ** -20) * np.float32(2 ** -20))
PI_C = TWO_PI - PI_A - PI_B
ROUND = 1.5 * 2 ** 23


def odd_layer(nc, x, positions, w_in, ret_g, w_pool, pool_scale, w_out, ln_g, ln_b, consts, x_next):
    ident_d, inv_d, dmat_d, winter_d, wstate_d, gammac_d, band_d = consts
    O_QK, O_V, O_GC, O_P, O_GD = 0, 512, 1024, 1536, 2048
    W = w_in.shape[1]
    wv = w_in.rearrange("(k p) n -> p k n", p=P)
    with ExitStack() as ctx:
        sem = ctx.enter_context(Semaphores(nc, "o_"))

        def sb(name, shape, dt=F32):
            return ctx.enter_context(nc.sbuf_tensor("o_" + name, shape, dt))

        def sig(name, per=1):
            return Signal(sem(name), per)

        W_in = sb("w_in", [P, KT, W])
        W_out = sb("w_out", [P, KT, D])
        xb = sb("xb", [P, 2, D])
        xT = sb("xT", [P, KT * P])
        qk = sb("qk", [P, 2, 512])
        v = sb("v", [P, 2, 512])
        gates = sb("gates", [P, 2, 1024])
        pp = sb("pp", [P, 2, 512])
        ident = sb("ident", [P, P])
        inv = sb("inv", [P, 32])
        dmat = sb("dmat", [P, 4, P])
        winter = sb("winter", [P, 4, P])
        wstate = sb("wstate", [P, 4])
        gammac = sb("gammac", [P, 2])
        band = sb("band", [P, 12, P])
        poolw = sb("poolw", [P, 4, P])
        ret_row = sb("ret_row", [P, 512])
        scale_row = sb("scale_row", [P, 512])
        ln_grow = sb("ln_grow", [P, D])
        ln_brow = sb("ln_brow", [P, D])
        eps = sb("eps", [P, 1])
        halfpi = sb("halfpi", [P, 1])
        posi = sb("posi", [P, BLOCKS], I32)
        posf = sb("posf", [P, BLOCKS])
        ang = sb("ang", [P, BLOCKS, 32])
        red = sb("red", [P, BLOCKS, 32])
        turns = sb("turns", [P, BLOCKS, 32])
        sin = sb("sin", [P, BLOCKS, 32])
        cos = sb("cos", [P, BLOCKS, 32])
        ra = sb("ra", [P, 8, 32])
        rb = sb("rb", [P, 8, 32])
        rc = sb("rc", [P, 8, 32])
        rd = sb("rd", [P, 8, 32])
        rot = sb("rot", [P, 8, 64])
        qT = sb("qT", [P, 2, P])
        kT = sb("kT", [P, 2, P])
        qz = sb("qz", [P, 4, P])
        qw = sb("qw", [P, 4, P])
        kst = sb("kst", [P, 256])
        probs = sb("probs", [P, 4, P])
        S = sb("S", [P, 2, P])
        pT = sb("pT", [P, 4, P])
        gt = sb("gt", [P, 1024])
        cat = sb("cat", [P, 1024])
        catT = gt
        st6 = sb("st6", [P, 4, 6])
        mv = sb("mv", [P, 4, 2])
        rs = sb("rs", [P, 4])
        lnst = sb("lnst", [P, 2, 6])
        lnmv = sb("lnmv", [P, 2])
        lnrs = sb("lnrs", [P, 1])
        bank = [ctx.enter_context(nc.psum_tensor(f"o_ps{n}", [P, 512], F32)) for n in range(8)]
        y0, y1, qkTp, scp, Up, op = bank[2], bank[3], bank[4], bank[5], bank[6], bank[7]

        loaded, wloaded = sig("loaded"), sig("wloaded")
        x_in = [sig("x_in0"), sig("x_in1")]
        stored, setup, tables = sig("stored"), sig("setup"), sig("tables", 2)
        xT_made, xT_ready = sig("xT_made", 2), sig("xT_ready", 2)
        proj_made, proj_ready = sig("proj_made", 5), sig("proj_ready", 5)
        rot_ready, qkT_made, qk_ready, kst_ready = sig("rot"), sig("qkT_made"), sig("qk_ready"), sig("kst")
        rot_part = sig("rot_part")
        sc_made, probs_ready, U_made, o_made, S_ready = sig("sc_made"), sig("probs"), sig("U_made"), sig("o_made"), sig("S_ready")
        gexp_ready, gsig_ready, gate_ready = sig("gexp"), sig("gsig"), sig("gate")
        mv_ready, rs_ready, oc_ready = sig("mv"), sig("rs"), sig("oc")
        pT_made, pT_ready, pd_made, od_ready = sig("pT_made"), sig("pT_ready"), sig("pd_made"), sig("od")
        catT_made, catT_ready = sig("catT_made", 2), sig("catT_ready", 2)
        y_made, r_ready, lnmv_ready, lnrs_ready, lnn_ready, out_ready = (
            sig("y_made"), sig("r_ready"), sig("lnmv"), sig("lnrs"), sig("lnn"), sig("out_ready"))
        orders = {n: sem("order_" + n) for n in ("act", "dve", "pool")}

        def chunks(p):
            return [(O_QK, qk[:, p, :]), (O_GC, gates[:, p, 0:512]), (O_GD, gates[:, p, 512:1024]),
                    (O_V, v[:, p, :]), (O_P, pp[:, p, :])]

        block = ctx.enter_context(nc.Block())
        small = [(ident[:], ident_d), (inv[:], inv_d), (dmat[:], dmat_d), (winter[:], winter_d), (wstate[:], wstate_d),
                 (gammac[:], gammac_d), (band[:], band_d), (poolw[:], w_pool.rearrange("g c d -> c g d")),
                 (ret_row[:], row(ret_g.rearrange("h e -> (h e)"))), (scale_row[:], row(pool_scale)),
                 (ln_grow[:], row(ln_g)), (ln_brow[:], row(ln_b)),
                 (posi[:], positions.rearrange("(b p) -> p b", p=P))]
        NSMALL = 16 * len(small)

        @block.sync
        def _(sp):
            sp.dma_start(xb[:, 0, :], x[0:P, :]).then_inc(x_in[0].sem, 16)
            sp.dma_start(xb[:, 1, :], x[P:2 * P, :]).then_inc(x_in[1].sem, 16)
            with nc.allow_non_contiguous_dma(reason="small tables"):
                for dst, src in small:
                    sp.dma_start(dst, src).then_inc(loaded.sem, 16)
            for k in range(KT):
                sp.dma_start(W_in[:, k, :], wv[:, k, :]).then_inc(wloaded.sem, 16)
            sp.dma_start(W_out[:], w_out.rearrange("(k p) n -> p k n", p=P)).then_inc(wloaded.sem, 16)

            def body(b, load=True):
                sp.wait_ge(*out_ready.upto(b.i))
                sp.dma_start(x_next[bass.ds(b.i * P, P), :], xb[:, b.p, :]).then_inc(stored.sem, 16)
                if load:
                    sp.wait_ge(stored.sem, b.i * 16 + 16)
                    sp.dma_start(xb[:, b.p, :], x[bass.ds(b.i * P + 2 * P, P), :]).then_inc(x_in[b.p].sem, 16)

            with sp.Fori(0, BLOCKS // 2 - 1) as r:
                body(Blk(r, 0))
                body(Blk(r, 1))
            body(Blk(BLOCKS // 2 - 1, 0), load=False)
            body(Blk(BLOCKS // 2 - 1, 1), load=False)
            sp.wait_ge(stored.sem, 16 * BLOCKS)

        @block.tensor
        def _(pe):
            def turn_x(i, r, p):
                pe.wait_ge(x_in[p].sem, 16 * r + 16)
                pe.wait_ge(*proj_ready.before(i))
                for half in range(2):
                    for k in range(4):
                        t = 4 * half + k
                        m = pe.transpose(bank[half][:, k * P:(k + 1) * P], xb[:, p, t * P:(t + 1) * P], ident[:])
                    m.then_inc(*xT_made.inc())

            def project(i, p, c):
                off, _ = chunks(p)[c]
                if c < 2:
                    pe.wait_ge(*xT_ready.upto(i))
                else:
                    pe.wait_ge(*proj_ready.upto(i, c - 1))
                for k in range(KT):
                    m = pe.matmul(bank[c % 2][:], xT[:, k * P:(k + 1) * P], W_in[:, k, off:off + 512],
                                  start=(k == 0), stop=(k == KT - 1))
                m.then_inc(*proj_made.inc())

            pe.wait_ge(loaded.sem, NSMALL)
            turn_x(0, 0, 0)
            pe.wait_ge(wloaded.sem, 16 * (KT + 1))
            for c in range(5):
                project(0, 0, c)
            pe.wait_ge(*setup.upto(0))

            def body(b, first=False):
                i, p = b.i, b.p
                nxt = []
                if not b.last:
                    r1, i1 = (b.r, b.i + 1) if p == 0 else (b.r + 1, b.i + 1)
                    nxt = [lambda: turn_x(i1, r1, b.q)] + [(lambda c=c: project(i1, b.q, c)) for c in range(5)]

                def fill():
                    if nxt:
                        nxt.pop(0)()

                pe.wait_ge(*proj_ready.upto(i))
                pe.wait_ge(*S_ready.before(i))
                for w in range(4):
                    m = pe.matmul(Up[:, w * P:(w + 1) * P], pp[:, p, w * P:(w + 1) * P], band[:, (8 if first else 0) + w, :],
                                  start=True, stop=first)
                    if not first:
                        m = pe.matmul(Up[:, w * P:(w + 1) * P], pp[:, b.q, w * P:(w + 1) * P], band[:, 4 + w, :],
                                      start=False, stop=True)
                m.then_inc(*pT_made.inc())
                fill()
                fill()
                pe.wait_ge(*rot_ready.upto(i))
                pe.wait_ge(*catT_ready.before(i))
                for g in range(4):
                    m = pe.transpose(qkTp[:, g * P:(g + 1) * P], rot[:, 2 * g:2 * g + 2, :].rearrange("p a b -> p (a b)"), ident[:])
                m.then_inc(*qkT_made.inc())
                fill()
                pe.wait_ge(*qk_ready.upto(i))
                for h in range(4):
                    m = pe.matmul(scp[:, h * P:(h + 1) * P], kT[:, h // 2, :], qz[:, h, :], start=True, stop=True)
                m.then_inc(*sc_made.inc())
                pe.wait_ge(*kst_ready.upto(i))
                pe.wait_ge(*pT_ready.upto(i))
                for h in range(4):
                    a, g = 64 * (h % 2), h // 2
                    m = pe.matmul(Up[a:a + 64, g * P:(g + 1) * P], kst[:, h * 64:h * 64 + 64],
                                  v[:, p, h * P:(h + 1) * P], start=True, stop=True)
                m.then_inc(*U_made.inc())
                pe.wait_ge(*r_ready.before(i))
                for w in range(4):
                    m = pe.matmul(y0[:, w * P:(w + 1) * P], pT[:, w, :], poolw[:, w, :], start=True, stop=True)
                m.then_inc(*pd_made.inc())
                fill()
                pe.wait_ge(*probs_ready.upto(i))
                for h in range(4):
                    g = h // 2
                    pe.matmul(op[:, h * P:(h + 1) * P], probs[:, h, :], v[:, p, h * P:(h + 1) * P], start=True, stop=False)
                    m = pe.matmul(op[:, h * P:(h + 1) * P], qw[:, h, :], S[:, g, :], start=False, stop=True)
                m.then_inc(*o_made.inc())
                fill()
                for half, ready in ((1, od_ready), (0, oc_ready)):
                    pe.wait_ge(*ready.upto(i))
                    for k in range(4):
                        t = 4 * half + k
                        m = pe.transpose((qkTp, scp)[half][:, k * P:(k + 1) * P], cat[:, t * P:(t + 1) * P], ident[:])
                    m.then_inc(*catT_made.inc())
                while nxt:
                    fill()
                pe.wait_ge(*catT_ready.upto(i))
                for half in range(2):
                    for k in range(KT):
                        m = pe.matmul((y0, y1)[half][:], catT[:, k * P:(k + 1) * P],
                                      W_out[:, k, half * 512:(half + 1) * 512], start=(k == 0), stop=(k == KT - 1))
                m.then_inc(*y_made.inc())

            body(Blk(0, 0), first=True)
            body(Blk(0, 1))
            with pe.Fori(1, BLOCKS // 2 - 1) as r:
                body(Blk(r, 0))
                body(Blk(r, 1))
            body(Blk(BLOCKS // 2 - 1, 0))
            body(Blk(BLOCKS // 2 - 1, 1, last=True))

        @block.scalar
        def _(act):
            o = Order(act, orders["act"])

            def turn_x(i, p):
                for half in range(2):
                    act.wait_ge(*xT_made.upto(i, half + 1))
                    act.activation(xT[:, half * 512:(half + 1) * 512], bank[half][:], ACT.Copy).then_inc(*xT_ready.inc())

            def project(i, p, c):
                act.wait_ge(*proj_made.upto(i, c + 1))
                act.activation(chunks(p)[c][1], bank[c % 2][:], ACT.Copy).then_inc(*proj_ready.inc())

            act.wait_ge(*tables.upto(0, 2))
            act.activation(sin[:], red[:], ACT.Sin).then_inc(*o.inc())
            act.activation(cos[:], turns[:], ACT.Sin).then_inc(*o.inc())
            o.settle()
            act.preload_act_table_set(TABLES)
            turn_x(0, 0)
            for c in range(5):
                project(0, 0, c)
            act.activation(lnrs[:], eps[:], ACT.Copy).then_inc(*setup.inc())
            o.end_block()

            def body(b):
                i, p = b.i, b.p
                nxt = []
                if not b.last:
                    nxt = [lambda: turn_x(b.i + 1, b.q)] + [(lambda c=c: project(b.i + 1, b.q, c)) for c in range(5)]

                def fill():
                    if nxt:
                        nxt.pop(0)()

                act.wait_ge(*y_made.before(i))
                act.wait_ge(*proj_ready.upto(i))
                act.activation(gt[:], gates[:, p, :], ACT.Exp, scale=-1.0).then_inc(*gexp_ready.inc())
                act.wait_ge(*pT_made.upto(i))
                act.activation(pT[:], Up[:].rearrange("p (g t) -> p g t", g=4), ACT.Copy).then_inc(*pT_ready.inc())
                fill()
                fill()
                fill()
                fill()
                act.wait_ge(*mv_ready.upto(i))
                act.activation(rs[:], mv[:, :, 1], ACT.Ln, bias=eps[:, 0:1]).then_inc(*o.inc())
                o.settle()
                act.activation(rs[:], rs[:], ACT.Exp, scale=-0.5).then_inc(*rs_ready.inc())
                fill()
                for half in (1, 0):
                    act.wait_ge(*catT_made.upto(i, 2 - half))
                    act.activation(catT[:, half * 512:(half + 1) * 512], (qkTp, scp)[half][:], ACT.Copy)\
                       .then_inc(*catT_ready.inc())
                while nxt:
                    fill()
                act.wait_ge(*lnmv_ready.upto(i))
                act.activation(lnrs[:], lnmv[:, 1:2], ACT.Ln, bias=eps[:, 0:1]).then_inc(*o.inc())
                o.settle()
                act.activation(lnrs[:], lnrs[:], ACT.Exp, scale=-0.5).then_inc(*lnrs_ready.inc())
                o.end_block()

            over_blocks(act, body)

        @block.vector
        def _(dve):
            o = Order(dve, orders["dve"])
            dve.memset(S[:], 0.0).then_inc(*o.inc())
            dve.memset(qz[:], 0.0).then_inc(*o.inc())
            dve.memset(eps[:], LN_EPS).then_inc(*o.inc())
            dve.wait_ge(loaded.sem, NSMALL)
            dve.tensor_copy(posf[:], posi[:]).then_inc(*o.inc())
            o.settle()
            dve.tensor_tensor(ang[:], spread(posf[:], 32), over_heads(inv[:], BLOCKS), ALU.mult).then_inc(*o.inc())
            o.settle()

            def reduce(dst, quarter, done):
                dve.tensor_scalar(rnd, ang[:], 1 / TWO_PI, quarter, ALU.mult, ALU.add).then_inc(*o.inc())
                o.settle()
                dve.tensor_scalar(rnd, rnd, ROUND, ROUND, ALU.add, ALU.subtract).then_inc(*o.inc())
                o.settle()
                dve.scalar_tensor_tensor(dst, rnd, -PI_A, ang[:], ALU.mult, ALU.add).then_inc(*o.inc())
                o.settle()
                dve.scalar_tensor_tensor(dst, rnd, -PI_B, dst, ALU.mult, ALU.add).then_inc(*o.inc())
                o.settle()
                dve.scalar_tensor_tensor(dst, rnd, -PI_C, dst, ALU.mult, ALU.add).then_inc(*o.inc())
                o.settle()
                dve.tensor_scalar(dst, dst, quarter * TWO_PI, math.pi * (1 - 1e-7), ALU.add, ALU.min).then_inc(*o.inc())
                o.settle()
                dve.tensor_scalar(dst, dst, -math.pi * (1 - 1e-7), None, ALU.max).then_inc(*done.inc())

            rnd = cos[:]
            reduce(red[:], 0.0, tables)
            reduce(turns[:], 0.25, tables)
            o.end_block()

            def body(b):
                i, p = b.i, b.p
                x12 = qk[:, p, :].rearrange("p (h a j) -> p h a j", h=8, a=2)
                cs, sn = (over_heads(t[:, bass.ds(i, 1), :].rearrange("p a j -> p (a j)"), 8) for t in (cos, sin))
                dve.wait_ge(*proj_ready.upto(i, 1))
                dve.wait_ge(*qkT_made.before(i))
                dve.tensor_tensor(rb[:], x12[:, :, 1, :], sn, ALU.mult).then_inc(*o.inc())
                dve.tensor_tensor(rc[:], x12[:, :, 0, :], sn, ALU.mult).then_inc(*o.inc())
                o.settle()
                dve.wait_ge(*rot_part.upto(i))
                dve.tensor_tensor(rot[:, :, 0:32], ra[:], rb[:], ALU.subtract).then_inc(*o.inc())
                dve.tensor_tensor(rot[:, :, 32:64], rc[:], rd[:], ALU.add).then_inc(*rot_ready.inc())
                dve.wait_ge(*gexp_ready.upto(i))
                dve.tensor_scalar_add(gt[:], gt[:], 1.0).then_inc(*o.inc())
                o.settle()
                dve.reciprocal(gt[:], gt[:]).then_inc(*gsig_ready.inc())
                dve.wait_ge(*qkT_made.upto(i))
                for a in (0, 64):
                    dve.tensor_copy(qz[a:a + 64].rearrange("p (g b) t -> p b g t", b=2)[:, a // 64],
                                    qkTp[a:a + 64, 0:256].rearrange("p (g t) -> p g t", g=2)).then_inc(*o.inc())
                dve.tensor_copy(kT[:], qkTp[:, 256:512].rearrange("p (g t) -> p g t", g=2)).then_inc(*qk_ready.inc())
                o.settle()
                dve.tensor_tensor(qw[:], qz[:], winter[:], ALU.mult).then_inc(*o.inc())
                dve.wait_ge(*sc_made.upto(i))
                dve.tensor_tensor(probs[:], scp[:].rearrange("p (h t) -> p h t", h=4), dmat[:], ALU.mult)\
                   .then_inc(*probs_ready.inc())
                dve.wait_ge(*gate_ready.upto(i))
                dve.wait_ge(*pd_made.upto(i))
                dve.tensor_tensor(cat[:, 512:1024], y0[:], gates[:, p, 512:1024], ALU.mult).then_inc(*od_ready.inc())
                dve.wait_ge(*o_made.upto(i))
                for g in range(4):
                    dve.bn_stats(st6[:, g, :], op[:, g * P:(g + 1) * P]).then_inc(*o.inc())
                o.settle()
                for g in range(4):
                    dve.bn_aggr(mv[:, g, :], st6[:, g, :]).then_inc(*(mv_ready if g == 3 else o).inc())
                dve.wait_ge(*U_made.upto(i))
                for g in range(2):
                    dve.scalar_tensor_tensor(S[:, g, :], S[:, g, :], gammac[:, g:g + 1], Up[:, g * P:(g + 1) * P],
                                             ALU.mult, ALU.add).then_inc(*(S_ready if g else o).inc())
                dve.wait_ge(*rs_ready.upto(i))
                for h in range(4):
                    dve.tensor_scalar(cat[:, h * P:(h + 1) * P], op[:, h * P:(h + 1) * P], mv[:, h, 0:1], rs[:, h:h + 1],
                                      ALU.subtract, ALU.mult).then_inc(*o.inc())
                o.settle()
                dve.tensor_tensor(cat[:, 0:512], cat[:, 0:512], gates[:, p, 0:512], ALU.mult).then_inc(*oc_ready.inc())
                dve.wait_ge(*y_made.upto(i))
                for half in range(2):
                    dve.scalar_tensor_tensor(xb[:, p, half * 512:(half + 1) * 512], xb[:, p, half * 512:(half + 1) * 512],
                                             ALPHA, (y0, y1)[half][:], ALU.mult, ALU.add)\
                       .then_inc(*(r_ready if half else o).inc())
                dve.wait_ge(*r_ready.upto(i))
                for half in range(2):
                    dve.bn_stats(lnst[:, half, :], xb[:, p, half * 512:(half + 1) * 512]).then_inc(*o.inc())
                o.settle()
                dve.bn_aggr(lnmv[:], lnst[:].rearrange("p a b -> p (a b)")).then_inc(*lnmv_ready.inc())
                dve.wait_ge(*lnrs_ready.upto(i))
                dve.tensor_scalar(xb[:, p, :], xb[:, p, :], lnmv[:, 0:1], lnrs[:, 0:1], ALU.subtract, ALU.mult)\
                   .then_inc(*lnn_ready.inc())
                o.end_block()

            over_blocks(dve, body)

        @block.gpsimd
        def _(pool):
            o = Order(pool, orders["pool"])
            pool.wait_ge(loaded.sem, NSMALL)
            pool.wait_ge(*setup.upto(0))

            def body(b):
                i, p = b.i, b.p
                x12 = qk[:, p, :].rearrange("p (h a j) -> p h a j", h=8, a=2)
                cs = over_heads(cos[:, bass.ds(i, 1), :].rearrange("p a j -> p (a j)"), 8)
                pool.wait_ge(*proj_ready.upto(i, 1))
                pool.wait_ge(*rot_ready.before(i))
                pool.tensor_tensor(ra[:], x12[:, :, 0, :], cs, ALU.mult).then_inc(*o.inc())
                pool.tensor_tensor(rd[:], x12[:, :, 1, :], cs, ALU.mult).then_inc(*rot_part.inc())
                pool.wait_ge(*rot_ready.upto(i))
                pool.tensor_tensor(kst[:].rearrange("p (h d) -> p h d", h=4), rot[:, 4:8, :], spread(wstate[:], 64), ALU.mult)\
                    .then_inc(*kst_ready.inc())
                pool.wait_ge(*gsig_ready.upto(i))
                pool.tensor_tensor(gates[:, p, :], gates[:, p, :], gt[:], ALU.mult).then_inc(*o.inc())
                o.settle()
                pool.tensor_tensor(gates[:, p, 0:512], gates[:, p, 0:512], ret_row[:], ALU.mult).then_inc(*o.inc())
                pool.tensor_tensor(gates[:, p, 512:1024], gates[:, p, 512:1024], scale_row[:], ALU.mult)\
                    .then_inc(*gate_ready.inc())
                pool.wait_ge(*lnn_ready.upto(i))
                pool.tensor_tensor(xb[:, p, :], xb[:, p, :], ln_grow[:], ALU.mult).then_inc(*o.inc())
                o.settle()
                pool.tensor_tensor(xb[:, p, :], xb[:, p, :], ln_brow[:], ALU.add).then_inc(*out_ready.inc())
                o.end_block()

            over_blocks(pool, body)


LEVELS = (1, 2, 4, 8, 16, 32)
QKV = 1536


def delta_layer(nc, x, c, w_ada, b_ada, g_pre, w_in, conv_w, a_log, dt_bias, g_gdn, g_post, consts, gate_row,
                hT_out, oa_out):
    ident_d, seg_d, big_d, lev_d = consts
    WA = 2056
    wv = w_in.rearrange("(k p) n -> p k n", p=P)
    with ExitStack() as ctx:
        sem = ctx.enter_context(Semaphores(nc, "d_"))

        def sb(name, shape, dt=F32):
            return ctx.enter_context(nc.sbuf_tensor("d_" + name, shape, dt))

        def sig(name, per=1):
            return Signal(sem(name), per)

        W_in = sb("w_in", [P, KT, WA])
        ada = sb("ada", [P, 2, 3 * D])
        ccol = sb("ccol", [P, KT])
        ctmp = sb("ctmp", [P, KT])
        cB = sb("cB", [P, KT, P])
        scale_row = sb("scale_row", [P, D])
        shift_row = sb("shift_row", [P, D])
        xb = sb("xb", [P, 2, D])
        hb = sb("hb", [P, D])
        hT = sb("hT", [P, KT * P])
        xss = sb("xss", [P, 1])
        xrs = sb("xrs", [P, 1])
        eps = sb("eps", [P, 1])
        cv = sb("cv", [P, 2, 12, P + 3])
        convw = sb("convw", [P, 4, 12])
        z = sb("z", [P, 2, 512])
        ba = sb("ba", [P, 2, 8])
        ident = sb("ident", [P, P])
        seg = sb("seg", [P, 4, P])
        big = sb("big", [P, 2, P])
        lev = sb("lev", [P, 6, P])
        eal = sb("eal", [P, 4])
        dtb = sb("dtb", [P, 4])
        gdn_row = sb("gdn_row", [P, P])
        cT = sb("cT", [P, 12, P])
        sg = sb("sg", [P, 12, P])
        ss = sb("ss", [P, 8])
        rs = sb("rs", [P, 8])
        beta = sb("beta", [P, 4])
        ya = sb("ya", [P, 4])
        yb = sb("yb", [P, 4])
        g = sb("g", [P, 4])
        gc = sb("gc", [P, 4])
        ngc = sb("ngc", [P, 4])
        egc = sb("egc", [P, 12])
        bg = sb("bg", [P, 4])
        eG = sb("eG", [P, 4, P])
        gU = sb("gU", [P, 4, P])
        D1 = sb("D1", [P, 4, P])
        D2 = sb("D2", [P, 4, P])
        qn = sb("qn", [P, 4, P])
        kn = sb("kn", [P, 4, P])
        kbg = sb("kbg", [P, 4, P])
        kg = sb("kg", [P, 4, P])
        vb = sb("vb", [P, 4, P])
        qT = sb("qT", [P, 4, P])
        kT = sb("kT", [P, 4, P])
        qgT = qn
        L = sb("L", [P, 4, P])
        Lm = sb("Lm", [P, 4, P])
        Lm2 = sb("Lm2", [P, 4, P])
        T = sb("T", [P, 4, P])
        R = sb("R", [P, 4, P])
        X = sb("X", [P, 4, P])
        attn = sb("attn", [P, 4, P])
        wT = sb("wT", [P, 4, P])
        u = sb("u", [P, 4, P])
        vnew = sb("vnew", [P, 4, P])
        S = sb("S", [P, 4, P])
        sgz = sb("sgz", [P, 512])
        gz = sb("gz", [P, 4, P])
        so = sb("so", [P, 4])
        ro = sb("ro", [P, 4])
        oa = sb("oa", [P, 512])
        ones = sb("ones", [P, P])
        bank = [ctx.enter_context(nc.psum_tensor(f"d_ps{n}", [P, 512], F32)) for n in range(8)]
        by_head = [b[:].rearrange("p (h t) -> p h t", h=4) for b in bank]

        loaded, wloaded, aloaded = sig("loaded"), sig("wloaded"), [sig("ada0"), sig("ada1")]
        c_ready, ada_used, mod_made, mod_ready = sig("c_ready", 3), sig("ada_used"), sig("mod_made"), sig("mod_ready", 3)
        x_in = [sig("x_in0"), sig("x_in1")]
        h_stored, oa_stored, setup = sig("h_stored"), sig("oa_stored"), sig("setup")
        xss_ready, hs_ready, h_ready = sig("xss"), sig("hs"), sig("h_ready")
        hT_made, hT_ready = sig("hT_made", 2), sig("hT_ready", 2)
        proj_made, proj_ready = sig("proj_made", 5), sig("proj_ready", 5)
        halo_ready, conv_ready, csig_ready, act_ready = sig("halo"), sig("conv"), sig("csig"), sig("silu")
        rows_made, sq_ready, ss_ready, rs_ready = sig("rows_made"), sig("sq"), sig("ss"), sig("rs")
        ba_ready, g_ready, gs_made, ge_ready, gU_ready, G_made = (
            sig("ba"), sig("g"), sig("gs_made"), sig("ge"), sig("gU"), sig("G_made"))
        D_ready, dec_ready, eG_ready = sig("D", 2), sig("dec", 2), sig("eG")
        qkn_ready, kg_ready, vb_ready = sig("qkn"), sig("kg"), sig("vb")
        qkT_made, qT_ready, kT_ready, qg_ready = sig("qkT_made"), sig("qT"), sig("kT"), sig("qg")
        kk_made, L_ready, attn_ready = sig("kk_made"), sig("L"), sig("attn")
        T_ready, T_turned, R_ready = sig("T"), sig("T_turned"), sig("R")
        Lm_ready, X_made, X_ready, RX_made, join_ready = sig("Lm", 5), sig("X_made", 5), sig("X", 5), sig("RX_made", 5), sig("join", 5)
        wu_made, wT_ready, u_ready = sig("wu_made"), sig("wT"), sig("u")
        wS_made, vnew_ready, U_made, S_ready = sig("wS_made", 2), sig("vnew", 2), sig("U_made", 2), sig("S", 2)
        o_made, so_ready, ro_ready, gz_ready, oa_ready = sig("o_made"), sig("so"), sig("ro"), sig("gz"), sig("oa")
        zsig_ready, osq_ready, sp_ready = sig("zsig"), sig("osq"), sig("sp")
        orders = {n: sem("order_" + n) for n in ("act", "dve", "pool")}

        block = ctx.enter_context(nc.Block())
        small = [(ccol[:], c.rearrange("(k p) -> p k", p=P)), (ident[:], ident_d), (seg[:], seg_d), (big[:], big_d),
                 (lev[:], lev_d), (eal[:], row(a_log)), (dtb[:], row(dt_bias)), (gdn_row[:], row(g_gdn)),
                 (shift_row[:], row(b_ada[0:D])), (scale_row[:], row(b_ada[D:2 * D])), (gate_row[:], row(b_ada[2 * D:3 * D])),
                 (xb[:, 0, :], row(g_pre)), (xb[:, 1, :], row(g_post))] + [
                 (convw[:, j, :], conv_w[j].rearrange("(k p) -> p k", p=P)) for j in range(4)]
        NSMALL = 16 * len(small)

        @block.sync
        def _(sp):
            with nc.allow_non_contiguous_dma(reason="small tables"):
                for dst, src in small:
                    sp.dma_start(dst, src).then_inc(loaded.sem, 16)
            for k in range(KT):
                if k >= 2:
                    sp.wait_ge(ada_used.sem, k - 1)
                sp.dma_start(ada[:, k % 2, :], w_ada[k * P:(k + 1) * P, :]).then_inc(aloaded[k % 2].sem, 16)
            for k in range(KT):
                sp.dma_start(W_in[:, k, :], wv[:, k, 0:WA]).then_inc(wloaded.sem, 16)
            sp.wait_ge(*mod_ready.upto(0))
            sp.dma_start(xb[:, 0, :], x[0:P, :]).then_inc(x_in[0].sem, 16)
            sp.dma_start(xb[:, 1, :], x[P:2 * P, :]).then_inc(x_in[1].sem, 16)
            sp.wait_ge(*hT_ready.upto(0))
            sp.dma_start(hT_out[0], hT[:]).then_inc(h_stored.sem, 16)
            sp.dma_start(xb[:, 0, :], x[2 * P:3 * P, :]).then_inc(x_in[0].sem, 16)

            def body(b, load=True, last=False):
                if not last:
                    sp.wait_ge(*hT_ready.upto(b.i + 1))
                    sp.dma_start(hT_out[b.i + 1], hT[:]).then_inc(h_stored.sem, 16)
                    if load:
                        sp.dma_start(xb[:, b.q, :], x[bass.ds(b.i * P + 3 * P, P), :]).then_inc(x_in[b.q].sem, 16)
                sp.wait_ge(*oa_ready.upto(b.i))
                sp.dma_start(oa_out[bass.ds(b.i * P, P), :], oa[:]).then_inc(oa_stored.sem, 16)

            with sp.Fori(0, 6) as r:
                body(Blk(r, 0))
                body(Blk(r, 1))
            body(Blk(6, 0))
            body(Blk(6, 1), load=False)
            body(Blk(7, 0), load=False)
            body(Blk(7, 1), load=False, last=True)
            sp.wait_ge(oa_stored.sem, 16 * BLOCKS)
            sp.wait_ge(h_stored.sem, 16 * BLOCKS)

        @block.tensor
        def _(pe):
            pe.wait_ge(*c_ready.upto(0))
            for k in range(KT):
                pe.wait_ge(aloaded[k % 2].sem, 16 * (k // 2) + 16)
                for n in range(6):
                    m = pe.matmul(bank[n][:], cB[:, k, :], ada[:, k % 2, n * 512:(n + 1) * 512], start=(k == 0), stop=(k == KT - 1))
                m.then_inc(*ada_used.inc())

            def turn_h(i):
                pe.wait_ge(*h_ready.upto(i))
                pe.wait_ge(*proj_ready.before(i))
                for half in range(2):
                    for k in range(4):
                        t = 4 * half + k
                        m = pe.transpose(bank[half][:, k * P:(k + 1) * P], hb[:, t * P:(t + 1) * P], ident[:])
                    m.then_inc(*hT_made.inc())

            def project(i, c):
                if c < 2:
                    pe.wait_ge(*hT_ready.upto(i))
                else:
                    pe.wait_ge(*proj_ready.upto(i, c - 1))
                if c < 3:
                    for t in range(4):
                        for k in range(KT):
                            m = pe.matmul(bank[c % 2][:, t * P:(t + 1) * P], W_in[:, k, (4 * c + t) * P:(4 * c + t + 1) * P],
                                          hT[:, k * P:(k + 1) * P], start=(k == 0), stop=(k == KT - 1))
                else:
                    a, n = ((QKV, 512), (2048, 8))[c - 3]
                    for k in range(KT):
                        m = pe.matmul(bank[c % 2][:, 0:n], hT[:, k * P:(k + 1) * P], W_in[:, k, a:a + n],
                                      start=(k == 0), stop=(k == KT - 1))
                m.then_inc(*proj_made.inc())

            pe.wait_ge(*mod_ready.upto(0))
            turn_h(0)
            pe.wait_ge(wloaded.sem, 16 * KT)
            for c_ in range(5):
                project(0, c_)
            pe.wait_ge(*setup.upto(0))

            def body(b):
                i, p = b.i, b.p
                nxt = []
                if not b.last:
                    nxt = [lambda: turn_h(b.i + 1)] + [(lambda c=c: project(b.i + 1, c)) for c in range(5)]

                def fill():
                    if nxt:
                        nxt.pop(0)()

                pe.wait_ge(*oa_ready.before(i))
                pe.wait_ge(*g_ready.upto(i))
                for n in range(4):
                    m = pe.matmul(bank[7][:, 4 * n:4 * n + 4], seg[:, n, :], g[:], start=True, stop=True)
                m.then_inc(*gs_made.inc())
                pe.wait_ge(*gU_ready.upto(i))
                pe.matmul(bank[5][:], ones[:], gU[:].rearrange("p h t -> p (h t)"), start=True, stop=True).then_inc(*G_made.inc())
                fill()
                pe.wait_ge(*act_ready.upto(i))
                for n in range(12):
                    m = pe.transpose(bank[2 + n // 4][:, (n % 4) * P:(n % 4 + 1) * P], cT[:, n, :], ident[:])
                m.then_inc(*rows_made.inc())
                fill()
                pe.wait_ge(*qkn_ready.upto(i))
                for n in range(8):
                    m = pe.transpose(bank[2 + n // 4][:, (n % 4) * P:(n % 4 + 1) * P], (qn, kn)[n // 4][:, n % 4, :], ident[:])
                m.then_inc(*qkT_made.inc())
                pe.wait_ge(*kT_ready.upto(i))
                pe.wait_ge(*vb_ready.upto(i))
                for h in range(4):
                    pe.matmul(bank[4][:, h * P:(h + 1) * P], kT[:, h, :], kT[:, h, :], start=True, stop=True)
                pe.wait_ge(*qT_ready.upto(i))
                for h in range(4):
                    m = pe.matmul(bank[6][:, h * P:(h + 1) * P], kT[:, h, :], qT[:, h, :], start=True, stop=True)
                m.then_inc(*kk_made.inc())
                fill()
                pe.wait_ge(*T_ready.upto(i))
                for h in range(4):
                    m = pe.transpose(bank[5][:, h * P:(h + 1) * P], T[:, h, :], ident[:])
                m.then_inc(*T_turned.inc())
                pe.wait_ge(*R_ready.upto(i))
                for s in range(5):
                    pe.wait_ge(*Lm_ready.upto(i, s + 1))
                    if s:
                        pe.wait_ge(*join_ready.upto(i, s))
                    for h in range(4):
                        m = pe.matmul(bank[2][:, h * P:(h + 1) * P], (Lm, Lm2)[s % 2][:, h, :], R[:, h, :], start=True, stop=True)
                    m.then_inc(*X_made.inc())
                    if s in (1, 3):
                        fill()
                    pe.wait_ge(*X_ready.upto(i, s + 1))
                    for h in range(4):
                        m = pe.matmul(bank[3][:, h * P:(h + 1) * P], T[:, h, :], X[:, h, :], start=True, stop=True)
                    if s < 4:
                        for h in range(4):
                            m = pe.matmul(bank[5][:, h * P:(h + 1) * P], X[:, h, :], T[:, h, :], start=True, stop=True)
                    m.then_inc(*RX_made.inc())
                pe.wait_ge(*join_ready.upto(i))
                pe.wait_ge(*kg_ready.upto(i))
                pe.wait_ge(*attn_ready.upto(i))
                for h in range(4):
                    pe.matmul(bank[4][:, h * P:(h + 1) * P], kbg[:, h, :], R[:, h, :], start=True, stop=True)
                for h in range(4):
                    m = pe.matmul(bank[6][:, h * P:(h + 1) * P], R[:, h, :], vb[:, h, :], start=True, stop=True)
                m.then_inc(*wu_made.inc())
                fill()
                pe.wait_ge(*wT_ready.upto(i))
                pe.wait_ge(*qg_ready.upto(i))
                for n in range(2):
                    a = 64 * n
                    if n:
                        pe.wait_ge(*S_ready.upto(i, 1))
                    for h in range(4):
                        m = pe.matmul(bank[2][a:a + 64, h * P:(h + 1) * P], wT[:, h, a:a + 64], S[:, h, :], start=True, stop=True)
                    m.then_inc(*wS_made.inc())
                    for h in range(4):
                        pe.matmul(bank[7][a:a + 64, h * P:(h + 1) * P], qgT[:, h, a:a + 64], S[:, h, :],
                                  start=(h == 0), stop=False, skip_group_check=True)
                    pe.wait_ge(*vnew_ready.upto(i, n + 1))
                    for h in range(4):
                        m = pe.matmul(bank[3][:, h * P:(h + 1) * P], kg[a:a + 64, h, :], vnew[a:a + 64, h, :], start=True, stop=True)
                    m.then_inc(*U_made.inc())
                for h in range(4):
                    m = pe.matmul(bank[7][:, h * P:(h + 1) * P], attn[:, h, :], vnew[:, h, :], start=False, stop=True,
                                  skip_group_check=True)
                m.then_inc(*o_made.inc())
                while nxt:
                    fill()

            over_blocks(pe, body)

        @block.scalar
        def _(act):
            o = Order(act, orders["act"])
            act.preload_act_table_set(TABLES)

            def sigmoid(dst, src, done):
                act.activation(dst, src, ACT.Exp, scale=-1.0).then_inc(*o.inc())
                o.settle()
                act.activation(dst, dst, ACT.Ln, bias=1.0).then_inc(*o.inc())
                o.settle()
                act.activation(dst, dst, ACT.Exp, scale=-1.0).then_inc(*done.inc())

            act.wait_ge(loaded.sem, NSMALL)
            act.activation(eal[:], eal[:], ACT.Exp).then_inc(*o.inc())
            sigmoid(ctmp[:], ccol[:], c_ready)
            o.settle()

            def norm_x(p):
                act.activation(hb[:], xb[:, p, :], ACT.Square, accum_out=xss[:]).then_inc(*o.inc())
                o.settle()
                act.activation(xrs[:], xss[:], ACT.Ln, bias=eps[:, 0:1], scale=1.0 / D).then_inc(*o.inc())
                o.settle()
                act.activation(xrs[:], xrs[:], ACT.Exp, scale=-0.5).then_inc(*xss_ready.inc())

            def turn_h(i):
                act.wait_ge(h_stored.sem, 16 * i)
                for half in range(2):
                    act.wait_ge(*hT_made.upto(i, half + 1))
                    act.activation(hT[:, half * 512:(half + 1) * 512], bank[half][:], ACT.Copy).then_inc(*hT_ready.inc())

            def project(i, p, c):
                act.wait_ge(*proj_made.upto(i, c + 1))
                if c < 3:
                    act.activation(cv[:, p, 4 * c:4 * c + 4, 3:P + 3], by_head[c % 2], ACT.Copy).then_inc(*proj_ready.inc())
                elif c == 3:
                    act.activation(z[:, p, :], bank[1][:], ACT.Copy).then_inc(*proj_ready.inc())
                else:
                    act.activation(ba[:, p, :], bank[0][:, 0:8], ACT.Copy).then_inc(*proj_ready.inc())

            act.wait_ge(*setup.upto(0))
            act.wait_ge(x_in[0].sem, 16)
            norm_x(0)
            turn_h(0)
            for c_ in range(5):
                project(0, 0, c_)
            o.end_block()

            def body(b):
                i, p = b.i, b.p
                nxt = []
                if not b.last:
                    nxt = [lambda: turn_h(b.i + 1)] + [(lambda c=c: project(b.i + 1, b.q, c)) for c in range(5)]

                def fill():
                    if nxt:
                        nxt.pop(0)()

                act.wait_ge(*oa_ready.before(i))
                act.wait_ge(*proj_ready.upto(i))
                act.wait_ge(*ba_ready.upto(i))
                act.activation(beta[:], ba[:, p, 0:4], ACT.Exp, scale=-1.0).then_inc(*o.inc())
                act.activation(yb[:], ya[:], ACT.Abs).then_inc(*o.inc())
                o.settle()
                act.activation(beta[:], beta[:], ACT.Ln, bias=1.0).then_inc(*o.inc())
                act.activation(yb[:], yb[:], ACT.Exp, scale=-1.0).then_inc(*o.inc())
                o.settle()
                act.activation(beta[:], beta[:], ACT.Exp, scale=-1.0).then_inc(*o.inc())
                act.activation(yb[:], yb[:], ACT.Ln, bias=1.0).then_inc(*sp_ready.inc())
                if not b.last:
                    act.wait_ge(x_in[b.q].sem, 16 * (b.r + p) + 16)
                    norm_x(b.q)
                act.wait_ge(*gs_made.upto(i))
                act.activation(gc[:], bank[7][:, 0:4], ACT.Copy).then_inc(*o.inc())
                act.activation(ngc[:], bank[7][:, 0:4], ACT.Copy, scale=-1.0).then_inc(*o.inc())
                act.activation(bg[:], bank[7][:, 0:4], ACT.Exp).then_inc(*o.inc())
                act.activation(egc[:], bank[7][:, 4:16], ACT.Exp).then_inc(*ge_ready.inc())
                act.wait_ge(*G_made.upto(i))
                act.activation(eG[:], by_head[5], ACT.Exp).then_inc(*eG_ready.inc())
                fill()
                act.wait_ge(*conv_ready.upto(i))
                sigmoid(sg[:], cT[:], csig_ready)
                act.wait_ge(*rows_made.upto(i))
                for n in range(2):
                    act.activation(sg[:, 4 * n:4 * n + 4, :], by_head[2 + n], ACT.Square)\
                        .then_inc(*(sq_ready if n else o).inc())
                act.wait_ge(*ss_ready.upto(i))
                act.activation(rs[:], ss[:], ACT.Ln, bias=eps[:, 0:1]).then_inc(*o.inc())
                o.settle()
                act.activation(rs[:], rs[:], ACT.Exp, scale=-0.5).then_inc(*rs_ready.inc())
                fill()
                act.wait_ge(*D_ready.upto(i))
                for h in range(4):
                    act.activation(D1[:, h, :], D1[:, h, :], ACT.Exp, scale=-1.0, bias=gc[:, h:h + 1])\
                        .then_inc(*(dec_ready if h == 3 else o).inc())
                for h in range(4):
                    act.activation(D2[:, h, :], D2[:, h, :], ACT.Exp, bias=ngc[:, h:h + 1])\
                        .then_inc(*(dec_ready if h == 3 else o).inc())
                act.wait_ge(*qkT_made.upto(i))
                act.activation(qT[:], by_head[2], ACT.Copy).then_inc(*qT_ready.inc())
                fill()
                act.wait_ge(*T_turned.upto(i))
                act.activation(R[:], by_head[5], ACT.Copy).then_inc(*R_ready.inc())
                for s in range(5):
                    act.wait_ge(*X_made.upto(i, s + 1))
                    act.activation(X[:], by_head[2], ACT.Copy).then_inc(*X_ready.inc())
                    if s in (1, 3):
                        fill()
                act.wait_ge(*wu_made.upto(i))
                act.activation(wT[:], by_head[4], ACT.Copy).then_inc(*wT_ready.inc())
                act.activation(u[:], by_head[6], ACT.Copy).then_inc(*u_ready.inc())
                sigmoid(sgz[:], z[:, p, :], zsig_ready)
                fill()
                act.wait_ge(*o_made.upto(i))
                act.activation(sg[:, 0:4, :], by_head[7], ACT.Square).then_inc(*osq_ready.inc())
                act.wait_ge(*so_ready.upto(i))
                act.activation(ro[:], so[:], ACT.Ln, bias=eps[:, 0:1], scale=1.0 / P).then_inc(*o.inc())
                o.settle()
                act.activation(ro[:], ro[:], ACT.Exp, scale=-0.5).then_inc(*ro_ready.inc())
                while nxt:
                    fill()
                o.end_block()

            over_blocks(act, body)

        @block.vector
        def _(dve):
            o = Order(dve, orders["dve"])
            dve.memset(S[:], 0.0).then_inc(*o.inc())
            dve.memset(eps[:], RMS_EPS).then_inc(*o.inc())
            dve.memset(ones[:], 1.0).then_inc(*o.inc())
            dve.memset(cv[:, 0, :, 0:3], 0.0).then_inc(*o.inc())
            o.settle()
            dve.wait_ge(*c_ready.upto(0, 1))
            dve.wait_ge(loaded.sem, NSMALL)
            dve.tensor_tensor(ctmp[:], ctmp[:], ccol[:], ALU.mult).then_inc(*c_ready.inc())
            dve.wait_ge(*c_ready.upto(0, 2))
            dve.tensor_copy(cB[:], spread(ctmp[:], P)).then_inc(*c_ready.inc())
            dve.wait_ge(ada_used.sem, KT)
            for n in range(6):
                dst = ((shift_row, scale_row, gate_row)[n // 2])[:, (n % 2) * 512:(n % 2 + 1) * 512]
                dve.tensor_tensor(dst, dst, bank[n][:], ALU.add).then_inc(*(mod_ready if n == 5 else o).inc())
            dve.wait_ge(*mod_ready.upto(0, 1))
            dve.scalar_tensor_tensor(scale_row[:], scale_row[:], 1.0, xb[:, 0, :], ALU.add, ALU.mult).then_inc(*mod_ready.inc())
            dve.tensor_tensor(gate_row[:], gate_row[:], xb[:, 1, :], ALU.mult).then_inc(*mod_ready.inc())
            dve.wait_ge(*mod_ready.upto(0))
            dve.tensor_scalar_mul(eal[:], eal[:], -1.0).then_inc(*setup.inc())

            def make_h(i, p):
                dve.wait_ge(*hT_made.before(i))
                dve.wait_ge(*xss_ready.upto(i))
                dve.scalar_tensor_tensor(hb[:], xb[:, p, :], xrs[:, 0:1], scale_row[:], ALU.mult, ALU.mult)\
                   .then_inc(*hs_ready.inc())

            make_h(0, 0)
            o.end_block()

            def body(b):
                i, p = b.i, b.p
                dve.wait_ge(*proj_ready.upto(i))
                dve.tensor_tensor(ya[:], ba[:, p, 4:8], dtb[:], ALU.add).then_inc(*ba_ready.inc())
                if not b.last:
                    dve.tensor_copy(cv[:, b.q, :, 0:3], cv[:, p, :, P:P + 3]).then_inc(*o.inc())
                for t in range(12):
                    dve.tensor_scalar(cT[:, t, :], cv[:, p, t, 0:P], convw[:, 0, t:t + 1], None, ALU.mult).then_inc(*o.inc())
                for j in range(1, 4):
                    o.settle()
                    for t in range(12):
                        dve.scalar_tensor_tensor(cT[:, t, :], cv[:, p, t, j:j + P], convw[:, j, t:t + 1], cT[:, t, :],
                                                 ALU.mult, ALU.add).then_inc(*(conv_ready if j == 3 and t == 11 else o).inc())
                dve.wait_ge(*sp_ready.upto(i))
                dve.scalar_tensor_tensor(g[:], ya[:], 0.0, yb[:], ALU.max, ALU.add).then_inc(*o.inc())
                o.settle()
                dve.tensor_tensor(g[:], g[:], eal[:], ALU.mult).then_inc(*g_ready.inc())
                if not b.last:
                    make_h(b.i + 1, b.q)
                dve.wait_ge(*ge_ready.upto(i))
                dve.tensor_tensor(bg[:], bg[:], beta[:], ALU.mult).then_inc(*o.inc())
                dve.wait_ge(*eG_ready.upto(i))
                dve.tensor_tensor(D1[:], by_head[5], over_heads(big[:, 0, :], 4), ALU.add).then_inc(*D_ready.inc())
                dve.tensor_tensor(D2[:], by_head[5], over_heads(big[:, 1, :], 4), ALU.subtract).then_inc(*D_ready.inc())
                dve.wait_ge(*csig_ready.upto(i))
                dve.tensor_tensor(cT[:], cT[:], sg[:], ALU.mult).then_inc(*act_ready.inc())
                dve.wait_ge(*sq_ready.upto(i))
                dve.tensor_reduce(ss[:], sg[:, 0:8, :], AX.X, ALU.add).then_inc(*ss_ready.inc())
                dve.tensor_tensor(vb[:], by_head[4], spread(beta[:], P), ALU.mult).then_inc(*vb_ready.inc())
                dve.wait_ge(*rs_ready.upto(i))
                dve.tensor_scalar_mul(rs[:, 0:4], rs[:, 0:4], float(P) ** -0.5).then_inc(*o.inc())
                dve.tensor_tensor(kn[:], by_head[3], spread(rs[:, 4:8], P), ALU.mult).then_inc(*o.inc())
                o.settle()
                dve.tensor_tensor(qn[:], by_head[2], spread(rs[:, 0:4], P), ALU.mult).then_inc(*qkn_ready.inc())
                dve.wait_ge(*qkT_made.upto(i))
                dve.tensor_copy(kT[:], by_head[3]).then_inc(*kT_ready.inc())
                dve.wait_ge(*dec_ready.upto(i))
                dve.wait_ge(*kk_made.upto(i))
                for h in range(4):
                    dve.scalar_tensor_tensor(L[:, h, :], by_head[4][:, h, :], beta[:, h:h + 1], D1[:, h, :],
                                             ALU.mult, ALU.mult).then_inc(*(L_ready if h == 3 else o).inc())
                dve.wait_ge(*L_ready.upto(i))
                dve.tensor_tensor(T[:], L[:], over_heads(lev[:, 0, :], 4), ALU.mult).then_inc(*o.inc())
                o.settle()
                dve.tensor_tensor(T[:], over_heads(ident[:], 4), T[:], ALU.subtract).then_inc(*T_ready.inc())
                dve.tensor_tensor(attn[:], by_head[6], D2[:], ALU.mult).then_inc(*attn_ready.inc())
                dve.wait_ge(*R_ready.upto(i))
                for s in range(5):
                    dve.wait_ge(*RX_made.upto(i, s + 1))
                    if s < 4:
                        dve.tensor_tensor(T[:], T[:], by_head[5], ALU.subtract).then_inc(*o.inc())
                    dve.tensor_tensor(R[:], R[:], by_head[3], ALU.subtract).then_inc(*join_ready.inc())
                    dve.wait_ge(*join_ready.upto(i, s + 1))
                dve.wait_ge(*u_ready.upto(i))
                for n in range(2):
                    a = 64 * n
                    dve.wait_ge(*wS_made.upto(i, n + 1))
                    dve.tensor_tensor(vnew[a:a + 64], u[a:a + 64], by_head[2][a:a + 64], ALU.subtract).then_inc(*vnew_ready.inc())
                    dve.wait_ge(*U_made.upto(i, n + 1))
                    for h in range(4):
                        dve.scalar_tensor_tensor(S[:, h, :], S[:, h, :], egc[:, 4 + 4 * n + h:5 + 4 * n + h],
                                                 by_head[3][:, h, :], ALU.mult, ALU.add)\
                           .then_inc(*(S_ready if h == 3 else o).inc())
                    dve.wait_ge(*S_ready.upto(i, n + 1))
                dve.wait_ge(*osq_ready.upto(i))
                dve.tensor_reduce(so[:], sg[:, 0:4, :], AX.X, ALU.add).then_inc(*so_ready.inc())
                dve.wait_ge(*ro_ready.upto(i))
                dve.wait_ge(*gz_ready.upto(i))
                dve.wait_ge(oa_stored.sem, 16 * i)
                for h in range(4):
                    dve.scalar_tensor_tensor(oa[:, h * P:(h + 1) * P], by_head[7][:, h, :], ro[:, h:h + 1], gz[:, h, :],
                                             ALU.mult, ALU.mult).then_inc(*(oa_ready if h == 3 else o).inc())
                o.end_block()

            over_blocks(dve, body)

        @block.gpsimd
        def _(pool):
            o = Order(pool, orders["pool"])
            pool.wait_ge(loaded.sem, NSMALL)
            pool.wait_ge(*mod_ready.upto(0))

            def shift_h(i):
                pool.wait_ge(*hs_ready.upto(i))
                pool.tensor_tensor(hb[:], hb[:], shift_row[:], ALU.add).then_inc(*h_ready.inc())

            shift_h(0)

            def body(b):
                i, p = b.i, b.p
                pool.wait_ge(*oa_ready.before(i))
                pool.wait_ge(*g_ready.upto(i))
                pool.tensor_tensor(gU[:], over_heads(seg[:, 0, :], 4), spread(g[:], P), ALU.mult).then_inc(*gU_ready.inc())
                if not b.last:
                    shift_h(b.i + 1)
                pool.wait_ge(*qkn_ready.upto(i))
                pool.tensor_tensor(kbg[:], kn[:], spread(bg[:], P), ALU.mult).then_inc(*o.inc())
                pool.tensor_tensor(kg[:], kn[:], spread(egc[:, 0:4], P), ALU.mult).then_inc(*kg_ready.inc())
                pool.wait_ge(*L_ready.upto(i))
                for s in range(5):
                    if s >= 2:
                        pool.wait_ge(*X_made.upto(i, s - 1))
                    pool.tensor_tensor((Lm, Lm2)[s % 2][:], L[:], over_heads(lev[:, s + 1, :], 4), ALU.mult)\
                        .then_inc(*Lm_ready.inc())
                    if s == 1:
                        pool.wait_ge(*qT_ready.upto(i))
                        pool.wait_ge(*eG_ready.upto(i))
                        pool.tensor_tensor(qgT[:], qT[:], eG[:], ALU.mult).then_inc(*qg_ready.inc())
                pool.wait_ge(*zsig_ready.upto(i))
                pool.tensor_tensor(sgz[:], sgz[:], z[:, p, :], ALU.mult).then_inc(*o.inc())
                o.settle()
                pool.tensor_tensor(gz[:], sgz[:].rearrange("p (h t) -> p h t", h=4), over_heads(gdn_row[:], 4), ALU.mult)\
                    .then_inc(*gz_ready.inc())
                o.end_block()

            over_blocks(pool, body)


IDX_HEADS, IDX_DIM = 8, 64
TOPK = 256
N_BUCKETS = 32
WIDE = 4
ROUNDS = 12
FAR = 1e30


class Stepped(Signal):

    def base(self, b):
        return 2 * b.G * (b.G + 1) * self.per + (b.i - WIDE * b.G) * (b.G + 1) * self.per

    def upto(self, b, k=None):
        return self.sem, self.base(b) + (self.per * (b.G + 1) if k is None else k)


def sparse_layer(nc, x, w_in, g_kv, w_uv, rel_bias, w_out, consts, gate_row, hT_in, oa_in, bias_scratch, out):
    ident_d, flip_d, late_d, onehot_d, iota_d, halves_d = consts
    C0 = 2056
    O_QB, O_CKV, O_Z, O_IQ, O_IK, O_IW = 0, 512, 640, 1152, 1664, 1792
    WB = 1800
    wv = w_in.rearrange("(k p) n -> p k n", p=P)
    with ExitStack() as ctx:
        def sb(name, shape, dt=F32):
            return ctx.enter_context(nc.sbuf_tensor("s_" + name, shape, dt))

        sem = ctx.enter_context(Semaphores(nc, "s_"))

        def sig(name, per=1):
            return Signal(sem(name), per)

        W_in = sb("w_in", [P, KT, WB])
        W_out = sb("w_out", [P, KT, D])
        ikT = sb("ikT", [P, SEQ])
        ckvT = sb("ckvT", [P, SEQ])
        ckvr = sb("ckvr", [P, BLOCKS, P])
        hT = sb("hT", [P, KT * P])
        pT = sb("pT", [P, 2, BLOCKS, P])
        Lg = sb("Lg", [P, 2, P + SEQ])
        acc = sb("acc", [P, SEQ])
        selb = sb("selb", [P, SEQ])
        cat = sb("cat", [P, D])
        catT = pT[:, 0].rearrange("p b t -> p (b t)")[:, 0:D]
        sgz = pT[:, 1].rearrange("p b t -> p (b t)")[:, 0:512]
        xb = sb("xb", [P, D])
        squares = [pT[:, 1].rearrange("p b t -> p (b t)")[:, n * 512:(n + 1) * 512] for n in range(2)]
        iqT = sb("iqT", [P, 2, 4, P])
        qbT = sb("qbT", [P, 2, 4, P])
        z = sb("z", [P, 2, 512])
        kvw = sb("kvw", [P, 2, P + IDX_HEADS])
        ident = sb("ident", [P, P])
        flip = sb("flip", [P, P])
        late = sb("late", [P, 896])
        onehot = sb("onehot", [N_BUCKETS, 384])
        rb = sb("rb", [N_BUCKETS, 4])
        rb31 = sb("rb31", [N_BUCKETS, 4])
        bias = sb("bias", [P, 4, 2 * P])
        vec = sb("vec", [4, 384])
        iota = sb("iota", [P, 8])
        halves = sb("halves", [P, ROUNDS + 1])
        kv_row = sb("kv_row", [P, P])
        uv = sb("uv", [P, 4, P])
        ones = sb("ones", [P, 1])
        eps = sb("eps", [P, 1])
        css = sb("css", [P, 1])
        crs = sb("crs", [P, 1])
        cn = sb("cn", [P, P])
        lo = sb("lo", [P, 1])
        hi = sb("hi", [P, 1])
        mid = sb("mid", [P, 1])
        cnt = sb("cnt", [P, 1])
        step = sb("step", [P, 1])
        steps = sb("steps", [P, ROUNDS + 1])
        best = sb("best", [P, 8])
        thr = sb("thr", [P, 1])
        bad = sb("bad", [P, 1])
        nbad = sb("nbad", [1, 1], I32)
        mx = sb("mx", [P, 4])
        psum_ = sb("psums", [P, 4])
        prec = sb("prec", [P, 4])
        oT = sb("oT", [P, 4, P])
        mss = sb("mss", [P, 2])
        mrs = sb("mrs", [P, 1])
        junk = cn
        relu = Lg[:, 1, 0:2048].rearrange("p (n c) -> p n c", n=4)
        work, other = Lg[:, 0, :], Lg[:, 1, :]
        bank = [ctx.enter_context(nc.psum_tensor(f"s_ps{n}", [P, 512], F32)) for n in range(8)]
        by_head = [b[:].rearrange("p (h t) -> p h t", h=4) for b in bank]

        loaded, loaded2, wloaded = sig("loaded"), sig("loaded2"), sig("wloaded")
        h_in, x_in, oa_in_s, stored = sig("h_in"), sig("x_in"), sig("oa_in"), sig("stored")
        zeroed, rb_ready, vec_made, vec_ready, vec_stored, bias_made, bias_ready = (
            sig("zeroed", 4), sig("rb"), sig("vec_made"), sig("vec"), sig("vec_stored"), sig("bias_made", 2), sig("bias", 2))
        proj_made, proj_ready = sig("proj_made", 4), sig("proj_ready", 4)
        crs_ready, cn_ready, ckvr_ready, cT_made, cT_ready = sig("crs"), sig("cn"), sig("ckvr"), sig("cT_made"), sig("cT")
        idx_made, relu_ready, relu_used = (Stepped(sem(n), 8) for n in ("idx_made", "relu", "relu_used"))
        bad_ready, nbad_made, nbad_ready, selb_ready = sig("bad"), sig("nbad_made"), sig("nbad"), sig("selb")
        lg_made, lg_read, pt_made, pt_ready = (Stepped(sem(n), 4) for n in ("lg_made", "lg_read", "pt_made", "pt"))
        mx_ready, exp_ready, pv_made = sig("mx", 4), sig("exp", 4), sig("pv_made", 4)
        zsig_ready, gz_ready, oT_ready, uv_made, ob_ready = sig("zsig"), sig("gz"), sig("oT"), sig("uv_made"), sig("ob")
        catT_made, catT_ready, y_made, mss_ready, mrs_ready, mix_ready, out_ready = (
            sig("catT_made", 2), sig("catT", 2), sig("y_made"), sig("mss"), sig("mrs"), sig("mix"), sig("out_ready"))
        branch = sem("branch")
        orders = {n: sem("order_" + n) for n in ("act", "dve", "pool")}

        def block_at(r, p, G):
            b = Blk(r, p, last=isinstance(r, int) and 2 * r + p == BLOCKS - 1)
            b.G, b.W, b.topk = G, 512 * (G + 1), not (isinstance(r, int) and (2 * r + p + 1) * P <= TOPK)
            return b

        def over_sections(eng, body):
            for r in range(2):
                for p in range(2):
                    body(block_at(r, p, 0))
            for G in (1, 2):
                with eng.Fori(2 * G, 2 * G + 2) as r:
                    body(block_at(r, 0, G))
                    body(block_at(r, 1, G))
            for r in (6, 7):
                for p in range(2):
                    body(block_at(r, p, 3))

        block = ctx.enter_context(nc.Block())
        small = [(ident[:], ident_d), (flip[:], flip_d), (late[:], late_d), (onehot[:], onehot_d), (iota[:], iota_d),
                 (halves[:], halves_d), (kv_row[:], row(g_kv)), (uv[:], w_uv.rearrange("h r d -> r h d")),
                 (rb[:], rel_bias), (rb31[:], row(rel_bias[N_BUCKETS - 1], N_BUCKETS))]
        NSMALL = 16 * len(small)

        @block.sync
        def _(sp):
            with nc.allow_non_contiguous_dma(reason="small tables"):
                for dst, src in small:
                    sp.dma_start(dst, src).then_inc(loaded.sem, 16)
                sp.dma_start(hT[:], hT_in[0]).then_inc(h_in.sem, 16)
                for k in range(KT):
                    sp.dma_start(W_in[:, k, 0:O_IK + 64], wv[:, k, C0:C0 + O_IK + 64]).then_inc(wloaded.sem, 16)
                    sp.dma_start(W_in[:, k, O_IK + 64:O_IW + 8], wv[:, k, C0 + O_IK:C0 + O_IK + 72]).then_inc(wloaded.sem, 16)
                sp.wait_ge(*vec_ready.upto(0))
                sp.dma_start(bias_scratch, vec[:]).then_inc(vec_stored.sem, 16)
                sp.wait_ge(vec_stored.sem, 16)
                for h in range(4):
                    src = bias_scratch[h]
                    src = bass.AP(src.tensor, src.offset, [[1, P], [1, 2 * P]])
                    sp.dma_start(acc[:, h * 2 * P:(h + 1) * 2 * P], src).then_inc(loaded2.sem, 16)
            sp.dma_start(W_out[:], w_out.rearrange("(k p) n -> p k n", p=P)).then_inc(wloaded.sem, 16)

            def body(b):
                if not b.last:
                    sp.wait_ge(*proj_ready.upto(b.i))
                    sp.dma_start(hT[:], hT_in[bass.ds(b.i + 1, 1)].rearrange("a p n -> (a p) n")).then_inc(h_in.sem, 16)
                sp.wait_ge(stored.sem, 16 * b.i)
                sp.dma_start(xb[:], x[bass.ds(b.i * P, P), :]).then_inc(x_in.sem, 16)
                sp.dma_start(cat[:, 0:512], oa_in[bass.ds(b.i * P, P), :]).then_inc(oa_in_s.sem, 16)
                sp.wait_ge(*out_ready.upto(b.i))
                sp.dma_start(out[bass.ds(b.i * P, P), :], xb[:]).then_inc(stored.sem, 16)

            over_sections(sp, body)
            sp.wait_ge(stored.sem, 16 * BLOCKS)

        @block.tensor
        def _(pe):
            def tile_of(c, t):
                a = (O_IQ, O_IK, O_QB)[c] + t * P
                return slice(a, a + P)

            def project(i, c):
                if c == 0:
                    pe.wait_ge(h_in.sem, 16 * i + 16)
                if c < 2:
                    pe.wait_ge(*proj_ready.before(i))
                else:
                    pe.wait_ge(*proj_ready.upto(i, c - 1))
                out_ = bank[c % 2]
                if c < 3:
                    for t in range((4, 1, 4)[c]):
                        for k in range(KT):
                            m = pe.matmul(out_[:, t * P:(t + 1) * P], W_in[:, k, tile_of(c, t)], hT[:, k * P:(k + 1) * P],
                                          start=(k == 0), stop=(k == KT - 1))
                for a, n, at in {1: [(O_CKV, P, P), (O_IW, 8, 2 * P)], 3: [(O_Z, 512, 0)]}.get(c, []):
                    for k in range(KT):
                        m = pe.matmul(out_[:, at:at + n], hT[:, k * P:(k + 1) * P], W_in[:, k, a:a + n],
                                      start=(k == 0), stop=(k == KT - 1))
                m.then_inc(*proj_made.inc())

            pe.wait_ge(loaded.sem, NSMALL)
            pe.wait_ge(*rb_ready.upto(0))
            pe.matmul(bank[2][0:4, 0:384], rb[:], onehot[:], start=True, stop=True).then_inc(*vec_made.inc())
            pe.wait_ge(loaded2.sem, 64)
            for n in range(2):
                pe.matmul(bank[3 + n][:], flip[:], acc[:, n * 512:(n + 1) * 512], start=True, stop=True).then_inc(*bias_made.inc())
            pe.wait_ge(wloaded.sem, 16 * (2 * KT + 1))
            for c in range(4):
                project(0, c)
            pe.wait_ge(*zeroed.upto(0))
            pe.wait_ge(*bias_ready.upto(0))

            def body(b):
                i, p, nk = b.i, b.p, b.G + 1
                nxt = [] if b.last else [(lambda c=c: project(b.i + 1, c)) for c in range(4)]

                def fill():
                    if nxt:
                        nxt.pop(0)()

                pe.wait_ge(*mix_ready.before(i))
                pe.wait_ge(*cn_ready.upto(i))
                pe.transpose(bank[6][:, 0:P], cn[:], ident[:]).then_inc(*cT_made.inc())
                pe.wait_ge(*proj_ready.upto(i))
                if b.topk:
                    for n in range(8 * nk):
                        kc, h = n // 8, n % 8
                        a = 64 * (h % 2)
                        if n >= 4:
                            pe.wait_ge(*relu_ready.upto(b, n - 3))
                        pe.matmul(bank[2 + n % 4][:], iqT[a:a + 64, p, h // 2, :], ikT[a:a + 64, kc * 512:(kc + 1) * 512],
                                  start=True, stop=True).then_inc(*idx_made.inc())
                else:
                    pe.matmul(bank[2][0:1, 0:1], ones[:], ones[:], start=True, stop=True).then_inc(idx_made.sem, 8 * nk)
                while nxt:
                    fill()
                pe.wait_ge(*bad_ready.upto(i))
                pe.matmul(bank[7][0:1, 0:1], bad[:], ones[:], start=True, stop=True).then_inc(*nbad_made.inc())
                pe.wait_ge(*selb_ready.upto(i))
                pe.wait_ge(*cT_ready.upto(i))
                pe.wait_ge(*ckvr_ready.upto(i))

                def logits(h):
                    for kc in range(nk):
                        n = h * nk + kc
                        if n >= 3:
                            pe.wait_ge(*lg_read.upto(b, n - 2))
                        pe.matmul(bank[2 + n % 3][:], qbT[:, p, h, :], ckvT[:, kc * 512:(kc + 1) * 512],
                                  start=True, stop=True).then_inc(*lg_made.inc())

                logits(0)
                for h in range(4):
                    if h < 3:
                        logits(h + 1)
                    pe.wait_ge(*exp_ready.upto(i, h + 1))
                    for kc in range(nk):
                        n = h * nk + kc
                        if n >= 2:
                            pe.wait_ge(*pt_ready.upto(b, n - 1))
                        for t in range(4):
                            s = P + (4 * kc + t) * P
                            m = pe.transpose(bank[6 + n % 2][:, t * P:(t + 1) * P], Lg[:, h % 2, s:s + P], ident[:])
                        m.then_inc(*pt_made.inc())
                    pe.wait_ge(*pt_ready.upto(b, (h + 1) * nk))
                    for t in range(4 * nk):
                        m = pe.matmul(bank[5][:, h * P:(h + 1) * P], ckvr[:, t, :], pT[:, h % 2, t, :],
                                      start=(t == 0), stop=(t == 4 * nk - 1))
                    m.then_inc(*pv_made.inc())
                pe.wait_ge(*oT_ready.upto(i))
                for h in range(4):
                    m = pe.matmul(bank[6][:, h * P:(h + 1) * P], oT[:, h, :], uv[:, h, :], start=True, stop=True)
                m.then_inc(*uv_made.inc())
                pe.wait_ge(oa_in_s.sem, 16 * i + 16)
                for half in range(2):
                    if half:
                        pe.wait_ge(*ob_ready.upto(i))
                    for k in range(4):
                        t = 4 * half + k
                        m = pe.transpose((bank[7], bank[2])[half][:, k * P:(k + 1) * P], cat[:, t * P:(t + 1) * P], ident[:])
                    m.then_inc(*catT_made.inc())
                pe.wait_ge(*catT_ready.upto(i))
                for half in range(2):
                    for k in range(KT):
                        m = pe.matmul(bank[3 + half][:], catT[:, k * P:(k + 1) * P],
                                      W_out[:, k, half * 512:(half + 1) * 512], start=(k == 0), stop=(k == KT - 1))
                m.then_inc(*y_made.inc())

            over_sections(pe, body)

        @block.scalar
        def _(act):
            o = Order(act, orders["act"])
            act.preload_act_table_set(TABLES)

            def project(i, p, c):
                act.wait_ge(*proj_made.upto(i, c + 1))
                if c == 0:
                    act.activation(iqT[:, p], by_head[0], ACT.Copy).then_inc(*proj_ready.inc())
                elif c == 1:
                    act.activation(ikT[:, bass.ds(i * P, P)], bank[1][:, 0:P], ACT.Copy).then_inc(*o.inc())
                    act.activation(kvw[:, p, 0:P], bank[1][:, P:2 * P], ACT.Copy).then_inc(*o.inc())
                    act.activation(kvw[:, p, P:P + 8], bank[1][:, 2 * P:2 * P + 8], ACT.Copy,
                                   scale=IDX_HEADS ** -0.5 * IDX_DIM ** -0.5).then_inc(*proj_ready.inc())
                elif c == 2:
                    act.activation(qbT[:, p], by_head[0], ACT.Copy).then_inc(*proj_ready.inc())
                else:
                    act.activation(z[:, p, :], bank[1][:], ACT.Copy).then_inc(*proj_ready.inc())

            act.wait_ge(*zeroed.upto(0))
            for c in range(4):
                project(0, 0, c)
            o.end_block()

            def body(b):
                i, p, nk = b.i, b.p, b.G + 1
                act.wait_ge(*mix_ready.before(i))
                act.wait_ge(*proj_ready.upto(i))
                act.activation(oT[:, 0, :], kvw[:, p, 0:P], ACT.Square, accum_out=css[:]).then_inc(*o.inc())
                o.settle()
                act.activation(crs[:], css[:], ACT.Ln, bias=eps[:, 0:1], scale=1.0 / P).then_inc(*o.inc())
                o.settle()
                act.activation(crs[:], crs[:], ACT.Exp, scale=-0.5).then_inc(*crs_ready.inc())
                act.wait_ge(*cT_made.upto(i))
                act.activation(ckvT[:, bass.ds(i * P, P)], bank[6][:, 0:P], ACT.Copy).then_inc(*cT_ready.inc())
                if b.topk:
                    for n in range(8 * nk):
                        act.wait_ge(*idx_made.upto(b, n + 1))
                        if n >= 4:
                            act.wait_ge(*relu_used.upto(b, n - 3))
                        act.activation(relu[:, n % 4, :], bank[2 + n % 4][:], ACT.Relu).then_inc(*relu_ready.inc())
                else:
                    act.wait_ge(*idx_made.upto(b))
                    act.activation(crs[:], crs[:], ACT.Copy).then_inc(relu_ready.sem, 8 * nk)
                act.activation(sgz[:], z[:, p, :], ACT.Exp, scale=-1.0).then_inc(*o.inc())
                o.settle()
                act.activation(sgz[:], sgz[:], ACT.Ln, bias=1.0).then_inc(*o.inc())
                o.settle()
                act.activation(sgz[:], sgz[:], ACT.Exp, scale=-1.0).then_inc(*zsig_ready.inc())
                if not b.last:
                    for c in range(4):
                        project(b.i + 1, b.q, c)
                for h in range(4):
                    act.wait_ge(*mx_ready.upto(i, h + 1))
                    act.activation(Lg[:, h % 2, P:P + b.W], Lg[:, h % 2, P:P + b.W], ACT.Exp, bias=mx[:, h:h + 1],
                                   accum_out=psum_[:, h:h + 1]).then_inc(*exp_ready.inc())
                    if h == 1:
                        act.wait_ge(*gz_ready.upto(i))
                    for kc in range(nk):
                        n = h * nk + kc
                        act.wait_ge(*pt_made.upto(b, n + 1))
                        if h >= 2:
                            act.wait_ge(*pv_made.upto(i, h - 1))
                        act.activation(pT[:, h % 2, 4 * kc:4 * kc + 4, :], by_head[6 + n % 2], ACT.Copy).then_inc(*pt_ready.inc())
                act.wait_ge(*pv_made.upto(i))
                act.activation(oT[:], by_head[5], ACT.Copy).then_inc(*oT_ready.inc())
                for half in range(2):
                    act.wait_ge(*catT_made.upto(i, half + 1))
                    act.activation(catT[:, half * 512:(half + 1) * 512], (bank[7], bank[2])[half][:], ACT.Copy)\
                       .then_inc(*catT_ready.inc())
                act.wait_ge(*y_made.upto(i))
                for half in range(2):
                    act.activation(squares[half], bank[3 + half][:], ACT.Square, accum_out=mss[:, half:half + 1])\
                       .then_inc(*(mss_ready if half else o).inc())
                act.wait_ge(*mss_ready.upto(i))
                act.activation(mss[:, 0:1], mss[:, 0:1], ACT.Identity, bias=mss[:, 1:2]).then_inc(*o.inc())
                o.settle()
                act.activation(mrs[:], mss[:, 0:1], ACT.Ln, bias=eps[:, 0:1], scale=1.0 / D).then_inc(*o.inc())
                o.settle()
                act.activation(mrs[:], mrs[:], ACT.Exp, scale=-0.5).then_inc(*mrs_ready.inc())
                o.end_block()

            over_sections(act, body)

        @block.vector
        def _(dve):
            o = Order(dve, orders["dve"])
            dve.memset(ikT[:], 0.0).then_inc(*zeroed.inc())
            dve.memset(ckvT[:], 0.0).then_inc(*zeroed.inc())
            dve.memset(ones[:], 1.0).then_inc(*o.inc())
            dve.memset(eps[:], RMS_EPS).then_inc(*zeroed.inc())
            dve.memset(bad[:], 0.0).then_inc(*o.inc())
            dve.wait_ge(loaded.sem, NSMALL)
            dve.tensor_tensor(rb[:], rb[:], rb31[:], ALU.subtract).then_inc(*rb_ready.inc())
            dve.wait_ge(*vec_made.upto(0))
            dve.tensor_copy(vec[:], bank[2][0:4, 0:384]).then_inc(*vec_ready.inc())
            for n in range(2):
                dve.wait_ge(*bias_made.upto(0, n + 1))
                dve.tensor_copy(bias[:, 2 * n:2 * n + 2, :].rearrange("p h c -> p (h c)"), bank[3 + n][:]).then_inc(*bias_ready.inc())
            o.end_block()

            def general(b):
                W = b.W
                dve.tensor_copy(work[:, 0:W], acc[:, 0:W]).then_inc(branch, 1)
                dve.wait_ge(branch, 1)
                dve.sem_clear(branch)
                with dve.Fori(0, TOPK // 8):
                    dve.max(best[:], work[:, 0:W]).then_inc(branch, 1)
                    dve.wait_ge(branch, 1)
                    dve.match_replace(work[:, 0:W], best[:], work[:, 0:W], -3e38).then_inc(branch, 1)
                    dve.wait_ge(branch, 2)
                    dve.sem_clear(branch)
                dve.tensor_tensor(other[:, 0:W], work[:, 0:W], acc[:, 0:W], ALU.is_equal).then_inc(branch, 1)
                dve.wait_ge(branch, 1)
                dve.tensor_scalar_mul(selb[:, 0:W], other[:, 0:W], -FAR).then_inc(branch, 1)
                dve.wait_ge(branch, 2)
                dve.sem_clear(branch)

            def choose(b):
                i, W, nk = b.i, b.W, b.G + 1
                dve.tensor_reduce(lo[:], acc[:, 0:W], AX.X, ALU.min).then_inc(*o.inc())
                o.settle()
                last = acc[:, W - 512:W]
                dve.tensor_tensor(last, last, late[:, bass.ds(384 + 512 * b.G - i * P, 512)], ALU.add).then_inc(*o.inc())
                o.settle()
                dve.tensor_reduce(hi[:], acc[:, 0:W], AX.X, ALU.max).then_inc(*o.inc())
                o.settle()
                dve.tensor_tensor(hi[:], hi[:], lo[:], ALU.subtract).then_inc(*o.inc())
                o.settle()
                dve.tensor_scalar(steps[:], halves[:], hi[:, 0:1], None, ALU.mult).then_inc(*o.inc())
                o.settle()
                dve.tensor_tensor(mid[:], lo[:], steps[:, 0:1], ALU.add).then_inc(*o.inc())
                o.settle()
                for n in range(ROUNDS):
                    dve.tensor_scalar(work[:, 0:W], acc[:, 0:W], mid[:, 0:1], 0.0, ALU.is_ge, ALU.add,
                                      accum_out=cnt[:]).then_inc(*o.inc())
                    o.settle()
                    dve.tensor_scalar(step[:], cnt[:], TOPK - 0.5, steps[:, n:n + 1], ALU.is_ge, ALU.mult).then_inc(*o.inc())
                    o.settle()
                    if n < ROUNDS - 1:
                        dve.scalar_tensor_tensor(mid[:], mid[:], step[:, 0:1], steps[:, n + 1:n + 2], ALU.add, ALU.subtract)\
                           .then_inc(*o.inc())
                    else:
                        dve.tensor_tensor(hi[:], mid[:], step[:], ALU.add).then_inc(*o.inc())
                    o.settle()
                dve.tensor_scalar(work[:, 0:W], acc[:, 0:W], hi[:, 0:1], 0.0, ALU.is_ge, ALU.add, accum_out=cnt[:])\
                   .then_inc(*o.inc())
                o.settle()
                dve.scalar_tensor_tensor(work[:, 0:W], work[:, 0:W], -FAR, acc[:, 0:W], ALU.mult, ALU.add).then_inc(*o.inc())
                dve.tensor_scalar(cnt[:], cnt[:], -1.0, float(TOPK), ALU.mult, ALU.add).then_inc(*o.inc())
                o.settle()
                dve.max(best[:], work[:, 0:W]).then_inc(*o.inc())
                o.settle()
                dve.scalar_tensor_tensor(best[:], iota[:], cnt[:, 0:1], best[:], ALU.is_equal, ALU.mult, accum_out=thr[:])\
                   .then_inc(*o.inc())
                o.settle()
                dve.tensor_scalar(work[:, 0:W], acc[:, 0:W], thr[:, 0:1], 0.0, ALU.is_ge, ALU.add, accum_out=cnt[:])\
                   .then_inc(*o.inc())
                o.settle()
                dve.tensor_scalar(bad[:], cnt[:], float(TOPK), None, ALU.not_equal).then_inc(*bad_ready.inc())
                dve.tensor_scalar(selb[:, 0:W], acc[:, 0:W], thr[:, 0:1], -FAR, ALU.is_lt, ALU.mult).then_inc(*o.inc())
                dve.wait_ge(*nbad_made.upto(i))
                dve.tensor_copy(nbad[:], bank[7][0:1, 0:1]).then_inc(*nbad_ready.inc())
                dve.wait_ge(*nbad_ready.upto(i))
                dve.tensor_copy(lo[:], thr[:]).then_inc(*o.inc())
                o.settle()
                rows = dve.value_load(nbad[0:1, 0:1], min_val=0, max_val=P)
                with dve.If(rows > 0):
                    general(b)
                dve.tensor_copy(lo[:], thr[:]).then_inc(*selb_ready.inc())

            def body(b):
                i, p, nk, W = b.i, b.p, b.G + 1, b.W
                dve.wait_ge(*mix_ready.before(i))
                dve.wait_ge(*crs_ready.upto(i))
                dve.scalar_tensor_tensor(cn[:], kvw[:, p, 0:P], crs[:, 0:1], kv_row[:], ALU.mult, ALU.mult).then_inc(*cn_ready.inc())
                if b.topk:
                    for n in range(8 * nk):
                        kc, h = n // 8, n % 8
                        dve.wait_ge(*relu_ready.upto(b, n + 1))
                        dst, w = acc[:, kc * 512:(kc + 1) * 512], kvw[:, p, P + h:P + h + 1]
                        if h == 0:
                            dve.tensor_scalar(dst, relu[:, n % 4, :], w, None, ALU.mult).then_inc(*relu_used.inc())
                        else:
                            dve.wait_ge(*relu_used.upto(b, n))
                            dve.scalar_tensor_tensor(dst, relu[:, n % 4, :], w, dst, ALU.mult, ALU.add).then_inc(*relu_used.inc())
                    dve.wait_ge(*relu_used.upto(b))
                    choose(b)
                else:
                    dve.wait_ge(*relu_ready.upto(b))
                    dve.tensor_copy(selb[:, 0:W], late[:, bass.ds(384 - i * P, 512)]).then_inc(relu_used.sem, 8 * nk)
                    dve.wait_ge(*relu_used.upto(b))
                    dve.tensor_copy(bad[:], bad[:]).then_inc(*bad_ready.inc())
                    dve.wait_ge(*nbad_made.upto(i))
                    dve.tensor_copy(nbad[:], bank[7][0:1, 0:1]).then_inc(*nbad_ready.inc())
                    dve.wait_ge(*nbad_ready.upto(i))
                    dve.memset(Lg[:, :, 0:P], 0.0).then_inc(*selb_ready.inc())
                for h in range(4):
                    lg = Lg[:, h % 2, P:P + W]
                    if h >= 2:
                        dve.wait_ge(*pt_made.upto(b, (h - 1) * nk))
                    for kc in range(nk):
                        n = h * nk + kc
                        dve.wait_ge(*lg_made.upto(b, n + 1))
                        dve.scalar_tensor_tensor(lg[:, kc * 512:(kc + 1) * 512], bank[2 + n % 3][:], float(P) ** -0.5,
                                                 selb[:, kc * 512:(kc + 1) * 512], ALU.mult, ALU.add).then_inc(*lg_read.inc())
                    dve.wait_ge(*lg_read.upto(b, (h + 1) * nk))
                    near = Lg[:, h % 2, bass.ds(i * P, 2 * P)]
                    dve.tensor_tensor(near, near, bias[:, h, :], ALU.add).then_inc(*o.inc())
                    o.settle()
                    dve.tensor_reduce(mx[:, h:h + 1], lg, AX.X, ALU.max, negate=True).then_inc(*mx_ready.inc())
                dve.wait_ge(*exp_ready.upto(i))
                dve.reciprocal(prec[:], psum_[:]).then_inc(*o.inc())
                o.settle()
                dve.wait_ge(*uv_made.upto(i))
                dve.wait_ge(*gz_ready.upto(i))
                for h in range(4):
                    dve.scalar_tensor_tensor(cat[:, 512 + h * P:512 + (h + 1) * P], by_head[6][:, h, :], prec[:, h:h + 1],
                                             z[:, p, h * P:(h + 1) * P], ALU.mult, ALU.mult)\
                       .then_inc(*(ob_ready if h == 3 else o).inc())
                dve.wait_ge(*mrs_ready.upto(i))
                for half in range(2):
                    sl = slice(half * 512, (half + 1) * 512)
                    dve.scalar_tensor_tensor(cat[:, sl], bank[3 + half][:], mrs[:, 0:1], gate_row[:, sl], ALU.mult, ALU.mult)\
                       .then_inc(*(mix_ready if half else o).inc())
                o.end_block()

            over_sections(dve, body)

        @block.gpsimd
        def _(pool):
            o = Order(pool, orders["pool"])
            pool.memset(ckvr[:], 0.0).then_inc(*zeroed.inc())
            pool.wait_ge(*zeroed.upto(0))

            def body(b):
                i, p = b.i, b.p
                pool.wait_ge(*cn_ready.upto(i))
                pool.tensor_copy(ckvr[:, bass.ds(i, 1), :].rearrange("p a r -> p (a r)"), cn[:]).then_inc(*ckvr_ready.inc())
                pool.wait_ge(*zsig_ready.upto(i))
                pool.tensor_tensor(z[:, p, :], z[:, p, :], sgz[:], ALU.mult).then_inc(*gz_ready.inc())
                pool.wait_ge(*mix_ready.upto(i))
                pool.wait_ge(x_in.sem, 16 * i + 16)
                pool.tensor_tensor(xb[:], xb[:], cat[:], ALU.add).then_inc(*out_ready.inc())

            over_sections(pool, body)


def shape_constants():
    f = lambda m: np.ascontiguousarray(np.asarray(m).astype(np.float32))
    j = np.arange(P)
    up = j[:, None] <= j[None, :]
    same = (j[:, None] // GLA_CHUNK) == (j[None, :] // GLA_CHUNK)
    c = dict(c_ident=f(np.eye(P)), c_chunk=f(np.stack([(same & up) / 16, (same & ~up) / 16], 1)),
             c_causal=f(same & up), c_tril=f(up))
    half = 32
    inv = (np.float32(10000.0) ** (-np.arange(half, dtype=np.float32) / np.float32(half))).astype(np.float32)
    c["c_inv"] = f(np.tile(inv, (P, 1)))
    lg = np.log(1.0 - 2.0 ** (-5.0 - np.arange(HEADS, dtype=np.float64)))
    rel = j[None, :] - j[:, None]
    c["c_dmat"] = f(np.stack([np.where(rel >= 0, np.exp(np.maximum(rel, 0) * g), 0) / 8 for g in lg], 1))
    w = np.zeros((P, HEADS, P))
    for h in range(HEADS):
        w[64 * (h % 2):64 * (h % 2) + 64, h, :] = np.exp((j + 1.0) * lg[h]) / 8
    c["c_winter"] = f(w)
    c["c_wstate"] = f(np.exp((P - 1.0 - j)[:, None] * lg[None, :]))
    c["c_gammac"] = f(np.exp(P * lg)[2 * np.arange(2)[None, :] + (j // 64)[:, None]])
    band = np.zeros((P, 12, P))
    for w_, win in enumerate(POOL_WINDOWS):
        d = j[None, :] - j[:, None]
        band[:, w_] = ((d >= 0) & (d < win)) / win - np.eye(P)
        band[:, 4 + w_] = ((d + P >= 0) & (d + P < win)) / win
        band[:, 8 + w_] = ((d >= 0) & (d < win)) / np.minimum(j + 1, win)[None, :] - np.eye(P)
    c["c_band"] = f(band)
    late = same & ~up
    first = np.broadcast_to((j < GLA_CHUNK)[:, None], (P, P))
    c["c_seg"] = f(np.stack([same & up, late, first, ~first], 1))
    c["c_big"] = f(np.stack([~(same & (j[:, None] > j[None, :])), ~(same & up)], 1) * 1e30)
    c["c_lev"] = f(np.stack([((j[:, None] // (2 * n)) == (j[None, :] // (2 * n))) & (j[:, None] // n % 2 == 1)
                             & (j[None, :] // n % 2 == 0) for n in LEVELS], 1))
    c["c_flip"] = f(np.eye(P)[::-1])
    c["c_late"] = f((np.arange(896)[None, :] - 384 > j[:, None]) * -FAR)
    dist = 255 - np.arange(384)
    n = np.maximum(dist, 1).astype(np.float32)
    big = 16 + (np.log(n / np.float32(16)) / np.float32(math.log(8)) * np.float32(16)).astype(np.int32)
    bucket = np.where(dist < 16, dist, np.minimum(big, N_BUCKETS - 1))
    c["c_onehot"] = f((np.arange(N_BUCKETS)[:, None] == bucket[None, :]) & (dist >= 0)[None, :])
    c["c_iota"] = f(np.tile(np.arange(1, 9), (P, 1)))
    c["c_halves"] = f(np.tile(0.5 ** np.arange(1, ROUNDS + 2), (P, 1)))
    return c


def build(nc, t, out, x1, x2, hT, oa, bias_scratch):
    def layer(prefix, names):
        return [t[prefix + n] for n in names.split()]

    def last(names):
        return [t[n + "_2"][0] for n in names.split()]

    def const(names):
        return tuple(t["c_" + n] for n in names.split())

    even_layer(nc, t["x"].rearrange("a s d -> (a s) d"),
               *layer("l0_", "w_in w_a2 b_a gla_norm_g sgu_ln_g sgu_ln_b w_s b_s w_out ln_g ln_b"),
               const("ident chunk causal tril"), x1)
    odd_layer(nc, x1, t["positions"].rearrange("a s -> (a s)"),
              *layer("l1_", "w_in ret_norm_g w_pool pool_scale w_out ln_g ln_b"),
              const("ident inv dmat winter wstate gammac band"), x2)
    with nc.sbuf_tensor("gate_row", [P, D], F32) as gate_row:
        delta_layer(nc, x2, *last("c w_ada b_ada g_pre w_in conv_w a_log dt_bias g_gdn g_post"),
                    const("ident seg big lev"), gate_row, hT, oa)
        sparse_layer(nc, x2, *last("w_in g_kv w_uv"), t["rel_bias_2"], *last("w_out"),
                     const("ident flip late onehot iota halves"), gate_row, hT, oa, bias_scratch,
                     out.rearrange("a s d -> (a s) d"))


def kernel(**inputs):
    import numpy as _np
    import concourse.bacc as _bacc
    from concourse import mybir as _mybir
    from concourse.bass_utils import run_bass_kernel_spmd as _run

    nc = _bacc.Bacc("TRN2", target_bir_lowering=False, num_devices=1)
    arrays, t = {}, {}
    for name, a in list(inputs.items()) + list(shape_constants().items()):
        arrays[name] = _np.ascontiguousarray(a)
        t[name] = nc.dram_tensor(name, list(arrays[name].shape), _mybir.dt.from_np(arrays[name].dtype),
                                 kind="ExternalInput").ap()
    out = nc.dram_tensor("out", [1, SEQ, D], F32, kind="ExternalOutput").ap()
    x1 = nc.dram_tensor("x1", [SEQ, D], F32).ap()
    x2 = nc.dram_tensor("x2", [SEQ, D], F32).ap()
    hT = nc.dram_tensor("hT", [BLOCKS, P, D], F32).ap()
    oa = nc.dram_tensor("oa", [SEQ, D // 2], F32).ap()
    bias_scratch = nc.dram_tensor("bias_scratch", [4, 384], F32).ap()
    build(nc, t, out, x1, x2, hT, oa, bias_scratch)
    r = _run(nc, [arrays], core_ids=[0])
    return r.results[0]["out"]
```

```python
import math
from contextlib import ExitStack

import numpy as np
import concourse.bass as bass
from concourse import mybir

F32 = mybir.dt.float32
BF16 = mybir.dt.bfloat16
I32 = mybir.dt.int32
ALU = mybir.AluOpType
ACT = mybir.ActivationFunctionType
AX = mybir.AxisListType

P = 128
SEQ, D = 2048, 1024
BLOCKS = SEQ // P
KT = D // P
HEADS = 4
LN_EPS = 1e-5
RMS_EPS = 1e-6
ALPHA = 4 ** 0.25
GELU_C = math.sqrt(2 / math.pi)
GELU_A = math.sqrt(0.044715)
TABLES = "natural_log_exp_and_others"


class Signal:

    def __init__(self, sem, per=1):
        self.sem, self.per, self.first = sem, per, 0

    def start(self):
        self.first = 1
        return self.sem

    def inc(self):
        return self.sem, 1

    def upto(self, i, k=None):
        return self.sem, i * self.per + (self.per if k is None else k) + self.first

    def before(self, i):
        assert self.first
        return self.sem, i * self.per + self.first


class Semaphores:

    def __init__(self, nc, prefix):
        self.nc, self.prefix, self.taken = nc, prefix, []

    def __enter__(self):
        return self

    def __call__(self, name):
        self.taken.append(self.nc.alloc_semaphore(name=self.prefix + name))
        return self.taken[-1]

    def __exit__(self, *_):
        self.nc.clear_and_free_semaphores(self.taken)
        self.nc.all_engine_barrier()


class Order:

    def __init__(self, eng, sem):
        self.eng, self.sem, self.count = eng, sem, 0

    def inc(self):
        self.count += 1
        return self.sem, 1

    def settle(self):
        self.eng.wait_ge(self.sem, self.count)

    def end_block(self):
        self.settle()
        self.eng.sem_clear(self.sem)
        self.count = 0


class Blk:

    def __init__(self, r, p, last=False):
        self.r, self.p, self.i, self.last = r, p, 2 * r + p, last
        self.q = 1 - p


def over_blocks(eng, body):
    with eng.Fori(0, BLOCKS // 2 - 1) as r:
        body(Blk(r, 0))
        body(Blk(r, 1))
    body(Blk(BLOCKS // 2 - 1, 0))
    body(Blk(BLOCKS // 2 - 1, 1, last=True))


def spread(ap, n):
    return ap.unsqueeze(2).broadcast_to([ap.shape[0], ap.shape[1], n])


def over_heads(ap, g):
    return ap.unsqueeze(1).broadcast_to([ap.shape[0], g, ap.shape[1]])


def row(ap, n=P):
    return ap.unsqueeze(0).broadcast_to([n, ap.shape[0]])


GLA_CHUNK = 64


def even_layer(nc, x, w_in, w_a2, b_a, gla_g, sgu_g, sgu_b, w_s, b_s, w_out, ln_g, ln_b, consts, x_next):
    ident_d, chunk_d, causal_d, tril_d = consts
    O_QK, O_V, O_GA, O_ALR, O_USV, O_GB = 0, 512, 1024, 1536, 1552, 2576
    W = w_in.shape[1]
    wv = w_in.rearrange("(k p) n -> p k n", p=P)
    with ExitStack() as ctx:
        sem = ctx.enter_context(Semaphores(nc, "e_"))

        def sb(name, shape, dt=F32):
            return ctx.enter_context(nc.sbuf_tensor("e_" + name, shape, dt))

        def sig(name, per=1):
            return Signal(sem(name), per)

        W_in = sb("w_in", [P, KT, W])
        W_out = sb("w_out", [P, KT, D])
        xb = sb("xb", [P, 2, D])
        xT = sb("xT", [P, KT * P])
        qk = sb("qk", [P, 512])
        v = sb("v", [P, 2, 512])
        gates = sb("gates", [P, 2, 1024])
        usv = sb("usv", [P, 2, 1024])
        alrT = sb("alrT", [17, 2, P])
        w2 = sb("w2", [17, 256])
        ident = sb("ident", [P, P])
        chunkm = sb("chunkm", [P, 2, P])
        causal = sb("causal", [P, P])
        tril = sb("tril", [P, P])
        gla_row = sb("gla_row", [P, 512])
        sgu_grow = sb("sgu_grow", [P, 512])
        sgu_brow = sb("sgu_brow", [P, 512])
        ln_grow = sb("ln_grow", [P, D])
        ln_brow = sb("ln_brow", [P, D])
        wsT = sb("wsT", [P, 4, P])
        bsT = sb("bsT", [P, 4])
        eps = sb("eps", [P, 1])
        la = sb("la", [P, 256])
        lt = sb("lt", [P, 256])
        eks = sb("eks", [P, 256])
        ebT = sb("ebT", [P, 2, P])
        enT = sb("enT", [P, 2, P])
        qz = sb("qz", [P, 4, P])
        kdT = sb("kdT", [P, 2, P])
        kst = sb("kst", [P, 256])
        probs = sb("probs", [P, 4, P])
        S = sb("S", [P, 2, P])
        Smid = sb("Smid", [P, 2, P])
        gt = sb("gt", [P, 1024])
        gl = sb("gl", [P, 1024])
        catT, cat = gt, gl
        sq = sb("sq", [P, 512])
        ws_in = sq[:].rearrange("p (g s) -> p g s", g=4)
        ss = sb("ss", [P, 4])
        rs = sb("rs", [P, 4])
        st6 = sb("st6", [P, 4, 6])
        mv = sb("mv", [P, 4, 2])
        rs2 = sb("rs2", [P, 4])
        lnst = sb("lnst", [P, 2, 6])
        lnmv = sb("lnmv", [P, 2])
        lnrs = sb("lnrs", [P, 1])
        bank = [ctx.enter_context(nc.psum_tensor(f"e_ps{n}", [P, 512], F32)) for n in range(8)]
        zk, bTp, qkTp, scp, Up, op = bank[2], bank[3], bank[4], bank[5], bank[6], bank[7]
        Uc = Up[:, 0:256], bTp[:, 256:512]

        loaded, wout_loaded = sig("loaded"), sig("w_out")
        w_parts = [(O_V, 512), (O_GA, 528), (O_GB, 512), (O_USV, 512), (O_USV + 512, 512), (O_QK, 512)]
        w_loaded = [sig(f"w_in{n}") for n in range(len(w_parts))]
        x_in = [sig("x_in0"), sig("x_in1")]
        stored = sig("stored")
        setup = sig("setup")
        ws_turned, ws_ready = sig("ws_turned"), sig("ws_ready")
        xT_made, xT_ready = sig("xT_made", 2), sig("xT_ready", 2)
        proj_made, proj_ready = sig("proj_made", 7), sig("proj_ready", 7)
        z_made, lse_ready, la_ready = sig("z_made"), sig("lse"), sig("la_ready")
        decay_made, decay_ready = sig("decay_made"), sig("decay_ready", 3)
        qkT_made, qkd_ready, kst_ready = sig("qkT_made"), sig("qkd_ready"), sig("kst_ready")
        sc_made, probs_ready = sig("sc_made"), sig("probs_ready")
        U_made, Smid_ready, S_ready = sig("U_made"), sig("Smid_ready"), sig("S_ready")
        o_made, sq_ready, ss_ready, rs_ready = sig("o_made"), sig("sq_ready"), sig("ss_ready"), sig("rs_ready")
        gsig_ready, gate_ready = sig("gsig"), sig("gate_ready")
        usq_ready, inner_ready, usig_ready, gelu_ready = (
            sig("usq"), sig("inner"), sig("usig"), sig("gelu_ready"))
        mv_ready, rs2_ready, norm_ready, sn_ready = sig("mv_ready"), sig("rs2_ready"), sig("norm_ready"), sig("sn_ready")
        s_made, ob_ready, oa_ready, cb_ready = sig("s_made"), sig("ob_ready"), sig("oa_ready"), sig("cb_ready")
        catT_made, catT_ready = sig("catT_made", 2), sig("catT_ready", 2)
        y_made, r_ready, lnmv_ready, lnrs_ready, lnn_ready, out_ready = (
            sig("y_made"), sig("r_ready"), sig("lnmv"), sig("lnrs"), sig("lnn"), sig("out_ready"))
        orders = {n: sem("order_" + n) for n in ("act", "dve", "pool")}

        def chunks(p):
            return [
                (O_V, v[:, p, :]), (O_GA, gates[:, p, 0:512]), (O_GB, gates[:, p, 512:1024]),
                (O_USV, usv[:, p, 0:512]), (O_USV + 512, usv[:, p, 512:1024]), (O_QK, qk[:]),
            ]

        started = [s.start() for s in (proj_ready, r_ready, kst_ready, y_made, stored)]
        block = ctx.enter_context(nc.Block())
        small = [(ident[:], ident_d), (chunkm[:], chunk_d), (causal[:], causal_d), (tril[:], tril_d), (w2[0:16, :], w_a2),
                 (w2[16:17, :], b_a.unsqueeze(0)), (gla_row[:], row(gla_g.rearrange("h e -> (h e)"))),
                 (sgu_grow[:], row(sgu_g.rearrange("h e -> (h e)"))), (sgu_brow[:], row(sgu_b.rearrange("h e -> (h e)"))),
                 (ln_grow[:], row(ln_g)), (ln_brow[:], row(ln_b)), (ws_in, w_s.rearrange("g t s -> t g s")),
                 (bsT[:], b_s.rearrange("g t -> t g"))]
        NSMALL = 16 * len(small)

        @block.sync
        def _(sp):
            for s in started:
                sp.sem_inc(s, 1)
            sp.dma_start(xb[:, 0, :], x[0:P, :]).then_inc(x_in[0].sem, 16)
            sp.dma_start(xb[:, 1, :], x[P:2 * P, :]).then_inc(x_in[1].sem, 16)
            with nc.allow_non_contiguous_dma(reason="small tables"):
                for dst, src in small:
                    sp.dma_start(dst, src).then_inc(loaded.sem, 16)
            for (a, n), part in zip(w_parts, w_loaded):
                sp.dma_start(W_in[:, :, a:a + n], wv[:, :, a:a + n]).then_inc(part.sem, 16)
            sp.dma_start(W_out[:], w_out.rearrange("(k p) n -> p k n", p=P)).then_inc(wout_loaded.sem, 16)

            def body(b, load=True):
                if load:
                    sp.wait_ge(*r_ready.upto(b.i))
                    sp.dma_start(xb[:, b.p, :], x[bass.ds(b.i * P + 2 * P, P), :]).then_inc(x_in[b.p].sem, 16)
                sp.wait_ge(*out_ready.upto(b.i))
                sp.dma_start(x_next[bass.ds(b.i * P, P), :], cat[:]).then_inc(stored.sem, 16)

            with sp.Fori(0, BLOCKS // 2 - 1) as r:
                body(Blk(r, 0))
                body(Blk(r, 1))
            body(Blk(BLOCKS // 2 - 1, 0), load=False)
            body(Blk(BLOCKS // 2 - 1, 1), load=False)
            sp.wait_ge(stored.sem, 16 * BLOCKS + 1)

        @block.tensor
        def _(pe):
            def turn_x(i, r, p):
                pe.wait_ge(x_in[p].sem, 16 * r + 16)
                for half in range(2):
                    pe.wait_ge(*proj_ready.before(i))
                    for k in range(4):
                        t = 4 * half + k
                        m = pe.transpose(bank[half][:, k * P:(k + 1) * P], xb[:, p, t * P:(t + 1) * P], ident[:])
                    m.then_inc(*xT_made.inc())

            def project(i, p, c):
                if c < 6:
                    off, _ = chunks(p)[c]
                    if c < 2:
                        pe.wait_ge(*xT_ready.upto(i))
                    else:
                        pe.wait_ge(*proj_ready.upto(i, c - 1))
                    for k in range(KT):
                        m = pe.matmul(bank[c % 2][:], xT[:, k * P:(k + 1) * P], W_in[:, k, off:off + 512],
                                      start=(k == 0), stop=(k == KT - 1))
                    m.then_inc(*proj_made.inc())
                else:
                    pe.wait_ge(*proj_ready.upto(i, 5))
                    for k in range(KT):
                        m = pe.matmul(bank[0][0:16, 0:P], W_in[:, k, O_ALR:O_ALR + 16], xT[:, k * P:(k + 1) * P],
                                      start=(k == 0), stop=(k == KT - 1))
                    m.then_inc(*proj_made.inc())

            pe.wait_ge(loaded.sem, NSMALL)
            for g in range(4):
                m = pe.transpose(bank[2][:, g * P:(g + 1) * P], ws_in[:, g, :], ident[:])
            m.then_inc(*ws_turned.inc())
            turn_x(0, 0, 0)
            for c in range(7):
                if c < 6:
                    pe.wait_ge(w_loaded[c].sem, 16)
                project(0, 0, c)
            pe.wait_ge(wout_loaded.sem, 16)
            pe.wait_ge(*setup.upto(0))
            pe.wait_ge(*ws_ready.upto(0))

            def body(b):
                i, p = b.i, b.p
                nxt = []
                if not b.last:
                    r1, i1 = (b.r, b.i + 1) if p == 0 else (b.r + 1, b.i + 1)
                    nxt = [lambda: turn_x(i1, r1, b.q)] + [(lambda c=c: project(i1, b.q, c)) for c in range(7)]

                def fill():
                    if nxt:
                        nxt.pop(0)()

                pe.wait_ge(*proj_ready.upto(i))
                pe.wait_ge(*r_ready.before(i))
                pe.matmul(zk[:, 0:256], alrT[:, p, :], w2[:], start=True, stop=True).then_inc(*z_made.inc())
                fill()
                for g in range(4):
                    m = pe.transpose(qkTp[:, g * P:(g + 1) * P], qk[:, g * P:(g + 1) * P], ident[:])
                m.then_inc(*qkT_made.inc())
                fill()
                pe.wait_ge(*la_ready.upto(i))
                pe.matmul(zk[:, 256:512], chunkm[:, 1, :], la[:], start=True, stop=True)
                for g in range(2):
                    m = pe.matmul(bTp[:, g * P:(g + 1) * P], la[:, g * P:(g + 1) * P], chunkm[:, 0, :],
                                  start=True, stop=True)
                m.then_inc(*decay_made.inc())
                fill()
                pe.wait_ge(*kst_ready.upto(i))
                pe.wait_ge(*qkd_ready.upto(i))
                for h in range(4):
                    m = pe.matmul(scp[:, h * P:(h + 1) * P], kdT[:, h // 2, :], qz[:, h, :], start=True, stop=True)
                m.then_inc(*sc_made.inc())
                for c in range(2):
                    for h in range(4):
                        a, g = 64 * (h % 2), h // 2
                        m = pe.matmul(Uc[c][a:a + 64, g * P:(g + 1) * P],
                                      kst[64 * c:64 * c + 64, h * 64:h * 64 + 64],
                                      v[64 * c:64 * c + 64, p, h * P:(h + 1) * P], start=True, stop=True)
                m.then_inc(*U_made.inc())
                fill()
                pe.wait_ge(*probs_ready.upto(i))
                pe.wait_ge(*Smid_ready.upto(i))
                for h in range(4):
                    g = h // 2
                    pe.matmul(op[:, h * P:(h + 1) * P], probs[:, h, :], v[:, p, h * P:(h + 1) * P],
                              start=True, stop=False, skip_group_check=True)
                    pe.matmul(op[0:64, h * P:(h + 1) * P], qz[:, h, 0:64], S[:, g, :],
                              start=False, stop=False, skip_group_check=True)
                    m = pe.matmul(op[64:128, h * P:(h + 1) * P], qz[:, h, 64:128], Smid[:, g, :],
                                  start=False, stop=True, skip_group_check=True)
                m.then_inc(*o_made.inc())
                fill()
                pe.wait_ge(*sn_ready.upto(i))
                pe.wait_ge(*S_ready.upto(i))
                for g in range(4):
                    m = pe.matmul(Up[:, g * P:(g + 1) * P], wsT[:, g, :], usv[:, p, 512 + g * P:512 + (g + 1) * P],
                                  start=True, stop=True)
                m.then_inc(*s_made.inc())
                fill()
                for half, ready in enumerate((oa_ready, cb_ready)):
                    pe.wait_ge(*ready.upto(i))
                    for k in range(4):
                        t = 4 * half + k
                        m = pe.transpose((qkTp, scp)[half][:, k * P:(k + 1) * P], cat[:, t * P:(t + 1) * P], ident[:])
                    m.then_inc(*catT_made.inc())
                    fill()
                pe.wait_ge(*catT_ready.upto(i))
                for half in range(2):
                    for k in range(KT):
                        m = pe.matmul((zk, bTp)[half][:], catT[:, k * P:(k + 1) * P],
                                      W_out[:, k, half * 512:(half + 1) * 512], start=(k == 0), stop=(k == KT - 1))
                m.then_inc(*y_made.inc())
                while nxt:
                    fill()

            over_blocks(pe, body)

        @block.scalar
        def _(act):
            o = Order(act, orders["act"])
            act.preload_act_table_set(TABLES)

            def sigmoid(dst, src, scale, ready):
                act.activation(dst, src, ACT.Exp, scale=scale).then_inc(*o.inc())
                o.settle()
                act.activation(dst, dst, ACT.Ln, bias=1.0).then_inc(*o.inc())
                o.settle()
                act.activation(dst, dst, ACT.Exp, scale=-1.0).then_inc(*ready.inc())

            def turn_x(i, p):
                for half in range(2):
                    act.wait_ge(*xT_made.upto(i, half + 1))
                    act.activation(xT[:, half * 512:(half + 1) * 512], bank[half][:], ACT.Copy).then_inc(*xT_ready.inc())

            def project(i, p, c):
                act.wait_ge(*proj_made.upto(i, c + 1))
                if c == 5:
                    act.wait_ge(*kst_ready.before(i))
                if c < 6:
                    act.activation(chunks(p)[c][1], bank[c % 2][:], ACT.Copy).then_inc(*proj_ready.inc())
                else:
                    act.activation(alrT[0:16, p, :], bank[0][0:16, 0:P], ACT.Copy).then_inc(*proj_ready.inc())

            turn_x(0, 0)
            act.wait_ge(*setup.upto(0))
            for c in range(7):
                project(0, 0, c)

            def body(b):
                i, p = b.i, b.p
                nxt = []
                if not b.last:
                    nxt = [lambda: turn_x(b.i + 1, b.q)] + [(lambda c=c: project(b.i + 1, b.q, c)) for c in range(7)]

                def fill():
                    if nxt:
                        nxt.pop(0)()

                act.wait_ge(*y_made.before(i))
                act.wait_ge(*z_made.upto(i))
                act.activation(lt[:], zk[:, 0:256], ACT.Abs).then_inc(*o.inc())
                o.settle()
                act.activation(eks[:], lt[:], ACT.Exp, scale=-1.0).then_inc(*o.inc())
                o.settle()
                act.activation(lt[:], eks[:], ACT.Ln, bias=1.0).then_inc(*lse_ready.inc())
                fill()
                act.wait_ge(*proj_ready.upto(i))
                sigmoid(gt[:], gates[:, p, :], -1.0, gsig_ready)
                fill()
                act.wait_ge(*decay_made.upto(i))
                act.activation(eks[:], zk[:, 256:512], ACT.Exp).then_inc(*decay_ready.inc())
                act.activation(ebT[:], bTp[:, 0:256].rearrange("p (g t) -> p g t", g=2), ACT.Exp).then_inc(*decay_ready.inc())
                act.activation(enT[:], bTp[:, 0:256].rearrange("p (g t) -> p g t", g=2), ACT.Exp, scale=-1.0)\
                   .then_inc(*decay_ready.inc())
                act.wait_ge(stored.sem, 16 * i + 1)
                act.activation(gl[:], usv[:, p, :], ACT.Square, scale=GELU_A).then_inc(*usq_ready.inc())
                fill()
                act.wait_ge(*inner_ready.upto(i))
                sigmoid(gl[:], gl[:], -2.0 * GELU_C, usig_ready)
                fill()
                act.wait_ge(*o_made.upto(i))
                act.activation(sq[:], op[:], ACT.Square).then_inc(*sq_ready.inc())
                act.wait_ge(*mv_ready.upto(i))
                act.activation(rs2[:], mv[:, :, 1], ACT.Ln, bias=eps[:, 0:1]).then_inc(*o.inc())
                o.settle()
                act.activation(rs2[:], rs2[:], ACT.Exp, scale=-0.5).then_inc(*rs2_ready.inc())
                act.wait_ge(*ss_ready.upto(i))
                act.activation(rs[:], ss[:], ACT.Ln, bias=eps[:, 0:1], scale=1.0 / P).then_inc(*o.inc())
                o.settle()
                act.activation(rs[:], rs[:], ACT.Exp, scale=-0.5).then_inc(*rs_ready.inc())
                fill()
                fill()
                for half in range(2):
                    act.wait_ge(*catT_made.upto(i, half + 1))
                    act.activation(catT[:, half * 512:(half + 1) * 512], (qkTp, scp)[half][:], ACT.Copy)\
                       .then_inc(*catT_ready.inc())
                    fill()
                act.wait_ge(*lnmv_ready.upto(i))
                act.activation(lnrs[:], lnmv[:, 1:2], ACT.Ln, bias=eps[:, 0:1]).then_inc(*o.inc())
                o.settle()
                act.activation(lnrs[:], lnrs[:], ACT.Exp, scale=-0.5).then_inc(*lnrs_ready.inc())
                while nxt:
                    fill()
                o.end_block()

            over_blocks(act, body)

        @block.vector
        def _(dve):
            o = Order(dve, orders["dve"])
            dve.memset(S[:], 0.0).then_inc(*o.inc())
            dve.memset(qz[:], 0.0).then_inc(*o.inc())
            dve.memset(eps[:], LN_EPS).then_inc(*o.inc())
            dve.memset(alrT[:], 1.0).then_inc(*o.inc())
            o.settle()
            dve.memset(st6[:], 0.0).then_inc(*setup.inc())
            dve.wait_ge(*ws_turned.upto(0))
            dve.wait_ge(loaded.sem, NSMALL)
            dve.tensor_tensor(wsT[:], bank[2][:].rearrange("p (g t) -> p g t", g=4), over_heads(tril[:, :], 4),
                              ALU.mult).then_inc(*ws_ready.inc())
            o.end_block()

            def body(b):
                i, p = b.i, b.p
                dve.wait_ge(*lse_ready.upto(i))
                dve.scalar_tensor_tensor(la[:], zk[:, 0:256], 0.0, lt[:], ALU.min, ALU.subtract).then_inc(*la_ready.inc())
                dve.wait_ge(*qkT_made.upto(i))
                dve.wait_ge(*decay_ready.upto(i))
                for a in (0, 64):
                    dve.scalar_tensor_tensor(qz[a:a + 64].rearrange("p (g b) t -> p b g t", b=2)[:, a // 64],
                                             qkTp[a:a + 64, 0:256].rearrange("p (g t) -> p g t", g=2), 0.125,
                                             ebT[a:a + 64], ALU.mult, ALU.mult).then_inc(*o.inc())
                dve.tensor_tensor(kdT[:], qkTp[:, 256:512].rearrange("p (g t) -> p g t", g=2), enT[:], ALU.mult)\
                   .then_inc(*qkd_ready.inc())
                dve.wait_ge(*sc_made.upto(i))
                dve.tensor_tensor(probs[:], scp[:].rearrange("p (h t) -> p h t", h=4), over_heads(causal[:, :], 4),
                                  ALU.mult).then_inc(*probs_ready.inc())
                dve.wait_ge(*U_made.upto(i))
                for g in range(2):
                    dve.scalar_tensor_tensor(Smid[:, g, :], S[:, g, :], ebT[:, g, 63:64], Uc[0][:, g * P:(g + 1) * P],
                                             ALU.mult, ALU.add).then_inc(*(Smid_ready if g else o).inc())
                dve.wait_ge(*gelu_ready.upto(i))
                for g in range(4):
                    dve.bn_stats(st6[:, g, :], usv[:, p, 512 + g * P:512 + (g + 1) * P]).then_inc(*o.inc())
                o.settle()
                for g in range(4):
                    dve.bn_aggr(mv[:, g, :], st6[:, g, :]).then_inc(*(mv_ready if g == 3 else o).inc())
                dve.wait_ge(*rs2_ready.upto(i))
                for g in range(4):
                    dve.tensor_scalar(usv[:, p, 512 + g * P:512 + (g + 1) * P], usv[:, p, 512 + g * P:512 + (g + 1) * P], mv[:, g, 0:1],
                                      rs2[:, g:g + 1], ALU.subtract, ALU.mult)\
                       .then_inc(*(norm_ready if g == 3 else o).inc())
                dve.wait_ge(*o_made.upto(i))
                for g in range(2):
                    dve.scalar_tensor_tensor(S[:, g, :], Smid[:, g, :], ebT[:, g, 127:128],
                                             Uc[1][:, g * P:(g + 1) * P], ALU.mult, ALU.add)\
                       .then_inc(*(S_ready if g else o).inc())
                dve.wait_ge(*sq_ready.upto(i))
                dve.tensor_reduce(ss[:], sq[:].rearrange("p (h e) -> p h e", h=4), AX.X, ALU.add).then_inc(*ss_ready.inc())
                dve.wait_ge(stored.sem, 16 * i + 1)
                dve.wait_ge(*rs_ready.upto(i))
                dve.wait_ge(*gate_ready.upto(i))
                for h in range(4):
                    dve.scalar_tensor_tensor(cat[:, h * P:(h + 1) * P], op[:, h * P:(h + 1) * P], rs[:, h:h + 1],
                                             gates[:, p, h * P:(h + 1) * P], ALU.mult, ALU.mult)\
                       .then_inc(*(oa_ready if h == 3 else o).inc())
                dve.wait_ge(*s_made.upto(i))
                for g in range(4):
                    dve.scalar_tensor_tensor(cat[:, 512 + g * P:512 + (g + 1) * P], Up[:, g * P:(g + 1) * P], bsT[:, g:g + 1],
                                             usv[:, p, g * P:(g + 1) * P], ALU.add, ALU.mult)\
                       .then_inc(*(ob_ready if g == 3 else o).inc())
                dve.wait_ge(*y_made.upto(i))
                for half in range(2):
                    dve.scalar_tensor_tensor(cat[:, half * 512:(half + 1) * 512], xb[:, p, half * 512:(half + 1) * 512],
                                             ALPHA, (zk, bTp)[half][:], ALU.mult, ALU.add)\
                       .then_inc(*(r_ready if half else o).inc())
                dve.wait_ge(*r_ready.upto(i))
                for half in range(2):
                    dve.bn_stats(lnst[:, half, :], cat[:, half * 512:(half + 1) * 512]).then_inc(*o.inc())
                o.settle()
                dve.bn_aggr(lnmv[:], lnst[:].rearrange("p a b -> p (a b)")).then_inc(*lnmv_ready.inc())
                dve.wait_ge(*lnrs_ready.upto(i))
                dve.tensor_scalar(cat[:], cat[:], lnmv[:, 0:1], lnrs[:, 0:1], ALU.subtract, ALU.mult)\
                   .then_inc(*lnn_ready.inc())
                o.end_block()

            over_blocks(dve, body)

        @block.gpsimd
        def _(pool):
            o = Order(pool, orders["pool"])
            pool.wait_ge(loaded.sem, NSMALL)

            def body(b):
                i, p = b.i, b.p
                pool.wait_ge(*usq_ready.upto(i))
                pool.tensor_tensor(gl[:], gl[:], usv[:, p, :], ALU.mult).then_inc(*o.inc())
                o.settle()
                pool.tensor_tensor(gl[:], gl[:], usv[:, p, :], ALU.add).then_inc(*inner_ready.inc())
                pool.wait_ge(*decay_ready.upto(i, 1))
                pool.tensor_tensor(kst[:], qk[:, 256:512], eks[:], ALU.mult).then_inc(*kst_ready.inc())
                pool.wait_ge(*usig_ready.upto(i))
                pool.tensor_tensor(usv[:, p, :], usv[:, p, :], gl[:], ALU.mult).then_inc(*gelu_ready.inc())
                pool.wait_ge(*gsig_ready.upto(i))
                pool.tensor_tensor(gates[:, p, :], gates[:, p, :], gt[:], ALU.mult).then_inc(*o.inc())
                o.settle()
                pool.tensor_tensor(gates[:, p, 0:512], gates[:, p, 0:512], gla_row[:], ALU.mult).then_inc(*gate_ready.inc())
                pool.wait_ge(*norm_ready.upto(i))
                pool.tensor_tensor(usv[:, p, 512:1024], usv[:, p, 512:1024], sgu_grow[:], ALU.mult).then_inc(*o.inc())
                o.settle()
                pool.tensor_tensor(usv[:, p, 512:1024], usv[:, p, 512:1024], sgu_brow[:], ALU.add).then_inc(*sn_ready.inc())
                pool.wait_ge(*ob_ready.upto(i))
                pool.tensor_tensor(cat[:, 512:1024], cat[:, 512:1024], gates[:, p, 512:1024], ALU.mult).then_inc(*cb_ready.inc())
                pool.wait_ge(*lnn_ready.upto(i))
                pool.tensor_tensor(cat[:], cat[:], ln_grow[:], ALU.mult).then_inc(*o.inc())
                o.settle()
                pool.tensor_tensor(cat[:], cat[:], ln_brow[:], ALU.add).then_inc(*out_ready.inc())
                o.end_block()

            over_blocks(pool, body)


POOL_WINDOWS = (2, 4, 8, 16)
TWO_PI = 2 * math.pi
PI_A = 6.28125
PI_B = float(np.float32(TWO_PI - PI_A) // np.float32(2 ** -20) * np.float32(2 ** -20))
PI_C = TWO_PI - PI_A - PI_B
ROUND = 1.5 * 2 ** 23


def odd_layer(nc, x, positions, w_in, ret_g, w_pool, pool_scale, w_out, ln_g, ln_b, consts, x_next):
    ident_d, inv_d, dmat_d, winter_d, wstate_d, gammac_d, band_d = consts
    O_QK, O_V, O_GC, O_P, O_GD = 0, 512, 1024, 1536, 2048
    W = w_in.shape[1]
    wv = w_in.rearrange("(k p) n -> p k n", p=P)
    with ExitStack() as ctx:
        sem = ctx.enter_context(Semaphores(nc, "o_"))

        def sb(name, shape, dt=F32):
            return ctx.enter_context(nc.sbuf_tensor("o_" + name, shape, dt))

        def sig(name, per=1):
            return Signal(sem(name), per)

        W_in = sb("w_in", [P, KT, W])
        W_out = sb("w_out", [P, KT, D])
        xb = sb("xb", [P, 2, D])
        xT = sb("xT", [P, KT * P])
        qk = sb("qk", [P, 2, 512])
        v = sb("v", [P, 2, 512])
        gates = sb("gates", [P, 2, 1024])
        pp = sb("pp", [P, 2, 512])
        ident = sb("ident", [P, P])
        inv = sb("inv", [P, 32])
        dmat = sb("dmat", [P, 4, P])
        winter = sb("winter", [P, 4, P])
        wstate = sb("wstate", [P, 4])
        gammac = sb("gammac", [P, 2])
        band = sb("band", [P, 12, P])
        poolw = sb("poolw", [P, 4, P])
        ret_row = sb("ret_row", [P, 512])
        scale_row = sb("scale_row", [P, 512])
        ln_grow = sb("ln_grow", [P, D])
        ln_brow = sb("ln_brow", [P, D])
        eps = sb("eps", [P, 1])
        halfpi = sb("halfpi", [P, 1])
        posi = sb("posi", [P, BLOCKS], I32)
        posf = sb("posf", [P, BLOCKS])
        ang = sb("ang", [P, BLOCKS, 32])
        red = sb("red", [P, BLOCKS, 32])
        turns = sb("turns", [P, BLOCKS, 32])
        sin = sb("sin", [P, BLOCKS, 32])
        cos = sb("cos", [P, BLOCKS, 32])
        ra = sb("ra", [P, 8, 32])
        rb = sb("rb", [P, 8, 32])
        rc = sb("rc", [P, 8, 32])
        rd = sb("rd", [P, 8, 32])
        rot = sb("rot", [P, 8, 64])
        qT = sb("qT", [P, 2, P])
        kT = sb("kT", [P, 2, P])
        qz = sb("qz", [P, 4, P])
        qw = sb("qw", [P, 4, P])
        kst = sb("kst", [P, 256])
        probs = sb("probs", [P, 4, P])
        S = sb("S", [P, 2, P])
        pT = sb("pT", [P, 4, P])
        gt = sb("gt", [P, 1024])
        cat = sb("cat", [P, 1024])
        catT = gt
        st6 = sb("st6", [P, 4, 6])
        mv = sb("mv", [P, 4, 2])
        rs = sb("rs", [P, 4])
        lnst = sb("lnst", [P, 2, 6])
        lnmv = sb("lnmv", [P, 2])
        lnrs = sb("lnrs", [P, 1])
        bank = [ctx.enter_context(nc.psum_tensor(f"o_ps{n}", [P, 512], F32)) for n in range(8)]
        y0, y1, qkTp, scp, Up, op = bank[2], bank[3], bank[4], bank[5], bank[6], bank[7]

        loaded, wout_loaded = sig("loaded"), sig("w_out")
        w_parts = (O_QK, O_GC, O_GD, O_V, O_P)
        w_loaded = [sig(f"w_in{n}") for n in range(len(w_parts))]
        x_in = [sig("x_in0"), sig("x_in1")]
        stored, setup, tables = sig("stored"), sig("setup"), sig("tables", 2)
        xT_made, xT_ready = sig("xT_made", 2), sig("xT_ready", 2)
        proj_made, proj_ready = sig("proj_made", 5), sig("proj_ready", 5)
        rot_ready, qkT_made, qk_ready, kst_ready = sig("rot"), sig("qkT_made"), sig("qk_ready"), sig("kst")
        rot_part = sig("rot_part")
        sc_made, probs_ready, U_made, o_made, S_ready = sig("sc_made"), sig("probs"), sig("U_made"), sig("o_made"), sig("S_ready")
        gsig_ready, gate_ready = sig("gsig"), sig("gate")
        mv_ready, rs_ready, oc_ready = sig("mv"), sig("rs"), sig("oc")
        pT_made, pT_ready, pd_made, od_ready = sig("pT_made"), sig("pT_ready"), sig("pd_made"), sig("od")
        catT_made, catT_ready = sig("catT_made", 2), sig("catT_ready", 2)
        y_made, r_ready, lnmv_ready, lnrs_ready, lnn_ready, out_ready = (
            sig("y_made"), sig("r_ready"), sig("lnmv"), sig("lnrs"), sig("lnn"), sig("out_ready"))
        orders = {n: sem("order_" + n) for n in ("act", "dve", "pool")}

        def chunks(p):
            return [(O_QK, qk[:, p, :]), (O_GC, gates[:, p, 0:512]), (O_GD, gates[:, p, 512:1024]),
                    (O_V, v[:, p, :]), (O_P, pp[:, p, :])]

        started = [s.start() for s in (proj_ready, S_ready, catT_ready, r_ready, y_made, qkT_made, rot_ready, stored)]
        block = ctx.enter_context(nc.Block())
        small = [(ident[:], ident_d), (inv[:], inv_d), (dmat[:], dmat_d), (winter[:], winter_d), (wstate[:], wstate_d),
                 (gammac[:], gammac_d), (band[:], band_d), (poolw[:], w_pool.rearrange("g c d -> c g d")),
                 (ret_row[:], row(ret_g.rearrange("h e -> (h e)"))), (scale_row[:], row(pool_scale)),
                 (ln_grow[:], row(ln_g)), (ln_brow[:], row(ln_b)),
                 (posi[:], positions.rearrange("(b p) -> p b", p=P))]
        NSMALL = 16 * len(small)

        @block.sync
        def _(sp):
            for s in started:
                sp.sem_inc(s, 1)
            sp.dma_start(xb[:, 0, :], x[0:P, :]).then_inc(x_in[0].sem, 16)
            sp.dma_start(xb[:, 1, :], x[P:2 * P, :]).then_inc(x_in[1].sem, 16)
            with nc.allow_non_contiguous_dma(reason="small tables"):
                for dst, src in small:
                    sp.dma_start(dst, src).then_inc(loaded.sem, 16)
            for a, part in zip(w_parts, w_loaded):
                sp.dma_start(W_in[:, :, a:a + 512], wv[:, :, a:a + 512]).then_inc(part.sem, 16)
            sp.dma_start(W_out[:], w_out.rearrange("(k p) n -> p k n", p=P)).then_inc(wout_loaded.sem, 16)

            def body(b, load=True):
                if load:
                    sp.wait_ge(*r_ready.upto(b.i))
                    sp.dma_start(xb[:, b.p, :], x[bass.ds(b.i * P + 2 * P, P), :]).then_inc(x_in[b.p].sem, 16)
                sp.wait_ge(*out_ready.upto(b.i))
                sp.dma_start(x_next[bass.ds(b.i * P, P), :], cat[:]).then_inc(stored.sem, 16)

            with sp.Fori(0, BLOCKS // 2 - 1) as r:
                body(Blk(r, 0))
                body(Blk(r, 1))
            body(Blk(BLOCKS // 2 - 1, 0), load=False)
            body(Blk(BLOCKS // 2 - 1, 1), load=False)
            sp.wait_ge(stored.sem, 16 * BLOCKS + 1)

        @block.tensor
        def _(pe):
            def turn_x(i, r, p):
                pe.wait_ge(x_in[p].sem, 16 * r + 16)
                pe.wait_ge(*proj_ready.before(i))
                for half in range(2):
                    for k in range(4):
                        t = 4 * half + k
                        m = pe.transpose(bank[half][:, k * P:(k + 1) * P], xb[:, p, t * P:(t + 1) * P], ident[:])
                    m.then_inc(*xT_made.inc())

            def project(i, p, c):
                off, _ = chunks(p)[c]
                if c < 2:
                    pe.wait_ge(*xT_ready.upto(i))
                else:
                    pe.wait_ge(*proj_ready.upto(i, c - 1))
                for k in range(KT):
                    m = pe.matmul(bank[c % 2][:], xT[:, k * P:(k + 1) * P], W_in[:, k, off:off + 512],
                                  start=(k == 0), stop=(k == KT - 1))
                m.then_inc(*proj_made.inc())

            pe.wait_ge(loaded.sem, NSMALL)
            turn_x(0, 0, 0)
            for c in range(5):
                pe.wait_ge(w_loaded[c].sem, 16)
                project(0, 0, c)
            pe.wait_ge(wout_loaded.sem, 16)
            pe.wait_ge(*setup.upto(0))

            def body(b, first=False):
                i, p = b.i, b.p
                nxt = []
                if not b.last:
                    r1, i1 = (b.r, b.i + 1) if p == 0 else (b.r + 1, b.i + 1)
                    nxt = [lambda: turn_x(i1, r1, b.q)] + [(lambda c=c: project(i1, b.q, c)) for c in range(5)]

                def fill():
                    if nxt:
                        nxt.pop(0)()

                pe.wait_ge(*proj_ready.upto(i))
                pe.wait_ge(*S_ready.before(i))
                for w in range(4):
                    m = pe.matmul(Up[:, w * P:(w + 1) * P], pp[:, p, w * P:(w + 1) * P], band[:, (8 if first else 0) + w, :],
                                  start=True, stop=first)
                    if not first:
                        m = pe.matmul(Up[:, w * P:(w + 1) * P], pp[:, b.q, w * P:(w + 1) * P], band[:, 4 + w, :],
                                      start=False, stop=True)
                m.then_inc(*pT_made.inc())
                fill()
                fill()
                pe.wait_ge(*rot_ready.upto(i))
                pe.wait_ge(*catT_ready.before(i))
                for g in range(4):
                    m = pe.transpose(qkTp[:, g * P:(g + 1) * P], rot[:, 2 * g:2 * g + 2, :].rearrange("p a b -> p (a b)"), ident[:])
                m.then_inc(*qkT_made.inc())
                fill()
                pe.wait_ge(*qk_ready.upto(i))
                for h in range(4):
                    m = pe.matmul(scp[:, h * P:(h + 1) * P], kT[:, h // 2, :], qz[:, h, :], start=True, stop=True)
                m.then_inc(*sc_made.inc())
                pe.wait_ge(*kst_ready.upto(i))
                pe.wait_ge(*pT_ready.upto(i))
                for h in range(4):
                    a, g = 64 * (h % 2), h // 2
                    m = pe.matmul(Up[a:a + 64, g * P:(g + 1) * P], kst[:, h * 64:h * 64 + 64],
                                  v[:, p, h * P:(h + 1) * P], start=True, stop=True)
                m.then_inc(*U_made.inc())
                pe.wait_ge(*r_ready.before(i))
                for w in range(4):
                    m = pe.matmul(y0[:, w * P:(w + 1) * P], pT[:, w, :], poolw[:, w, :], start=True, stop=True)
                m.then_inc(*pd_made.inc())
                fill()
                pe.wait_ge(*probs_ready.upto(i))
                for h in range(4):
                    g = h // 2
                    pe.matmul(op[:, h * P:(h + 1) * P], probs[:, h, :], v[:, p, h * P:(h + 1) * P], start=True, stop=False)
                    m = pe.matmul(op[:, h * P:(h + 1) * P], qw[:, h, :], S[:, g, :], start=False, stop=True)
                m.then_inc(*o_made.inc())
                fill()
                for half, ready in ((1, od_ready), (0, oc_ready)):
                    pe.wait_ge(*ready.upto(i))
                    for k in range(4):
                        t = 4 * half + k
                        m = pe.transpose((qkTp, scp)[half][:, k * P:(k + 1) * P], cat[:, t * P:(t + 1) * P], ident[:])
                    m.then_inc(*catT_made.inc())
                while nxt:
                    fill()
                pe.wait_ge(*catT_ready.upto(i))
                for half in range(2):
                    for k in range(KT):
                        m = pe.matmul((y0, y1)[half][:], catT[:, k * P:(k + 1) * P],
                                      W_out[:, k, half * 512:(half + 1) * 512], start=(k == 0), stop=(k == KT - 1))
                m.then_inc(*y_made.inc())

            body(Blk(0, 0), first=True)
            body(Blk(0, 1))
            with pe.Fori(1, BLOCKS // 2 - 1) as r:
                body(Blk(r, 0))
                body(Blk(r, 1))
            body(Blk(BLOCKS // 2 - 1, 0))
            body(Blk(BLOCKS // 2 - 1, 1, last=True))

        @block.scalar
        def _(act):
            o = Order(act, orders["act"])

            def turn_x(i, p):
                for half in range(2):
                    act.wait_ge(*xT_made.upto(i, half + 1))
                    act.activation(xT[:, half * 512:(half + 1) * 512], bank[half][:], ACT.Copy).then_inc(*xT_ready.inc())

            def project(i, p, c):
                act.wait_ge(*proj_made.upto(i, c + 1))
                act.activation(chunks(p)[c][1], bank[c % 2][:], ACT.Copy).then_inc(*proj_ready.inc())

            act.wait_ge(*tables.upto(0, 2))
            act.activation(sin[:], red[:], ACT.Sin).then_inc(*o.inc())
            act.activation(cos[:], turns[:], ACT.Sin).then_inc(*o.inc())
            o.settle()
            act.preload_act_table_set(TABLES)

            def sigmoid(dst, src, scale, ready):
                act.activation(dst, src, ACT.Exp, scale=scale).then_inc(*o.inc())
                o.settle()
                act.activation(dst, dst, ACT.Ln, bias=1.0).then_inc(*o.inc())
                o.settle()
                act.activation(dst, dst, ACT.Exp, scale=-1.0).then_inc(*ready.inc())
            turn_x(0, 0)
            for c in range(5):
                project(0, 0, c)
            act.activation(lnrs[:], eps[:], ACT.Copy).then_inc(*setup.inc())
            o.end_block()

            def body(b):
                i, p = b.i, b.p
                nxt = []
                if not b.last:
                    nxt = [lambda: turn_x(b.i + 1, b.q)] + [(lambda c=c: project(b.i + 1, b.q, c)) for c in range(5)]

                def fill():
                    if nxt:
                        nxt.pop(0)()

                act.wait_ge(*y_made.before(i))
                act.wait_ge(*proj_ready.upto(i))
                sigmoid(gt[:], gates[:, p, :], -1.0, gsig_ready)
                act.wait_ge(*pT_made.upto(i))
                act.activation(pT[:], Up[:].rearrange("p (g t) -> p g t", g=4), ACT.Copy).then_inc(*pT_ready.inc())
                fill()
                fill()
                fill()
                fill()
                act.wait_ge(*mv_ready.upto(i))
                act.activation(rs[:], mv[:, :, 1], ACT.Ln, bias=eps[:, 0:1]).then_inc(*o.inc())
                o.settle()
                act.activation(rs[:], rs[:], ACT.Exp, scale=-0.5).then_inc(*rs_ready.inc())
                fill()
                for half in (1, 0):
                    act.wait_ge(*catT_made.upto(i, 2 - half))
                    act.activation(catT[:, half * 512:(half + 1) * 512], (qkTp, scp)[half][:], ACT.Copy)\
                       .then_inc(*catT_ready.inc())
                while nxt:
                    fill()
                act.wait_ge(*lnmv_ready.upto(i))
                act.activation(lnrs[:], lnmv[:, 1:2], ACT.Ln, bias=eps[:, 0:1]).then_inc(*o.inc())
                o.settle()
                act.activation(lnrs[:], lnrs[:], ACT.Exp, scale=-0.5).then_inc(*lnrs_ready.inc())
                o.end_block()

            over_blocks(act, body)

        @block.vector
        def _(dve):
            o = Order(dve, orders["dve"])
            dve.memset(S[:], 0.0).then_inc(*o.inc())
            dve.memset(qz[:], 0.0).then_inc(*o.inc())
            dve.memset(eps[:], LN_EPS).then_inc(*o.inc())
            dve.wait_ge(loaded.sem, NSMALL)
            dve.tensor_copy(posf[:], posi[:]).then_inc(*o.inc())
            o.settle()
            dve.tensor_tensor(ang[:], spread(posf[:], 32), over_heads(inv[:], BLOCKS), ALU.mult).then_inc(*o.inc())
            o.settle()

            def reduce(dst, quarter, done):
                dve.tensor_scalar(rnd, ang[:], 1 / TWO_PI, quarter, ALU.mult, ALU.add).then_inc(*o.inc())
                o.settle()
                dve.tensor_scalar(rnd, rnd, ROUND, ROUND, ALU.add, ALU.subtract).then_inc(*o.inc())
                o.settle()
                dve.scalar_tensor_tensor(dst, rnd, -PI_A, ang[:], ALU.mult, ALU.add).then_inc(*o.inc())
                o.settle()
                dve.scalar_tensor_tensor(dst, rnd, -PI_B, dst, ALU.mult, ALU.add).then_inc(*o.inc())
                o.settle()
                dve.scalar_tensor_tensor(dst, rnd, -PI_C, dst, ALU.mult, ALU.add).then_inc(*o.inc())
                o.settle()
                dve.tensor_scalar(dst, dst, quarter * TWO_PI, math.pi * (1 - 1e-7), ALU.add, ALU.min).then_inc(*o.inc())
                o.settle()
                dve.tensor_scalar(dst, dst, -math.pi * (1 - 1e-7), None, ALU.max).then_inc(*done.inc())

            rnd = cos[:]
            reduce(red[:], 0.0, tables)
            reduce(turns[:], 0.25, tables)
            o.end_block()

            def body(b):
                i, p = b.i, b.p
                x12 = qk[:, p, :].rearrange("p (h a j) -> p h a j", h=8, a=2)
                cs, sn = (over_heads(t[:, bass.ds(i, 1), :].rearrange("p a j -> p (a j)"), 8) for t in (cos, sin))
                dve.wait_ge(*proj_ready.upto(i, 1))
                dve.wait_ge(*qkT_made.before(i))
                dve.tensor_tensor(rb[:], x12[:, :, 1, :], sn, ALU.mult).then_inc(*o.inc())
                dve.tensor_tensor(rc[:], x12[:, :, 0, :], sn, ALU.mult).then_inc(*o.inc())
                o.settle()
                dve.wait_ge(*rot_part.upto(i))
                dve.tensor_tensor(rot[:, :, 0:32], ra[:], rb[:], ALU.subtract).then_inc(*o.inc())
                dve.tensor_tensor(rot[:, :, 32:64], rc[:], rd[:], ALU.add).then_inc(*rot_ready.inc())
                dve.wait_ge(*qkT_made.upto(i))
                for a in (0, 64):
                    dve.tensor_copy(qz[a:a + 64].rearrange("p (g b) t -> p b g t", b=2)[:, a // 64],
                                    qkTp[a:a + 64, 0:256].rearrange("p (g t) -> p g t", g=2)).then_inc(*o.inc())
                dve.tensor_copy(kT[:], qkTp[:, 256:512].rearrange("p (g t) -> p g t", g=2)).then_inc(*qk_ready.inc())
                o.settle()
                dve.tensor_tensor(qw[:], qz[:], winter[:], ALU.mult).then_inc(*o.inc())
                dve.wait_ge(*sc_made.upto(i))
                dve.tensor_tensor(probs[:], scp[:].rearrange("p (h t) -> p h t", h=4), dmat[:], ALU.mult)\
                   .then_inc(*probs_ready.inc())
                dve.wait_ge(stored.sem, 16 * i + 1)
                dve.wait_ge(*gate_ready.upto(i))
                dve.wait_ge(*pd_made.upto(i))
                dve.tensor_tensor(cat[:, 512:1024], y0[:], gates[:, p, 512:1024], ALU.mult).then_inc(*od_ready.inc())
                dve.wait_ge(*o_made.upto(i))
                for g in range(4):
                    dve.bn_stats(st6[:, g, :], op[:, g * P:(g + 1) * P]).then_inc(*o.inc())
                o.settle()
                for g in range(4):
                    dve.bn_aggr(mv[:, g, :], st6[:, g, :]).then_inc(*(mv_ready if g == 3 else o).inc())
                dve.wait_ge(*U_made.upto(i))
                for g in range(2):
                    dve.scalar_tensor_tensor(S[:, g, :], S[:, g, :], gammac[:, g:g + 1], Up[:, g * P:(g + 1) * P],
                                             ALU.mult, ALU.add).then_inc(*(S_ready if g else o).inc())
                dve.wait_ge(*rs_ready.upto(i))
                for h in range(4):
                    dve.tensor_scalar(cat[:, h * P:(h + 1) * P], op[:, h * P:(h + 1) * P], mv[:, h, 0:1], rs[:, h:h + 1],
                                      ALU.subtract, ALU.mult).then_inc(*o.inc())
                o.settle()
                dve.tensor_tensor(cat[:, 0:512], cat[:, 0:512], gates[:, p, 0:512], ALU.mult).then_inc(*oc_ready.inc())
                dve.wait_ge(*y_made.upto(i))
                for half in range(2):
                    dve.scalar_tensor_tensor(cat[:, half * 512:(half + 1) * 512], xb[:, p, half * 512:(half + 1) * 512],
                                             ALPHA, (y0, y1)[half][:], ALU.mult, ALU.add)\
                       .then_inc(*(r_ready if half else o).inc())
                dve.wait_ge(*r_ready.upto(i))
                for half in range(2):
                    dve.bn_stats(lnst[:, half, :], cat[:, half * 512:(half + 1) * 512]).then_inc(*o.inc())
                o.settle()
                dve.bn_aggr(lnmv[:], lnst[:].rearrange("p a b -> p (a b)")).then_inc(*lnmv_ready.inc())
                dve.wait_ge(*lnrs_ready.upto(i))
                dve.tensor_scalar(cat[:], cat[:], lnmv[:, 0:1], lnrs[:, 0:1], ALU.subtract, ALU.mult)\
                   .then_inc(*lnn_ready.inc())
                o.end_block()

            over_blocks(dve, body)

        @block.gpsimd
        def _(pool):
            o = Order(pool, orders["pool"])
            pool.wait_ge(loaded.sem, NSMALL)
            pool.wait_ge(*setup.upto(0))

            def body(b):
                i, p = b.i, b.p
                x12 = qk[:, p, :].rearrange("p (h a j) -> p h a j", h=8, a=2)
                cs = over_heads(cos[:, bass.ds(i, 1), :].rearrange("p a j -> p (a j)"), 8)
                pool.wait_ge(*proj_ready.upto(i, 1))
                pool.wait_ge(*rot_ready.before(i))
                pool.tensor_tensor(ra[:], x12[:, :, 0, :], cs, ALU.mult).then_inc(*o.inc())
                pool.tensor_tensor(rd[:], x12[:, :, 1, :], cs, ALU.mult).then_inc(*rot_part.inc())
                pool.wait_ge(*rot_ready.upto(i))
                pool.tensor_tensor(kst[:].rearrange("p (h d) -> p h d", h=4), rot[:, 4:8, :], spread(wstate[:], 64), ALU.mult)\
                    .then_inc(*kst_ready.inc())
                pool.wait_ge(*gsig_ready.upto(i))
                pool.tensor_tensor(gates[:, p, :], gates[:, p, :], gt[:], ALU.mult).then_inc(*o.inc())
                o.settle()
                pool.tensor_tensor(gates[:, p, 0:512], gates[:, p, 0:512], ret_row[:], ALU.mult).then_inc(*o.inc())
                pool.tensor_tensor(gates[:, p, 512:1024], gates[:, p, 512:1024], scale_row[:], ALU.mult)\
                    .then_inc(*gate_ready.inc())
                pool.wait_ge(*lnn_ready.upto(i))
                pool.tensor_tensor(cat[:], cat[:], ln_grow[:], ALU.mult).then_inc(*o.inc())
                o.settle()
                pool.tensor_tensor(cat[:], cat[:], ln_brow[:], ALU.add).then_inc(*out_ready.inc())
                o.end_block()

            over_blocks(pool, body)


LEVELS = (1, 2, 4, 8, 16, 32)
QKV = 1536


def delta_layer(nc, x, c, w_ada, b_ada, g_pre, w_in, conv_w, a_log, dt_bias, g_gdn, g_post, consts, gate_row,
                hT_out, oa_out):
    ident_d, seg_d, big_d, lev_d = consts
    WA = 2056
    wv = w_in.rearrange("(k p) n -> p k n", p=P)
    with ExitStack() as ctx:
        sem = ctx.enter_context(Semaphores(nc, "d_"))

        def sb(name, shape, dt=F32):
            return ctx.enter_context(nc.sbuf_tensor("d_" + name, shape, dt))

        def sig(name, per=1):
            return Signal(sem(name), per)

        W_in = sb("w_in", [P, KT, WA])
        ada = sb("ada", [P, 2, 3 * D])
        ccol = sb("ccol", [P, KT])
        ctmp = sb("ctmp", [P, KT])
        cB = sb("cB", [P, KT, P])
        scale_row = sb("scale_row", [P, D])
        shift_row = sb("shift_row", [P, D])
        xb = sb("xb", [P, 2, D])
        hb = sb("hb", [P, D])
        hT = sb("hT", [P, KT * P])
        xss = sb("xss", [P, 1])
        xrs = sb("xrs", [P, 1])
        eps = sb("eps", [P, 1])
        cv = sb("cv", [P, 2, 12, P + 3])
        convw = sb("convw", [P, 4, 12])
        z = sb("z", [P, 2, 512])
        ba = sb("ba", [P, 2, 8])
        ident = sb("ident", [P, P])
        seg = sb("seg", [P, 4, P])
        big = sb("big", [P, 2, P])
        lev = sb("lev", [P, 6, P])
        eal = sb("eal", [P, 4])
        dtb = sb("dtb", [P, 4])
        gdn_row = sb("gdn_row", [P, P])
        cT = sb("cT", [P, 12, P])
        sg = sb("sg", [P, 12, P])
        ss = sb("ss", [P, 8])
        rs = sb("rs", [P, 8])
        beta = sb("beta", [P, 4])
        ya = sb("ya", [P, 4])
        yb = sb("yb", [P, 4])
        g = sb("g", [P, 4])
        gc = sb("gc", [P, 4])
        ngc = sb("ngc", [P, 4])
        egc = sb("egc", [P, 12])
        bg = sb("bg", [P, 4])
        eG = sb("eG", [P, 4, P])
        gU = sb("gU", [P, 4, P])
        D1 = sb("D1", [P, 4, P])
        D2 = sb("D2", [P, 4, P])
        qn = sb("qn", [P, 4, P])
        kn = sb("kn", [P, 4, P])
        kbg = sb("kbg", [P, 4, P])
        kg = sb("kg", [P, 4, P])
        vb = sb("vb", [P, 4, P])
        qT = sb("qT", [P, 4, P])
        kT = sb("kT", [P, 4, P])
        qgT = qn
        L = sb("L", [P, 4, P])
        Lm = sb("Lm", [P, 4, P])
        Lm2 = sb("Lm2", [P, 4, P])
        T = sb("T", [P, 4, P])
        R = sb("R", [P, 4, P])
        X = sb("X", [P, 4, P])
        attn = sb("attn", [P, 4, P])
        wT = sb("wT", [P, 4, P])
        u = sb("u", [P, 4, P])
        vnew = sb("vnew", [P, 4, P])
        S = sb("S", [P, 4, P])
        sgz = sb("sgz", [P, 512])
        gz = sb("gz", [P, 4, P])
        so = sb("so", [P, 4])
        ro = sb("ro", [P, 4])
        oa = sb("oa", [P, 512])
        ones = sb("ones", [P, P])
        bank = [ctx.enter_context(nc.psum_tensor(f"d_ps{n}", [P, 512], F32)) for n in range(8)]
        by_head = [b[:].rearrange("p (h t) -> p h t", h=4) for b in bank]

        loaded, aloaded = sig("loaded"), [sig("ada0"), sig("ada1")]
        w_parts = [(0, 512), (512, 512), (1024, 512), (QKV, WA - QKV)]
        w_loaded = [sig(f"w_in{n}") for n in range(len(w_parts))]
        c_ready, ada_used, mod_made, mod_ready = sig("c_ready", 3), sig("ada_used"), sig("mod_made"), sig("mod_ready", 3)
        x_in = [sig("x_in0"), sig("x_in1")]
        h_stored, oa_stored, setup = sig("h_stored"), sig("oa_stored"), sig("setup")
        xss_ready, hs_ready, h_ready = sig("xss"), sig("hs"), sig("h_ready")
        hT_made, hT_ready = sig("hT_made", 2), sig("hT_ready", 2)
        proj_made, proj_ready = sig("proj_made", 5), sig("proj_ready", 5)
        halo_ready, conv_ready, csig_ready, act_ready = sig("halo"), sig("conv"), sig("csig"), sig("silu")
        rows_made, sq_ready, ss_ready, rs_ready = sig("rows_made"), sig("sq"), sig("ss"), sig("rs")
        ba_ready, g_ready, gs_made, ge_ready, gU_ready, G_made = (
            sig("ba"), sig("g"), sig("gs_made"), sig("ge"), sig("gU"), sig("G_made"))
        D_ready, dec_ready, eG_ready = sig("D", 2), sig("dec", 2), sig("eG")
        qkn_ready, kg_ready, vb_ready = sig("qkn"), sig("kg"), sig("vb")
        qkT_made, qT_ready, kT_ready, qg_ready = sig("qkT_made"), sig("qT"), sig("kT"), sig("qg")
        kk_made, L_ready, attn_ready = sig("kk_made"), sig("L"), sig("attn")
        T_ready, T_turned, R_ready = sig("T"), sig("T_turned"), sig("R")
        Lm_ready, X_made, X_ready, RX_made, join_ready = sig("Lm", 5), sig("X_made", 5), sig("X", 5), sig("RX_made", 5), sig("join", 5)
        wu_made, wT_ready, u_ready = sig("wu_made"), sig("wT"), sig("u")
        wS_made, vnew_ready, U_made, S_ready = sig("wS_made", 2), sig("vnew", 2), sig("U_made", 2), sig("S", 2)
        o_made, so_ready, ro_ready, gz_ready, oa_ready = sig("o_made"), sig("so"), sig("ro"), sig("gz"), sig("oa")
        zsig_ready, osq_ready, sp_ready = sig("zsig"), sig("osq"), sig("sp")
        orders = {n: sem("order_" + n) for n in ("act", "dve", "pool")}

        started = [s.start() for s in (proj_ready, oa_ready, hT_made, h_stored, oa_stored)]
        block = ctx.enter_context(nc.Block())
        small = [(ccol[:], c.rearrange("(k p) -> p k", p=P)), (ident[:], ident_d), (seg[:], seg_d), (big[:], big_d),
                 (lev[:], lev_d), (eal[:], row(a_log)), (dtb[:], row(dt_bias)), (gdn_row[:], row(g_gdn)),
                 (shift_row[:], row(b_ada[0:D])), (scale_row[:], row(b_ada[D:2 * D])), (gate_row[:], row(b_ada[2 * D:3 * D])),
                 (xb[:, 0, :], row(g_pre)), (xb[:, 1, :], row(g_post))] + [
                 (convw[:, j, :], conv_w[j].rearrange("(k p) -> p k", p=P)) for j in range(4)]
        NSMALL = 16 * len(small)

        @block.sync
        def _(sp):
            for s in started:
                sp.sem_inc(s, 1)
            with nc.allow_non_contiguous_dma(reason="small tables"):
                for dst, src in small:
                    sp.dma_start(dst, src).then_inc(loaded.sem, 16)
            for k in range(KT):
                if k >= 2:
                    sp.wait_ge(ada_used.sem, k - 1)
                sp.dma_start(ada[:, k % 2, :], w_ada[k * P:(k + 1) * P, :]).then_inc(aloaded[k % 2].sem, 16)
            for (a, n), part in zip(w_parts, w_loaded):
                sp.dma_start(W_in[:, :, a:a + n], wv[:, :, a:a + n]).then_inc(part.sem, 16)
            sp.wait_ge(*mod_ready.upto(0))
            sp.dma_start(xb[:, 0, :], x[0:P, :]).then_inc(x_in[0].sem, 16)
            sp.dma_start(xb[:, 1, :], x[P:2 * P, :]).then_inc(x_in[1].sem, 16)
            sp.wait_ge(*hT_ready.upto(0))
            sp.dma_start(hT_out[0], hT[:]).then_inc(h_stored.sem, 16)
            sp.dma_start(xb[:, 0, :], x[2 * P:3 * P, :]).then_inc(x_in[0].sem, 16)

            def body(b, load=True, last=False):
                if not last:
                    sp.wait_ge(*hT_ready.upto(b.i + 1))
                    sp.dma_start(hT_out[b.i + 1], hT[:]).then_inc(h_stored.sem, 16)
                    if load:
                        sp.dma_start(xb[:, b.q, :], x[bass.ds(b.i * P + 3 * P, P), :]).then_inc(x_in[b.q].sem, 16)
                sp.wait_ge(*oa_ready.upto(b.i))
                sp.dma_start(oa_out[bass.ds(b.i * P, P), :], oa[:]).then_inc(oa_stored.sem, 16)

            with sp.Fori(0, 6) as r:
                body(Blk(r, 0))
                body(Blk(r, 1))
            body(Blk(6, 0))
            body(Blk(6, 1), load=False)
            body(Blk(7, 0), load=False)
            body(Blk(7, 1), load=False, last=True)
            sp.wait_ge(oa_stored.sem, 16 * BLOCKS + 1)
            sp.wait_ge(h_stored.sem, 16 * BLOCKS + 1)

        @block.tensor
        def _(pe):
            pe.wait_ge(*c_ready.upto(0))
            for k in range(KT):
                pe.wait_ge(aloaded[k % 2].sem, 16 * (k // 2) + 16)
                for n in range(6):
                    m = pe.matmul(bank[n][:], cB[:, k, :], ada[:, k % 2, n * 512:(n + 1) * 512], start=(k == 0), stop=(k == KT - 1))
                m.then_inc(*ada_used.inc())

            def turn_h(i):
                pe.wait_ge(*h_ready.upto(i))
                pe.wait_ge(*proj_ready.before(i))
                for half in range(2):
                    for k in range(4):
                        t = 4 * half + k
                        m = pe.transpose(bank[half][:, k * P:(k + 1) * P], hb[:, t * P:(t + 1) * P], ident[:])
                    m.then_inc(*hT_made.inc())

            def project(i, c):
                if c < 2:
                    pe.wait_ge(*hT_ready.upto(i))
                else:
                    pe.wait_ge(*proj_ready.upto(i, c - 1))
                if c < 3:
                    for t in range(4):
                        for k in range(KT):
                            m = pe.matmul(bank[c % 2][:, t * P:(t + 1) * P], W_in[:, k, (4 * c + t) * P:(4 * c + t + 1) * P],
                                          hT[:, k * P:(k + 1) * P], start=(k == 0), stop=(k == KT - 1))
                else:
                    a, n = ((QKV, 512), (2048, 8))[c - 3]
                    for k in range(KT):
                        m = pe.matmul(bank[c % 2][:, 0:n], hT[:, k * P:(k + 1) * P], W_in[:, k, a:a + n],
                                      start=(k == 0), stop=(k == KT - 1))
                m.then_inc(*proj_made.inc())

            pe.wait_ge(*mod_ready.upto(0))
            turn_h(0)
            for c_ in range(5):
                if c_ < 4:
                    pe.wait_ge(w_loaded[c_].sem, 16)
                project(0, c_)
            pe.wait_ge(*setup.upto(0))

            def body(b):
                i, p = b.i, b.p
                nxt = []
                if not b.last:
                    nxt = [lambda: turn_h(b.i + 1)] + [(lambda c=c: project(b.i + 1, c)) for c in range(5)]

                def fill():
                    if nxt:
                        nxt.pop(0)()

                pe.wait_ge(*oa_ready.before(i))
                pe.wait_ge(*g_ready.upto(i))
                for n in range(4):
                    m = pe.matmul(bank[7][:, 4 * n:4 * n + 4], seg[:, n, :], g[:], start=True, stop=True)
                m.then_inc(*gs_made.inc())
                pe.wait_ge(*gU_ready.upto(i))
                pe.matmul(bank[5][:], ones[:], gU[:].rearrange("p h t -> p (h t)"), start=True, stop=True).then_inc(*G_made.inc())
                fill()
                pe.wait_ge(*act_ready.upto(i))
                for n in range(12):
                    m = pe.transpose(bank[2 + n // 4][:, (n % 4) * P:(n % 4 + 1) * P], cT[:, n, :], ident[:])
                m.then_inc(*rows_made.inc())
                fill()
                pe.wait_ge(*qkn_ready.upto(i))
                for n in range(8):
                    m = pe.transpose(bank[2 + n // 4][:, (n % 4) * P:(n % 4 + 1) * P], (qn, kn)[n // 4][:, n % 4, :], ident[:])
                m.then_inc(*qkT_made.inc())
                pe.wait_ge(*kT_ready.upto(i))
                pe.wait_ge(*vb_ready.upto(i))
                for h in range(4):
                    pe.matmul(bank[4][:, h * P:(h + 1) * P], kT[:, h, :], kT[:, h, :], start=True, stop=True)
                pe.wait_ge(*qT_ready.upto(i))
                for h in range(4):
                    m = pe.matmul(bank[6][:, h * P:(h + 1) * P], kT[:, h, :], qT[:, h, :], start=True, stop=True)
                m.then_inc(*kk_made.inc())
                fill()
                pe.wait_ge(*T_ready.upto(i))
                for h in range(4):
                    m = pe.transpose(bank[5][:, h * P:(h + 1) * P], T[:, h, :], ident[:])
                m.then_inc(*T_turned.inc())
                pe.wait_ge(*R_ready.upto(i))
                for s in range(5):
                    pe.wait_ge(*Lm_ready.upto(i, s + 1))
                    if s:
                        pe.wait_ge(*join_ready.upto(i, s))
                    for h in range(4):
                        m = pe.matmul(bank[2][:, h * P:(h + 1) * P], (Lm, Lm2)[s % 2][:, h, :], R[:, h, :], start=True, stop=True)
                    m.then_inc(*X_made.inc())
                    if s in (1, 3):
                        fill()
                    pe.wait_ge(*X_ready.upto(i, s + 1))
                    for h in range(4):
                        m = pe.matmul(bank[3][:, h * P:(h + 1) * P], T[:, h, :], X[:, h, :], start=True, stop=True)
                    if s < 4:
                        for h in range(4):
                            m = pe.matmul(bank[5][:, h * P:(h + 1) * P], X[:, h, :], T[:, h, :], start=True, stop=True)
                    m.then_inc(*RX_made.inc())
                pe.wait_ge(*join_ready.upto(i))
                pe.wait_ge(*kg_ready.upto(i))
                pe.wait_ge(*attn_ready.upto(i))
                for h in range(4):
                    pe.matmul(bank[4][:, h * P:(h + 1) * P], kbg[:, h, :], R[:, h, :], start=True, stop=True)
                for h in range(4):
                    m = pe.matmul(bank[6][:, h * P:(h + 1) * P], R[:, h, :], vb[:, h, :], start=True, stop=True)
                m.then_inc(*wu_made.inc())
                fill()
                pe.wait_ge(*wT_ready.upto(i))
                pe.wait_ge(*qg_ready.upto(i))
                for n in range(2):
                    a = 64 * n
                    if n:
                        pe.wait_ge(*S_ready.upto(i, 1))
                    for h in range(4):
                        m = pe.matmul(bank[2][a:a + 64, h * P:(h + 1) * P], wT[:, h, a:a + 64], S[:, h, :], start=True, stop=True)
                    m.then_inc(*wS_made.inc())
                    for h in range(4):
                        pe.matmul(bank[7][a:a + 64, h * P:(h + 1) * P], qgT[:, h, a:a + 64], S[:, h, :],
                                  start=(h == 0), stop=False, skip_group_check=True)
                    pe.wait_ge(*vnew_ready.upto(i, n + 1))
                    for h in range(4):
                        m = pe.matmul(bank[3][:, h * P:(h + 1) * P], kg[a:a + 64, h, :], vnew[a:a + 64, h, :], start=True, stop=True)
                    m.then_inc(*U_made.inc())
                for h in range(4):
                    m = pe.matmul(bank[7][:, h * P:(h + 1) * P], attn[:, h, :], vnew[:, h, :], start=False, stop=True,
                                  skip_group_check=True)
                m.then_inc(*o_made.inc())
                while nxt:
                    fill()

            over_blocks(pe, body)

        @block.scalar
        def _(act):
            o = Order(act, orders["act"])
            act.preload_act_table_set(TABLES)

            def sigmoid(dst, src, done):
                act.activation(dst, src, ACT.Exp, scale=-1.0).then_inc(*o.inc())
                o.settle()
                act.activation(dst, dst, ACT.Ln, bias=1.0).then_inc(*o.inc())
                o.settle()
                act.activation(dst, dst, ACT.Exp, scale=-1.0).then_inc(*done.inc())

            act.wait_ge(loaded.sem, NSMALL)
            act.activation(eal[:], eal[:], ACT.Exp).then_inc(*o.inc())
            sigmoid(ctmp[:], ccol[:], c_ready)
            o.settle()

            def norm_x(p):
                act.activation(hb[:], xb[:, p, :], ACT.Square, accum_out=xss[:]).then_inc(*o.inc())
                o.settle()
                act.activation(xrs[:], xss[:], ACT.Ln, bias=eps[:, 0:1], scale=1.0 / D).then_inc(*o.inc())
                o.settle()
                act.activation(xrs[:], xrs[:], ACT.Exp, scale=-0.5).then_inc(*xss_ready.inc())

            def turn_h(i):
                act.wait_ge(h_stored.sem, 16 * i + 1)
                for half in range(2):
                    act.wait_ge(*hT_made.upto(i, half + 1))
                    act.activation(hT[:, half * 512:(half + 1) * 512], bank[half][:], ACT.Copy).then_inc(*hT_ready.inc())

            def project(i, p, c):
                act.wait_ge(*proj_made.upto(i, c + 1))
                if c < 3:
                    act.activation(cv[:, p, 4 * c:4 * c + 4, 3:P + 3], by_head[c % 2], ACT.Copy).then_inc(*proj_ready.inc())
                elif c == 3:
                    act.activation(z[:, p, :], bank[1][:], ACT.Copy).then_inc(*proj_ready.inc())
                else:
                    act.activation(ba[:, p, :], bank[0][:, 0:8], ACT.Copy).then_inc(*proj_ready.inc())

            act.wait_ge(*setup.upto(0))
            act.wait_ge(x_in[0].sem, 16)
            norm_x(0)
            turn_h(0)
            for c_ in range(5):
                project(0, 0, c_)
            o.end_block()

            def body(b):
                i, p = b.i, b.p
                nxt = []
                if not b.last:
                    nxt = [lambda: turn_h(b.i + 1)] + [(lambda c=c: project(b.i + 1, b.q, c)) for c in range(5)]

                def fill():
                    if nxt:
                        nxt.pop(0)()

                act.wait_ge(*oa_ready.before(i))
                act.wait_ge(*proj_ready.upto(i))
                act.wait_ge(*ba_ready.upto(i))
                act.activation(beta[:], ba[:, p, 0:4], ACT.Exp, scale=-1.0).then_inc(*o.inc())
                act.activation(yb[:], ya[:], ACT.Abs).then_inc(*o.inc())
                o.settle()
                act.activation(beta[:], beta[:], ACT.Ln, bias=1.0).then_inc(*o.inc())
                act.activation(yb[:], yb[:], ACT.Exp, scale=-1.0).then_inc(*o.inc())
                o.settle()
                act.activation(beta[:], beta[:], ACT.Exp, scale=-1.0).then_inc(*o.inc())
                act.activation(yb[:], yb[:], ACT.Ln, bias=1.0).then_inc(*sp_ready.inc())
                if not b.last:
                    act.wait_ge(x_in[b.q].sem, 16 * (b.r + p) + 16)
                    norm_x(b.q)
                act.wait_ge(*gs_made.upto(i))
                act.activation(gc[:], bank[7][:, 0:4], ACT.Copy).then_inc(*o.inc())
                act.activation(ngc[:], bank[7][:, 0:4], ACT.Copy, scale=-1.0).then_inc(*o.inc())
                act.activation(bg[:], bank[7][:, 0:4], ACT.Exp).then_inc(*o.inc())
                act.activation(egc[:], bank[7][:, 4:16], ACT.Exp).then_inc(*ge_ready.inc())
                act.wait_ge(*G_made.upto(i))
                act.activation(eG[:], by_head[5], ACT.Exp).then_inc(*eG_ready.inc())
                fill()
                act.wait_ge(*conv_ready.upto(i))
                sigmoid(sg[:], cT[:], csig_ready)
                act.wait_ge(*rows_made.upto(i))
                for n in range(2):
                    act.activation(sg[:, 4 * n:4 * n + 4, :], by_head[2 + n], ACT.Square)\
                        .then_inc(*(sq_ready if n else o).inc())
                act.wait_ge(*ss_ready.upto(i))
                act.activation(rs[:], ss[:], ACT.Ln, bias=eps[:, 0:1]).then_inc(*o.inc())
                o.settle()
                act.activation(rs[:], rs[:], ACT.Exp, scale=-0.5).then_inc(*rs_ready.inc())
                fill()
                act.wait_ge(*D_ready.upto(i))
                for h in range(4):
                    act.activation(D1[:, h, :], D1[:, h, :], ACT.Exp, scale=-1.0, bias=gc[:, h:h + 1])\
                        .then_inc(*(dec_ready if h == 3 else o).inc())
                for h in range(4):
                    act.activation(D2[:, h, :], D2[:, h, :], ACT.Exp, bias=ngc[:, h:h + 1])\
                        .then_inc(*(dec_ready if h == 3 else o).inc())
                act.wait_ge(*qkT_made.upto(i))
                act.activation(qT[:], by_head[2], ACT.Copy).then_inc(*qT_ready.inc())
                fill()
                act.wait_ge(*T_turned.upto(i))
                act.activation(R[:], by_head[5], ACT.Copy).then_inc(*R_ready.inc())
                for s in range(5):
                    act.wait_ge(*X_made.upto(i, s + 1))
                    act.activation(X[:], by_head[2], ACT.Copy).then_inc(*X_ready.inc())
                    if s in (1, 3):
                        fill()
                act.wait_ge(*wu_made.upto(i))
                act.activation(wT[:], by_head[4], ACT.Copy).then_inc(*wT_ready.inc())
                act.activation(u[:], by_head[6], ACT.Copy).then_inc(*u_ready.inc())
                sigmoid(sgz[:], z[:, p, :], zsig_ready)
                fill()
                act.wait_ge(*o_made.upto(i))
                act.activation(sg[:, 0:4, :], by_head[7], ACT.Square).then_inc(*osq_ready.inc())
                act.wait_ge(*so_ready.upto(i))
                act.activation(ro[:], so[:], ACT.Ln, bias=eps[:, 0:1], scale=1.0 / P).then_inc(*o.inc())
                o.settle()
                act.activation(ro[:], ro[:], ACT.Exp, scale=-0.5).then_inc(*ro_ready.inc())
                while nxt:
                    fill()
                o.end_block()

            over_blocks(act, body)

        @block.vector
        def _(dve):
            o = Order(dve, orders["dve"])
            dve.memset(S[:], 0.0).then_inc(*o.inc())
            dve.memset(eps[:], RMS_EPS).then_inc(*o.inc())
            dve.memset(ones[:], 1.0).then_inc(*o.inc())
            dve.memset(cv[:, 0, :, 0:3], 0.0).then_inc(*o.inc())
            o.settle()
            dve.wait_ge(*c_ready.upto(0, 1))
            dve.wait_ge(loaded.sem, NSMALL)
            dve.tensor_tensor(ctmp[:], ctmp[:], ccol[:], ALU.mult).then_inc(*c_ready.inc())
            dve.wait_ge(*c_ready.upto(0, 2))
            dve.tensor_copy(cB[:], spread(ctmp[:], P)).then_inc(*c_ready.inc())
            dve.wait_ge(ada_used.sem, KT)
            for n in range(6):
                dst = ((shift_row, scale_row, gate_row)[n // 2])[:, (n % 2) * 512:(n % 2 + 1) * 512]
                dve.tensor_tensor(dst, dst, bank[n][:], ALU.add).then_inc(*(mod_ready if n == 5 else o).inc())
            dve.wait_ge(*mod_ready.upto(0, 1))
            dve.scalar_tensor_tensor(scale_row[:], scale_row[:], 1.0, xb[:, 0, :], ALU.add, ALU.mult).then_inc(*mod_ready.inc())
            dve.tensor_tensor(gate_row[:], gate_row[:], xb[:, 1, :], ALU.mult).then_inc(*mod_ready.inc())
            dve.wait_ge(*mod_ready.upto(0))
            dve.tensor_scalar_mul(eal[:], eal[:], -1.0).then_inc(*setup.inc())

            def make_h(i, p):
                dve.wait_ge(*hT_made.before(i))
                dve.wait_ge(*xss_ready.upto(i))
                dve.scalar_tensor_tensor(hb[:], xb[:, p, :], xrs[:, 0:1], scale_row[:], ALU.mult, ALU.mult)\
                   .then_inc(*hs_ready.inc())

            make_h(0, 0)
            o.end_block()

            def body(b):
                i, p = b.i, b.p
                dve.wait_ge(*proj_ready.upto(i))
                dve.tensor_tensor(ya[:], ba[:, p, 4:8], dtb[:], ALU.add).then_inc(*ba_ready.inc())
                if not b.last:
                    dve.tensor_copy(cv[:, b.q, :, 0:3], cv[:, p, :, P:P + 3]).then_inc(*o.inc())
                for t in range(12):
                    dve.tensor_scalar(cT[:, t, :], cv[:, p, t, 0:P], convw[:, 0, t:t + 1], None, ALU.mult).then_inc(*o.inc())
                for j in range(1, 4):
                    o.settle()
                    for t in range(12):
                        dve.scalar_tensor_tensor(cT[:, t, :], cv[:, p, t, j:j + P], convw[:, j, t:t + 1], cT[:, t, :],
                                                 ALU.mult, ALU.add).then_inc(*(conv_ready if j == 3 and t == 11 else o).inc())
                dve.wait_ge(*sp_ready.upto(i))
                dve.scalar_tensor_tensor(g[:], ya[:], 0.0, yb[:], ALU.max, ALU.add).then_inc(*o.inc())
                o.settle()
                dve.tensor_tensor(g[:], g[:], eal[:], ALU.mult).then_inc(*g_ready.inc())
                if not b.last:
                    make_h(b.i + 1, b.q)
                dve.wait_ge(*ge_ready.upto(i))
                dve.tensor_tensor(bg[:], bg[:], beta[:], ALU.mult).then_inc(*o.inc())
                dve.wait_ge(*eG_ready.upto(i))
                dve.tensor_tensor(D1[:], by_head[5], over_heads(big[:, 0, :], 4), ALU.add).then_inc(*D_ready.inc())
                dve.tensor_tensor(D2[:], by_head[5], over_heads(big[:, 1, :], 4), ALU.subtract).then_inc(*D_ready.inc())
                dve.wait_ge(*csig_ready.upto(i))
                dve.tensor_tensor(cT[:], cT[:], sg[:], ALU.mult).then_inc(*act_ready.inc())
                dve.wait_ge(*sq_ready.upto(i))
                dve.tensor_reduce(ss[:], sg[:, 0:8, :], AX.X, ALU.add).then_inc(*ss_ready.inc())
                dve.tensor_tensor(vb[:], by_head[4], spread(beta[:], P), ALU.mult).then_inc(*vb_ready.inc())
                dve.wait_ge(*rs_ready.upto(i))
                dve.tensor_scalar_mul(rs[:, 0:4], rs[:, 0:4], float(P) ** -0.5).then_inc(*o.inc())
                dve.tensor_tensor(kn[:], by_head[3], spread(rs[:, 4:8], P), ALU.mult).then_inc(*o.inc())
                o.settle()
                dve.tensor_tensor(qn[:], by_head[2], spread(rs[:, 0:4], P), ALU.mult).then_inc(*qkn_ready.inc())
                dve.wait_ge(*qkT_made.upto(i))
                dve.tensor_copy(kT[:], by_head[3]).then_inc(*kT_ready.inc())
                dve.wait_ge(*dec_ready.upto(i))
                dve.wait_ge(*kk_made.upto(i))
                for h in range(4):
                    dve.scalar_tensor_tensor(L[:, h, :], by_head[4][:, h, :], beta[:, h:h + 1], D1[:, h, :],
                                             ALU.mult, ALU.mult).then_inc(*(L_ready if h == 3 else o).inc())
                dve.wait_ge(*L_ready.upto(i))
                dve.tensor_tensor(T[:], L[:], over_heads(lev[:, 0, :], 4), ALU.mult).then_inc(*o.inc())
                o.settle()
                dve.tensor_tensor(T[:], over_heads(ident[:], 4), T[:], ALU.subtract).then_inc(*T_ready.inc())
                dve.tensor_tensor(attn[:], by_head[6], D2[:], ALU.mult).then_inc(*attn_ready.inc())
                dve.wait_ge(*R_ready.upto(i))
                for s in range(5):
                    dve.wait_ge(*RX_made.upto(i, s + 1))
                    if s < 4:
                        dve.tensor_tensor(T[:], T[:], by_head[5], ALU.subtract).then_inc(*o.inc())
                    dve.tensor_tensor(R[:], R[:], by_head[3], ALU.subtract).then_inc(*join_ready.inc())
                    dve.wait_ge(*join_ready.upto(i, s + 1))
                dve.wait_ge(*u_ready.upto(i))
                for n in range(2):
                    a = 64 * n
                    dve.wait_ge(*wS_made.upto(i, n + 1))
                    dve.tensor_tensor(vnew[a:a + 64], u[a:a + 64], by_head[2][a:a + 64], ALU.subtract).then_inc(*vnew_ready.inc())
                    dve.wait_ge(*U_made.upto(i, n + 1))
                    for h in range(4):
                        dve.scalar_tensor_tensor(S[:, h, :], S[:, h, :], egc[:, 4 + 4 * n + h:5 + 4 * n + h],
                                                 by_head[3][:, h, :], ALU.mult, ALU.add)\
                           .then_inc(*(S_ready if h == 3 else o).inc())
                    dve.wait_ge(*S_ready.upto(i, n + 1))
                dve.wait_ge(*osq_ready.upto(i))
                dve.tensor_reduce(so[:], sg[:, 0:4, :], AX.X, ALU.add).then_inc(*so_ready.inc())
                dve.wait_ge(*ro_ready.upto(i))
                dve.wait_ge(*gz_ready.upto(i))
                dve.wait_ge(oa_stored.sem, 16 * i + 1)
                for h in range(4):
                    dve.scalar_tensor_tensor(oa[:, h * P:(h + 1) * P], by_head[7][:, h, :], ro[:, h:h + 1], gz[:, h, :],
                                             ALU.mult, ALU.mult).then_inc(*(oa_ready if h == 3 else o).inc())
                o.end_block()

            over_blocks(dve, body)

        @block.gpsimd
        def _(pool):
            o = Order(pool, orders["pool"])
            pool.wait_ge(loaded.sem, NSMALL)
            pool.wait_ge(*mod_ready.upto(0))

            def shift_h(i):
                pool.wait_ge(*hs_ready.upto(i))
                pool.tensor_tensor(hb[:], hb[:], shift_row[:], ALU.add).then_inc(*h_ready.inc())

            shift_h(0)

            def body(b):
                i, p = b.i, b.p
                pool.wait_ge(*oa_ready.before(i))
                pool.wait_ge(*g_ready.upto(i))
                pool.tensor_tensor(gU[:], over_heads(seg[:, 0, :], 4), spread(g[:], P), ALU.mult).then_inc(*gU_ready.inc())
                if not b.last:
                    shift_h(b.i + 1)
                pool.wait_ge(*qkn_ready.upto(i))
                pool.tensor_tensor(kbg[:], kn[:], spread(bg[:], P), ALU.mult).then_inc(*o.inc())
                pool.tensor_tensor(kg[:], kn[:], spread(egc[:, 0:4], P), ALU.mult).then_inc(*kg_ready.inc())
                pool.wait_ge(*L_ready.upto(i))
                for s in range(5):
                    if s >= 2:
                        pool.wait_ge(*X_made.upto(i, s - 1))
                    pool.tensor_tensor((Lm, Lm2)[s % 2][:], L[:], over_heads(lev[:, s + 1, :], 4), ALU.mult)\
                        .then_inc(*Lm_ready.inc())
                    if s == 1:
                        pool.wait_ge(*qT_ready.upto(i))
                        pool.wait_ge(*eG_ready.upto(i))
                        pool.tensor_tensor(qgT[:], qT[:], eG[:], ALU.mult).then_inc(*qg_ready.inc())
                pool.wait_ge(*zsig_ready.upto(i))
                pool.tensor_tensor(sgz[:], sgz[:], z[:, p, :], ALU.mult).then_inc(*o.inc())
                o.settle()
                pool.tensor_tensor(gz[:], sgz[:].rearrange("p (h t) -> p h t", h=4), over_heads(gdn_row[:], 4), ALU.mult)\
                    .then_inc(*gz_ready.inc())
                o.end_block()

            over_blocks(pool, body)


IDX_HEADS, IDX_DIM = 8, 64
TOPK = 256
N_BUCKETS = 32
WIDE = 512
ROUNDS = 14
FIRST_TOPK = TOPK // P
FAR = 1e30


def key_chunks(i):
    return [(a, min(WIDE, (i + 1) * P - a)) for a in range(0, (i + 1) * P, WIDE)]


class Varied(Signal):

    def __init__(self, sem, counts):
        self.sem, self.counts, self.first = sem, counts, 0

    def upto(self, i, k=None):
        return self.sem, sum(self.counts[:i]) + (self.counts[i] if k is None else k)


def sparse_layer(nc, x, w_in, g_kv, w_uv, rel_bias, w_out, consts, gate_row, hT_in, oa_in, bias_scratch, out):
    ident_d, flip_d, late_d, onehot_d, iota_d, halves_d = consts
    C0 = 2056
    O_QB, O_CKV, O_Z, O_IQ, O_IK, O_IW = 0, 512, 640, 1152, 1664, 1792
    WB = 1800
    wv = w_in.rearrange("(k p) n -> p k n", p=P)
    with ExitStack() as ctx:
        sem = ctx.enter_context(Semaphores(nc, "s_"))

        def sb(name, shape, dt=F32):
            return ctx.enter_context(nc.sbuf_tensor("s_" + name, shape, dt))

        def sig(name, per=1):
            return Signal(sem(name), per)

        W_in = sb("w_in", [P, KT, WB])
        W_out = sb("w_out", [P, KT, D])
        ikT = sb("ikT", [P, SEQ])
        ckvT = sb("ckvT", [P, SEQ])
        ckvr = sb("ckvr", [P, BLOCKS, P])
        hT = sb("hT", [P, KT * P])
        pT = sb("pT", [P, 4, 4, P])
        Lg = sb("Lg", [P, 2, SEQ])
        acc = sb("acc", [P, SEQ])
        selb = sb("selb", [P, SEQ])
        passed = sb("passed", [P, SEQ], BF16)
        cat = sb("cat", [P, D])
        catT = sb("catT", [P, D])
        xb = sb("xb", [P, D])
        sgz = sb("sgz", [P, 512])
        iqT = sb("iqT", [P, 4, P])
        qbT = sb("qbT", [P, 2, 4, P])
        z = sb("z", [P, 2, 512])
        ckv = sb("ckv", [P, P])
        iw = sb("iw", [P, IDX_HEADS])
        ident = sb("ident", [P, P])
        flip = sb("flip", [P, P])
        late = sb("late", [P, P])
        onehot = sb("onehot", [N_BUCKETS, 384])
        rb = sb("rb", [N_BUCKETS, 4])
        rb31 = sb("rb31", [N_BUCKETS, 4])
        bias = sb("bias", [P, 4, 2 * P])
        vec = sb("vec", [4, 384])
        iota = sb("iota", [P, 8])
        halves = sb("halves", [P, ROUNDS + 1])
        kv_row = sb("kv_row", [P, P])
        uv = sb("uv", [P, 4, P])
        ones = sb("ones", [P, 1])
        eps = sb("eps", [P, 1])
        css = sb("css", [P, 1])
        crs = sb("crs", [P, 1])
        cn = sb("cn", [P, P])
        csq = sb("csq", [P, P])
        lo = sb("lo", [P, 1])
        hi = sb("hi", [P, 1])
        mid = sb("mid", [P, 1])
        cnt = sb("cnt", [P, 1])
        step = sb("step", [P, 1])
        steps = sb("steps", [P, ROUNDS + 1])
        best = sb("best", [P, 8])
        match = sb("match", [P, 8])
        thr = sb("thr", [P, 1])
        bad = sb("bad", [P, 2])
        nbad = sb("nbad", [1, 2], I32)
        mx = sb("mx", [P, 4])
        psum_ = sb("psums", [P, 4])
        prec = sb("prec", [P, 4])
        oT = sb("oT", [P, 4, P])
        mss = sb("mss", [P, 2])
        mrs = sb("mrs", [P, 1])
        squares = catT
        relu = Lg[:, 1, :].rearrange("p (n c) -> p n c", n=4)
        work, other = Lg[:, 0, :], pT[:].rearrange("p n b t -> p (n b t)")
        bank = [ctx.enter_context(nc.psum_tensor(f"s_ps{n}", [P, 512], F32)) for n in range(8)]
        by_head = [b[:].rearrange("p (h t) -> p h t", h=4) for b in bank]
        LG_BANKS, IDX_BANKS = (2, 3, 4), (2, 3, 5, 4)

        pieces = [len(key_chunks(i)) for i in range(BLOCKS)]
        scored = [8 * n if i >= FIRST_TOPK else 0 for i, n in enumerate(pieces)]
        loaded, loaded2, wout_loaded = sig("loaded"), sig("loaded2"), sig("w_out")
        w_parts = [[(O_IQ, C0 + O_IQ, 576)], [(O_CKV, C0 + O_CKV, 128), (O_IK + 64, C0 + O_IK, 72)],
                   [(O_QB, C0 + O_QB, 512)], [(O_Z, C0 + O_Z, 512)]]
        w_loaded = [sig(f"w_in{n}") for n in range(len(w_parts))]
        h_in, x_in, oa_in_s, stored = sig("h_in"), sig("x_in"), sig("oa_in"), sig("stored")
        rb_ready, vec_made, vec_ready, vec_stored, bias_made, bias_ready = (
            sig("rb"), sig("vec_made"), sig("vec"), sig("vec_stored"), sig("bias_made", 2), sig("bias", 2))
        proj_made, proj_ready = sig("proj_made", 4), sig("proj_ready", 4)
        crs_ready, cn_ready, ckvr_ready, cT_made, cT_ready = sig("crs"), sig("cn"), sig("ckvr"), sig("cT_made"), sig("cT")
        idx_made, relu_ready, relu_used = (Varied(sem(n), scored) for n in ("idx_made", "relu", "relu_used"))
        found = [1 if i >= FIRST_TOPK else 0 for i in range(BLOCKS)]
        bad_ready, nbad_made, nbad_ready = (Varied(sem(n), found) for n in ("bad", "nbad_made", "nbad"))
        eps_ready, selb_ready = sig("eps"), sig("selb")
        lg_made, lg_read, pt_made, pt_ready, pv_made = (
            Varied(sem(n), [4 * n for n in pieces]) for n in ("lg_made", "lg_read", "pt_made", "pt", "pv_made"))
        mx_ready, exp_ready = sig("mx", 4), sig("exp", 4)
        zsig_ready, gz_ready, oT_ready, uv_made, ob_ready = sig("zsig"), sig("gz"), sig("oT"), sig("uv_made"), sig("ob")
        catT_made, catT_ready, y_made, mss_ready, mrs_ready, mix_ready, out_ready = (
            sig("catT_made", 2), sig("catT", 2), sig("y_made"), sig("mss"), sig("mrs"), sig("mix"), sig("out_ready"))
        branch = sem("branch")
        orders = {n: sem("order_" + n) for n in ("act", "dve", "pool")}

        block = ctx.enter_context(nc.Block())
        small = [(rb[:], rel_bias), (rb31[:], row(rel_bias[N_BUCKETS - 1], N_BUCKETS)), (onehot[:], onehot_d),
                 (flip[:], flip_d), (ident[:], ident_d), (late[:], late_d), (iota[:], iota_d),
                 (halves[:], halves_d), (kv_row[:], row(g_kv)), (uv[:], w_uv.rearrange("h r d -> r h d"))]
        NSMALL = 16 * len(small)

        @block.sync
        def _(sp):
            with nc.allow_non_contiguous_dma(reason="small tables"):
                for dst, src in small:
                    sp.dma_start(dst, src).then_inc(loaded.sem, 16)
                sp.dma_start(hT[:], hT_in[0]).then_inc(h_in.sem, 16)
                for part, ready in zip(w_parts, w_loaded):
                    for to, a, n in part:
                        sp.dma_start(W_in[:, :, to:to + n], wv[:, :, a:a + n]).then_inc(ready.sem, 16)
                sp.dma_start(W_out[:], w_out.rearrange("(k p) n -> p k n", p=P)).then_inc(wout_loaded.sem, 16)
                sp.wait_ge(*vec_ready.upto(0))
                sp.dma_start(bias_scratch, vec[:]).then_inc(vec_stored.sem, 16)
                sp.wait_ge(vec_stored.sem, 16)
                for h in range(4):
                    src = bias_scratch[h]
                    src = bass.AP(src.tensor, src.offset, [[1, P], [1, 2 * P]])
                    sp.dma_start(acc[:, h * 2 * P:(h + 1) * 2 * P], src).then_inc(loaded2.sem, 16)
            sp.wait_ge(*proj_ready.upto(0))
            sp.dma_start(hT[:], hT_in[1]).then_inc(h_in.sem, 16)
            for i in range(BLOCKS):
                sp.dma_start(xb[:], x[i * P:(i + 1) * P, :]).then_inc(x_in.sem, 16)
                sp.dma_start(cat[:, 0:512], oa_in[i * P:(i + 1) * P, :]).then_inc(oa_in_s.sem, 16)
                if i + 2 < BLOCKS:
                    sp.wait_ge(*proj_ready.upto(i + 1))
                    sp.dma_start(hT[:], hT_in[i + 2]).then_inc(h_in.sem, 16)
                sp.wait_ge(*out_ready.upto(i))
                sp.dma_start(out[i * P:(i + 1) * P, :], xb[:]).then_inc(stored.sem, 16)
                sp.wait_ge(stored.sem, 16 * (i + 1))

        @block.tensor
        def _(pe):
            def tile_of(c, t):
                a = (O_IQ, O_IK, O_QB)[c] + t * P
                return slice(a, a + P)

            def project(i, c):
                if i >= BLOCKS:
                    return
                if c == 0:
                    pe.wait_ge(h_in.sem, 16 * i + 16)
                if 4 * i + c >= 2:
                    pe.wait_ge(*proj_ready.upto(0, 4 * i + c - 1))
                out_ = bank[c % 2]
                if c < 3:
                    for t in range((4, 1, 4)[c]):
                        for k in range(KT):
                            m = pe.matmul(out_[:, t * P:(t + 1) * P], W_in[:, k, tile_of(c, t)], hT[:, k * P:(k + 1) * P],
                                          start=(k == 0), stop=(k == KT - 1))
                for a, n, at in {1: [(O_CKV, P, P), (O_IW, 8, 2 * P)], 3: [(O_Z, 512, 0)]}.get(c, []):
                    for k in range(KT):
                        m = pe.matmul(out_[:, at:at + n], hT[:, k * P:(k + 1) * P], W_in[:, k, a:a + n],
                                      start=(k == 0), stop=(k == KT - 1))
                m.then_inc(*proj_made.inc())

            def transpose_ckv(i):
                if i >= BLOCKS:
                    return
                pe.wait_ge(*cn_ready.upto(i))
                pe.transpose(bank[4][:, 0:P], cn[:], ident[:]).then_inc(*cT_made.inc())

            pe.wait_ge(loaded.sem, NSMALL)
            pe.wait_ge(*rb_ready.upto(0))
            pe.matmul(bank[2][0:4, 0:384], rb[:], onehot[:], start=True, stop=True).then_inc(*vec_made.inc())
            for c in range(4):
                pe.wait_ge(w_loaded[c].sem, 16 * len(w_parts[c]))
                project(0, c)
            pe.wait_ge(loaded2.sem, 64)
            for n in range(2):
                pe.matmul(bank[3 + n][:], flip[:], acc[:, n * 512:(n + 1) * 512], start=True, stop=True).then_inc(*bias_made.inc())
            pe.wait_ge(*bias_ready.upto(0))
            transpose_ckv(0)
            for c in range(4):
                project(1, c)
            pe.wait_ge(*cT_ready.upto(0))
            transpose_ckv(1)
            pe.wait_ge(wout_loaded.sem, 16)

            for i in range(BLOCKS):
                n_pieces = pieces[i]
                pe.wait_ge(*cT_ready.upto(min(i + 1, BLOCKS - 1)))
                pe.wait_ge(*ckvr_ready.upto(i))
                pe.wait_ge(*proj_ready.upto(i))
                if FIRST_TOPK <= i + 1 < BLOCKS:
                    pe.wait_ge(*relu_ready.upto(i + 1))
                if i >= FIRST_TOPK:
                    pe.wait_ge(*nbad_ready.upto(i))

                def logits(h):
                    for c, (a, w) in enumerate(key_chunks(i)):
                        n = h * n_pieces + c
                        if n >= 3:
                            pe.wait_ge(*lg_read.upto(i, n - 2))
                        pe.matmul(bank[LG_BANKS[n % 3]][:, 0:w], qbT[:, i % 2, h, :], ckvT[:, a:a + w],
                                  start=True, stop=True).then_inc(*lg_made.inc())

                def transpose(h, c):
                    n = h * n_pieces + c
                    if n >= 2:
                        pe.wait_ge(*pt_ready.upto(i, n - 1))
                    a, w = key_chunks(i)[c]
                    for t in range(w // P):
                        m = pe.transpose(bank[6 + n % 2][:, t * P:(t + 1) * P], Lg[:, h % 2, a + t * P:a + (t + 1) * P], ident[:])
                    m.then_inc(*pt_made.inc())

                def values(h, c):
                    n = h * n_pieces + c
                    pe.wait_ge(*pt_ready.upto(i, n + 1))
                    a, w = key_chunks(i)[c]
                    for t in range(w // P):
                        m = pe.matmul(bank[5][:, h * P:(h + 1) * P], ckvr[:, a // P + t, :], pT[:, n % 4, t, :],
                                      start=(c == 0 and t == 0), stop=(a + (t + 1) * P == (i + 1) * P))
                    m.then_inc(*pv_made.inc())

                logits(0)
                for h in range(4):
                    if h < 3:
                        logits(h + 1)
                    if h in (0, 1):
                        project(i + 2, h)
                    if h == 3:
                        project(i + 2, 2)
                    if h == 0 and i:
                        pe.wait_ge(*mix_ready.upto(i - 1))
                    pe.wait_ge(*exp_ready.upto(i, h + 1))
                    transpose(h, 0)
                    for c in range(n_pieces):
                        if c + 1 < n_pieces:
                            transpose(h, c + 1)
                        values(h, c)
                pe.wait_ge(oa_in_s.sem, 16 * i + 16)
                pe.wait_ge(*lg_read.upto(i))
                for half in range(2):
                    if half:
                        pe.wait_ge(*oT_ready.upto(i))
                        for h in range(4):
                            m = pe.matmul(bank[5][:, h * P:(h + 1) * P], oT[:, h, :], uv[:, h, :], start=True, stop=True)
                        m.then_inc(*uv_made.inc())
                        transpose_ckv(i + 2)
                        pe.wait_ge(*ob_ready.upto(i))
                    for k in range(4):
                        t = 4 * half + k
                        m = pe.transpose(bank[2 + half][:, k * P:(k + 1) * P], cat[:, t * P:(t + 1) * P], ident[:])
                    m.then_inc(*catT_made.inc())
                project(i + 2, 3)
                pe.wait_ge(*catT_ready.upto(i))
                for half in range(2):
                    for k in range(KT):
                        m = pe.matmul(bank[6 + half][:], catT[:, k * P:(k + 1) * P],
                                      W_out[:, k, half * 512:(half + 1) * 512], start=(k == 0), stop=(k == KT - 1))
                m.then_inc(*y_made.inc())
                if FIRST_TOPK <= i + 1 < BLOCKS:
                    pe.wait_ge(*cT_ready.upto(min(i + 2, BLOCKS - 1)))
                    pe.wait_ge(*bad_ready.upto(i + 1))
                    pe.matmul(bank[4][0:1, 0:2], ones[:], bad[:], start=True, stop=True).then_inc(*nbad_made.inc())
                if i + 2 < BLOCKS:
                    pe.wait_ge(*proj_ready.upto(i + 2, 2))
                    for n in range(scored[i + 2]):
                        (a, w), h = key_chunks(i + 2)[n // 8], n % 8
                        o = 64 * (h % 2)
                        if n >= 4:
                            pe.wait_ge(*relu_ready.upto(i + 2, n - 3))
                        if n == 3:
                            pe.wait_ge(*cT_ready.upto(i + 2))
                            if FIRST_TOPK <= i + 1:
                                pe.wait_ge(*nbad_ready.upto(i + 1))
                        pe.matmul(bank[IDX_BANKS[n % 4]][:, 0:w], iqT[o:o + 64, h // 2, :], ikT[o:o + 64, a:a + w],
                                  start=True, stop=True).then_inc(*idx_made.inc())

        @block.scalar
        def _(act):
            o = Order(act, orders["act"])
            act.preload_act_table_set(TABLES)

            def project(i, c):
                if i >= BLOCKS:
                    return
                act.wait_ge(*proj_made.upto(i, c + 1))
                if c == 0:
                    act.activation(iqT[:], by_head[0], ACT.Copy).then_inc(*proj_ready.inc())
                elif c == 1:
                    act.activation(ikT[:, i * P:(i + 1) * P], bank[1][:, 0:P], ACT.Copy).then_inc(*o.inc())
                    act.activation(ckv[:], bank[1][:, P:2 * P], ACT.Copy).then_inc(*o.inc())
                    act.activation(iw[:], bank[1][:, 2 * P:2 * P + 8], ACT.Copy,
                                   scale=IDX_HEADS ** -0.5 * IDX_DIM ** -0.5).then_inc(*o.inc())
                    o.settle()
                    act.activation(csq[:], ckv[:], ACT.Square, accum_out=css[:]).then_inc(*proj_ready.inc())
                    act.wait_ge(*proj_ready.upto(i, 2))
                    act.activation(crs[:], css[:], ACT.Ln, bias=eps[:, 0:1], scale=1.0 / P).then_inc(*o.inc())
                    o.settle()
                    act.activation(crs[:], crs[:], ACT.Exp, scale=-0.5).then_inc(*crs_ready.inc())
                elif c == 2:
                    act.activation(qbT[:, i % 2], by_head[0], ACT.Copy).then_inc(*proj_ready.inc())
                else:
                    act.activation(z[:, i % 2, :], bank[1][:], ACT.Copy).then_inc(*proj_ready.inc())

            def copy_ckvT(i):
                if i >= BLOCKS:
                    return
                act.wait_ge(*cT_made.upto(i))
                act.activation(ckvT[:, i * P:(i + 1) * P], bank[4][:, 0:P], ACT.Copy).then_inc(*cT_ready.inc())

            act.wait_ge(*eps_ready.upto(0))
            for i in range(2):
                for c in range(4):
                    project(i, c)
                copy_ckvT(i)
            o.end_block()

            for i in range(BLOCKS):
                n_pieces = pieces[i]
                act.wait_ge(*proj_ready.upto(i))
                if i:
                    act.wait_ge(*gz_ready.upto(i - 1))
                act.activation(sgz[:], z[:, i % 2, :], ACT.Exp, scale=-1.0).then_inc(*o.inc())
                o.settle()
                act.activation(sgz[:], sgz[:], ACT.Ln, bias=1.0).then_inc(*o.inc())
                o.settle()
                act.activation(sgz[:], sgz[:], ACT.Exp, scale=-1.0).then_inc(*zsig_ready.inc())
                for h in range(4):
                    act.wait_ge(*mx_ready.upto(i, h + 1))
                    act.activation(Lg[:, h % 2, 0:(i + 1) * P], Lg[:, h % 2, 0:(i + 1) * P], ACT.Exp, bias=mx[:, h:h + 1],
                                   accum_out=psum_[:, h:h + 1]).then_inc(*exp_ready.inc())
                    if h in (0, 1):
                        project(i + 2, h)
                    if h == 3:
                        project(i + 2, 2)
                    for c, (a, w) in enumerate(key_chunks(i)):
                        n = h * n_pieces + c
                        act.wait_ge(*pt_made.upto(i, n + 1))
                        if n >= 4:
                            act.wait_ge(*pv_made.upto(i, n - 3))
                        act.activation(pT[:, n % 4, 0:w // P, :], by_head[6 + n % 2][:, 0:w // P, :], ACT.Copy)\
                           .then_inc(*pt_ready.inc())
                act.wait_ge(*catT_made.upto(i, 1))
                act.activation(catT[:, 0:512], bank[2][:], ACT.Copy).then_inc(*catT_ready.inc())
                act.wait_ge(*pv_made.upto(i))
                act.activation(oT[:], by_head[5], ACT.Copy).then_inc(*oT_ready.inc())
                copy_ckvT(i + 2)
                act.wait_ge(*catT_made.upto(i))
                act.activation(catT[:, 512:1024], bank[3][:], ACT.Copy).then_inc(*catT_ready.inc())
                project(i + 2, 3)
                act.wait_ge(*y_made.upto(i))
                for half in range(2):
                    act.activation(squares[:, half * 512:(half + 1) * 512], bank[6 + half][:], ACT.Square,
                                   accum_out=mss[:, half:half + 1]).then_inc(*(mss_ready if half else o).inc())
                act.wait_ge(*mss_ready.upto(i))
                act.activation(mss[:, 0:1], mss[:, 0:1], ACT.Identity, bias=mss[:, 1:2]).then_inc(*o.inc())
                o.settle()
                act.activation(mrs[:], mss[:, 0:1], ACT.Ln, bias=eps[:, 0:1], scale=1.0 / D).then_inc(*o.inc())
                o.settle()
                act.activation(mrs[:], mrs[:], ACT.Exp, scale=-0.5).then_inc(*mrs_ready.inc())
                if i + 2 < BLOCKS:
                    for n in range(scored[i + 2]):
                        w = key_chunks(i + 2)[n // 8][1]
                        act.wait_ge(*idx_made.upto(i + 2, n + 1))
                        if n >= 4:
                            act.wait_ge(*relu_used.upto(i + 2, n - 3))
                        act.activation(relu[:, n % 4, 0:w], bank[IDX_BANKS[n % 4]][:, 0:w], ACT.Relu).then_inc(*relu_ready.inc())
                o.end_block()

        @block.vector
        def _(dve):
            o = Order(dve, orders["dve"])
            dve.memset(eps[:], RMS_EPS).then_inc(*eps_ready.inc())
            dve.memset(ones[:], 1.0).then_inc(*o.inc())
            dve.wait_ge(loaded.sem, NSMALL)
            dve.tensor_tensor(rb[:], rb[:], rb31[:], ALU.subtract).then_inc(*rb_ready.inc())
            dve.wait_ge(*vec_made.upto(0))
            dve.tensor_copy(vec[:], bank[2][0:4, 0:384]).then_inc(*vec_ready.inc())
            for n in range(2):
                dve.wait_ge(*bias_made.upto(0, n + 1))
                dve.tensor_copy(bias[:, 2 * n:2 * n + 2, :].rearrange("p h c -> p (h c)"), bank[3 + n][:]).then_inc(*bias_ready.inc())

            def do(instruction):
                instruction.then_inc(*o.inc())
                o.settle()

            def normalise_ckv(i):
                if i >= BLOCKS:
                    return
                dve.wait_ge(*crs_ready.upto(i))
                if i:
                    dve.wait_ge(*cT_made.upto(i - 1))
                    dve.wait_ge(*ckvr_ready.upto(i - 1))
                dve.scalar_tensor_tensor(cn[:], ckv[:], crs[:, 0:1], kv_row[:], ALU.mult, ALU.mult).then_inc(*cn_ready.inc())

            normalise_ckv(0)
            normalise_ckv(1)
            do(dve.tensor_copy(selb[:, 0:P], late[:]))
            dve.tensor_copy(lo[:], ones[:]).then_inc(*selb_ready.inc())
            o.end_block()

            def equal_scores(W):
                def step_(instruction, n):
                    instruction.then_inc(branch, 1)
                    dve.wait_ge(branch, n)
                step_(dve.tensor_scalar(selb[:, 0:W], acc[:, 0:W], thr[:, 0:1], 0.0, ALU.is_gt, ALU.add, accum_out=cnt[:]), 1)
                step_(dve.tensor_scalar(cnt[:], cnt[:], -1.0, float(TOPK), ALU.mult, ALU.add), 2)
                step_(dve.tensor_scalar(work[:, 0:W], acc[:, 0:W], thr[:, 0:1], None, ALU.is_equal), 3)
                step_(dve.tensor_tensor_scan(other[:, 0:W], work[:, 0:W], work[:, 0:W], 0.0, ALU.add, ALU.max), 4)
                step_(dve.scalar_tensor_tensor(work[:, 0:W], other[:, 0:W], cnt[:, 0:1], work[:, 0:W], ALU.is_le, ALU.mult), 5)
                step_(dve.tensor_tensor(selb[:, 0:W], selb[:, 0:W], work[:, 0:W], ALU.add), 6)
                step_(dve.tensor_scalar(selb[:, 0:W], selb[:, 0:W], -1.0, FAR, ALU.add, ALU.mult), 7)
                dve.sem_clear(branch)

            def general(W):
                dve.tensor_copy(work[:, 0:W], acc[:, 0:W]).then_inc(branch, 1)
                dve.wait_ge(branch, 1)
                dve.sem_clear(branch)
                with dve.Fori(0, TOPK // 8):
                    dve.max(best[:], work[:, 0:W]).then_inc(branch, 1)
                    dve.wait_ge(branch, 1)
                    dve.match_replace(work[:, 0:W], best[:], work[:, 0:W], -3e38).then_inc(branch, 1)
                    dve.wait_ge(branch, 2)
                    dve.sem_clear(branch)
                dve.tensor_tensor(other[:, 0:W], work[:, 0:W], acc[:, 0:W], ALU.is_equal).then_inc(branch, 1)
                dve.wait_ge(branch, 1)
                dve.tensor_scalar_mul(selb[:, 0:W], other[:, 0:W], -FAR).then_inc(branch, 1)
                dve.wait_ge(branch, 2)
                dve.sem_clear(branch)

            def start_search(j):
                W = (j + 1) * P
                last = acc[:, j * P:W]
                do(dve.tensor_reduce(lo[:], acc[:, 0:W], AX.X, ALU.min))
                do(dve.tensor_tensor(last, last, late[:], ALU.add))
                do(dve.tensor_reduce(hi[:], acc[:, 0:W], AX.X, ALU.max))
                do(dve.tensor_tensor(hi[:], hi[:], lo[:], ALU.subtract))
                do(dve.tensor_scalar(steps[:], halves[:], hi[:, 0:1], None, ALU.mult))
                do(dve.tensor_tensor(mid[:], lo[:], steps[:, 0:1], ALU.add))

            def search(j, rounds):
                W = (j + 1) * P
                for n in rounds:
                    do(dve.tensor_scalar(passed[:, 0:W], acc[:, 0:W], mid[:, 0:1], 0.0, ALU.is_ge, ALU.add, accum_out=cnt[:]))
                    do(dve.tensor_scalar(step[:], cnt[:], TOPK - 0.5, steps[:, n:n + 1], ALU.is_ge, ALU.mult))
                    if n < ROUNDS - 1:
                        do(dve.scalar_tensor_tensor(mid[:], mid[:], step[:, 0:1], steps[:, n + 1:n + 2], ALU.add, ALU.subtract))
                    else:
                        do(dve.tensor_tensor(hi[:], mid[:], step[:], ALU.add))

            def choose(j):
                W = (j + 1) * P
                do(dve.tensor_scalar(passed[:, 0:W], acc[:, 0:W], hi[:, 0:1], 0.0, ALU.is_ge, ALU.add, accum_out=cnt[:]))
                dve.scalar_tensor_tensor(work[:, 0:W], passed[:, 0:W], -FAR, acc[:, 0:W], ALU.mult, ALU.add).then_inc(*o.inc())
                do(dve.tensor_scalar(cnt[:], cnt[:], -1.0, float(TOPK), ALU.mult, ALU.add))
                do(dve.tensor_scalar(cnt[:], cnt[:], 8.0, None, ALU.min))
                do(dve.max(best[:], work[:, 0:W]))
                dve.tensor_scalar(match[:], iota[:], cnt[:, 0:1], 0.0, ALU.is_equal, ALU.add, accum_out=step[:]).then_inc(*o.inc())
                do(dve.scalar_tensor_tensor(best[:], iota[:], cnt[:, 0:1], best[:], ALU.is_equal, ALU.mult, accum_out=thr[:]))
                do(dve.tensor_scalar(passed[:, 0:W], acc[:, 0:W], thr[:, 0:1], 0.0, ALU.is_ge, ALU.add, accum_out=cnt[:]))
                dve.tensor_scalar(bad[:, 1:2], cnt[:], step[:, 0:1], TOPK - 0.5, ALU.mult, ALU.is_lt).then_inc(*o.inc())
                dve.tensor_scalar(bad[:, 0:1], cnt[:], float(TOPK), None, ALU.not_equal).then_inc(*bad_ready.inc())
                dve.tensor_scalar(selb[:, 0:W], acc[:, 0:W], thr[:, 0:1], -FAR, ALU.is_lt, ALU.mult).then_inc(*o.inc())

            def check_chosen(j):
                W = (j + 1) * P
                dve.wait_ge(*nbad_made.upto(j))
                dve.tensor_copy(nbad[:], bank[4][0:1, 0:2]).then_inc(*nbad_ready.inc())
                dve.wait_ge(*nbad_ready.upto(j))
                o.settle()
                equal = dve.value_load(nbad[0:1, 0:1], min_val=0, max_val=P)
                unfound = dve.value_load(nbad[0:1, 1:2], min_val=0, max_val=P)
                with dve.If(equal > 0):
                    equal_scores(W)
                with dve.If(unfound > 0):
                    general(W)

            for i in range(BLOCKS):
                W, n_pieces, j = (i + 1) * P, pieces[i], i + 1
                searched = FIRST_TOPK <= j < BLOCKS
                for h in range(4):
                    lg = Lg[:, h % 2, 0:W]
                    if h >= 2:
                        dve.wait_ge(*pt_made.upto(i, (h - 1) * n_pieces))
                    for c, (a, w) in enumerate(key_chunks(i)):
                        n = h * n_pieces + c
                        dve.wait_ge(*lg_made.upto(i, n + 1))
                        dve.scalar_tensor_tensor(lg[:, a:a + w], bank[LG_BANKS[n % 3]][:, 0:w], float(P) ** -0.5,
                                                 selb[:, a:a + w], ALU.mult, ALU.add).then_inc(*lg_read.inc())
                    dve.wait_ge(*lg_read.upto(i, (h + 1) * n_pieces))
                    near = max(0, (i - 1) * P)
                    do(dve.tensor_tensor(lg[:, near:W], lg[:, near:W], bias[:, h, 2 * P - (W - near):], ALU.add))
                    dve.tensor_reduce(mx[:, h:h + 1], lg, AX.X, ALU.max, negate=True).then_inc(*mx_ready.inc())
                    if searched:
                        if h == 0:
                            start_search(j)
                        search(j, range(ROUNDS * h // 4, ROUNDS * (h + 1) // 4))
                    if h == 2:
                        normalise_ckv(i + 2)
                dve.wait_ge(*exp_ready.upto(i))
                do(dve.reciprocal(prec[:], psum_[:]))
                dve.wait_ge(*uv_made.upto(i))
                dve.wait_ge(*gz_ready.upto(i))
                for h in range(4):
                    dve.scalar_tensor_tensor(cat[:, 512 + h * P:512 + (h + 1) * P], by_head[5][:, h, :], prec[:, h:h + 1],
                                             z[:, i % 2, h * P:(h + 1) * P], ALU.mult, ALU.mult)\
                       .then_inc(*(ob_ready if h == 3 else o).inc())
                if searched:
                    dve.wait_ge(*pt_made.upto(i))
                    choose(j)
                    dve.wait_ge(*pv_made.upto(i))
                    check_chosen(j)
                elif j < BLOCKS:
                    dve.memset(selb[:, 0:j * P], 0.0).then_inc(*o.inc())
                    do(dve.tensor_copy(selb[:, j * P:(j + 1) * P], late[:]))
                if j < BLOCKS:
                    dve.tensor_copy(lo[:], ones[:]).then_inc(*selb_ready.inc())
                dve.wait_ge(*mrs_ready.upto(i))
                for half in range(2):
                    sl = slice(half * 512, (half + 1) * 512)
                    dve.scalar_tensor_tensor(cat[:, sl], bank[6 + half][:], mrs[:, 0:1], gate_row[:, sl], ALU.mult, ALU.mult)\
                       .then_inc(*(mix_ready if half else o).inc())
                if i + 2 < BLOCKS:
                    for n in range(scored[i + 2]):
                        (a, w), h = key_chunks(i + 2)[n // 8], n % 8
                        dve.wait_ge(*relu_ready.upto(i + 2, n + 1))
                        dst, weight = acc[:, a:a + w], iw[:, h:h + 1]
                        if h == 0:
                            dve.tensor_scalar(dst, relu[:, n % 4, 0:w], weight, None, ALU.mult).then_inc(*relu_used.inc())
                        else:
                            dve.wait_ge(*relu_used.upto(i + 2, n))
                            dve.scalar_tensor_tensor(dst, relu[:, n % 4, 0:w], weight, dst, ALU.mult, ALU.add)\
                               .then_inc(*relu_used.inc())
                    if scored[i + 2]:
                        dve.wait_ge(*relu_used.upto(i + 2))
                o.end_block()

        @block.gpsimd
        def _(pool):
            def ckv_rows(i):
                if i >= BLOCKS:
                    return
                pool.wait_ge(*cn_ready.upto(i))
                pool.tensor_copy(ckvr[:, i, :], cn[:]).then_inc(*ckvr_ready.inc())

            ckv_rows(0)
            ckv_rows(1)
            for i in range(BLOCKS):
                pool.wait_ge(*zsig_ready.upto(i))
                pool.tensor_tensor(z[:, i % 2, :], z[:, i % 2, :], sgz[:], ALU.mult).then_inc(*gz_ready.inc())
                ckv_rows(i + 2)
                pool.wait_ge(*mix_ready.upto(i))
                pool.wait_ge(x_in.sem, 16 * i + 16)
                pool.tensor_tensor(xb[:], xb[:], cat[:], ALU.add).then_inc(*out_ready.inc())


def shape_constants():
    f = lambda m: np.ascontiguousarray(np.asarray(m).astype(np.float32))
    j = np.arange(P)
    up = j[:, None] <= j[None, :]
    same = (j[:, None] // GLA_CHUNK) == (j[None, :] // GLA_CHUNK)
    c = dict(c_ident=f(np.eye(P)), c_chunk=f(np.stack([(same & up) / 16, (same & ~up) / 16], 1)),
             c_causal=f(same & up), c_tril=f(up))
    half = 32
    inv = (np.float32(10000.0) ** (-np.arange(half, dtype=np.float32) / np.float32(half))).astype(np.float32)
    c["c_inv"] = f(np.tile(inv, (P, 1)))
    lg = np.log(1.0 - 2.0 ** (-5.0 - np.arange(HEADS, dtype=np.float64)))
    rel = j[None, :] - j[:, None]
    c["c_dmat"] = f(np.stack([np.where(rel >= 0, np.exp(np.maximum(rel, 0) * g), 0) / 8 for g in lg], 1))
    w = np.zeros((P, HEADS, P))
    for h in range(HEADS):
        w[64 * (h % 2):64 * (h % 2) + 64, h, :] = np.exp((j + 1.0) * lg[h]) / 8
    c["c_winter"] = f(w)
    c["c_wstate"] = f(np.exp((P - 1.0 - j)[:, None] * lg[None, :]))
    c["c_gammac"] = f(np.exp(P * lg)[2 * np.arange(2)[None, :] + (j // 64)[:, None]])
    band = np.zeros((P, 12, P))
    for w_, win in enumerate(POOL_WINDOWS):
        d = j[None, :] - j[:, None]
        band[:, w_] = ((d >= 0) & (d < win)) / win - np.eye(P)
        band[:, 4 + w_] = ((d + P >= 0) & (d + P < win)) / win
        band[:, 8 + w_] = ((d >= 0) & (d < win)) / np.minimum(j + 1, win)[None, :] - np.eye(P)
    c["c_band"] = f(band)
    late = same & ~up
    first = np.broadcast_to((j < GLA_CHUNK)[:, None], (P, P))
    c["c_seg"] = f(np.stack([same & up, late, first, ~first], 1))
    c["c_big"] = f(np.stack([~(same & (j[:, None] > j[None, :])), ~(same & up)], 1) * 1e30)
    c["c_lev"] = f(np.stack([((j[:, None] // (2 * n)) == (j[None, :] // (2 * n))) & (j[:, None] // n % 2 == 1)
                             & (j[None, :] // n % 2 == 0) for n in LEVELS], 1))
    c["c_flip"] = f(np.eye(P)[::-1])
    c["c_late"] = f((j[None, :] > j[:, None]) * -FAR)
    dist = 255 - np.arange(384)
    n = np.maximum(dist, 1).astype(np.float32)
    big = 16 + (np.log(n / np.float32(16)) / np.float32(math.log(8)) * np.float32(16)).astype(np.int32)
    bucket = np.where(dist < 16, dist, np.minimum(big, N_BUCKETS - 1))
    c["c_onehot"] = f((np.arange(N_BUCKETS)[:, None] == bucket[None, :]) & (dist >= 0)[None, :])
    c["c_iota"] = f(np.tile(np.arange(1, 9), (P, 1)))
    c["c_halves"] = f(np.tile(0.5 ** np.arange(1, ROUNDS + 2), (P, 1)))
    return c


def build(nc, t, out, x1, x2, hT, oa, bias_scratch):
    def layer(prefix, names):
        return [t[prefix + n] for n in names.split()]

    def last(names):
        return [t[n + "_2"][0] for n in names.split()]

    def const(names):
        return tuple(t["c_" + n] for n in names.split())

    even_layer(nc, t["x"].rearrange("a s d -> (a s) d"),
               *layer("l0_", "w_in w_a2 b_a gla_norm_g sgu_ln_g sgu_ln_b w_s b_s w_out ln_g ln_b"),
               const("ident chunk causal tril"), x1)
    odd_layer(nc, x1, t["positions"].rearrange("a s -> (a s)"),
              *layer("l1_", "w_in ret_norm_g w_pool pool_scale w_out ln_g ln_b"),
              const("ident inv dmat winter wstate gammac band"), x2)
    with nc.sbuf_tensor("gate_row", [P, D], F32) as gate_row:
        delta_layer(nc, x2, *last("c w_ada b_ada g_pre w_in conv_w a_log dt_bias g_gdn g_post"),
                    const("ident seg big lev"), gate_row, hT, oa)
        sparse_layer(nc, x2, *last("w_in g_kv w_uv"), t["rel_bias_2"], *last("w_out"),
                     const("ident flip late onehot iota halves"), gate_row, hT, oa, bias_scratch,
                     out.rearrange("a s d -> (a s) d"))


def kernel(**inputs):
    import numpy as _np
    import concourse.bacc as _bacc
    from concourse import mybir as _mybir
    from concourse.bass_utils import run_bass_kernel_spmd as _run

    nc = _bacc.Bacc("TRN2", target_bir_lowering=False, num_devices=1)
    arrays, t = {}, {}
    for name, a in list(inputs.items()) + list(shape_constants().items()):
        arrays[name] = _np.ascontiguousarray(a)
        t[name] = nc.dram_tensor(name, list(arrays[name].shape), _mybir.dt.from_np(arrays[name].dtype),
                                 kind="ExternalInput").ap()
    out = nc.dram_tensor("out", [1, SEQ, D], F32, kind="ExternalOutput").ap()
    x1 = nc.dram_tensor("x1", [SEQ, D], F32).ap()
    x2 = nc.dram_tensor("x2", [SEQ, D], F32).ap()
    hT = nc.dram_tensor("hT", [BLOCKS, P, D], F32).ap()
    oa = nc.dram_tensor("oa", [SEQ, D // 2], F32).ap()
    bias_scratch = nc.dram_tensor("bias_scratch", [4, 384], F32).ap()
    build(nc, t, out, x1, x2, hT, oa, bias_scratch)
    r = _run(nc, [arrays], core_ids=[0])
    return r.results[0]["out"]
```

```python
import math
from contextlib import ExitStack

import numpy as np
import concourse.bass as bass
from concourse import mybir

F32 = mybir.dt.float32
BF16 = mybir.dt.bfloat16
I32 = mybir.dt.int32
ALU = mybir.AluOpType
ACT = mybir.ActivationFunctionType
AX = mybir.AxisListType

P = 128
SEQ, D = 2048, 1024
BLOCKS = SEQ // P
KT = D // P
HEADS = 4
LN_EPS = 1e-5
RMS_EPS = 1e-6
ALPHA = 4 ** 0.25
GELU_C = math.sqrt(2 / math.pi)
GELU_A = math.sqrt(0.044715)
TABLES = "natural_log_exp_and_others"


class Signal:

    def __init__(self, sem, per=1):
        self.sem, self.per, self.first = sem, per, 0

    def start(self):
        self.first = 1
        return self.sem

    def inc(self):
        return self.sem, 1

    def upto(self, i, k=None):
        return self.sem, i * self.per + (self.per if k is None else k) + self.first

    def before(self, i):
        assert self.first
        return self.sem, i * self.per + self.first


class Semaphores:

    def __init__(self, nc, prefix):
        self.nc, self.prefix, self.taken = nc, prefix, []

    def __enter__(self):
        return self

    def __call__(self, name):
        self.taken.append(self.nc.alloc_semaphore(name=self.prefix + name))
        return self.taken[-1]

    def __exit__(self, *_):
        self.nc.clear_and_free_semaphores(self.taken)
        self.nc.all_engine_barrier()


class Order:

    def __init__(self, eng, sem):
        self.eng, self.sem, self.count = eng, sem, 0

    def inc(self):
        self.count += 1
        return self.sem, 1

    def settle(self):
        self.eng.wait_ge(self.sem, self.count)

    def end_block(self):
        self.settle()
        self.eng.sem_clear(self.sem)
        self.count = 0


class Blk:

    def __init__(self, r, p, last=False):
        self.r, self.p, self.i, self.last = r, p, 2 * r + p, last
        self.q = 1 - p


def over_blocks(eng, body):
    with eng.Fori(0, BLOCKS // 2 - 1) as r:
        body(Blk(r, 0))
        body(Blk(r, 1))
    body(Blk(BLOCKS // 2 - 1, 0))
    body(Blk(BLOCKS // 2 - 1, 1, last=True))


def spread(ap, n):
    return ap.unsqueeze(2).broadcast_to([ap.shape[0], ap.shape[1], n])


def over_heads(ap, g):
    return ap.unsqueeze(1).broadcast_to([ap.shape[0], g, ap.shape[1]])


def row(ap, n=P):
    return ap.unsqueeze(0).broadcast_to([n, ap.shape[0]])


GLA_CHUNK = 64
ALR = 5


def even_layer(nc, x, w_in, w_a2, b_a, gla_g, sgu_g, sgu_b, w_s, b_s, w_out, ln_g, ln_b, consts, x_next):
    ident_d, chunk_d, causal_d, tril_d = consts
    O_QK, O_V, O_GA, O_ALR, O_USV, O_GB = 0, 512, 1024, 1536, 1552, 2576
    W = w_in.shape[1]
    wv = w_in.rearrange("(k p) n -> p k n", p=P)
    with ExitStack() as ctx:
        sem = ctx.enter_context(Semaphores(nc, "e_"))

        def sb(name, shape, dt=F32):
            return ctx.enter_context(nc.sbuf_tensor("e_" + name, shape, dt))

        def sig(name, per=1):
            return Signal(sem(name), per)

        W_in = sb("w_in", [P, KT, W])
        W_out = sb("w_out", [P, KT, D])
        xb = sb("xb", [P, 2, D])
        xT = sb("xT", [P, KT * P])
        qk = sb("qk", [P, 512])
        v = sb("v", [P, 2, 512])
        gates = sb("gates", [P, 2, 1024])
        usv = sb("usv", [P, 2, 1024])
        alrT = sb("alrT", [17, 2, P])
        w2 = sb("w2", [17, 256])
        ident = sb("ident", [P, P])
        chunkm = sb("chunkm", [P, 2, P])
        causal = sb("causal", [P, P])
        tril = sb("tril", [P, P])
        gla_row = sb("gla_row", [P, 512])
        sgu_grow = sb("sgu_grow", [P, 512])
        sgu_brow = sb("sgu_brow", [P, 512])
        ln_grow = sb("ln_grow", [P, D])
        ln_brow = sb("ln_brow", [P, D])
        wsT = sb("wsT", [P, 4, P])
        bsT = sb("bsT", [P, 4])
        eps = sb("eps", [P, 1])
        la = sb("la", [P, 256])
        lt = sb("lt", [P, 256])
        eks = sb("eks", [P, 256])
        ebT = sb("ebT", [P, 2, P])
        enT = sb("enT", [P, 2, P])
        qz = sb("qz", [P, 4, P])
        kdT = sb("kdT", [P, 2, P])
        kst = sb("kst", [P, 256])
        probs = sb("probs", [P, 4, P])
        S = sb("S", [P, 2, P])
        Smid = sb("Smid", [P, 2, P])
        gt = sb("gt", [P, 1024])
        gl = sb("gl", [P, 1024])
        catT, cat = gt, gl
        sq = sb("sq", [P, 512])
        ws_in = sq[:].rearrange("p (g s) -> p g s", g=4)
        ss = sb("ss", [P, 4])
        rs = sb("rs", [P, 4])
        st6 = sb("st6", [P, 4, 6])
        mv = sb("mv", [P, 4, 2])
        rs2 = sb("rs2", [P, 4])
        lnst = sb("lnst", [P, 2, 6])
        lnmv = sb("lnmv", [P, 2])
        lnrs = sb("lnrs", [P, 1])
        bank = [ctx.enter_context(nc.psum_tensor(f"e_ps{n}", [P, 512], F32)) for n in range(8)]
        zk, bTp, qkTp, scp, Up, op = bank[2], bank[3], bank[4], bank[5], bank[6], bank[7]
        Uc = Up[:, 0:256], bTp[:, 256:512]

        loaded, wout_loaded = sig("loaded"), sig("w_out")
        w_parts = [(O_V, 512), (O_GA, 528), (O_USV, 512), (O_USV + 512, 512), (O_QK, 512), (O_GB, 512)]
        w_loaded = [sig(f"w_in{n}") for n in range(len(w_parts))]
        x_in = [sig("x_in0"), sig("x_in1")]
        stored = sig("stored")
        setup = sig("setup")
        ws_turned, ws_ready = sig("ws_turned"), sig("ws_ready")
        xT_made, xT_ready = sig("xT_made", 2), sig("xT_ready", 2)
        proj_made, proj_ready = sig("proj_made", 7), sig("proj_ready", 7)
        z_made, lse_ready, la_ready = sig("z_made"), sig("lse"), sig("la_ready")
        decay_made, decay_ready = sig("decay_made"), sig("decay_ready", 3)
        qkT_made, qkd_ready, kst_ready = sig("qkT_made"), sig("qkd_ready"), sig("kst_ready")
        sc_made, probs_ready = sig("sc_made"), sig("probs_ready")
        U_made, Smid_ready, S_ready = sig("U_made"), sig("Smid_ready"), sig("S_ready")
        o_made, sq_ready, ss_ready, rs_ready = sig("o_made"), sig("sq_ready"), sig("ss_ready"), sig("rs_ready")
        gsig_ready, gate_ready = sig("gsig"), sig("gate_ready")
        usq_ready, inner_ready, usig_ready, gelu_ready = (
            sig("usq"), sig("inner"), sig("usig"), sig("gelu_ready"))
        mv_ready, rs2_ready, norm_ready, sn_ready = sig("mv_ready"), sig("rs2_ready"), sig("norm_ready"), sig("sn_ready")
        s_made, ob_ready, oa_ready, cb_ready = sig("s_made"), sig("ob_ready"), sig("oa_ready"), sig("cb_ready")
        catT_made, catT_ready = sig("catT_made", 2), sig("catT_ready", 2)
        y_made, r_ready, lnmv_ready, lnrs_ready, lnn_ready, out_ready = (
            sig("y_made"), sig("r_ready"), sig("lnmv"), sig("lnrs"), sig("lnn"), sig("out_ready"))
        orders = {n: sem("order_" + n) for n in ("act", "dve", "pool")}

        def chunks(p):
            return [
                (O_V, v[:, p, :]), (O_GA, gates[:, p, 0:512]), (O_USV, usv[:, p, 0:512]),
                (O_USV + 512, usv[:, p, 512:1024]), (O_QK, qk[:]), None, (O_GB, gates[:, p, 512:1024]),
            ]

        started = [s.start() for s in (proj_ready, r_ready, kst_ready, y_made, stored)]
        block = ctx.enter_context(nc.Block())
        small = [(ident[:], ident_d), (chunkm[:], chunk_d), (causal[:], causal_d), (tril[:], tril_d), (w2[0:16, :], w_a2),
                 (w2[16:17, :], b_a.unsqueeze(0)), (gla_row[:], row(gla_g.rearrange("h e -> (h e)"))),
                 (sgu_grow[:], row(sgu_g.rearrange("h e -> (h e)"))), (sgu_brow[:], row(sgu_b.rearrange("h e -> (h e)"))),
                 (ln_grow[:], row(ln_g)), (ln_brow[:], row(ln_b)), (ws_in, w_s.rearrange("g t s -> t g s")),
                 (bsT[:], b_s.rearrange("g t -> t g"))]
        NSMALL = 16 * len(small)

        @block.sync
        def _(sp):
            for s in started:
                sp.sem_inc(s, 1)
            sp.dma_start(xb[:, 0, :], x[0:P, :]).then_inc(x_in[0].sem, 16)
            sp.dma_start(xb[:, 1, :], x[P:2 * P, :]).then_inc(x_in[1].sem, 16)
            with nc.allow_non_contiguous_dma(reason="small tables"):
                for dst, src in small:
                    sp.dma_start(dst, src).then_inc(loaded.sem, 16)
            for (a, n), part in zip(w_parts, w_loaded):
                sp.dma_start(W_in[:, :, a:a + n], wv[:, :, a:a + n]).then_inc(part.sem, 16)
            sp.dma_start(W_out[:], w_out.rearrange("(k p) n -> p k n", p=P)).then_inc(wout_loaded.sem, 16)

            def body(b, load=True):
                if load:
                    sp.wait_ge(*r_ready.upto(b.i))
                    sp.dma_start(xb[:, b.p, :], x[bass.ds(b.i * P + 2 * P, P), :]).then_inc(x_in[b.p].sem, 16)
                sp.wait_ge(*out_ready.upto(b.i))
                sp.dma_start(x_next[bass.ds(b.i * P, P), :], cat[:]).then_inc(stored.sem, 16)

            with sp.Fori(0, BLOCKS // 2 - 1) as r:
                body(Blk(r, 0))
                body(Blk(r, 1))
            body(Blk(BLOCKS // 2 - 1, 0), load=False)
            body(Blk(BLOCKS // 2 - 1, 1), load=False)
            sp.wait_ge(stored.sem, 16 * BLOCKS + 1)

        @block.tensor
        def _(pe):
            def turn_x(i, r, p):
                pe.wait_ge(x_in[p].sem, 16 * r + 16)
                for half in range(2):
                    pe.wait_ge(*proj_ready.before(i))
                    for k in range(4):
                        t = 4 * half + k
                        m = pe.transpose(bank[half][:, k * P:(k + 1) * P], xb[:, p, t * P:(t + 1) * P], ident[:])
                    m.then_inc(*xT_made.inc())

            def project(i, p, c):
                if c != ALR:
                    off, _ = chunks(p)[c]
                    if c < 2:
                        pe.wait_ge(*xT_ready.upto(i))
                    else:
                        pe.wait_ge(*proj_ready.upto(i, c - 1))
                    for k in range(KT):
                        m = pe.matmul(bank[c % 2][:], xT[:, k * P:(k + 1) * P], W_in[:, k, off:off + 512],
                                      start=(k == 0), stop=(k == KT - 1))
                    m.then_inc(*proj_made.inc())
                else:
                    pe.wait_ge(*proj_ready.upto(i, c - 1))
                    for k in range(KT):
                        m = pe.matmul(bank[c % 2][0:16, 0:P], W_in[:, k, O_ALR:O_ALR + 16], xT[:, k * P:(k + 1) * P],
                                      start=(k == 0), stop=(k == KT - 1))
                    m.then_inc(*proj_made.inc())

            pe.wait_ge(loaded.sem, NSMALL)
            for g in range(4):
                m = pe.transpose(bank[2][:, g * P:(g + 1) * P], ws_in[:, g, :], ident[:])
            m.then_inc(*ws_turned.inc())
            turn_x(0, 0, 0)
            for c in range(6):
                if c != ALR:
                    pe.wait_ge(w_loaded[c].sem, 16)
                project(0, 0, c)
            pe.wait_ge(w_loaded[5].sem, 16)
            pe.wait_ge(wout_loaded.sem, 16)
            pe.wait_ge(*setup.upto(0))
            pe.wait_ge(*ws_ready.upto(0))

            def body(b):
                i, p = b.i, b.p
                nxt = []
                if not b.last:
                    r1, i1 = (b.r, b.i + 1) if p == 0 else (b.r + 1, b.i + 1)
                    nxt = [lambda: turn_x(i1, r1, b.q)] + [(lambda c=c: project(i1, b.q, c)) for c in range(6)]

                def fill():
                    if nxt:
                        nxt.pop(0)()

                project(i, p, 6)
                fill()
                pe.wait_ge(*proj_ready.upto(i, 6))
                for g in range(4):
                    m = pe.transpose(qkTp[:, g * P:(g + 1) * P], qk[:, g * P:(g + 1) * P], ident[:])
                m.then_inc(*qkT_made.inc())
                pe.wait_ge(*r_ready.before(i))
                pe.matmul(zk[:, 0:256], alrT[:, p, :], w2[:], start=True, stop=True).then_inc(*z_made.inc())
                fill()
                pe.wait_ge(*la_ready.upto(i))
                pe.matmul(zk[:, 256:512], chunkm[:, 1, :], la[:], start=True, stop=True)
                for g in range(2):
                    m = pe.matmul(bTp[:, g * P:(g + 1) * P], la[:, g * P:(g + 1) * P], chunkm[:, 0, :],
                                  start=True, stop=True)
                m.then_inc(*decay_made.inc())
                fill()
                pe.wait_ge(*kst_ready.upto(i))
                pe.wait_ge(*qkd_ready.upto(i))
                for h in range(4):
                    m = pe.matmul(scp[:, h * P:(h + 1) * P], kdT[:, h // 2, :], qz[:, h, :], start=True, stop=True)
                m.then_inc(*sc_made.inc())
                for c in range(2):
                    for h in range(4):
                        a, g = 64 * (h % 2), h // 2
                        m = pe.matmul(Uc[c][a:a + 64, g * P:(g + 1) * P],
                                      kst[64 * c:64 * c + 64, h * 64:h * 64 + 64],
                                      v[64 * c:64 * c + 64, p, h * P:(h + 1) * P], start=True, stop=True)
                m.then_inc(*U_made.inc())
                fill()
                pe.wait_ge(*probs_ready.upto(i))
                pe.wait_ge(*Smid_ready.upto(i))
                for h in range(4):
                    g = h // 2
                    pe.matmul(op[:, h * P:(h + 1) * P], probs[:, h, :], v[:, p, h * P:(h + 1) * P],
                              start=True, stop=False, skip_group_check=True)
                    pe.matmul(op[0:64, h * P:(h + 1) * P], qz[:, h, 0:64], S[:, g, :],
                              start=False, stop=False, skip_group_check=True)
                    m = pe.matmul(op[64:128, h * P:(h + 1) * P], qz[:, h, 64:128], Smid[:, g, :],
                                  start=False, stop=True, skip_group_check=True)
                m.then_inc(*o_made.inc())
                fill()
                pe.wait_ge(*sn_ready.upto(i))
                pe.wait_ge(*S_ready.upto(i))
                for g in range(4):
                    m = pe.matmul(Up[:, g * P:(g + 1) * P], wsT[:, g, :], usv[:, p, 512 + g * P:512 + (g + 1) * P],
                                  start=True, stop=True)
                m.then_inc(*s_made.inc())
                fill()
                for half, ready in enumerate((oa_ready, cb_ready)):
                    pe.wait_ge(*ready.upto(i))
                    for k in range(4):
                        t = 4 * half + k
                        m = pe.transpose((qkTp, scp)[half][:, k * P:(k + 1) * P], cat[:, t * P:(t + 1) * P], ident[:])
                    m.then_inc(*catT_made.inc())
                    fill()
                for half in range(2):
                    for k in range(KT):
                        if half == 0 and k % 4 == 0:
                            pe.wait_ge(*catT_ready.upto(i, 1 + k // 4))
                        m = pe.matmul((zk, bTp)[half][:], catT[:, k * P:(k + 1) * P],
                                      W_out[:, k, half * 512:(half + 1) * 512], start=(k == 0), stop=(k == KT - 1))
                m.then_inc(*y_made.inc())
                while nxt:
                    fill()

            over_blocks(pe, body)

        @block.scalar
        def _(act):
            o = Order(act, orders["act"])
            act.preload_act_table_set(TABLES)

            def sigmoid(dst, src, scale, ready):
                act.activation(dst, src, ACT.Exp, scale=scale).then_inc(*o.inc())
                o.settle()
                act.activation(dst, dst, ACT.Ln, bias=1.0).then_inc(*o.inc())
                o.settle()
                act.activation(dst, dst, ACT.Exp, scale=-1.0).then_inc(*ready.inc())

            def turn_x(i, p):
                for half in range(2):
                    act.wait_ge(*xT_made.upto(i, half + 1))
                    act.activation(xT[:, half * 512:(half + 1) * 512], bank[half][:], ACT.Copy).then_inc(*xT_ready.inc())

            def project(i, p, c):
                act.wait_ge(*proj_made.upto(i, c + 1))
                if c == 4:
                    act.wait_ge(*kst_ready.before(i))
                if c != ALR:
                    act.activation(chunks(p)[c][1], bank[c % 2][:], ACT.Copy).then_inc(*proj_ready.inc())
                else:
                    act.activation(alrT[0:16, p, :], bank[c % 2][0:16, 0:P], ACT.Copy).then_inc(*proj_ready.inc())

            turn_x(0, 0)
            act.wait_ge(*setup.upto(0))
            for c in range(6):
                project(0, 0, c)

            def body(b):
                i, p = b.i, b.p
                nxt = []
                if not b.last:
                    nxt = [lambda: turn_x(b.i + 1, b.q)] + [(lambda c=c: project(b.i + 1, b.q, c)) for c in range(6)]

                def fill():
                    if nxt:
                        nxt.pop(0)()

                act.wait_ge(*y_made.before(i))
                project(i, p, 6)
                fill()
                act.wait_ge(*z_made.upto(i))
                act.activation(lt[:], zk[:, 0:256], ACT.Abs).then_inc(*o.inc())
                o.settle()
                act.activation(eks[:], lt[:], ACT.Exp, scale=-1.0).then_inc(*o.inc())
                o.settle()
                act.activation(lt[:], eks[:], ACT.Ln, bias=1.0).then_inc(*lse_ready.inc())
                act.wait_ge(*proj_ready.upto(i))
                sigmoid(gt[:], gates[:, p, :], -1.0, gsig_ready)
                fill()
                act.wait_ge(*decay_made.upto(i))
                act.activation(eks[:], zk[:, 256:512], ACT.Exp).then_inc(*decay_ready.inc())
                act.activation(ebT[:], bTp[:, 0:256].rearrange("p (g t) -> p g t", g=2), ACT.Exp).then_inc(*decay_ready.inc())
                act.activation(enT[:], bTp[:, 0:256].rearrange("p (g t) -> p g t", g=2), ACT.Exp, scale=-1.0)\
                   .then_inc(*decay_ready.inc())
                act.wait_ge(stored.sem, 16 * i + 1)
                act.activation(gl[:], usv[:, p, :], ACT.Square, scale=GELU_A).then_inc(*usq_ready.inc())
                fill()
                act.wait_ge(*inner_ready.upto(i))
                sigmoid(gl[:], gl[:], -2.0 * GELU_C, usig_ready)
                fill()
                act.wait_ge(*o_made.upto(i))
                act.activation(sq[:], op[:], ACT.Square).then_inc(*sq_ready.inc())
                act.wait_ge(*mv_ready.upto(i))
                act.activation(rs2[:], mv[:, :, 1], ACT.Ln, bias=eps[:, 0:1]).then_inc(*o.inc())
                o.settle()
                act.activation(rs2[:], rs2[:], ACT.Exp, scale=-0.5).then_inc(*rs2_ready.inc())
                act.wait_ge(*ss_ready.upto(i))
                act.activation(rs[:], ss[:], ACT.Ln, bias=eps[:, 0:1], scale=1.0 / P).then_inc(*o.inc())
                o.settle()
                act.activation(rs[:], rs[:], ACT.Exp, scale=-0.5).then_inc(*rs_ready.inc())
                fill()
                fill()
                for half in range(2):
                    act.wait_ge(*catT_made.upto(i, half + 1))
                    act.activation(catT[:, half * 512:(half + 1) * 512], (qkTp, scp)[half][:], ACT.Copy)\
                       .then_inc(*catT_ready.inc())
                    fill()
                act.wait_ge(*lnmv_ready.upto(i))
                act.activation(lnrs[:], lnmv[:, 1:2], ACT.Ln, bias=eps[:, 0:1]).then_inc(*o.inc())
                o.settle()
                act.activation(lnrs[:], lnrs[:], ACT.Exp, scale=-0.5).then_inc(*lnrs_ready.inc())
                while nxt:
                    fill()
                o.end_block()

            over_blocks(act, body)

        @block.vector
        def _(dve):
            o = Order(dve, orders["dve"])
            dve.memset(S[:], 0.0).then_inc(*o.inc())
            dve.memset(qz[:], 0.0).then_inc(*o.inc())
            dve.memset(eps[:], LN_EPS).then_inc(*o.inc())
            dve.memset(alrT[:], 1.0).then_inc(*o.inc())
            o.settle()
            dve.memset(st6[:], 0.0).then_inc(*setup.inc())
            dve.wait_ge(*ws_turned.upto(0))
            dve.wait_ge(loaded.sem, NSMALL)
            dve.tensor_tensor(wsT[:], bank[2][:].rearrange("p (g t) -> p g t", g=4), over_heads(tril[:, :], 4),
                              ALU.mult).then_inc(*ws_ready.inc())
            o.end_block()

            def body(b):
                i, p = b.i, b.p
                dve.wait_ge(*lse_ready.upto(i))
                dve.scalar_tensor_tensor(la[:], zk[:, 0:256], 0.0, lt[:], ALU.min, ALU.subtract).then_inc(*la_ready.inc())
                dve.wait_ge(*qkT_made.upto(i))
                dve.wait_ge(*decay_ready.upto(i))
                for a in (0, 64):
                    dve.scalar_tensor_tensor(qz[a:a + 64].rearrange("p (g b) t -> p b g t", b=2)[:, a // 64],
                                             qkTp[a:a + 64, 0:256].rearrange("p (g t) -> p g t", g=2), 0.125,
                                             ebT[a:a + 64], ALU.mult, ALU.mult).then_inc(*o.inc())
                dve.tensor_tensor(kdT[:], qkTp[:, 256:512].rearrange("p (g t) -> p g t", g=2), enT[:], ALU.mult)\
                   .then_inc(*qkd_ready.inc())
                dve.wait_ge(*sc_made.upto(i))
                dve.tensor_tensor(probs[:], scp[:].rearrange("p (h t) -> p h t", h=4), over_heads(causal[:, :], 4),
                                  ALU.mult).then_inc(*probs_ready.inc())
                dve.wait_ge(*U_made.upto(i))
                for g in range(2):
                    dve.scalar_tensor_tensor(Smid[:, g, :], S[:, g, :], ebT[:, g, 63:64], Uc[0][:, g * P:(g + 1) * P],
                                             ALU.mult, ALU.add).then_inc(*(Smid_ready if g else o).inc())
                dve.wait_ge(*gelu_ready.upto(i))
                for g in range(4):
                    dve.bn_stats(st6[:, g, :], usv[:, p, 512 + g * P:512 + (g + 1) * P]).then_inc(*o.inc())
                o.settle()
                for g in range(4):
                    dve.bn_aggr(mv[:, g, :], st6[:, g, :]).then_inc(*(mv_ready if g == 3 else o).inc())
                dve.wait_ge(*rs2_ready.upto(i))
                for g in range(4):
                    dve.tensor_scalar(usv[:, p, 512 + g * P:512 + (g + 1) * P], usv[:, p, 512 + g * P:512 + (g + 1) * P], mv[:, g, 0:1],
                                      rs2[:, g:g + 1], ALU.subtract, ALU.mult)\
                       .then_inc(*(norm_ready if g == 3 else o).inc())
                dve.wait_ge(*o_made.upto(i))
                for g in range(2):
                    dve.scalar_tensor_tensor(S[:, g, :], Smid[:, g, :], ebT[:, g, 127:128],
                                             Uc[1][:, g * P:(g + 1) * P], ALU.mult, ALU.add)\
                       .then_inc(*(S_ready if g else o).inc())
                dve.wait_ge(*sq_ready.upto(i))
                dve.tensor_reduce(ss[:], sq[:].rearrange("p (h e) -> p h e", h=4), AX.X, ALU.add).then_inc(*ss_ready.inc())
                dve.wait_ge(stored.sem, 16 * i + 1)
                dve.wait_ge(*rs_ready.upto(i))
                dve.wait_ge(*gate_ready.upto(i))
                for h in range(4):
                    dve.scalar_tensor_tensor(cat[:, h * P:(h + 1) * P], op[:, h * P:(h + 1) * P], rs[:, h:h + 1],
                                             gates[:, p, h * P:(h + 1) * P], ALU.mult, ALU.mult)\
                       .then_inc(*(oa_ready if h == 3 else o).inc())
                dve.wait_ge(*s_made.upto(i))
                for g in range(4):
                    dve.scalar_tensor_tensor(cat[:, 512 + g * P:512 + (g + 1) * P], Up[:, g * P:(g + 1) * P], bsT[:, g:g + 1],
                                             usv[:, p, g * P:(g + 1) * P], ALU.add, ALU.mult)\
                       .then_inc(*(ob_ready if g == 3 else o).inc())
                dve.wait_ge(*y_made.upto(i))
                for half in range(2):
                    dve.scalar_tensor_tensor(cat[:, half * 512:(half + 1) * 512], xb[:, p, half * 512:(half + 1) * 512],
                                             ALPHA, (zk, bTp)[half][:], ALU.mult, ALU.add)\
                       .then_inc(*(r_ready if half else o).inc())
                dve.wait_ge(*r_ready.upto(i))
                for half in range(2):
                    dve.bn_stats(lnst[:, half, :], cat[:, half * 512:(half + 1) * 512]).then_inc(*o.inc())
                o.settle()
                dve.bn_aggr(lnmv[:], lnst[:].rearrange("p a b -> p (a b)")).then_inc(*lnmv_ready.inc())
                dve.wait_ge(*lnrs_ready.upto(i))
                dve.tensor_scalar(cat[:], cat[:], lnmv[:, 0:1], lnrs[:, 0:1], ALU.subtract, ALU.mult)\
                   .then_inc(*lnn_ready.inc())
                o.end_block()

            over_blocks(dve, body)

        @block.gpsimd
        def _(pool):
            o = Order(pool, orders["pool"])
            pool.wait_ge(loaded.sem, NSMALL)

            def body(b):
                i, p = b.i, b.p
                pool.wait_ge(*usq_ready.upto(i))
                pool.tensor_tensor(gl[:], gl[:], usv[:, p, :], ALU.mult).then_inc(*o.inc())
                o.settle()
                pool.tensor_tensor(gl[:], gl[:], usv[:, p, :], ALU.add).then_inc(*inner_ready.inc())
                pool.wait_ge(*decay_ready.upto(i, 1))
                pool.tensor_tensor(kst[:], qk[:, 256:512], eks[:], ALU.mult).then_inc(*kst_ready.inc())
                pool.wait_ge(*usig_ready.upto(i))
                pool.tensor_tensor(usv[:, p, :], usv[:, p, :], gl[:], ALU.mult).then_inc(*gelu_ready.inc())
                pool.wait_ge(*gsig_ready.upto(i))
                pool.tensor_tensor(gates[:, p, :], gates[:, p, :], gt[:], ALU.mult).then_inc(*o.inc())
                o.settle()
                pool.tensor_tensor(gates[:, p, 0:512], gates[:, p, 0:512], gla_row[:], ALU.mult).then_inc(*gate_ready.inc())
                pool.wait_ge(*norm_ready.upto(i))
                pool.tensor_tensor(usv[:, p, 512:1024], usv[:, p, 512:1024], sgu_grow[:], ALU.mult).then_inc(*o.inc())
                o.settle()
                pool.tensor_tensor(usv[:, p, 512:1024], usv[:, p, 512:1024], sgu_brow[:], ALU.add).then_inc(*sn_ready.inc())
                pool.wait_ge(*ob_ready.upto(i))
                pool.tensor_tensor(cat[:, 512:1024], cat[:, 512:1024], gates[:, p, 512:1024], ALU.mult).then_inc(*cb_ready.inc())
                pool.wait_ge(*lnn_ready.upto(i))
                pool.tensor_tensor(cat[:], cat[:], ln_grow[:], ALU.mult).then_inc(*o.inc())
                o.settle()
                pool.tensor_tensor(cat[:], cat[:], ln_brow[:], ALU.add).then_inc(*out_ready.inc())
                o.end_block()

            over_blocks(pool, body)


POOL_WINDOWS = (2, 4, 8, 16)
TWO_PI = 2 * math.pi
PI_A = 6.28125
PI_B = float(np.float32(TWO_PI - PI_A) // np.float32(2 ** -20) * np.float32(2 ** -20))
PI_C = TWO_PI - PI_A - PI_B
ROUND = 1.5 * 2 ** 23


def odd_layer(nc, x, positions, w_in, ret_g, w_pool, pool_scale, w_out, ln_g, ln_b, consts, x_next):
    ident_d, inv_d, dmat_d, winter_d, wstate_d, gammac_d, band_d = consts
    O_QK, O_V, O_GC, O_P, O_GD = 0, 512, 1024, 1536, 2048
    W = w_in.shape[1]
    wv = w_in.rearrange("(k p) n -> p k n", p=P)
    with ExitStack() as ctx:
        sem = ctx.enter_context(Semaphores(nc, "o_"))

        def sb(name, shape, dt=F32):
            return ctx.enter_context(nc.sbuf_tensor("o_" + name, shape, dt))

        def sig(name, per=1):
            return Signal(sem(name), per)

        W_in = sb("w_in", [P, KT, W])
        W_out = sb("w_out", [P, KT, D])
        xb = sb("xb", [P, 2, D])
        xT = sb("xT", [P, KT * P])
        qk = sb("qk", [P, 2, 512])
        v = sb("v", [P, 2, 512])
        gates = sb("gates", [P, 2, 1024])
        pp = sb("pp", [P, 2, 512])
        ident = sb("ident", [P, P])
        inv = sb("inv", [P, 32])
        dmat = sb("dmat", [P, 4, P])
        winter = sb("winter", [P, 4, P])
        wstate = sb("wstate", [P, 4])
        gammac = sb("gammac", [P, 2])
        band = sb("band", [P, 12, P])
        poolw = sb("poolw", [P, 4, P])
        ret_row = sb("ret_row", [P, 512])
        scale_row = sb("scale_row", [P, 512])
        ln_grow = sb("ln_grow", [P, D])
        ln_brow = sb("ln_brow", [P, D])
        eps = sb("eps", [P, 1])
        halfpi = sb("halfpi", [P, 1])
        posi = sb("posi", [P, BLOCKS], I32)
        posf = sb("posf", [P, BLOCKS])
        ang = sb("ang", [P, BLOCKS, 32])
        red = sb("red", [P, BLOCKS, 32])
        turns = sb("turns", [P, BLOCKS, 32])
        sin = sb("sin", [P, BLOCKS, 32])
        cos = sb("cos", [P, BLOCKS, 32])
        ra = sb("ra", [P, 8, 32])
        rb = sb("rb", [P, 8, 32])
        rc = sb("rc", [P, 8, 32])
        rd = sb("rd", [P, 8, 32])
        rot = sb("rot", [P, 8, 64])
        qT = sb("qT", [P, 2, P])
        kT = sb("kT", [P, 2, P])
        qz = sb("qz", [P, 4, P])
        qw = sb("qw", [P, 4, P])
        kst = sb("kst", [P, 256])
        probs = sb("probs", [P, 4, P])
        S = sb("S", [P, 2, P])
        pT = sb("pT", [P, 4, P])
        gt = sb("gt", [P, 1024])
        cat = sb("cat", [P, 1024])
        catT = gt
        st6 = sb("st6", [P, 4, 6])
        mv = sb("mv", [P, 4, 2])
        rs = sb("rs", [P, 4])
        lnst = sb("lnst", [P, 2, 6])
        lnmv = sb("lnmv", [P, 2])
        lnrs = sb("lnrs", [P, 1])
        bank = [ctx.enter_context(nc.psum_tensor(f"o_ps{n}", [P, 512], F32)) for n in range(8)]
        y0, y1, qkTp, scp, Up, op = bank[2], bank[3], bank[4], bank[5], bank[6], bank[7]

        loaded, wout_loaded = sig("loaded"), sig("w_out")
        w_parts = (O_QK, O_V, O_P, O_GC, O_GD)
        w_loaded = [sig(f"w_in{n}") for n in range(len(w_parts))]
        x_in = [sig("x_in0"), sig("x_in1")]
        stored, setup, tables = sig("stored"), sig("setup"), sig("tables", 2)
        xT_made, xT_ready = sig("xT_made", 2), sig("xT_ready", 2)
        proj_made, proj_ready = sig("proj_made", 5), sig("proj_ready", 5)
        rot_ready, qkT_made, qk_ready, kst_ready = sig("rot"), sig("qkT_made"), sig("qk_ready"), sig("kst")
        rot_part = sig("rot_part")
        sc_made, probs_ready, U_made, o_made, S_ready = sig("sc_made"), sig("probs"), sig("U_made"), sig("o_made"), sig("S_ready")
        gsig_ready, gate_ready = sig("gsig"), sig("gate")
        mv_ready, rs_ready, oc_ready = sig("mv"), sig("rs"), sig("oc")
        pT_made, pT_ready, pd_made, od_ready = sig("pT_made"), sig("pT_ready"), sig("pd_made"), sig("od")
        catT_made, catT_ready = sig("catT_made", 2), sig("catT_ready", 2)
        y_made, r_ready, lnmv_ready, lnrs_ready, lnn_ready, out_ready = (
            sig("y_made"), sig("r_ready"), sig("lnmv"), sig("lnrs"), sig("lnn"), sig("out_ready"))
        orders = {n: sem("order_" + n) for n in ("act", "dve", "pool")}

        def chunks(p):
            return [(O_QK, qk[:, p, :]), (O_V, v[:, p, :]), (O_P, pp[:, p, :]), (O_GC, gates[:, p, 0:512]),
                    (O_GD, gates[:, p, 512:1024])]

        started = [s.start() for s in (proj_ready, S_ready, catT_ready, r_ready, y_made, qkT_made, rot_ready, stored)]
        block = ctx.enter_context(nc.Block())
        small = [(ident[:], ident_d), (inv[:], inv_d), (dmat[:], dmat_d), (winter[:], winter_d), (wstate[:], wstate_d),
                 (gammac[:], gammac_d), (band[:], band_d), (poolw[:], w_pool.rearrange("g c d -> c g d")),
                 (ret_row[:], row(ret_g.rearrange("h e -> (h e)"))), (scale_row[:], row(pool_scale)),
                 (ln_grow[:], row(ln_g)), (ln_brow[:], row(ln_b)),
                 (posi[:], positions.rearrange("(b p) -> p b", p=P))]
        NSMALL = 16 * len(small)

        @block.sync
        def _(sp):
            for s in started:
                sp.sem_inc(s, 1)
            sp.dma_start(xb[:, 0, :], x[0:P, :]).then_inc(x_in[0].sem, 16)
            sp.dma_start(xb[:, 1, :], x[P:2 * P, :]).then_inc(x_in[1].sem, 16)
            with nc.allow_non_contiguous_dma(reason="small tables"):
                for dst, src in small:
                    sp.dma_start(dst, src).then_inc(loaded.sem, 16)
            for a, part in zip(w_parts, w_loaded):
                sp.dma_start(W_in[:, :, a:a + 512], wv[:, :, a:a + 512]).then_inc(part.sem, 16)
            sp.dma_start(W_out[:], w_out.rearrange("(k p) n -> p k n", p=P)).then_inc(wout_loaded.sem, 16)

            def body(b, load=True):
                if load:
                    sp.wait_ge(*r_ready.upto(b.i))
                    sp.dma_start(xb[:, b.p, :], x[bass.ds(b.i * P + 2 * P, P), :]).then_inc(x_in[b.p].sem, 16)
                sp.wait_ge(*out_ready.upto(b.i))
                sp.dma_start(x_next[bass.ds(b.i * P, P), :], cat[:]).then_inc(stored.sem, 16)

            with sp.Fori(0, BLOCKS // 2 - 1) as r:
                body(Blk(r, 0))
                body(Blk(r, 1))
            body(Blk(BLOCKS // 2 - 1, 0), load=False)
            body(Blk(BLOCKS // 2 - 1, 1), load=False)
            sp.wait_ge(stored.sem, 16 * BLOCKS + 1)

        @block.tensor
        def _(pe):
            def turn_x(i, r, p):
                pe.wait_ge(x_in[p].sem, 16 * r + 16)
                pe.wait_ge(*proj_ready.before(i))
                for half in range(2):
                    for k in range(4):
                        t = 4 * half + k
                        m = pe.transpose(bank[half][:, k * P:(k + 1) * P], xb[:, p, t * P:(t + 1) * P], ident[:])
                    m.then_inc(*xT_made.inc())

            def project(i, p, c):
                off, _ = chunks(p)[c]
                if c < 2:
                    pe.wait_ge(*xT_ready.upto(i))
                else:
                    pe.wait_ge(*proj_ready.upto(i, c - 1))
                for k in range(KT):
                    m = pe.matmul(bank[c % 2][:], xT[:, k * P:(k + 1) * P], W_in[:, k, off:off + 512],
                                  start=(k == 0), stop=(k == KT - 1))
                m.then_inc(*proj_made.inc())

            pe.wait_ge(loaded.sem, NSMALL)
            turn_x(0, 0, 0)
            for c in range(4):
                pe.wait_ge(w_loaded[c].sem, 16)
                project(0, 0, c)
            pe.wait_ge(w_loaded[4].sem, 16)
            pe.wait_ge(wout_loaded.sem, 16)
            pe.wait_ge(*setup.upto(0))

            def body(b, first=False):
                i, p = b.i, b.p
                nxt = []
                if not b.last:
                    r1, i1 = (b.r, b.i + 1) if p == 0 else (b.r + 1, b.i + 1)
                    nxt = [lambda: turn_x(i1, r1, b.q)] + [(lambda c=c: project(i1, b.q, c)) for c in range(4)]

                def fill():
                    if nxt:
                        nxt.pop(0)()

                project(i, p, 4)
                fill()
                pe.wait_ge(*proj_ready.upto(i, 4))
                pe.wait_ge(*S_ready.before(i))
                for w in range(4):
                    m = pe.matmul(Up[:, w * P:(w + 1) * P], pp[:, p, w * P:(w + 1) * P], band[:, (8 if first else 0) + w, :],
                                  start=True, stop=first)
                    if not first:
                        m = pe.matmul(Up[:, w * P:(w + 1) * P], pp[:, b.q, w * P:(w + 1) * P], band[:, 4 + w, :],
                                      start=False, stop=True)
                m.then_inc(*pT_made.inc())
                fill()
                pe.wait_ge(*rot_ready.upto(i))
                pe.wait_ge(*catT_ready.before(i))
                for g in range(4):
                    m = pe.transpose(qkTp[:, g * P:(g + 1) * P], rot[:, 2 * g:2 * g + 2, :].rearrange("p a b -> p (a b)"), ident[:])
                m.then_inc(*qkT_made.inc())
                fill()
                pe.wait_ge(*qk_ready.upto(i))
                for h in range(4):
                    m = pe.matmul(scp[:, h * P:(h + 1) * P], kT[:, h // 2, :], qz[:, h, :], start=True, stop=True)
                m.then_inc(*sc_made.inc())
                pe.wait_ge(*kst_ready.upto(i))
                pe.wait_ge(*pT_ready.upto(i))
                for h in range(4):
                    a, g = 64 * (h % 2), h // 2
                    m = pe.matmul(Up[a:a + 64, g * P:(g + 1) * P], kst[:, h * 64:h * 64 + 64],
                                  v[:, p, h * P:(h + 1) * P], start=True, stop=True)
                m.then_inc(*U_made.inc())
                pe.wait_ge(*r_ready.before(i))
                for w in range(4):
                    m = pe.matmul(y0[:, w * P:(w + 1) * P], pT[:, w, :], poolw[:, w, :], start=True, stop=True)
                m.then_inc(*pd_made.inc())
                fill()
                pe.wait_ge(*probs_ready.upto(i))
                for h in range(4):
                    g = h // 2
                    pe.matmul(op[:, h * P:(h + 1) * P], probs[:, h, :], v[:, p, h * P:(h + 1) * P], start=True, stop=False)
                    m = pe.matmul(op[:, h * P:(h + 1) * P], qw[:, h, :], S[:, g, :], start=False, stop=True)
                m.then_inc(*o_made.inc())
                fill()
                for half, ready in ((1, od_ready), (0, oc_ready)):
                    pe.wait_ge(*ready.upto(i))
                    for k in range(4):
                        t = 4 * half + k
                        m = pe.transpose((qkTp, scp)[half][:, k * P:(k + 1) * P], cat[:, t * P:(t + 1) * P], ident[:])
                    m.then_inc(*catT_made.inc())
                while nxt:
                    fill()
                for half in range(2):
                    for n, k in enumerate((4, 5, 6, 7, 0, 1, 2, 3)):
                        if half == 0 and n % 4 == 0:
                            pe.wait_ge(*catT_ready.upto(i, 1 + n // 4))
                        m = pe.matmul((y0, y1)[half][:], catT[:, k * P:(k + 1) * P],
                                      W_out[:, k, half * 512:(half + 1) * 512], start=(n == 0), stop=(n == KT - 1))
                m.then_inc(*y_made.inc())

            body(Blk(0, 0), first=True)
            body(Blk(0, 1))
            with pe.Fori(1, BLOCKS // 2 - 1) as r:
                body(Blk(r, 0))
                body(Blk(r, 1))
            body(Blk(BLOCKS // 2 - 1, 0))
            body(Blk(BLOCKS // 2 - 1, 1, last=True))

        @block.scalar
        def _(act):
            o = Order(act, orders["act"])

            def turn_x(i, p):
                for half in range(2):
                    act.wait_ge(*xT_made.upto(i, half + 1))
                    act.activation(xT[:, half * 512:(half + 1) * 512], bank[half][:], ACT.Copy).then_inc(*xT_ready.inc())

            def project(i, p, c):
                act.wait_ge(*proj_made.upto(i, c + 1))
                act.activation(chunks(p)[c][1], bank[c % 2][:], ACT.Copy).then_inc(*proj_ready.inc())

            act.wait_ge(*tables.upto(0, 2))
            act.activation(sin[:], red[:], ACT.Sin).then_inc(*o.inc())
            act.activation(cos[:], turns[:], ACT.Sin).then_inc(*o.inc())
            o.settle()
            act.preload_act_table_set(TABLES)

            def sigmoid(dst, src, scale, ready):
                act.activation(dst, src, ACT.Exp, scale=scale).then_inc(*o.inc())
                o.settle()
                act.activation(dst, dst, ACT.Ln, bias=1.0).then_inc(*o.inc())
                o.settle()
                act.activation(dst, dst, ACT.Exp, scale=-1.0).then_inc(*ready.inc())
            turn_x(0, 0)
            for c in range(4):
                project(0, 0, c)
            act.activation(lnrs[:], eps[:], ACT.Copy).then_inc(*setup.inc())
            o.end_block()

            def body(b):
                i, p = b.i, b.p
                nxt = []
                if not b.last:
                    nxt = [lambda: turn_x(b.i + 1, b.q)] + [(lambda c=c: project(b.i + 1, b.q, c)) for c in range(4)]

                def fill():
                    if nxt:
                        nxt.pop(0)()

                act.wait_ge(*y_made.before(i))
                project(i, p, 4)
                fill()
                act.wait_ge(*pT_made.upto(i))
                act.activation(pT[:], Up[:].rearrange("p (g t) -> p g t", g=4), ACT.Copy).then_inc(*pT_ready.inc())
                act.wait_ge(*proj_ready.upto(i))
                sigmoid(gt[:], gates[:, p, :], -1.0, gsig_ready)
                fill()
                fill()
                fill()
                act.wait_ge(*mv_ready.upto(i))
                act.activation(rs[:], mv[:, :, 1], ACT.Ln, bias=eps[:, 0:1]).then_inc(*o.inc())
                o.settle()
                act.activation(rs[:], rs[:], ACT.Exp, scale=-0.5).then_inc(*rs_ready.inc())
                fill()
                for half in (1, 0):
                    act.wait_ge(*catT_made.upto(i, 2 - half))
                    act.activation(catT[:, half * 512:(half + 1) * 512], (qkTp, scp)[half][:], ACT.Copy)\
                       .then_inc(*catT_ready.inc())
                while nxt:
                    fill()
                act.wait_ge(*lnmv_ready.upto(i))
                act.activation(lnrs[:], lnmv[:, 1:2], ACT.Ln, bias=eps[:, 0:1]).then_inc(*o.inc())
                o.settle()
                act.activation(lnrs[:], lnrs[:], ACT.Exp, scale=-0.5).then_inc(*lnrs_ready.inc())
                o.end_block()

            over_blocks(act, body)

        @block.vector
        def _(dve):
            o = Order(dve, orders["dve"])
            dve.memset(S[:], 0.0).then_inc(*o.inc())
            dve.memset(qz[:], 0.0).then_inc(*o.inc())
            dve.memset(eps[:], LN_EPS).then_inc(*o.inc())
            dve.wait_ge(loaded.sem, NSMALL)
            dve.tensor_copy(posf[:], posi[:]).then_inc(*o.inc())
            o.settle()
            dve.tensor_tensor(ang[:], spread(posf[:], 32), over_heads(inv[:], BLOCKS), ALU.mult).then_inc(*o.inc())
            o.settle()

            def reduce(dst, quarter, done):
                dve.tensor_scalar(rnd, ang[:], 1 / TWO_PI, quarter, ALU.mult, ALU.add).then_inc(*o.inc())
                o.settle()
                dve.tensor_scalar(rnd, rnd, ROUND, ROUND, ALU.add, ALU.subtract).then_inc(*o.inc())
                o.settle()
                dve.scalar_tensor_tensor(dst, rnd, -PI_A, ang[:], ALU.mult, ALU.add).then_inc(*o.inc())
                o.settle()
                dve.scalar_tensor_tensor(dst, rnd, -PI_B, dst, ALU.mult, ALU.add).then_inc(*o.inc())
                o.settle()
                dve.scalar_tensor_tensor(dst, rnd, -PI_C, dst, ALU.mult, ALU.add).then_inc(*o.inc())
                o.settle()
                dve.tensor_scalar(dst, dst, quarter * TWO_PI, math.pi * (1 - 1e-7), ALU.add, ALU.min).then_inc(*o.inc())
                o.settle()
                dve.tensor_scalar(dst, dst, -math.pi * (1 - 1e-7), None, ALU.max).then_inc(*done.inc())

            rnd = cos[:]
            reduce(red[:], 0.0, tables)
            reduce(turns[:], 0.25, tables)
            o.end_block()

            def body(b):
                i, p = b.i, b.p
                x12 = qk[:, p, :].rearrange("p (h a j) -> p h a j", h=8, a=2)
                cs, sn = (over_heads(t[:, bass.ds(i, 1), :].rearrange("p a j -> p (a j)"), 8) for t in (cos, sin))
                dve.wait_ge(*proj_ready.upto(i, 1))
                dve.wait_ge(*qkT_made.before(i))
                dve.tensor_tensor(rb[:], x12[:, :, 1, :], sn, ALU.mult).then_inc(*o.inc())
                dve.tensor_tensor(rc[:], x12[:, :, 0, :], sn, ALU.mult).then_inc(*o.inc())
                o.settle()
                dve.wait_ge(*rot_part.upto(i))
                dve.tensor_tensor(rot[:, :, 0:32], ra[:], rb[:], ALU.subtract).then_inc(*o.inc())
                dve.tensor_tensor(rot[:, :, 32:64], rc[:], rd[:], ALU.add).then_inc(*rot_ready.inc())
                dve.wait_ge(*qkT_made.upto(i))
                for a in (0, 64):
                    dve.tensor_copy(qz[a:a + 64].rearrange("p (g b) t -> p b g t", b=2)[:, a // 64],
                                    qkTp[a:a + 64, 0:256].rearrange("p (g t) -> p g t", g=2)).then_inc(*o.inc())
                dve.tensor_copy(kT[:], qkTp[:, 256:512].rearrange("p (g t) -> p g t", g=2)).then_inc(*qk_ready.inc())
                o.settle()
                dve.tensor_tensor(qw[:], qz[:], winter[:], ALU.mult).then_inc(*o.inc())
                dve.wait_ge(*sc_made.upto(i))
                dve.tensor_tensor(probs[:], scp[:].rearrange("p (h t) -> p h t", h=4), dmat[:], ALU.mult)\
                   .then_inc(*probs_ready.inc())
                dve.wait_ge(stored.sem, 16 * i + 1)
                dve.wait_ge(*gate_ready.upto(i))
                dve.wait_ge(*pd_made.upto(i))
                dve.tensor_tensor(cat[:, 512:1024], y0[:], gates[:, p, 512:1024], ALU.mult).then_inc(*od_ready.inc())
                dve.wait_ge(*o_made.upto(i))
                for g in range(4):
                    dve.bn_stats(st6[:, g, :], op[:, g * P:(g + 1) * P]).then_inc(*o.inc())
                o.settle()
                for g in range(4):
                    dve.bn_aggr(mv[:, g, :], st6[:, g, :]).then_inc(*(mv_ready if g == 3 else o).inc())
                dve.wait_ge(*U_made.upto(i))
                for g in range(2):
                    dve.scalar_tensor_tensor(S[:, g, :], S[:, g, :], gammac[:, g:g + 1], Up[:, g * P:(g + 1) * P],
                                             ALU.mult, ALU.add).then_inc(*(S_ready if g else o).inc())
                dve.wait_ge(*rs_ready.upto(i))
                for h in range(4):
                    dve.tensor_scalar(cat[:, h * P:(h + 1) * P], op[:, h * P:(h + 1) * P], mv[:, h, 0:1], rs[:, h:h + 1],
                                      ALU.subtract, ALU.mult).then_inc(*o.inc())
                o.settle()
                dve.tensor_tensor(cat[:, 0:512], cat[:, 0:512], gates[:, p, 0:512], ALU.mult).then_inc(*oc_ready.inc())
                dve.wait_ge(*y_made.upto(i))
                for half in range(2):
                    dve.scalar_tensor_tensor(cat[:, half * 512:(half + 1) * 512], xb[:, p, half * 512:(half + 1) * 512],
                                             ALPHA, (y0, y1)[half][:], ALU.mult, ALU.add)\
                       .then_inc(*(r_ready if half else o).inc())
                dve.wait_ge(*r_ready.upto(i))
                for half in range(2):
                    dve.bn_stats(lnst[:, half, :], cat[:, half * 512:(half + 1) * 512]).then_inc(*o.inc())
                o.settle()
                dve.bn_aggr(lnmv[:], lnst[:].rearrange("p a b -> p (a b)")).then_inc(*lnmv_ready.inc())
                dve.wait_ge(*lnrs_ready.upto(i))
                dve.tensor_scalar(cat[:], cat[:], lnmv[:, 0:1], lnrs[:, 0:1], ALU.subtract, ALU.mult)\
                   .then_inc(*lnn_ready.inc())
                o.end_block()

            over_blocks(dve, body)

        @block.gpsimd
        def _(pool):
            o = Order(pool, orders["pool"])
            pool.wait_ge(loaded.sem, NSMALL)
            pool.wait_ge(*setup.upto(0))

            def body(b):
                i, p = b.i, b.p
                x12 = qk[:, p, :].rearrange("p (h a j) -> p h a j", h=8, a=2)
                cs = over_heads(cos[:, bass.ds(i, 1), :].rearrange("p a j -> p (a j)"), 8)
                pool.wait_ge(*proj_ready.upto(i, 1))
                pool.wait_ge(*rot_ready.before(i))
                pool.tensor_tensor(ra[:], x12[:, :, 0, :], cs, ALU.mult).then_inc(*o.inc())
                pool.tensor_tensor(rd[:], x12[:, :, 1, :], cs, ALU.mult).then_inc(*rot_part.inc())
                pool.wait_ge(*rot_ready.upto(i))
                pool.tensor_tensor(kst[:].rearrange("p (h d) -> p h d", h=4), rot[:, 4:8, :], spread(wstate[:], 64), ALU.mult)\
                    .then_inc(*kst_ready.inc())
                pool.wait_ge(*gsig_ready.upto(i))
                pool.tensor_tensor(gates[:, p, :], gates[:, p, :], gt[:], ALU.mult).then_inc(*o.inc())
                o.settle()
                pool.tensor_tensor(gates[:, p, 0:512], gates[:, p, 0:512], ret_row[:], ALU.mult).then_inc(*o.inc())
                pool.tensor_tensor(gates[:, p, 512:1024], gates[:, p, 512:1024], scale_row[:], ALU.mult)\
                    .then_inc(*gate_ready.inc())
                pool.wait_ge(*lnn_ready.upto(i))
                pool.tensor_tensor(cat[:], cat[:], ln_grow[:], ALU.mult).then_inc(*o.inc())
                o.settle()
                pool.tensor_tensor(cat[:], cat[:], ln_brow[:], ALU.add).then_inc(*out_ready.inc())
                o.end_block()

            over_blocks(pool, body)


LEVELS = (1, 2, 4, 8, 16, 32)
QKV = 1536


def delta_layer(nc, x, c, w_ada, b_ada, g_pre, w_in, conv_w, a_log, dt_bias, g_gdn, g_post, consts, gate_row,
                hT_out, oa_out):
    ident_d, seg_d, big_d, lev_d = consts
    WA = 2056
    wv = w_in.rearrange("(k p) n -> p k n", p=P)
    with ExitStack() as ctx:
        sem = ctx.enter_context(Semaphores(nc, "d_"))

        def sb(name, shape, dt=F32):
            return ctx.enter_context(nc.sbuf_tensor("d_" + name, shape, dt))

        def sig(name, per=1):
            return Signal(sem(name), per)

        W_in = sb("w_in", [P, KT, WA])
        ada = sb("ada", [P, 2, 3 * D])
        ccol = sb("ccol", [P, KT])
        ctmp = sb("ctmp", [P, KT])
        cB = sb("cB", [P, KT, P])
        scale_row = sb("scale_row", [P, D])
        shift_row = sb("shift_row", [P, D])
        xb = sb("xb", [P, 2, D])
        hb = sb("hb", [P, D])
        hT = sb("hT", [P, KT * P])
        xss = sb("xss", [P, 1])
        xrs = sb("xrs", [P, 1])
        eps = sb("eps", [P, 1])
        cv = sb("cv", [P, 2, 12, P + 3])
        convw = sb("convw", [P, 4, 12])
        z = sb("z", [P, 2, 512])
        ba = sb("ba", [P, 2, 8])
        ident = sb("ident", [P, P])
        seg = sb("seg", [P, 4, P])
        big = sb("big", [P, 2, P])
        lev = sb("lev", [P, 6, P])
        eal = sb("eal", [P, 4])
        dtb = sb("dtb", [P, 4])
        gdn_row = sb("gdn_row", [P, P])
        cT = sb("cT", [P, 12, P])
        sg = sb("sg", [P, 12, P])
        ss = sb("ss", [P, 8])
        rs = sb("rs", [P, 8])
        beta = sb("beta", [P, 4])
        ya = sb("ya", [P, 4])
        yb = sb("yb", [P, 4])
        g = sb("g", [P, 4])
        gc = sb("gc", [P, 4])
        ngc = sb("ngc", [P, 4])
        egc = sb("egc", [P, 2, 12])
        bg = sb("bg", [P, 4])
        eG = sb("eG", [P, 4, P])
        gU = sb("gU", [P, 4, P])
        D1 = sb("D1", [P, 4, P])
        D2 = sb("D2", [P, 4, P])
        qn = sb("qn", [P, 4, P])
        kn = sb("kn", [P, 4, P])
        kbg = sb("kbg", [P, 4, P])
        kg = sb("kg", [P, 4, P])
        vb = sb("vb", [P, 4, P])
        qT = sb("qT", [P, 4, P])
        kT = sb("kT", [P, 4, P])
        qgT = qn
        L = sb("L", [P, 4, P])
        Lm = sb("Lm", [P, 4, P])
        Lm2 = sb("Lm2", [P, 4, P])
        T = sb("T", [P, 4, P])
        R = sb("R", [P, 4, P])
        X = sb("X", [P, 4, P])
        attn = sb("attn", [P, 4, P])
        wT = sb("wT", [P, 4, P])
        u = sb("u", [P, 4, P])
        vnew = sb("vnew", [P, 4, P])
        S = sb("S", [P, 4, P])
        sgz = sb("sgz", [P, 512])
        gz = sb("gz", [P, 4, P])
        so = sb("so", [P, 4])
        ro = sb("ro", [P, 4])
        oa = sb("oa", [P, 512])
        ones = sb("ones", [P, P])
        pre_row, post_row = (t[:].rearrange("p n t -> p (n t)")[:, 0:D] for t in (sg, cT))
        bank = [ctx.enter_context(nc.psum_tensor(f"d_ps{n}", [P, 512], F32)) for n in range(8)]
        by_head = [b[:].rearrange("p (h t) -> p h t", h=4) for b in bank]

        loaded, c_loaded, aloaded = sig("loaded"), sig("c_loaded"), [sig("ada0"), sig("ada1")]
        w_parts = [(0, 512), (512, 512), (1024, 512), (QKV, WA - QKV)]
        w_loaded = [sig(f"w_in{n}") for n in range(len(w_parts))]
        c_ready, ada_used, mod_made, mod_ready = sig("c_ready", 3), sig("ada_used"), sig("mod_made"), sig("mod_ready", 3)
        x_in = [sig("x_in0"), sig("x_in1")]
        h_stored, oa_stored, setup = sig("h_stored"), sig("oa_stored"), sig("setup")
        eps_ready, eal_ready = sig("eps"), sig("eal")
        xss_ready, hs_ready, h_ready = sig("xss"), sig("hs"), sig("h_ready")
        hT_made, hT_ready = sig("hT_made", 2), sig("hT_ready", 2)
        proj_made, proj_ready = sig("proj_made", 5), sig("proj_ready", 5)
        halo_ready, conv_ready, cexp_ready, cln_ready, csig_ready, act_ready = sig("halo"), sig("conv"), sig("cexp"), sig("cln"), sig("csig"), sig("silu")
        v_made, rows_made, sq_ready, ss_ready, rs_ready = sig("v_made"), sig("rows_made"), sig("sq"), sig("ss"), sig("rs")
        ba_ready, g_ready, gs_made, ge_ready, gU_ready, G_made = (
            sig("ba"), sig("g"), sig("gs_made"), sig("ge"), sig("gU"), sig("G_made"))
        D_ready, dec_ready, eG_ready = sig("D", 2), sig("dec", 2), sig("eG")
        qkn_ready, kg_ready, vb_ready = sig("qkn"), sig("kg"), sig("vb")
        qkT_made, qT_ready, kT_ready, qg_ready = sig("qkT_made"), sig("qT"), sig("kT"), sig("qg")
        kk_made, L_ready, attn_ready = sig("kk_made"), sig("L"), sig("attn")
        T_ready, T_turned, R_ready = sig("T"), sig("T_turned"), sig("R")
        Lm_ready, X_made, X_ready, RX_made, join_ready = sig("Lm", 5), sig("X_made", 5), sig("X", 5), sig("RX_made", 5), sig("join", 5)
        wu_made, wT_ready, u_ready = sig("wu_made"), sig("wT"), sig("u")
        wS_made, vnew_ready, U_made, S_ready = sig("wS_made", 2), sig("vnew", 2), sig("U_made", 2), sig("S", 2)
        o_made, so_ready, ro_ready, gz_ready, oa_ready = sig("o_made"), sig("so"), sig("ro"), sig("gz"), sig("oa")
        zsig_ready, osq_ready, sp_ready = sig("zsig"), sig("osq"), sig("sp")
        orders = {n: sem("order_" + n) for n in ("act", "dve", "pool")}

        started = [s.start() for s in (proj_ready, oa_ready, hT_made, h_stored, oa_stored)]
        def over_pipeline(eng, body):
            def at(r, p):
                b = Blk(r, p)
                i = 2 * r + p if isinstance(r, int) else 0
                b.last, b.last2, b.last3, b.last5 = (i + n >= BLOCKS for n in (1, 2, 3, 5))
                return b

            with eng.Fori(0, 5) as r:
                body(at(r, 0))
                body(at(r, 1))
            for i in range(10, BLOCKS):
                body(at(i // 2, i % 2))

        block = ctx.enter_context(nc.Block())
        small = [(ident[:], ident_d), (seg[:], seg_d), (big[:], big_d),
                 (lev[:], lev_d), (eal[:], row(a_log)), (dtb[:], row(dt_bias)), (gdn_row[:], row(g_gdn)),
                 (shift_row[:], row(b_ada[0:D])), (scale_row[:], row(b_ada[D:2 * D])), (gate_row[:], row(b_ada[2 * D:3 * D])),
                 (pre_row, row(g_pre)), (post_row, row(g_post))] + [
                 (convw[:, j, :], conv_w[j].rearrange("(k p) -> p k", p=P)) for j in range(4)]
        NSMALL = 16 * len(small)

        @block.sync
        def _(sp):
            for s in started:
                sp.sem_inc(s, 1)
            def load_ada(k):
                sp.dma_start(ada[:, k % 2, :], w_ada[k * P:(k + 1) * P, :]).then_inc(aloaded[k % 2].sem, 16)

            with nc.allow_non_contiguous_dma(reason="small tables"):
                sp.dma_start(ccol[:], c.rearrange("(k p) -> p k", p=P)).then_inc(c_loaded.sem, 16)
                load_ada(0)
                load_ada(1)
                for dst, src in small:
                    sp.dma_start(dst, src).then_inc(loaded.sem, 16)
            sp.dma_start(xb[:, 0, :], x[0:P, :]).then_inc(x_in[0].sem, 16)
            sp.dma_start(xb[:, 1, :], x[P:2 * P, :]).then_inc(x_in[1].sem, 16)
            for k in range(2, KT):
                sp.wait_ge(ada_used.sem, k - 1)
                load_ada(k)
            for (a, n), part in zip(w_parts, w_loaded):
                sp.dma_start(W_in[:, :, a:a + n], wv[:, :, a:a + n]).then_inc(part.sem, 16)
            for i in range(3):
                sp.wait_ge(*hs_ready.upto(i))
                sp.dma_start(xb[:, i % 2, :], x[(i + 2) * P:(i + 3) * P, :]).then_inc(x_in[i % 2].sem, 16)
                if i < 2:
                    sp.wait_ge(*hT_ready.upto(i))
                    sp.dma_start(hT_out[i], hT[:]).then_inc(h_stored.sem, 16)

            def body(b):
                if not b.last2:
                    sp.wait_ge(*hT_ready.upto(b.i + 2))
                    sp.dma_start(hT_out[b.i + 2], hT[:]).then_inc(h_stored.sem, 16)
                if not b.last5:
                    sp.wait_ge(*hs_ready.upto(b.i + 3))
                    sp.dma_start(xb[:, b.q, :], x[bass.ds(b.i * P + 5 * P, P), :]).then_inc(x_in[b.q].sem, 16)
                sp.wait_ge(*oa_ready.upto(b.i))
                sp.dma_start(oa_out[bass.ds(b.i * P, P), :], oa[:]).then_inc(oa_stored.sem, 16)

            over_pipeline(sp, body)
            sp.wait_ge(oa_stored.sem, 16 * BLOCKS + 1)
            sp.wait_ge(h_stored.sem, 16 * BLOCKS + 1)

        @block.tensor
        def _(pe):
            pe.wait_ge(*c_ready.upto(0))
            for k in range(KT):
                pe.wait_ge(aloaded[k % 2].sem, 16 * (k // 2) + 16)
                for n in range(6):
                    m = pe.matmul(bank[n][:], cB[:, k, :], ada[:, k % 2, n * 512:(n + 1) * 512], start=(k == 0), stop=(k == KT - 1))
                m.then_inc(*ada_used.inc())

            def turn_h(i):
                pe.wait_ge(*h_ready.upto(i))
                pe.wait_ge(*proj_ready.before(i))
                for half in range(2):
                    for k in range(4):
                        t = 4 * half + k
                        m = pe.transpose(bank[half][:, k * P:(k + 1) * P], hb[:, t * P:(t + 1) * P], ident[:])
                    m.then_inc(*hT_made.inc())

            def project(i, n):
                c, t = n // 4, n % 4
                if t == 0:
                    if c < 2:
                        pe.wait_ge(*hT_ready.upto(i))
                    else:
                        pe.wait_ge(*proj_ready.upto(i, c - 1))
                if c < 3:
                    for k in range(KT):
                        m = pe.matmul(bank[c % 2][:, t * P:(t + 1) * P], W_in[:, k, (4 * c + t) * P:(4 * c + t + 1) * P],
                                      hT[:, k * P:(k + 1) * P], start=(k == 0), stop=(k == KT - 1))
                elif c == 3:
                    for k in (2 * t, 2 * t + 1):
                        m = pe.matmul(bank[1][:], hT[:, k * P:(k + 1) * P], W_in[:, k, QKV:QKV + 512],
                                      start=(k == 0), stop=(k == KT - 1))
                else:
                    for k in range(KT):
                        m = pe.matmul(bank[0][:, 0:8], hT[:, k * P:(k + 1) * P], W_in[:, k, 2048:2056],
                                      start=(k == 0), stop=(k == KT - 1))
                if t == 3 or c == 4:
                    m.then_inc(*proj_made.inc())

            def decay_sums(i):
                pe.wait_ge(*g_ready.upto(i))
                for n in range(4):
                    m = pe.matmul(bank[4][:, 4 * n:4 * n + 4], seg[:, n, :], g[:], start=True, stop=True)
                m.then_inc(*gs_made.inc())

            def decay_columns(i):
                pe.wait_ge(*gU_ready.upto(i))
                pe.matmul(bank[6][:], ones[:], gU[:].rearrange("p h t -> p (h t)"), start=True, stop=True).then_inc(*G_made.inc())

            def turn_rows(i, n, to, made):
                for t in range(4):
                    m = pe.transpose(bank[to][:, t * P:(t + 1) * P], cT[:, 4 * n + t, :], ident[:])
                if made:
                    m.then_inc(*made.inc())

            def turn_v(i):
                pe.wait_ge(*act_ready.upto(i))
                pe.wait_ge(*ge_ready.upto(i))
                turn_rows(i, 2, 4, v_made)

            def turn_qk(i):
                pe.wait_ge(*D_ready.upto(i))
                turn_rows(i, 1, 6, None)
                pe.wait_ge(*vb_ready.upto(i))
                turn_rows(i, 0, 4, rows_made)

            def turn_normalised(i):
                pe.wait_ge(*qkn_ready.upto(i))
                for n in range(8):
                    m = pe.transpose(bank[(4, 6)[n // 4]][:, (n % 4) * P:(n % 4 + 1) * P], (qn, kn)[n // 4][:, n % 4, :], ident[:])
                m.then_inc(*qkT_made.inc())

            def key_products(i):
                pe.wait_ge(*kT_ready.upto(i))
                pe.wait_ge(*qT_ready.upto(i))
                for h in range(4):
                    pe.matmul(bank[4][:, h * P:(h + 1) * P], kT[:, h, :], kT[:, h, :], start=True, stop=True)
                for h in range(4):
                    m = pe.matmul(bank[6][:, h * P:(h + 1) * P], kT[:, h, :], qT[:, h, :], start=True, stop=True)
                m.then_inc(*kk_made.inc())

            pe.wait_ge(*mod_ready.upto(0, 1))
            turn_h(0)
            for n in range(17):
                if n % 4 == 0 and n < 16:
                    pe.wait_ge(w_loaded[n // 4].sem, 16)
                project(0, n)
            pe.wait_ge(*setup.upto(0))
            turn_h(1)
            stages = {4: decay_sums, 6: decay_columns, 9: turn_v, 11: turn_qk, 13: turn_normalised, 15: key_products}
            for n in range(17):
                if n in stages:
                    stages[n](0)
                project(1, n)

            def body(b):
                i, j, p = b.i, b.i + 1, b.p
                pieces = [] if b.last2 else list(range(17))

                def fill(n=1):
                    for _ in range(n):
                        if pieces:
                            project(b.i + 2, pieces.pop(0))

                pe.wait_ge(*T_ready.upto(i))
                for h in range(4):
                    m = pe.transpose(bank[5][:, h * P:(h + 1) * P], T[:, h, :], ident[:])
                m.then_inc(*T_turned.inc())
                if not b.last2:
                    turn_h(b.i + 2)
                pe.wait_ge(*R_ready.upto(i))
                for s in range(5):
                    pe.wait_ge(*Lm_ready.upto(i, s + 1))
                    if s:
                        pe.wait_ge(*join_ready.upto(i, s))
                    for h in range(4):
                        m = pe.matmul(bank[2][:, h * P:(h + 1) * P], (Lm, Lm2)[s % 2][:, h, :], R[:, h, :], start=True, stop=True)
                    m.then_inc(*X_made.inc())
                    fill()
                    pe.wait_ge(*X_ready.upto(i, s + 1))
                    for h in range(4):
                        m = pe.matmul(bank[3][:, h * P:(h + 1) * P], T[:, h, :], X[:, h, :], start=True, stop=True)
                    if s < 4:
                        for h in range(4):
                            m = pe.matmul(bank[5][:, h * P:(h + 1) * P], X[:, h, :], T[:, h, :], start=True, stop=True)
                    m.then_inc(*RX_made.inc())
                    fill()
                    if not b.last:
                        if s == 1:
                            decay_sums(j)
                        if s == 3:
                            decay_columns(j)
                pe.wait_ge(*join_ready.upto(i))
                pe.wait_ge(*kg_ready.upto(i))
                for h in range(4):
                    pe.matmul(bank[5][:, h * P:(h + 1) * P], kbg[:, h, :], R[:, h, :], start=True, stop=True)
                for h in range(4):
                    m = pe.matmul(bank[3][:, h * P:(h + 1) * P], R[:, h, :], vb[:, h, :], start=True, stop=True)
                m.then_inc(*wu_made.inc())
                fill()
                pe.wait_ge(*u_ready.upto(i))
                pe.wait_ge(*qg_ready.upto(i))
                pe.wait_ge(*oa_ready.before(i))
                for n in range(2):
                    a = 64 * n
                    if n:
                        pe.wait_ge(*S_ready.upto(i, 1))
                    for h in range(4):
                        m = pe.matmul(bank[2][a:a + 64, h * P:(h + 1) * P], wT[:, h, a:a + 64], S[:, h, :], start=True, stop=True)
                    m.then_inc(*wS_made.inc())
                    for h in range(4):
                        pe.matmul(bank[7][a:a + 64, h * P:(h + 1) * P], qgT[:, h, a:a + 64], S[:, h, :],
                                  start=(h == 0), stop=False, skip_group_check=True)
                    if n and not b.last:
                        turn_v(j)
                    pe.wait_ge(*vnew_ready.upto(i, n + 1))
                    for h in range(4):
                        m = pe.matmul(bank[3][:, h * P:(h + 1) * P], kg[a:a + 64, h, :], vnew[a:a + 64, h, :], start=True, stop=True)
                    m.then_inc(*U_made.inc())
                    if n == 0:
                        fill()
                pe.wait_ge(*attn_ready.upto(i))
                for h in range(4):
                    m = pe.matmul(bank[7][:, h * P:(h + 1) * P], attn[:, h, :], vnew[:, h, :], start=False, stop=True,
                                  skip_group_check=True)
                m.then_inc(*o_made.inc())
                if not b.last:
                    turn_qk(j)
                    fill(3)
                    turn_normalised(j)
                    key_products(j)
                fill(17)

            over_pipeline(pe, body)

        @block.scalar
        def _(act):
            o = Order(act, orders["act"])
            act.preload_act_table_set(TABLES)

            def sigmoid(dst, src, done):
                act.activation(dst, src, ACT.Exp, scale=-1.0).then_inc(*o.inc())
                o.settle()
                act.activation(dst, dst, ACT.Ln, bias=1.0).then_inc(*o.inc())
                o.settle()
                act.activation(dst, dst, ACT.Exp, scale=-1.0).then_inc(*done.inc())

            act.wait_ge(c_loaded.sem, 16)
            sigmoid(ctmp[:], ccol[:], c_ready)
            act.wait_ge(loaded.sem, NSMALL)
            act.activation(eal[:], eal[:], ACT.Exp).then_inc(*eal_ready.inc())
            act.wait_ge(*eps_ready.upto(0))

            def norm_x(p):
                act.activation(hb[:], xb[:, p, :], ACT.Square, accum_out=xss[:]).then_inc(*o.inc())
                o.settle()
                act.activation(xrs[:], xss[:], ACT.Ln, bias=eps[:, 0:1], scale=1.0 / D).then_inc(*o.inc())
                o.settle()
                act.activation(xrs[:], xrs[:], ACT.Exp, scale=-0.5).then_inc(*xss_ready.inc())

            def turn_h(i):
                act.wait_ge(h_stored.sem, 16 * i + 1)
                for half in range(2):
                    act.wait_ge(*hT_made.upto(i, half + 1))
                    act.activation(hT[:, half * 512:(half + 1) * 512], bank[half][:], ACT.Copy).then_inc(*hT_ready.inc())

            def project(i, p, c):
                act.wait_ge(*proj_made.upto(i, c + 1))
                if c < 3:
                    act.activation(cv[:, p, 4 * c:4 * c + 4, 3:P + 3], by_head[c % 2], ACT.Copy).then_inc(*proj_ready.inc())
                elif c == 3:
                    act.activation(z[:, p, :], bank[1][:], ACT.Copy).then_inc(*proj_ready.inc())
                else:
                    act.activation(ba[:, p, :], bank[0][:, 0:8], ACT.Copy).then_inc(*proj_ready.inc())

            def softplus(i, p):
                act.wait_ge(*proj_ready.upto(i))
                act.wait_ge(*ba_ready.upto(i))
                act.activation(beta[:], ba[:, p, 0:4], ACT.Exp, scale=-1.0).then_inc(*o.inc())
                act.activation(yb[:], ya[:], ACT.Abs).then_inc(*o.inc())
                o.settle()
                act.activation(beta[:], beta[:], ACT.Ln, bias=1.0).then_inc(*o.inc())
                act.activation(yb[:], yb[:], ACT.Exp, scale=-1.0).then_inc(*o.inc())
                o.settle()
                act.activation(beta[:], beta[:], ACT.Exp, scale=-1.0).then_inc(*o.inc())
                act.activation(yb[:], yb[:], ACT.Ln, bias=1.0).then_inc(*sp_ready.inc())

            def decay_sums(i, p):
                act.wait_ge(*gs_made.upto(i))
                act.activation(gc[:], bank[4][:, 0:4], ACT.Copy).then_inc(*o.inc())
                act.activation(ngc[:], bank[4][:, 0:4], ACT.Copy, scale=-1.0).then_inc(*o.inc())
                act.activation(bg[:], bank[4][:, 0:4], ACT.Exp).then_inc(*o.inc())
                act.activation(egc[:, p, :], bank[4][:, 4:16], ACT.Exp).then_inc(*ge_ready.inc())

            def decay_columns(i):
                act.wait_ge(*G_made.upto(i))
                act.activation(eG[:], by_head[6], ACT.Exp).then_inc(*eG_ready.inc())

            def decays(i):
                act.wait_ge(*D_ready.upto(i))
                for h in range(4):
                    act.activation(D1[:, h, :], D1[:, h, :], ACT.Exp, scale=-1.0, bias=gc[:, h:h + 1])\
                        .then_inc(*(dec_ready if h == 3 else o).inc())
                for h in range(4):
                    act.activation(D2[:, h, :], D2[:, h, :], ACT.Exp, bias=ngc[:, h:h + 1])\
                        .then_inc(*(dec_ready if h == 3 else o).inc())

            def silu_step(i, n):
                if n == 0:
                    act.wait_ge(*conv_ready.upto(i))
                    act.activation(sg[:], cT[:], ACT.Exp, scale=-1.0).then_inc(*cexp_ready.inc())
                elif n == 1:
                    act.wait_ge(*cexp_ready.upto(i))
                    act.activation(sg[:], sg[:], ACT.Ln, bias=1.0).then_inc(*cln_ready.inc())
                else:
                    act.wait_ge(*cln_ready.upto(i))
                    act.activation(sg[:], sg[:], ACT.Exp, scale=-1.0).then_inc(*csig_ready.inc())

            def square_qk(i):
                act.wait_ge(*rows_made.upto(i))
                for n in range(2):
                    act.activation(sg[:, 4 * n:4 * n + 4, :], by_head[(4, 6)[n]], ACT.Square)\
                        .then_inc(*(sq_ready if n else o).inc())

            def root_qk(i):
                act.wait_ge(*ss_ready.upto(i))
                act.activation(rs[:], ss[:], ACT.Ln, bias=eps[:, 0:1]).then_inc(*o.inc())
                o.settle()
                act.activation(rs[:], rs[:], ACT.Exp, scale=-0.5).then_inc(*rs_ready.inc())

            def copy_qT(i):
                act.wait_ge(*qkT_made.upto(i))
                act.activation(qT[:], by_head[4], ACT.Copy).then_inc(*qT_ready.inc())

            def prepare_x(i):
                act.wait_ge(x_in[i % 2].sem, 16 * (i // 2) + 16)
                if i:
                    act.wait_ge(*hT_made.upto(i - 1))
                norm_x(i % 2)

            prepare_x(0)
            turn_h(0)
            prepare_x(1)
            for n in range(5):
                project(0, 0, n)
            softplus(0, 0)
            turn_h(1)
            prepare_x(2)
            decay_sums(0, 0)
            decay_columns(0)
            for n in range(3):
                silu_step(0, n)
            project(1, 1, 0)
            decays(0)
            project(1, 1, 1)
            square_qk(0)
            project(1, 1, 2)
            root_qk(0)
            copy_qT(0)
            project(1, 1, 3)
            project(1, 1, 4)
            o.end_block()

            def body(b):
                i, j, p, q = b.i, b.i + 1, b.p, b.q
                act.wait_ge(*T_turned.upto(i))
                act.activation(R[:], by_head[5], ACT.Copy).then_inc(*R_ready.inc())
                if not b.last:
                    softplus(j, q)
                if not b.last2:
                    turn_h(b.i + 2)
                for s in range(5):
                    act.wait_ge(*X_made.upto(i, s + 1))
                    act.activation(X[:], by_head[2], ACT.Copy).then_inc(*X_ready.inc())
                    if s == 0:
                        sigmoid(sgz[:], z[:, p, :], zsig_ready)
                    if s == 1 and not b.last3:
                        act.wait_ge(x_in[q].sem, 16 * (b.r + p) + 32)
                        act.wait_ge(*hT_made.upto(b.i + 2))
                        norm_x(q)
                    if s == 2:
                        if not b.last:
                            decay_sums(j, q)
                        if not b.last2:
                            project(b.i + 2, p, 0)
                    if s == 3 and not b.last:
                        silu_step(j, 0)
                    if s == 4:
                        if not b.last:
                            decay_columns(j)
                            silu_step(j, 1)
                        if not b.last2:
                            project(b.i + 2, p, 1)
                act.wait_ge(*wu_made.upto(i))
                act.activation(wT[:], by_head[5], ACT.Copy).then_inc(*wT_ready.inc())
                act.activation(u[:], by_head[3], ACT.Copy).then_inc(*u_ready.inc())
                if not b.last:
                    silu_step(j, 2)
                    decays(j)
                if not b.last2:
                    project(b.i + 2, p, 2)
                act.wait_ge(*o_made.upto(i))
                act.activation(X[:], by_head[7], ACT.Square).then_inc(*osq_ready.inc())
                if not b.last:
                    square_qk(j)
                act.wait_ge(*so_ready.upto(i))
                act.activation(ro[:], so[:], ACT.Ln, bias=eps[:, 0:1], scale=1.0 / P).then_inc(*o.inc())
                o.settle()
                act.activation(ro[:], ro[:], ACT.Exp, scale=-0.5).then_inc(*ro_ready.inc())
                if not b.last:
                    root_qk(j)
                    copy_qT(j)
                if not b.last2:
                    project(b.i + 2, p, 3)
                    project(b.i + 2, p, 4)
                o.end_block()

            over_pipeline(act, body)

        @block.vector
        def _(dve):
            o = Order(dve, orders["dve"])
            dve.memset(eps[:], RMS_EPS).then_inc(*eps_ready.inc())
            dve.wait_ge(*c_ready.upto(0, 1))
            dve.tensor_tensor(ctmp[:], ctmp[:], ccol[:], ALU.mult).then_inc(*c_ready.inc())
            dve.wait_ge(*c_ready.upto(0, 2))
            dve.tensor_copy(cB[:], spread(ctmp[:], P)).then_inc(*c_ready.inc())
            dve.memset(S[:], 0.0).then_inc(*o.inc())
            dve.memset(ones[:], 1.0).then_inc(*o.inc())
            dve.memset(cv[:, 0, :, 0:3], 0.0).then_inc(*o.inc())
            dve.wait_ge(loaded.sem, NSMALL)
            dve.wait_ge(ada_used.sem, KT)

            def add_row(which, dst, done):
                for half in range(2):
                    dve.tensor_tensor(dst[:, half * 512:(half + 1) * 512], dst[:, half * 512:(half + 1) * 512],
                                      bank[2 * which + half][:], ALU.add).then_inc(*(done if half else o).inc())

            add_row(1, scale_row, o)
            add_row(0, shift_row, mod_ready)
            dve.wait_ge(*mod_ready.upto(0, 1))
            dve.scalar_tensor_tensor(scale_row[:], scale_row[:], 1.0, pre_row, ALU.add, ALU.mult).then_inc(*mod_ready.inc())
            dve.wait_ge(*mod_ready.upto(0, 2))

            def make_h(i, p):
                dve.wait_ge(*hT_made.before(i))
                dve.wait_ge(*xss_ready.upto(i))
                dve.scalar_tensor_tensor(hb[:], xb[:, p, :], xrs[:, 0:1], scale_row[:], ALU.mult, ALU.mult)\
                   .then_inc(*hs_ready.inc())

            def add_dt_bias(i, p, last=False):
                dve.wait_ge(*proj_ready.upto(i))
                dve.tensor_tensor(ya[:], ba[:, p, 4:8], dtb[:], ALU.add).then_inc(*ba_ready.inc())
                if not last:
                    dve.tensor_copy(cv[:, 1 - p, :, 0:3], cv[:, p, :, P:P + 3]).then_inc(*o.inc())

            def convolve(i, p, j):
                o.settle()
                for t in range(12):
                    if j == 0:
                        m = dve.tensor_scalar(cT[:, t, :], cv[:, p, t, 0:P], convw[:, 0, t:t + 1], None, ALU.mult)
                    else:
                        m = dve.scalar_tensor_tensor(cT[:, t, :], cv[:, p, t, j:j + P], convw[:, j, t:t + 1], cT[:, t, :],
                                                     ALU.mult, ALU.add)
                    m.then_inc(*(conv_ready if j == 3 and t == 11 else o).inc())

            def log_decay(i):
                dve.wait_ge(*sp_ready.upto(i))
                dve.scalar_tensor_tensor(g[:], ya[:], 0.0, yb[:], ALU.max, ALU.add).then_inc(*o.inc())
                o.settle()
                dve.tensor_tensor(g[:], g[:], eal[:], ALU.mult).then_inc(*g_ready.inc())

            def decays(i):
                dve.wait_ge(*ge_ready.upto(i))
                dve.tensor_tensor(bg[:], bg[:], beta[:], ALU.mult).then_inc(*o.inc())
                dve.wait_ge(*eG_ready.upto(i))
                dve.tensor_tensor(D1[:], by_head[6], over_heads(big[:, 0, :], 4), ALU.add).then_inc(*D_ready.inc())
                dve.tensor_tensor(D2[:], by_head[6], over_heads(big[:, 1, :], 4), ALU.subtract).then_inc(*D_ready.inc())

            def silu(i):
                dve.wait_ge(*csig_ready.upto(i))
                dve.tensor_tensor(cT[:], cT[:], sg[:], ALU.mult).then_inc(*act_ready.inc())

            def weigh_v(i):
                dve.wait_ge(*v_made.upto(i))
                dve.tensor_tensor(vb[:], by_head[4], spread(beta[:], P), ALU.mult).then_inc(*vb_ready.inc())

            def sums_qk(i):
                dve.wait_ge(*sq_ready.upto(i))
                dve.tensor_reduce(ss[:], sg[:, 0:8, :], AX.X, ALU.add).then_inc(*ss_ready.inc())

            def normalise_qk(i):
                dve.wait_ge(*rs_ready.upto(i))
                dve.tensor_scalar_mul(rs[:, 0:4], rs[:, 0:4], float(P) ** -0.5).then_inc(*o.inc())
                dve.tensor_tensor(kn[:], by_head[6], spread(rs[:, 4:8], P), ALU.mult).then_inc(*o.inc())
                o.settle()
                dve.tensor_tensor(qn[:], by_head[4], spread(rs[:, 0:4], P), ALU.mult).then_inc(*qkn_ready.inc())

            def copy_kT(i):
                dve.wait_ge(*qkT_made.upto(i))
                dve.tensor_copy(kT[:], by_head[6]).then_inc(*kT_ready.inc())

            def mask_products(i):
                dve.wait_ge(*dec_ready.upto(i))
                dve.wait_ge(*kk_made.upto(i))
                for h in range(4):
                    dve.scalar_tensor_tensor(L[:, h, :], by_head[4][:, h, :], beta[:, h:h + 1], D1[:, h, :],
                                             ALU.mult, ALU.mult).then_inc(*(L_ready if h == 3 else o).inc())
                dve.tensor_tensor(attn[:], by_head[6], D2[:], ALU.mult).then_inc(*attn_ready.inc())

            make_h(0, 0)
            add_row(2, gate_row, o)
            o.settle()
            dve.tensor_tensor(gate_row[:], gate_row[:], post_row, ALU.mult).then_inc(*mod_ready.inc())
            dve.wait_ge(*mod_ready.upto(0))
            dve.wait_ge(*eal_ready.upto(0))
            dve.tensor_scalar_mul(eal[:], eal[:], -1.0).then_inc(*setup.inc())
            make_h(1, 1)
            add_dt_bias(0, 0)
            for j in range(4):
                convolve(0, 0, j)
            log_decay(0)
            make_h(2, 0)
            for stage in (decays, silu, weigh_v, sums_qk, normalise_qk, copy_kT, mask_products):
                stage(0)
            o.end_block()

            def body(b):
                i, j, p, q = b.i, b.i + 1, b.p, b.q
                dve.wait_ge(*L_ready.upto(i))
                dve.tensor_tensor(T[:], L[:], over_heads(lev[:, 0, :], 4), ALU.mult).then_inc(*o.inc())
                o.settle()
                dve.tensor_tensor(T[:], over_heads(ident[:], 4), T[:], ALU.subtract).then_inc(*T_ready.inc())
                if not b.last:
                    add_dt_bias(j, q, last=b.last2)
                    convolve(j, q, 0)
                dve.wait_ge(*R_ready.upto(i))
                for s in range(5):
                    dve.wait_ge(*RX_made.upto(i, s + 1))
                    if s < 4:
                        dve.tensor_tensor(T[:], T[:], by_head[5], ALU.subtract).then_inc(*o.inc())
                    dve.tensor_tensor(R[:], R[:], by_head[3], ALU.subtract).then_inc(*join_ready.inc())
                    dve.wait_ge(*join_ready.upto(i, s + 1))
                    if not b.last:
                        if s == 0:
                            log_decay(j)
                        if s < 3:
                            convolve(j, q, s + 1)
                    if s == 3 and not b.last3:
                        make_h(b.i + 3, q)
                if not b.last:
                    decays(j)
                dve.wait_ge(*u_ready.upto(i))
                for n in range(2):
                    a = 64 * n
                    dve.wait_ge(*wS_made.upto(i, n + 1))
                    dve.tensor_tensor(vnew[a:a + 64], u[a:a + 64], by_head[2][a:a + 64], ALU.subtract).then_inc(*vnew_ready.inc())
                    if not b.last:
                        (silu, weigh_v)[n](j)
                    dve.wait_ge(*U_made.upto(i, n + 1))
                    for h in range(4):
                        dve.scalar_tensor_tensor(S[:, h, :], S[:, h, :], egc[:, p, 4 + 4 * n + h:5 + 4 * n + h],
                                                 by_head[3][:, h, :], ALU.mult, ALU.add)\
                           .then_inc(*(S_ready if h == 3 else o).inc())
                    dve.wait_ge(*S_ready.upto(i, n + 1))
                dve.wait_ge(*osq_ready.upto(i))
                dve.tensor_reduce(so[:], X[:], AX.X, ALU.add).then_inc(*so_ready.inc())
                if not b.last:
                    sums_qk(j)
                dve.wait_ge(*ro_ready.upto(i))
                dve.wait_ge(*gz_ready.upto(i))
                dve.wait_ge(oa_stored.sem, 16 * i + 1)
                for h in range(4):
                    dve.scalar_tensor_tensor(oa[:, h * P:(h + 1) * P], by_head[7][:, h, :], ro[:, h:h + 1], gz[:, h, :],
                                             ALU.mult, ALU.mult).then_inc(*(oa_ready if h == 3 else o).inc())
                if not b.last:
                    for stage in (normalise_qk, copy_kT, mask_products):
                        stage(j)
                o.end_block()

            over_pipeline(dve, body)

        @block.gpsimd
        def _(pool):
            o = Order(pool, orders["pool"])
            pool.wait_ge(loaded.sem, NSMALL)
            pool.wait_ge(*mod_ready.upto(0, 1))

            def shift_h(i):
                pool.wait_ge(*hs_ready.upto(i))
                pool.tensor_tensor(hb[:], hb[:], shift_row[:], ALU.add).then_inc(*h_ready.inc())

            def spread_g(i):
                pool.wait_ge(*g_ready.upto(i))
                pool.tensor_tensor(gU[:], over_heads(seg[:, 0, :], 4), spread(g[:], P), ALU.mult).then_inc(*gU_ready.inc())

            def decay_keys(i, p):
                pool.wait_ge(*qkn_ready.upto(i))
                pool.tensor_tensor(kbg[:], kn[:], spread(bg[:], P), ALU.mult).then_inc(*o.inc())
                pool.tensor_tensor(kg[:], kn[:], spread(egc[:, p, 0:4], P), ALU.mult).then_inc(*kg_ready.inc())

            def decay_q(i):
                pool.wait_ge(*qT_ready.upto(i))
                pool.tensor_tensor(qgT[:], qT[:], eG[:], ALU.mult).then_inc(*qg_ready.inc())

            shift_h(0)
            shift_h(1)
            spread_g(0)
            shift_h(2)
            decay_keys(0, 0)
            decay_q(0)
            o.end_block()

            def body(b):
                i, j, p = b.i, b.i + 1, b.p
                pool.wait_ge(*L_ready.upto(i))
                for s in range(5):
                    if s >= 2:
                        pool.wait_ge(*X_made.upto(i, s - 1))
                    pool.tensor_tensor((Lm, Lm2)[s % 2][:], L[:], over_heads(lev[:, s + 1, :], 4), ALU.mult)\
                        .then_inc(*Lm_ready.inc())
                    if s == 1 and not b.last:
                        spread_g(j)
                pool.wait_ge(*zsig_ready.upto(i))
                pool.tensor_tensor(sgz[:], sgz[:], z[:, p, :], ALU.mult).then_inc(*o.inc())
                o.settle()
                pool.tensor_tensor(gz[:], sgz[:].rearrange("p (h t) -> p h t", h=4), over_heads(gdn_row[:], 4), ALU.mult)\
                    .then_inc(*gz_ready.inc())
                if not b.last3:
                    shift_h(b.i + 3)
                if not b.last:
                    decay_keys(j, b.q)
                    decay_q(j)
                o.end_block()

            over_pipeline(pool, body)


IDX_HEADS, IDX_DIM = 8, 64
TOPK = 256
N_BUCKETS = 32
WIDE = 512
ROUNDS = 14
FIRST_TOPK = TOPK // P
SHARES = ((1, 2), (2, 2), (2, 2), (3, 0))
FAR = 1e30


def key_chunks(i):
    return [(a, min(WIDE, (i + 1) * P - a)) for a in range(0, (i + 1) * P, WIDE)]


def score_order(i):
    pieces = key_chunks(i)
    return [(pieces[c], h) for first in range(0, len(pieces), 2) for h in range(IDX_HEADS)
            for c in range(first, min(first + 2, len(pieces)))]


class Varied(Signal):

    def __init__(self, sem, counts):
        self.sem, self.counts, self.first = sem, counts, 0

    def upto(self, i, k=None):
        return self.sem, sum(self.counts[:i]) + (self.counts[i] if k is None else k)


def sparse_layer(nc, x, w_in, g_kv, w_uv, rel_bias, w_out, consts, gate_row, hT_in, oa_in, bias_scratch, out):
    ident_d, flip_d, late_d, onehot_d, iota_d, halves_d = consts
    C0 = 2056
    O_QB, O_CKV, O_Z, O_IQ, O_IK, O_IW = 0, 512, 640, 1152, 1664, 1792
    WB = 1800
    wv = w_in.rearrange("(k p) n -> p k n", p=P)
    with ExitStack() as ctx:
        sem = ctx.enter_context(Semaphores(nc, "s_"))

        def sb(name, shape, dt=F32):
            return ctx.enter_context(nc.sbuf_tensor("s_" + name, shape, dt))

        def sig(name, per=1):
            return Signal(sem(name), per)

        W_in = sb("w_in", [P, KT, WB])
        W_out = sb("w_out", [P, KT, D])
        ikT = sb("ikT", [P, SEQ])
        ckvT = sb("ckvT", [P, SEQ])
        ckvr = sb("ckvr", [P, BLOCKS, P])
        hT = sb("hT", [P, KT * P])
        pT = sb("pT", [P, 4, 4, P])
        Lg = sb("Lg", [P, 2, SEQ])
        acc = sb("acc", [P, SEQ])
        selb = sb("selb", [P, SEQ])
        passed = sb("passed", [P, SEQ], BF16)
        cat = sb("cat", [P, D])
        catT = sb("catT", [P, D])
        xb = sb("xb", [P, D])
        sgz = sb("sgz", [P, 512])
        iqT = sb("iqT", [P, 4, P])
        qbT = sb("qbT", [P, 2, 4, P])
        z = sb("z", [P, 2, 512])
        ckv = sb("ckv", [P, P])
        iw = sb("iw", [P, IDX_HEADS])
        ident = sb("ident", [P, P])
        flip = sb("flip", [P, P])
        late = sb("late", [P, P])
        onehot = sb("onehot", [N_BUCKETS, 384])
        rb = sb("rb", [N_BUCKETS, 4])
        rb31 = sb("rb31", [N_BUCKETS, 4])
        bias = sb("bias", [P, 4, 2 * P])
        vec = sb("vec", [4, 384])
        iota = sb("iota", [P, 8])
        halves = sb("halves", [P, ROUNDS + 1])
        kv_row = sb("kv_row", [P, P])
        uv = sb("uv", [P, 4, P])
        ones = sb("ones", [P, 1])
        eps = sb("eps", [P, 1])
        css = sb("css", [P, 1])
        crs = sb("crs", [P, 1])
        cn = sb("cn", [P, P])
        csq = sb("csq", [P, P])
        lo = sb("lo", [P, 1])
        hi = sb("hi", [P, 1])
        mid = sb("mid", [P, 1])
        nmid = sb("nmid", [P, 1])
        excess = sb("excess", [P, 1])
        above = sb("above", [P, 1])
        few = sb("few", [P, 1])
        cnt = sb("cnt", [P, 1])
        step = sb("step", [P, 1])
        steps = sb("steps", [P, ROUNDS + 1])
        nsteps = sb("nsteps", [P, ROUNDS + 1])
        best = sb("best", [P, 8])
        match = sb("match", [P, 8])
        thr = sb("thr", [P, 1])
        bad = sb("bad", [P, 2])
        nbad = sb("nbad", [1, 2], I32)
        mx = sb("mx", [P, 4])
        psum_ = sb("psums", [P, 4])
        prec = sb("prec", [P, 4])
        oT = sb("oT", [P, 4, P])
        mss = sb("mss", [P, 2])
        mrs = sb("mrs", [P, 1])
        squares = catT
        relu = Lg[:, 1, :].rearrange("p (n c) -> p n c", n=4)
        work, other = Lg[:, 0, :], pT[:].rearrange("p n b t -> p (n b t)")
        bank = [ctx.enter_context(nc.psum_tensor(f"s_ps{n}", [P, 512], F32)) for n in range(8)]
        by_head = [b[:].rearrange("p (h t) -> p h t", h=4) for b in bank]
        LG_BANKS, IDX_BANKS = (2, 3, 4), (2, 3, 5, 4)

        pieces = [len(key_chunks(i)) for i in range(BLOCKS)]
        scored = [8 * n if i >= FIRST_TOPK else 0 for i, n in enumerate(pieces)]
        loaded, loaded2, wout_loaded = sig("loaded"), sig("loaded2"), sig("w_out")
        w_parts = [[(O_IQ, C0 + O_IQ, 576)], [(O_CKV, C0 + O_CKV, 128), (O_IK + 64, C0 + O_IK, 72)],
                   [(O_QB, C0 + O_QB, 512)], [(O_Z, C0 + O_Z, 512)]]
        w_loaded = [sig(f"w_in{n}") for n in range(len(w_parts))]
        h_in, x_in, oa_in_s, stored = sig("h_in"), sig("x_in"), sig("oa_in"), sig("stored")
        rb_ready, vec_made, vec_ready, vec_stored, bias_made, bias_ready = (
            sig("rb"), sig("vec_made"), sig("vec"), sig("vec_stored"), sig("bias_made", 2), sig("bias", 2))
        proj_made, proj_ready = sig("proj_made", 4), sig("proj_ready", 4)
        crs_ready, cn_ready, ckvr_ready, cT_made, cT_ready = sig("crs"), sig("cn"), sig("ckvr"), sig("cT_made"), sig("cT")
        idx_made, relu_ready, relu_used = (Varied(sem(n), scored) for n in ("idx_made", "relu", "relu_used"))
        found = [1 if i >= FIRST_TOPK else 0 for i in range(BLOCKS)]
        bad_ready, nbad_made, nbad_ready = (Varied(sem(n), found) for n in ("bad", "nbad_made", "nbad"))
        turn_act, turn_dve = (Varied(sem(n), [3 * f for f in found]) for n in ("turn_act", "turn_dve"))
        eps_ready, selb_ready = sig("eps"), sig("selb")
        lg_made, lg_read, pt_made, pt_ready, pv_made = (
            Varied(sem(n), [4 * n for n in pieces]) for n in ("lg_made", "lg_read", "pt_made", "pt", "pv_made"))
        mx_ready, exp_ready = sig("mx", 4), sig("exp", 4)
        zsig_ready, gz_ready, oT_ready, uv_made, ob_ready = sig("zsig"), sig("gz"), sig("oT"), sig("uv_made"), sig("ob")
        catT_made, catT_ready, y_made, mss_ready, mrs_ready, mix_ready, out_ready = (
            sig("catT_made", 2), sig("catT", 2), sig("y_made"), sig("mss"), sig("mrs"), sig("mix"), sig("out_ready"))
        branch = sem("branch")
        orders = {n: sem("order_" + n) for n in ("act", "dve", "pool")}

        block = ctx.enter_context(nc.Block())
        small = [(rb[:], rel_bias), (rb31[:], row(rel_bias[N_BUCKETS - 1], N_BUCKETS)), (onehot[:], onehot_d),
                 (flip[:], flip_d), (ident[:], ident_d), (late[:], late_d), (iota[:], iota_d),
                 (halves[:], halves_d), (kv_row[:], row(g_kv)), (uv[:], w_uv.rearrange("h r d -> r h d"))]
        NSMALL = 16 * len(small)

        @block.sync
        def _(sp):
            with nc.allow_non_contiguous_dma(reason="small tables"):
                for dst, src in small:
                    sp.dma_start(dst, src).then_inc(loaded.sem, 16)
                sp.dma_start(hT[:], hT_in[0]).then_inc(h_in.sem, 16)
                for part, ready in zip(w_parts, w_loaded):
                    for to, a, n in part:
                        sp.dma_start(W_in[:, :, to:to + n], wv[:, :, a:a + n]).then_inc(ready.sem, 16)
                sp.dma_start(W_out[:], w_out.rearrange("(k p) n -> p k n", p=P)).then_inc(wout_loaded.sem, 16)
                sp.wait_ge(*vec_ready.upto(0))
                sp.dma_start(bias_scratch, vec[:]).then_inc(vec_stored.sem, 16)
                sp.wait_ge(vec_stored.sem, 16)
                for h in range(4):
                    src = bias_scratch[h]
                    src = bass.AP(src.tensor, src.offset, [[1, P], [1, 2 * P]])
                    sp.dma_start(acc[:, h * 2 * P:(h + 1) * 2 * P], src).then_inc(loaded2.sem, 16)
            sp.wait_ge(*proj_ready.upto(0))
            sp.dma_start(hT[:], hT_in[1]).then_inc(h_in.sem, 16)
            for i in range(BLOCKS):
                if i == 0:
                    sp.dma_start(xb[:], x[0:P, :]).then_inc(x_in.sem, 16)
                    sp.dma_start(cat[:, 0:512], oa_in[0:P, :]).then_inc(oa_in_s.sem, 16)
                    sp.wait_ge(*proj_ready.upto(1))
                    sp.dma_start(hT[:], hT_in[2]).then_inc(h_in.sem, 16)
                if i + 3 < BLOCKS:
                    sp.wait_ge(*proj_ready.upto(i + 2))
                    sp.dma_start(hT[:], hT_in[i + 3]).then_inc(h_in.sem, 16)
                sp.wait_ge(*out_ready.upto(i))
                sp.dma_start(out[i * P:(i + 1) * P, :], xb[:]).then_inc(stored.sem, 16)
                if i + 1 < BLOCKS:
                    sp.dma_start(cat[:, 0:512], oa_in[(i + 1) * P:(i + 2) * P, :]).then_inc(oa_in_s.sem, 16)
                sp.wait_ge(stored.sem, 16 * (i + 1))
                if i + 1 < BLOCKS:
                    sp.dma_start(xb[:], x[(i + 1) * P:(i + 2) * P, :]).then_inc(x_in.sem, 16)

        @block.tensor
        def _(pe):
            def tile_of(c, t):
                a = (O_IQ, O_IK, O_QB)[c] + t * P
                return slice(a, a + P)

            def project(i, c, tiles=None):
                if i >= BLOCKS:
                    return
                tiles = tiles or range((4, 1, 4, 4)[c])
                last = c == 1 or 3 in tiles
                if c == 0:
                    pe.wait_ge(h_in.sem, 16 * i + 16)
                if 4 * i + c >= 2:
                    pe.wait_ge(*proj_ready.upto(0, 4 * i + c - 1))
                out_ = bank[c % 2]
                if c < 3:
                    for t in tiles:
                        for k in range(KT):
                            m = pe.matmul(out_[:, t * P:(t + 1) * P], W_in[:, k, tile_of(c, t)], hT[:, k * P:(k + 1) * P],
                                          start=(k == 0), stop=(k == KT - 1))
                for a, n, at in {1: [(O_CKV, P, P), (O_IW, 8, 2 * P)], 3: [(O_Z, 512, 0)]}.get(c, []):
                    for k in range(KT) if c == 1 else [2 * t + u for t in tiles for u in range(2)]:
                        m = pe.matmul(out_[:, at:at + n], hT[:, k * P:(k + 1) * P], W_in[:, k, a:a + n],
                                      start=(k == 0), stop=(k == KT - 1))
                if last:
                    m.then_inc(*proj_made.inc())

            def transpose_ckv(i):
                if i >= BLOCKS:
                    return
                pe.wait_ge(*cn_ready.upto(i))
                pe.transpose(bank[4][:, 0:P], cn[:], ident[:]).then_inc(*cT_made.inc())

            pe.wait_ge(loaded.sem, NSMALL)
            pe.wait_ge(*rb_ready.upto(0))
            pe.matmul(bank[2][0:4, 0:384], rb[:], onehot[:], start=True, stop=True).then_inc(*vec_made.inc())
            for c in range(4):
                pe.wait_ge(w_loaded[c].sem, 16 * len(w_parts[c]))
                project(0, c)
            pe.wait_ge(loaded2.sem, 64)
            for n in range(2):
                pe.matmul(bank[3 + n][:], flip[:], acc[:, n * 512:(n + 1) * 512], start=True, stop=True).then_inc(*bias_made.inc())
            pe.wait_ge(*bias_ready.upto(0))
            transpose_ckv(0)
            for c in range(4):
                project(1, c)
            pe.wait_ge(*cT_ready.upto(0))
            transpose_ckv(1)
            pe.wait_ge(wout_loaded.sem, 16)

            for i in range(BLOCKS):
                n_pieces = pieces[i]
                pe.wait_ge(*cT_ready.upto(min(i + 1, BLOCKS - 1)))
                pe.wait_ge(*ckvr_ready.upto(i))
                pe.wait_ge(*proj_ready.upto(i))
                if i >= FIRST_TOPK:
                    pe.wait_ge(*nbad_ready.upto(i))

                def logits(h, c):
                    if h == 4:
                        return
                    a, w = key_chunks(i)[c]
                    n = h * n_pieces + c
                    if n >= 3:
                        pe.wait_ge(*lg_read.upto(i, n - 2))
                    elif FIRST_TOPK <= i + 1 < BLOCKS:
                        pe.wait_ge(*relu_ready.upto(i + 1, scored[i + 1] - (3, 2, 0)[n]))
                    pe.matmul(bank[LG_BANKS[n % 3]][:, 0:w], qbT[:, i % 2, h, :], ckvT[:, a:a + w],
                              start=True, stop=True).then_inc(*lg_made.inc())

                def transpose(h, c):
                    n = h * n_pieces + c
                    if n >= 2:
                        pe.wait_ge(*pt_ready.upto(i, n - 1))
                    a, w = key_chunks(i)[c]
                    for t in range(w // P):
                        m = pe.transpose(bank[6 + n % 2][:, t * P:(t + 1) * P], Lg[:, h % 2, a + t * P:a + (t + 1) * P], ident[:])
                    m.then_inc(*pt_made.inc())

                def values(h, c):
                    n = h * n_pieces + c
                    pe.wait_ge(*pt_ready.upto(i, n + 1))
                    a, w = key_chunks(i)[c]
                    for t in range(w // P):
                        m = pe.matmul(bank[5][:, h * P:(h + 1) * P], ckvr[:, a // P + t, :], pT[:, n % 4, t, :],
                                      start=(c == 0 and t == 0), stop=(a + (t + 1) * P == (i + 1) * P))
                    m.then_inc(*pv_made.inc())

                for c in range(n_pieces):
                    logits(0, c)
                for h in range(4):
                    if h == 0:
                        project(i + 2, 0, (0, 1, 2))
                        if i:
                            pe.wait_ge(*mix_ready.upto(i - 1))
                    elif h == 1:
                        project(i + 2, 0, (3,))
                        project(i + 2, 1)
                    elif h == 2:
                        project(i + 2, 2, (0, 1))
                    else:
                        project(i + 2, 2, (2, 3))
                    lead = min(3, n_pieces) if i >= BLOCKS - 1 else 0
                    for c in range(lead):
                        logits(h + 1, c)
                    pe.wait_ge(*exp_ready.upto(i, h + 1))
                    transpose(h, 0)
                    for c in range(n_pieces):
                        if c + lead < n_pieces:
                            logits(h + 1, c + lead)
                        if c + 1 < n_pieces:
                            transpose(h, c + 1)
                        values(h, c)
                pe.wait_ge(oa_in_s.sem, 16 * i + 16)
                pe.wait_ge(*lg_read.upto(i))
                for half in range(2):
                    if half:
                        project(i + 2, 3, (0, 1))
                        pe.wait_ge(*oT_ready.upto(i))
                        for h in range(4):
                            m = pe.matmul(bank[5][:, h * P:(h + 1) * P], oT[:, h, :], uv[:, h, :], start=True, stop=True)
                        m.then_inc(*uv_made.inc())
                        transpose_ckv(i + 2)
                        project(i + 2, 3, (2, 3))
                        pe.wait_ge(*ob_ready.upto(i))
                    for k in range(4):
                        t = 4 * half + k
                        m = pe.transpose(bank[2 + half][:, k * P:(k + 1) * P], cat[:, t * P:(t + 1) * P], ident[:])
                    m.then_inc(*catT_made.inc())
                for half in range(2):
                    for k in range(KT):
                        if not half:
                            pe.wait_ge(*catT_ready.upto(i, 1 + k // 4))
                        m = pe.matmul(bank[6 + half][:], catT[:, k * P:(k + 1) * P],
                                      W_out[:, k, half * 512:(half + 1) * 512], start=(k == 0), stop=(k == KT - 1))
                        if (half, k) == (0, KT - 1) and FIRST_TOPK <= i + 1 < BLOCKS:
                            pe.wait_ge(*cT_ready.upto(min(i + 2, BLOCKS - 1)))
                            pe.wait_ge(*bad_ready.upto(i + 1))
                            pe.matmul(bank[4][0:1, 0:2], ones[:], bad[:], start=True, stop=True).then_inc(*nbad_made.inc())
                m.then_inc(*y_made.inc())
                if i + 2 < BLOCKS:
                    pe.wait_ge(*proj_ready.upto(i + 2, 2))
                    for n in range(scored[i + 2]):
                        (a, w), h = score_order(i + 2)[n]
                        o = 64 * (h % 2)
                        if n >= 4:
                            pe.wait_ge(*relu_ready.upto(i + 2, n - 3))
                        if n == 3:
                            pe.wait_ge(*cT_ready.upto(i + 2))
                            if FIRST_TOPK <= i + 1:
                                pe.wait_ge(*nbad_ready.upto(i + 1))
                        pe.matmul(bank[IDX_BANKS[n % 4]][:, 0:w], iqT[o:o + 64, h // 2, :], ikT[o:o + 64, a:a + w],
                                  start=True, stop=True).then_inc(*idx_made.inc())

        @block.scalar
        def _(act):
            o = Order(act, orders["act"])
            act.preload_act_table_set(TABLES)

            def project(i, c):
                if i >= BLOCKS:
                    return
                act.wait_ge(*proj_made.upto(i, c + 1))
                if c == 0:
                    act.activation(iqT[:], by_head[0], ACT.Copy).then_inc(*proj_ready.inc())
                elif c == 1:
                    act.activation(ikT[:, i * P:(i + 1) * P], bank[1][:, 0:P], ACT.Copy).then_inc(*o.inc())
                    act.activation(ckv[:], bank[1][:, P:2 * P], ACT.Copy).then_inc(*o.inc())
                    act.activation(iw[:], bank[1][:, 2 * P:2 * P + 8], ACT.Copy,
                                   scale=IDX_HEADS ** -0.5 * IDX_DIM ** -0.5).then_inc(*o.inc())
                    o.settle()
                    act.activation(csq[:], ckv[:], ACT.Square, accum_out=css[:]).then_inc(*proj_ready.inc())
                    act.wait_ge(*proj_ready.upto(i, 2))
                    act.activation(crs[:], css[:], ACT.Ln, bias=eps[:, 0:1], scale=1.0 / P).then_inc(*o.inc())
                    o.settle()
                    act.activation(crs[:], crs[:], ACT.Exp, scale=-0.5).then_inc(*crs_ready.inc())
                elif c == 2:
                    act.activation(qbT[:, i % 2], by_head[0], ACT.Copy).then_inc(*proj_ready.inc())
                else:
                    act.activation(z[:, i % 2, :], bank[1][:], ACT.Copy).then_inc(*proj_ready.inc())

            def copy_ckvT(i):
                if i >= BLOCKS:
                    return
                act.wait_ge(*cT_made.upto(i))
                act.activation(ckvT[:, i * P:(i + 1) * P], bank[4][:, 0:P], ACT.Copy).then_inc(*cT_ready.inc())

            def search(j, turn, k):
                n = sum(a + b for a, b in SHARES[:turn]) + SHARES[turn][0] + k
                if k == 0:
                    act.wait_ge(*turn_act.upto(j, turn + 1))
                o.settle()
                act.activation(passed[:, 0:(j + 1) * P], acc[:, 0:(j + 1) * P], ACT.Sign, bias=nmid[:, 0:1],
                               accum_out=excess[:]).then_inc(*o.inc())
                o.settle()
                act.activation(above[:], excess[:], ACT.Sign, bias=few[:, 0:1]).then_inc(*o.inc())
                o.settle()
                act.activation(nmid[:], above[:], ACT.Identity, scale=nsteps[:, n + 1:n + 2], bias=nmid[:, 0:1])\
                   .then_inc(*(turn_dve if k + 1 == SHARES[turn][1] else o).inc())

            act.wait_ge(*eps_ready.upto(0))
            for i in range(2):
                for c in range(4):
                    project(i, c)
                copy_ckvT(i)
            o.end_block()

            for i in range(BLOCKS):
                n_pieces = pieces[i]
                act.wait_ge(*proj_ready.upto(i))
                if i:
                    act.wait_ge(*gz_ready.upto(i - 1))
                act.activation(sgz[:], z[:, i % 2, :], ACT.Exp, scale=-1.0).then_inc(*o.inc())
                o.settle()
                act.activation(sgz[:], sgz[:], ACT.Ln, bias=1.0).then_inc(*o.inc())
                o.settle()
                act.activation(sgz[:], sgz[:], ACT.Exp, scale=-1.0).then_inc(*zsig_ready.inc())
                for h in range(4):
                    act.wait_ge(*mx_ready.upto(i, h + 1))
                    act.activation(Lg[:, h % 2, 0:(i + 1) * P], Lg[:, h % 2, 0:(i + 1) * P], ACT.Exp, bias=mx[:, h:h + 1],
                                   accum_out=psum_[:, h:h + 1]).then_inc(*exp_ready.inc())
                    if h == 1:
                        project(i + 2, 0)
                        project(i + 2, 1)
                    if h == 3:
                        project(i + 2, 2)
                    for c, (a, w) in enumerate(key_chunks(i)):
                        n = h * n_pieces + c
                        act.wait_ge(*pt_made.upto(i, n + 1))
                        if n >= 4:
                            act.wait_ge(*pv_made.upto(i, n - 3))
                        act.activation(pT[:, n % 4, 0:w // P, :], by_head[6 + n % 2][:, 0:w // P, :], ACT.Copy)\
                           .then_inc(*pt_ready.inc())
                        if FIRST_TOPK <= i + 1 < BLOCKS and SHARES[h][1]:
                            if c == (n_pieces - 1 if h == 0 else (n_pieces - 1) // 2):
                                search(i + 1, h, 0)
                            if c == n_pieces - 1:
                                search(i + 1, h, 1)
                act.wait_ge(*catT_made.upto(i, 1))
                act.activation(catT[:, 0:512], bank[2][:], ACT.Copy).then_inc(*catT_ready.inc())
                act.wait_ge(*pv_made.upto(i))
                act.activation(oT[:], by_head[5], ACT.Copy).then_inc(*oT_ready.inc())
                copy_ckvT(i + 2)
                act.wait_ge(*catT_made.upto(i))
                act.activation(catT[:, 512:1024], bank[3][:], ACT.Copy).then_inc(*catT_ready.inc())
                project(i + 2, 3)
                def rectify(numbers):
                    for n in numbers:
                        w = score_order(i + 2)[n][0][1]
                        act.wait_ge(*idx_made.upto(i + 2, n + 1))
                        if n >= 4:
                            act.wait_ge(*relu_used.upto(i + 2, n - 3))
                        act.activation(relu[:, n % 4, 0:w], bank[IDX_BANKS[n % 4]][:, 0:w], ACT.Relu).then_inc(*relu_ready.inc())

                scores = scored[i + 2] if i + 2 < BLOCKS else 0
                rectify(range(min(scores, 2)))
                act.wait_ge(*y_made.upto(i))
                for half in range(2):
                    act.activation(squares[:, half * 512:(half + 1) * 512], bank[6 + half][:], ACT.Square,
                                   accum_out=mss[:, half:half + 1]).then_inc(*(mss_ready if half else o).inc())
                act.wait_ge(*mss_ready.upto(i))
                act.activation(mss[:, 0:1], mss[:, 0:1], ACT.Identity, bias=mss[:, 1:2]).then_inc(*o.inc())
                o.settle()
                act.activation(mrs[:], mss[:, 0:1], ACT.Ln, bias=eps[:, 0:1], scale=1.0 / D).then_inc(*o.inc())
                o.settle()
                act.activation(mrs[:], mrs[:], ACT.Exp, scale=-0.5).then_inc(*mrs_ready.inc())
                rectify(range(min(scores, 2), scores))
                o.end_block()

        @block.vector
        def _(dve):
            o = Order(dve, orders["dve"])
            dve.memset(eps[:], RMS_EPS).then_inc(*eps_ready.inc())
            dve.memset(ones[:], 1.0).then_inc(*o.inc())
            dve.wait_ge(loaded.sem, NSMALL)
            dve.tensor_tensor(rb[:], rb[:], rb31[:], ALU.subtract).then_inc(*rb_ready.inc())
            dve.wait_ge(*vec_made.upto(0))
            dve.tensor_copy(vec[:], bank[2][0:4, 0:384]).then_inc(*vec_ready.inc())
            for n in range(2):
                dve.wait_ge(*bias_made.upto(0, n + 1))
                dve.tensor_copy(bias[:, 2 * n:2 * n + 2, :].rearrange("p h c -> p (h c)"), bank[3 + n][:]).then_inc(*bias_ready.inc())

            def do(instruction):
                instruction.then_inc(*o.inc())
                o.settle()

            def normalise_ckv(i):
                if i >= BLOCKS:
                    return
                dve.wait_ge(*crs_ready.upto(i))
                if i:
                    dve.wait_ge(*cT_made.upto(i - 1))
                    dve.wait_ge(*ckvr_ready.upto(i - 1))
                dve.scalar_tensor_tensor(cn[:], ckv[:], crs[:, 0:1], kv_row[:], ALU.mult, ALU.mult).then_inc(*cn_ready.inc())

            normalise_ckv(0)
            normalise_ckv(1)
            do(dve.tensor_copy(selb[:, 0:P], late[:]))
            dve.tensor_copy(lo[:], ones[:]).then_inc(*selb_ready.inc())
            o.end_block()

            def equal_scores(W):
                def step_(instruction, n):
                    instruction.then_inc(branch, 1)
                    dve.wait_ge(branch, n)
                step_(dve.tensor_scalar(selb[:, 0:W], acc[:, 0:W], thr[:, 0:1], 0.0, ALU.is_gt, ALU.add, accum_out=cnt[:]), 1)
                step_(dve.tensor_scalar(cnt[:], cnt[:], -1.0, float(TOPK), ALU.mult, ALU.add), 2)
                step_(dve.tensor_scalar(work[:, 0:W], acc[:, 0:W], thr[:, 0:1], None, ALU.is_equal), 3)
                step_(dve.tensor_tensor_scan(other[:, 0:W], work[:, 0:W], work[:, 0:W], 0.0, ALU.add, ALU.max), 4)
                step_(dve.scalar_tensor_tensor(work[:, 0:W], other[:, 0:W], cnt[:, 0:1], work[:, 0:W], ALU.is_le, ALU.mult), 5)
                step_(dve.tensor_tensor(selb[:, 0:W], selb[:, 0:W], work[:, 0:W], ALU.add), 6)
                step_(dve.tensor_scalar(selb[:, 0:W], selb[:, 0:W], -1.0, FAR, ALU.add, ALU.mult), 7)
                dve.sem_clear(branch)

            def general(W):
                dve.tensor_copy(work[:, 0:W], acc[:, 0:W]).then_inc(branch, 1)
                dve.wait_ge(branch, 1)
                dve.sem_clear(branch)
                with dve.Fori(0, TOPK // 8):
                    dve.max(best[:], work[:, 0:W]).then_inc(branch, 1)
                    dve.wait_ge(branch, 1)
                    dve.match_replace(work[:, 0:W], best[:], work[:, 0:W], -3e38).then_inc(branch, 1)
                    dve.wait_ge(branch, 2)
                    dve.sem_clear(branch)
                dve.tensor_tensor(other[:, 0:W], work[:, 0:W], acc[:, 0:W], ALU.is_equal).then_inc(branch, 1)
                dve.wait_ge(branch, 1)
                dve.tensor_scalar_mul(selb[:, 0:W], other[:, 0:W], -FAR).then_inc(branch, 1)
                dve.wait_ge(branch, 2)
                dve.sem_clear(branch)

            def start_search(j):
                W = (j + 1) * P
                last = acc[:, j * P:W]
                do(dve.tensor_reduce(lo[:], acc[:, 0:W], AX.X, ALU.min))
                do(dve.tensor_tensor(last, last, late[:], ALU.add))
                do(dve.tensor_reduce(hi[:], acc[:, 0:W], AX.X, ALU.max))
                do(dve.tensor_tensor(hi[:], hi[:], lo[:], ALU.subtract))
                dve.memset(few[:], W - 2 * TOPK + 1.5).then_inc(*o.inc())
                dve.tensor_scalar(nsteps[:], halves[:], hi[:, 0:1], -1.0, ALU.mult, ALU.mult).then_inc(*o.inc())
                do(dve.tensor_scalar(steps[:], halves[:], hi[:, 0:1], None, ALU.mult))
                do(dve.tensor_tensor(mid[:], lo[:], steps[:, 0:1], ALU.add))

            def search(j, turn):
                W = (j + 1) * P
                if turn:
                    dve.wait_ge(*turn_dve.upto(j, turn))
                    do(dve.tensor_scalar_mul(mid[:], nmid[:], -1.0))
                first = sum(a + b for a, b in SHARES[:turn])
                for n in range(first, first + SHARES[turn][0]):
                    do(dve.tensor_scalar(passed[:, 0:W], acc[:, 0:W], mid[:, 0:1], 0.0, ALU.is_ge, ALU.add, accum_out=cnt[:]))
                    do(dve.tensor_scalar(step[:], cnt[:], TOPK - 0.5, steps[:, n:n + 1], ALU.is_ge, ALU.mult))
                    if n < ROUNDS - 1:
                        do(dve.scalar_tensor_tensor(mid[:], mid[:], step[:, 0:1], steps[:, n + 1:n + 2], ALU.add, ALU.subtract))
                    else:
                        do(dve.tensor_tensor(hi[:], mid[:], step[:], ALU.add))
                if SHARES[turn][1]:
                    dve.tensor_scalar_mul(nmid[:], mid[:], -1.0).then_inc(*turn_act.inc())

            def set_aside(j):
                W = (j + 1) * P
                do(dve.tensor_scalar(passed[:, 0:W], acc[:, 0:W], hi[:, 0:1], 0.0, ALU.is_ge, ALU.add, accum_out=cnt[:]))
                do(dve.scalar_tensor_tensor(work[:, 0:W], passed[:, 0:W], -FAR, acc[:, 0:W], ALU.mult, ALU.add))

            def choose(j):
                W = (j + 1) * P
                do(dve.tensor_scalar(cnt[:], cnt[:], -1.0, float(TOPK), ALU.mult, ALU.add))
                do(dve.tensor_scalar(cnt[:], cnt[:], 8.0, None, ALU.min))
                do(dve.max(best[:], work[:, 0:W]))
                dve.tensor_scalar(match[:], iota[:], cnt[:, 0:1], 0.0, ALU.is_equal, ALU.add, accum_out=step[:]).then_inc(*o.inc())
                do(dve.scalar_tensor_tensor(best[:], iota[:], cnt[:, 0:1], best[:], ALU.is_equal, ALU.mult, accum_out=thr[:]))
                do(dve.tensor_scalar(passed[:, 0:W], acc[:, 0:W], thr[:, 0:1], 0.0, ALU.is_ge, ALU.add, accum_out=cnt[:]))
                dve.tensor_scalar(bad[:, 1:2], cnt[:], step[:, 0:1], TOPK - 0.5, ALU.mult, ALU.is_lt).then_inc(*o.inc())
                dve.tensor_scalar(bad[:, 0:1], cnt[:], float(TOPK), None, ALU.not_equal).then_inc(*bad_ready.inc())
                dve.tensor_scalar(selb[:, 0:W], acc[:, 0:W], thr[:, 0:1], -FAR, ALU.is_lt, ALU.mult).then_inc(*o.inc())

            def check_chosen(j):
                W = (j + 1) * P
                dve.wait_ge(*nbad_made.upto(j))
                dve.tensor_copy(nbad[:], bank[4][0:1, 0:2]).then_inc(*nbad_ready.inc())
                dve.wait_ge(*nbad_ready.upto(j))
                o.settle()
                equal = dve.value_load(nbad[0:1, 0:1], min_val=0, max_val=P)
                unfound = dve.value_load(nbad[0:1, 1:2], min_val=0, max_val=P)
                with dve.If(equal > 0):
                    equal_scores(W)
                with dve.If(unfound > 0):
                    general(W)

            for i in range(BLOCKS):
                W, n_pieces, j = (i + 1) * P, pieces[i], i + 1
                searched = FIRST_TOPK <= j < BLOCKS
                for h in range(4):
                    lg = Lg[:, h % 2, 0:W]
                    if h >= 2:
                        dve.wait_ge(*pt_made.upto(i, (h - 1) * n_pieces))
                    for c, (a, w) in enumerate(key_chunks(i)):
                        n = h * n_pieces + c
                        dve.wait_ge(*lg_made.upto(i, n + 1))
                        dve.scalar_tensor_tensor(lg[:, a:a + w], bank[LG_BANKS[n % 3]][:, 0:w], float(P) ** -0.5,
                                                 selb[:, a:a + w], ALU.mult, ALU.add).then_inc(*lg_read.inc())
                    dve.wait_ge(*lg_read.upto(i, (h + 1) * n_pieces))
                    near = max(0, (i - 1) * P)
                    do(dve.tensor_tensor(lg[:, near:W], lg[:, near:W], bias[:, h, 2 * P - (W - near):], ALU.add))
                    dve.tensor_reduce(mx[:, h:h + 1], lg, AX.X, ALU.max, negate=True).then_inc(*mx_ready.inc())
                    if searched:
                        if h == 0:
                            start_search(j)
                        search(j, h)
                    if h == 2:
                        normalise_ckv(i + 2)
                if searched:
                    dve.wait_ge(*pt_made.upto(i, 3 * n_pieces))
                    set_aside(j)
                dve.wait_ge(*exp_ready.upto(i))
                do(dve.reciprocal(prec[:], psum_[:]))
                dve.wait_ge(*uv_made.upto(i))
                dve.wait_ge(*gz_ready.upto(i))
                for h in range(4):
                    dve.scalar_tensor_tensor(cat[:, 512 + h * P:512 + (h + 1) * P], by_head[5][:, h, :], prec[:, h:h + 1],
                                             z[:, i % 2, h * P:(h + 1) * P], ALU.mult, ALU.mult)\
                       .then_inc(*(ob_ready if h == 3 else o).inc())
                if searched:
                    choose(j)
                    dve.wait_ge(*pv_made.upto(i))
                    check_chosen(j)
                elif j < BLOCKS:
                    dve.memset(selb[:, 0:j * P], 0.0).then_inc(*o.inc())
                    do(dve.tensor_copy(selb[:, j * P:(j + 1) * P], late[:]))
                if j < BLOCKS:
                    dve.tensor_copy(lo[:], ones[:]).then_inc(*selb_ready.inc())
                def weigh(numbers):
                    for n in numbers:
                        (a, w), h = score_order(i + 2)[n]
                        dve.wait_ge(*relu_ready.upto(i + 2, n + 1))
                        dst, weight = acc[:, a:a + w], iw[:, h:h + 1]
                        if h == 0:
                            dve.tensor_scalar(dst, relu[:, n % 4, 0:w], weight, None, ALU.mult).then_inc(*relu_used.inc())
                        else:
                            dve.wait_ge(*relu_used.upto(i + 2, score_order(i + 2).index(((a, w), h - 1)) + 1))
                            dve.scalar_tensor_tensor(dst, relu[:, n % 4, 0:w], weight, dst, ALU.mult, ALU.add)\
                               .then_inc(*relu_used.inc())

                scores = scored[i + 2] if i + 2 < BLOCKS else 0
                weigh(range(min(scores, 4)))
                dve.wait_ge(*mrs_ready.upto(i))
                for half in range(2):
                    sl = slice(half * 512, (half + 1) * 512)
                    dve.scalar_tensor_tensor(cat[:, sl], bank[6 + half][:], mrs[:, 0:1], gate_row[:, sl], ALU.mult, ALU.mult)\
                       .then_inc(*(mix_ready if half else o).inc())
                weigh(range(4, scores))
                if scores:
                    dve.wait_ge(*relu_used.upto(i + 2))
                o.end_block()

        @block.gpsimd
        def _(pool):
            def ckv_rows(i):
                if i >= BLOCKS:
                    return
                pool.wait_ge(*cn_ready.upto(i))
                pool.tensor_copy(ckvr[:, i, :], cn[:]).then_inc(*ckvr_ready.inc())

            ckv_rows(0)
            ckv_rows(1)
            for i in range(BLOCKS):
                pool.wait_ge(*zsig_ready.upto(i))
                pool.tensor_tensor(z[:, i % 2, :], z[:, i % 2, :], sgz[:], ALU.mult).then_inc(*gz_ready.inc())
                ckv_rows(i + 2)
                pool.wait_ge(*mix_ready.upto(i))
                pool.wait_ge(x_in.sem, 16 * i + 16)
                pool.tensor_tensor(xb[:], xb[:], cat[:], ALU.add).then_inc(*out_ready.inc())


def shape_constants():
    f = lambda m: np.ascontiguousarray(np.asarray(m).astype(np.float32))
    j = np.arange(P)
    up = j[:, None] <= j[None, :]
    same = (j[:, None] // GLA_CHUNK) == (j[None, :] // GLA_CHUNK)
    c = dict(c_ident=f(np.eye(P)), c_chunk=f(np.stack([(same & up) / 16, (same & ~up) / 16], 1)),
             c_causal=f(same & up), c_tril=f(up))
    half = 32
    inv = (np.float32(10000.0) ** (-np.arange(half, dtype=np.float32) / np.float32(half))).astype(np.float32)
    c["c_inv"] = f(np.tile(inv, (P, 1)))
    lg = np.log(1.0 - 2.0 ** (-5.0 - np.arange(HEADS, dtype=np.float64)))
    rel = j[None, :] - j[:, None]
    c["c_dmat"] = f(np.stack([np.where(rel >= 0, np.exp(np.maximum(rel, 0) * g), 0) / 8 for g in lg], 1))
    w = np.zeros((P, HEADS, P))
    for h in range(HEADS):
        w[64 * (h % 2):64 * (h % 2) + 64, h, :] = np.exp((j + 1.0) * lg[h]) / 8
    c["c_winter"] = f(w)
    c["c_wstate"] = f(np.exp((P - 1.0 - j)[:, None] * lg[None, :]))
    c["c_gammac"] = f(np.exp(P * lg)[2 * np.arange(2)[None, :] + (j // 64)[:, None]])
    band = np.zeros((P, 12, P))
    for w_, win in enumerate(POOL_WINDOWS):
        d = j[None, :] - j[:, None]
        band[:, w_] = ((d >= 0) & (d < win)) / win - np.eye(P)
        band[:, 4 + w_] = ((d + P >= 0) & (d + P < win)) / win
        band[:, 8 + w_] = ((d >= 0) & (d < win)) / np.minimum(j + 1, win)[None, :] - np.eye(P)
    c["c_band"] = f(band)
    late = same & ~up
    first = np.broadcast_to((j < GLA_CHUNK)[:, None], (P, P))
    c["c_seg"] = f(np.stack([same & up, late, first, ~first], 1))
    c["c_big"] = f(np.stack([~(same & (j[:, None] > j[None, :])), ~(same & up)], 1) * 1e30)
    c["c_lev"] = f(np.stack([((j[:, None] // (2 * n)) == (j[None, :] // (2 * n))) & (j[:, None] // n % 2 == 1)
                             & (j[None, :] // n % 2 == 0) for n in LEVELS], 1))
    c["c_flip"] = f(np.eye(P)[::-1])
    c["c_late"] = f((j[None, :] > j[:, None]) * -FAR)
    dist = 255 - np.arange(384)
    n = np.maximum(dist, 1).astype(np.float32)
    big = 16 + (np.log(n / np.float32(16)) / np.float32(math.log(8)) * np.float32(16)).astype(np.int32)
    bucket = np.where(dist < 16, dist, np.minimum(big, N_BUCKETS - 1))
    c["c_onehot"] = f((np.arange(N_BUCKETS)[:, None] == bucket[None, :]) & (dist >= 0)[None, :])
    c["c_iota"] = f(np.tile(np.arange(1, 9), (P, 1)))
    c["c_halves"] = f(np.tile(0.5 ** np.arange(1, ROUNDS + 2), (P, 1)))
    return c


def build(nc, t, out, x1, x2, hT, oa, bias_scratch):
    def layer(prefix, names):
        return [t[prefix + n] for n in names.split()]

    def last(names):
        return [t[n + "_2"][0] for n in names.split()]

    def const(names):
        return tuple(t["c_" + n] for n in names.split())

    even_layer(nc, t["x"].rearrange("a s d -> (a s) d"),
               *layer("l0_", "w_in w_a2 b_a gla_norm_g sgu_ln_g sgu_ln_b w_s b_s w_out ln_g ln_b"),
               const("ident chunk causal tril"), x1)
    odd_layer(nc, x1, t["positions"].rearrange("a s -> (a s)"),
              *layer("l1_", "w_in ret_norm_g w_pool pool_scale w_out ln_g ln_b"),
              const("ident inv dmat winter wstate gammac band"), x2)
    with nc.sbuf_tensor("gate_row", [P, D], F32) as gate_row:
        delta_layer(nc, x2, *last("c w_ada b_ada g_pre w_in conv_w a_log dt_bias g_gdn g_post"),
                    const("ident seg big lev"), gate_row, hT, oa)
        sparse_layer(nc, x2, *last("w_in g_kv w_uv"), t["rel_bias_2"], *last("w_out"),
                     const("ident flip late onehot iota halves"), gate_row, hT, oa, bias_scratch,
                     out.rearrange("a s d -> (a s) d"))


def kernel(**inputs):
    import numpy as _np
    import concourse.bacc as _bacc
    from concourse import mybir as _mybir
    from concourse.bass_utils import run_bass_kernel_spmd as _run

    nc = _bacc.Bacc("TRN2", target_bir_lowering=False, num_devices=1)
    arrays, t = {}, {}
    for name, a in list(inputs.items()) + list(shape_constants().items()):
        arrays[name] = _np.ascontiguousarray(a)
        t[name] = nc.dram_tensor(name, list(arrays[name].shape), _mybir.dt.from_np(arrays[name].dtype),
                                 kind="ExternalInput").ap()
    out = nc.dram_tensor("out", [1, SEQ, D], F32, kind="ExternalOutput").ap()
    x1 = nc.dram_tensor("x1", [SEQ, D], F32).ap()
    x2 = nc.dram_tensor("x2", [SEQ, D], F32).ap()
    hT = nc.dram_tensor("hT", [BLOCKS, P, D], F32).ap()
    oa = nc.dram_tensor("oa", [SEQ, D // 2], F32).ap()
    bias_scratch = nc.dram_tensor("bias_scratch", [4, 384], F32).ap()
    build(nc, t, out, x1, x2, hT, oa, bias_scratch)
    r = _run(nc, [arrays], core_ids=[0])
    return r.results[0]["out"]
```
